# Optimizing a Trainium2 kernel written in Bass

```python
import math
import jax
import jax.numpy as jnp
from jax import lax
import numpy as np
import jax, jax.numpy as jnp

D_MODEL = 1024
BATCH = 1
SEQ = 512
DEPTH = 2

HEAD_DIM = 64
DIFF_W = (D_MODEL * 3 // 8)
DELTA_W = (D_MODEL * 3 // 8)
CONV_CH = D_MODEL - DIFF_W - DELTA_W
DIFF_HEADS = DIFF_W // HEAD_DIM
DIFF_DIM = HEAD_DIM // 2
DELTA_HEADS = DELTA_W // HEAD_DIM
CONV_WIDTH = 31
SHORT_CONV = 3
CHUNK = 64
Q_BLOCK = 128
D_FF = 4 * D_MODEL
IN_W = 2 * CONV_CH + 3 * DIFF_W + 4 * DELTA_W + 4 * DELTA_HEADS
NORM_EPS = 1e-6


def rms_norm(x, w, eps=NORM_EPS):
    xf = x.astype(jnp.float32)
    y = xf * lax.rsqrt(jnp.mean(xf * xf, axis=-1, keepdims=True) + eps)
    return (y * w.astype(jnp.float32)).astype(x.dtype)

def layer_norm(x, w, b, eps=1e-5):
    xf = x.astype(jnp.float32)
    mu = jnp.mean(xf, axis=-1, keepdims=True)
    xc = xf - mu
    var = jnp.mean(xc * xc, axis=-1, keepdims=True)
    y = xc * lax.rsqrt(var + eps) * w.astype(jnp.float32) + b.astype(jnp.float32)
    return y.astype(x.dtype)

def l2norm(x, eps=1e-6):
    xf = x.astype(jnp.float32)
    return xf * lax.rsqrt(jnp.sum(xf * xf, axis=-1, keepdims=True) + eps)

def depthwise_conv(x, w):
    k, c = w.shape
    pad = (k - 1) // 2
    return lax.conv_general_dilated(
        x, w[:, None, :].astype(x.dtype), window_strides=(1,), padding=[(pad, pad)],
        dimension_numbers=("NWC", "WIO", "NWC"), feature_group_count=c)

def alibi_slopes(n):
    def pow2(m):
        start = 2.0 ** (-8.0 / m)
        return [start ** (i + 1) for i in range(m)]
    if math.log2(n).is_integer():
        s = pow2(n)
    else:
        c = 2 ** int(math.floor(math.log2(n)))
        s = pow2(c) + pow2(2 * c)[0::2][: n - c]
    return jnp.asarray(s, dtype=jnp.float32)

def conv_module(u, dw_w, dw_b, ln_w, ln_b):
    a, g = jnp.split(u, 2, axis=-1)
    h = a * jax.nn.sigmoid(g)
    h = depthwise_conv(h, dw_w) + dw_b.astype(h.dtype)
    h = layer_norm(h, ln_w, ln_b)
    return jax.nn.silu(h)

def diff_attention(q, k, v, lam_q1, lam_k1, lam_q2, lam_k2, subln_w, layer_idx):
    B, S = q.shape[0], q.shape[1]
    H = DIFF_HEADS
    f32 = jnp.float32
    lambda_init = 0.8 - 0.6 * math.exp(-0.3 * layer_idx)
    lam = (jnp.exp(jnp.sum(lam_q1.astype(f32) * lam_k1.astype(f32)))
           - jnp.exp(jnp.sum(lam_q2.astype(f32) * lam_k2.astype(f32))) + lambda_init)
    slopes = jnp.repeat(alibi_slopes(H), 2)
    n_blk = S // Q_BLOCK
    qf = q.astype(f32).reshape(B, n_blk, Q_BLOCK, 2 * H, DIFF_DIM) * (DIFF_DIM ** -0.5)
    qf = jnp.moveaxis(qf, 1, 0)
    kf = k.astype(f32).reshape(B, S, 2 * H, DIFF_DIM)
    vf = v.astype(f32).reshape(B, S, H, HEAD_DIM)
    kpos = jnp.arange(S)

    def block(args):
        q_blk, blk = args
        s = jnp.einsum("bqmd,bkmd->bmqk", q_blk, kf)
        qpos = blk * Q_BLOCK + jnp.arange(Q_BLOCK)
        dist = jnp.abs(qpos[:, None] - kpos[None, :]).astype(f32)
        p = jax.nn.softmax(s - slopes[:, None, None] * dist, axis=-1)
        p = p.reshape(B, H, 2, Q_BLOCK, S)
        a = p[:, :, 0] - lam * p[:, :, 1]
        return jnp.einsum("bhqk,bkhe->bqhe", a, vf)

    o = lax.map(block, (qf, jnp.arange(n_blk)))
    o = jnp.moveaxis(o, 0, 1).reshape(B, S, H, HEAD_DIM)
    o = rms_norm(o, subln_w, eps=1e-5) * (1.0 - lambda_init)
    return o.reshape(B, S, H * HEAD_DIM).astype(q.dtype)

def chunk_gated_delta(q, k, v, g, beta):
    B, S, H, Dk = q.shape
    Dv = v.shape[-1]
    N = S // CHUNK
    q = q * (Dk ** -0.5)

    def chunks(t):
        return t.reshape(B, N, CHUNK, H, -1).transpose(0, 3, 1, 2, 4)

    qc, kc, vc = chunks(q), chunks(k), chunks(v)
    gc = jnp.cumsum(g.reshape(B, N, CHUNK, H).transpose(0, 3, 1, 2), axis=-1)
    bc = beta.reshape(B, N, CHUNK, H).transpose(0, 3, 1, 2)
    idx = jnp.arange(CHUNK)
    lower = idx[:, None] >= idx[None, :]
    strict = idx[:, None] > idx[None, :]
    decay = jnp.exp(jnp.where(lower, gc[..., :, None] - gc[..., None, :], -jnp.inf))
    kb = kc * bc[..., None]
    A = jnp.where(strict, jnp.einsum("bhncd,bhnsd->bhncs", kb, kc) * decay, 0.0)
    rhs = jnp.concatenate([vc * bc[..., None], kb * jnp.exp(gc)[..., None]], axis=-1)
    sol = lax.linalg.triangular_solve(A, rhs, left_side=True, lower=True, unit_diagonal=True)
    u, w = sol[..., :Dv], sol[..., Dv:]
    Aqk = jnp.einsum("bhncd,bhnsd->bhncs", qc, kc) * decay
    qg = qc * jnp.exp(gc)[..., None]
    kdec = kc * jnp.exp(gc[..., -1:] - gc)[..., None]
    glast = jnp.exp(gc[..., -1])

    def step(state, inp):
        u_i, w_i, qg_i, aqk_i, kdec_i, gl_i = inp
        v_new = u_i - jnp.einsum("bhcd,bhde->bhce", w_i, state)
        o = jnp.einsum("bhcd,bhde->bhce", qg_i, state) + jnp.einsum("bhcs,bhse->bhce", aqk_i, v_new)
        state = state * gl_i[..., None, None] + jnp.einsum("bhcd,bhce->bhde", kdec_i, v_new)
        return state, o

    xs = tuple(jnp.moveaxis(t, 2, 0) for t in (u, w, qg, Aqk, kdec, glast))
    s0 = jnp.zeros((B, H, Dk, Dv), jnp.float32)
    _, o = lax.scan(step, s0, xs)
    return o.transpose(1, 0, 3, 2, 4).reshape(B, S, H, Dv)

def gated_deltanet(qkv, z, b_f, b_b, a_f, a_b, conv_w, A_log, dt_bias, norm_w):
    B, S, _ = qkv.shape
    H, D = DELTA_HEADS, HEAD_DIM
    f32 = jnp.float32
    out_dtype = qkv.dtype
    qkv = jax.nn.silu(depthwise_conv(qkv, conv_w))
    q, k, v = jnp.split(qkv, 3, axis=-1)
    q = l2norm(q.reshape(B, S, H, D))
    k = l2norm(k.reshape(B, S, H, D))
    v = v.reshape(B, S, H, D).astype(f32)

    def log_decay(a, a_log, dtb):
        return -jnp.exp(a_log.astype(f32)) * jax.nn.softplus(a.astype(f32) + dtb.astype(f32))

    g_f = log_decay(a_f, A_log[0], dt_bias[0])
    g_b = log_decay(a_b, A_log[1], dt_bias[1])
    beta_f = jax.nn.sigmoid(b_f.astype(f32))
    beta_b = jax.nn.sigmoid(b_b.astype(f32))
    o_f = chunk_gated_delta(q, k, v, g_f, beta_f)
    rev = lambda t: jnp.flip(t, axis=1)
    o_b = rev(chunk_gated_delta(rev(q), rev(k), rev(v), rev(g_b), rev(beta_b)))
    o = rms_norm(o_f + o_b, norm_w) * jax.nn.silu(z.astype(f32).reshape(B, S, H, D))
    return o.reshape(B, S, H * D).astype(out_dtype)

def first_inputs(seed: int = 0) -> dict:
    key = jax.random.key(seed)
    ks = jax.random.split(key, 24)
    f32 = jnp.float32
    nrm = lambda k, shape, scale: jax.random.normal(k, shape, f32) * scale
    gain = lambda k, shape: 1.0 + 0.05 * jax.random.normal(k, shape, f32)
    dt = jnp.exp(jax.random.uniform(ks[20], (DEPTH, 2, DELTA_HEADS), f32, math.log(1e-3), math.log(1e-1)))
    return {
        "x": nrm(ks[0], (BATCH, SEQ, D_MODEL), 1.0),
        "w_in": nrm(ks[1], (DEPTH, D_MODEL, IN_W), D_MODEL ** -0.5),
        "w_out": nrm(ks[2], (DEPTH, D_MODEL, D_MODEL), D_MODEL ** -0.5),
        "pre_mix_w": gain(ks[3], (DEPTH, D_MODEL)),
        "post_mix_w": gain(ks[4], (DEPTH, D_MODEL)),
        "pre_mlp_w": gain(ks[5], (DEPTH, D_MODEL)),
        "post_mlp_w": gain(ks[6], (DEPTH, D_MODEL)),
        "w_ff1": nrm(ks[7], (DEPTH, D_MODEL, D_FF), D_MODEL ** -0.5),
        "w_ff2": nrm(ks[8], (DEPTH, D_FF, D_MODEL), D_FF ** -0.5),
        "conv_dw_w": nrm(ks[9], (DEPTH, CONV_WIDTH, CONV_CH), CONV_WIDTH ** -0.5),
        "conv_dw_b": nrm(ks[10], (DEPTH, CONV_CH), 0.02),
        "conv_ln_w": gain(ks[11], (DEPTH, CONV_CH)),
        "conv_ln_b": nrm(ks[12], (DEPTH, CONV_CH), 0.02),
        "diff_lambda_q1": nrm(ks[13], (DEPTH, DIFF_DIM), 0.1),
        "diff_lambda_k1": nrm(ks[14], (DEPTH, DIFF_DIM), 0.1),
        "diff_lambda_q2": nrm(ks[15], (DEPTH, DIFF_DIM), 0.1),
        "diff_lambda_k2": nrm(ks[16], (DEPTH, DIFF_DIM), 0.1),
        "diff_subln_w": gain(ks[17], (DEPTH, HEAD_DIM)),
        "delta_conv_w": nrm(ks[18], (DEPTH, SHORT_CONV, 3 * DELTA_W), SHORT_CONV ** -0.5),
        "delta_A_log": jnp.log(jax.random.uniform(ks[19], (DEPTH, 2, DELTA_HEADS), f32, 1.0, 16.0)),
        "delta_dt_bias": dt + jnp.log(-jnp.expm1(-dt)),
        "delta_norm_w": gain(ks[21], (DEPTH, HEAD_DIM)),
    }

def first_block(x, w_in, w_out, pre_mix_w, post_mix_w, pre_mlp_w, post_mlp_w, w_ff1, w_ff2,
              conv_dw_w, conv_dw_b, conv_ln_w, conv_ln_b,
              diff_lambda_q1, diff_lambda_k1, diff_lambda_q2, diff_lambda_k2, diff_subln_w,
              delta_conv_w, delta_A_log, delta_dt_bias, delta_norm_w):
    sizes = [2 * CONV_CH, DIFF_W, DIFF_W, DIFF_W, 3 * DELTA_W, DELTA_W,
             DELTA_HEADS, DELTA_HEADS, DELTA_HEADS, DELTA_HEADS]
    offs = [sum(sizes[: i + 1]) for i in range(len(sizes) - 1)]
    for l in range(DEPTH):
        h = rms_norm(x, pre_mix_w[l])
        u = h @ w_in[l]
        (u_conv, dq, dk, dv, gqkv, gz, b_f, b_b, a_f, a_b) = jnp.split(u, offs, axis=-1)
        y_conv = conv_module(u_conv, conv_dw_w[l], conv_dw_b[l], conv_ln_w[l], conv_ln_b[l])
        y_diff = diff_attention(dq, dk, dv, diff_lambda_q1[l], diff_lambda_k1[l],
                                diff_lambda_q2[l], diff_lambda_k2[l], diff_subln_w[l], l)
        y_delta = gated_deltanet(gqkv, gz, b_f, b_b, a_f, a_b, delta_conv_w[l],
                                 delta_A_log[l], delta_dt_bias[l], delta_norm_w[l])
        y = jnp.concatenate([y_conv, y_diff, y_delta], axis=-1) @ w_out[l]
        x = x + rms_norm(y, post_mix_w[l])
        h = rms_norm(x, pre_mlp_w[l])
        y = jnp.square(jax.nn.relu(h @ w_ff1[l])) @ w_ff2[l]
        x = x + rms_norm(y, post_mlp_w[l])
    return x


N_EVEN = (DEPTH + 1) // 2
N_ODD = DEPTH // 2

MIX_WIDTH = 1024
A_GROUPS = 4
A_GROUP_DIM = 128
A_WIDTH = A_GROUPS * A_GROUP_DIM
CHUNK_2 = 128
SGU_LN_EPS = 1e-5
B_HEADS = 8
B_HEAD_DIM = 64
B_WIDTH = B_HEADS * B_HEAD_DIM
DECAY_LORA = 64
ICLR_LORA = 64
GATE_LORA = 128
B_IN = 3 * B_WIDTH + DECAY_LORA + ICLR_LORA + GATE_LORA
RWKV_GN_EPS = 64e-5
IN0 = 2 * A_WIDTH + B_IN
C_HEADS = 8
C_KV_HEADS = 2
C_GROUP = C_HEADS // C_KV_HEADS
C_HEAD_DIM = 64
C_WIDTH = C_HEADS * C_HEAD_DIM
KV_WIDTH = C_KV_HEADS * C_HEAD_DIM
N_BRANCH = 3
CMP_LEN = 32
CMP_STRIDE = 16
CMP_HIDDEN = 256
SLC_BLK = 64
SEL_TOPK = 8
WIN = 512
QBLK = 128
ROT_DIM = C_HEAD_DIM // 4
ROPE_THETA = 500000.0
D_WIDTH = 512
CONV_W = 3
IN1 = C_WIDTH + 6 * KV_WIDTH + C_HEADS * N_BRANCH + 3 * D_WIDTH
FFN_DIM = 2816
N_EXPERTS = 8
TOP_K = 2
EXPERT_DIM = 1408
MOE_BLK = 256
NEG_INF = -1e30
FORCE_BONUS = 1e6


def _split(p, sizes):
    offs = [int(o) for o in np.cumsum(sizes)[:-1]]
    return jnp.split(p, offs, axis=-1)

def _rms_norm(x, g):
    xf = x.astype(jnp.float32)
    y = xf * lax.rsqrt(jnp.mean(xf * xf, axis=-1, keepdims=True) + NORM_EPS)
    return (y * g.astype(jnp.float32)).astype(x.dtype)

def _masked_softmax(s, mask):
    s = jnp.where(mask, s, NEG_INF)
    m = jnp.max(s, axis=-1, keepdims=True)
    p = jnp.where(mask, jnp.exp(s - m), 0.0)
    return p / jnp.maximum(jnp.sum(p, axis=-1, keepdims=True), 1e-30)

def _rope_partial(x, cos, sin):
    half = ROT_DIM // 2
    c = cos[None, :, None, :].astype(x.dtype)
    s = sin[None, :, None, :].astype(x.dtype)
    x1 = x[..., :half]
    x2 = x[..., half:ROT_DIM]
    return jnp.concatenate([x1 * c - x2 * s, x1 * s + x2 * c, x[..., ROT_DIM:]], axis=-1)

def _chunked_sgu(u, v, ln_g, ln_b, w_s, b_s):
    bsz, t, _ = v.shape
    vf = v.reshape(bsz, t, A_GROUPS, A_GROUP_DIM).astype(jnp.float32)
    mu = jnp.mean(vf, axis=-1, keepdims=True)
    var = jnp.mean(jnp.square(vf - mu), axis=-1, keepdims=True)
    vn = ((vf - mu) * lax.rsqrt(var + SGU_LN_EPS)).reshape(bsz, t, A_WIDTH)
    vn = (vn * ln_g + ln_b).astype(v.dtype)
    vc = vn.reshape(bsz, t // CHUNK_2, CHUNK_2, A_GROUPS, A_GROUP_DIM)
    causal = jnp.tril(jnp.ones((CHUNK_2, CHUNK_2), dtype=bool))
    wm = jnp.where(causal[None], w_s, 0.0).astype(v.dtype)
    mixed = jnp.einsum('gts,bcsgd->bctgd', wm, vc) + b_s.T[:, :, None]
    return u * mixed.reshape(bsz, t, A_WIDTH)

def _rwkv7_scan(r, w, k, v, kk, a):
    bsz, _, h, n = r.shape

    def step(S, inp):
        r_t, w_t, k_t, v_t, kk_t, a_t = inp
        sa = jnp.einsum('bhij,bhj->bhi', S, kk_t)
        S = (S * w_t[:, :, None, :]
             - sa[..., None] * (kk_t * a_t)[:, :, None, :]
             + v_t[..., None] * k_t[:, :, None, :])
        return S, jnp.einsum('bhij,bhj->bhi', S, r_t)

    xs = tuple(jnp.moveaxis(z, 1, 0) for z in (r, w, k, v, kk, a))
    S0 = jnp.zeros((bsz, h, n, n), jnp.float32)
    _, ys = lax.scan(step, S0, xs)
    return jnp.moveaxis(ys, 0, 1)

def _rwkv7_time_mix(pb, mu, w0, w2, a0, a2, g2, k_k, k_a, r_k, gn_g, gn_b):
    bsz, t, _ = pb.shape
    prev = jnp.pad(pb, ((0, 0), (1, 0), (0, 0)))[:, :-1]
    pb = pb + (prev - pb) * mu
    r, k, v, wl, al, gl = _split(pb, [B_WIDTH, B_WIDTH, B_WIDTH, DECAY_LORA, ICLR_LORA, GATE_LORA])
    w = -jax.nn.softplus(-(w0 + jnp.tanh(wl) @ w2)) - 0.5
    decay = jnp.exp(-jnp.exp(w.astype(jnp.float32)))
    a = jax.nn.sigmoid(a0 + al @ a2)
    g = jax.nn.sigmoid(gl) @ g2

    def heads(z):
        return z.reshape(bsz, t, B_HEADS, B_HEAD_DIM).astype(jnp.float32)

    kk = heads(k * k_k)
    kk = kk / jnp.maximum(jnp.sqrt(jnp.sum(kk * kk, axis=-1, keepdims=True)), 1e-12)
    k = k * (1.0 + (a - 1.0) * k_a)
    rh, kh, vh, ah, wh = heads(r), heads(k), heads(v), heads(a), heads(decay)
    y = _rwkv7_scan(rh, wh, kh, vh, kk, ah)
    ym = jnp.mean(y, axis=-1, keepdims=True)
    yv = jnp.mean(jnp.square(y - ym), axis=-1, keepdims=True)
    y = ((y - ym) * lax.rsqrt(yv + RWKV_GN_EPS)).reshape(bsz, t, B_WIDTH)
    y = y * gn_g.astype(jnp.float32) + gn_b.astype(jnp.float32)
    bonus = jnp.sum(rh * kh * r_k.astype(jnp.float32), axis=-1, keepdims=True) * vh
    y = (y + bonus.reshape(bsz, t, B_WIDTH)) * g.astype(jnp.float32)
    return y.astype(pb.dtype)

def _nsa(q, kc, vc, ks, vs, kw, vw, gl, pos_k, pos_v, ck1, ck2, cv1, cv2, cos, sin):
    bsz, t, _ = q.shape
    f32 = jnp.float32
    scale = C_HEAD_DIM ** -0.5
    q = q.reshape(bsz, t, C_HEADS, C_HEAD_DIM)
    kc, vc, ks, vs, kw, vw = (z.reshape(bsz, t, C_KV_HEADS, C_HEAD_DIM) for z in (kc, vc, ks, vs, kw, vw))

    n_cmp = (t - CMP_LEN) // CMP_STRIDE + 1
    idx = np.arange(n_cmp)[:, None] * CMP_STRIDE + np.arange(CMP_LEN)[None, :]

    def compress(z, pos, w1, w2):
        zb = z[:, idx] + pos[None, None, :, None, :]
        zb = zb.transpose(0, 3, 1, 2, 4).reshape(bsz, C_KV_HEADS, n_cmp, CMP_LEN * C_HEAD_DIM)
        return jax.nn.gelu(zb @ w1) @ w2

    k_cmp = compress(kc, pos_k, ck1, ck2)
    v_cmp = compress(vc, pos_v, cv1, cv2).astype(f32)
    cmp_end = jnp.arange(n_cmp) * CMP_STRIDE + CMP_LEN - 1
    n_slc = t // SLC_BLK
    ci = jnp.arange(n_cmp)[:, None] * CMP_STRIDE
    sj = jnp.arange(n_slc)[None, :] * SLC_BLK
    overlap = ((ci < sj + SLC_BLK) & (ci + CMP_LEN > sj)).astype(f32)
    n_sel = min(SEL_TOPK, n_slc)

    q_rot = _rope_partial(q, cos, sin)
    ks = _rope_partial(ks, cos, sin)
    kw = _rope_partial(kw, cos, sin)
    n_qb = t // QBLK

    def to_qblocks(z):
        return z.reshape(bsz, n_qb, QBLK, C_KV_HEADS, C_GROUP, z.shape[-1]).transpose(1, 0, 3, 4, 2, 5)

    qr_b = to_qblocks(q_rot)
    qn_b = to_qblocks(q)
    g_b = to_qblocks(jax.nn.sigmoid(gl.reshape(bsz, t, C_HEADS, N_BRANCH)))
    ks_blk = ks.reshape(bsz, n_slc, SLC_BLK, C_KV_HEADS, C_HEAD_DIM).transpose(0, 3, 1, 2, 4)
    vs_blk = vs.reshape(bsz, n_slc, SLC_BLK, C_KV_HEADS, C_HEAD_DIM).transpose(0, 3, 1, 2, 4)
    pad = ((0, 0), (0, 0), (WIN, 0), (0, 0))
    kw_pad = jnp.pad(kw.transpose(0, 2, 1, 3), pad)
    vw_pad = jnp.pad(vw.transpose(0, 2, 1, 3), pad)
    b_ix = jnp.arange(bsz)[:, None, None, None]
    h_ix = jnp.arange(C_KV_HEADS)[None, :, None, None]
    jb = jnp.arange(n_slc)

    def body(args):
        qr, qn, gt, blk = args
        s0 = blk * QBLK
        t_pos = s0 + jnp.arange(QBLK)
        sc = jnp.einsum('bhgqd,bhnd->bhgqn', qn, k_cmp).astype(f32) * scale
        pc = _masked_softmax(sc, cmp_end[None, :] <= t_pos[:, None])
        o_c = jnp.einsum('bhgqn,bhnd->bhgqd', pc, v_cmp)
        imp = jnp.einsum('bhgqn,nj->bhqj', pc, overlap)
        cur = t_pos // SLC_BLK
        forced = (jb[None] == 0) | (jb[None] == cur[:, None]) | (jb[None] == cur[:, None] - 1)
        imp = jnp.where(jb[None] * SLC_BLK <= t_pos[:, None],
                        imp + jnp.where(forced, FORCE_BONUS, 0.0), NEG_INF)
        _, sel = lax.top_k(imp, n_sel)
        kg = ks_blk[b_ix, h_ix, sel]
        vg = vs_blk[b_ix, h_ix, sel]
        tok = sel[..., None] * SLC_BLK + jnp.arange(SLC_BLK)
        ms = (tok <= t_pos[:, None, None]).reshape(bsz, C_KV_HEADS, 1, QBLK, n_sel * SLC_BLK)
        ss = jnp.einsum('bhgqd,bhqnld->bhgqnl', qr, kg).astype(f32)
        ps = _masked_softmax(ss.reshape(bsz, C_KV_HEADS, C_GROUP, QBLK, n_sel * SLC_BLK) * scale, ms)
        o_s = jnp.einsum('bhgqm,bhqmd->bhgqd', ps,
                         vg.reshape(bsz, C_KV_HEADS, QBLK, n_sel * SLC_BLK, C_HEAD_DIM).astype(f32))
        kwb = lax.dynamic_slice_in_dim(kw_pad, s0, QBLK + WIN, axis=2)
        vwb = lax.dynamic_slice_in_dim(vw_pad, s0, QBLK + WIN, axis=2)
        key_pos = s0 - WIN + jnp.arange(QBLK + WIN)
        diff = t_pos[:, None] - key_pos[None, :]
        mw = (diff >= 0) & (diff < WIN) & (key_pos[None, :] >= 0)
        sw = jnp.einsum('bhgqd,bhkd->bhgqk', qr, kwb).astype(f32) * scale
        pw = _masked_softmax(sw, mw)
        o_w = jnp.einsum('bhgqk,bhkd->bhgqd', pw, vwb.astype(f32))
        gt = gt.astype(f32)
        return (gt[..., 0:1] * o_c + gt[..., 1:2] * o_s + gt[..., 2:3] * o_w).astype(qr.dtype)

    out = lax.map(body, (qr_b, qn_b, g_b, jnp.arange(n_qb)))
    return out.transpose(1, 0, 4, 2, 3, 5).reshape(bsz, t, C_WIDTH)

def _short_conv(bg, cg, hd, conv_w):
    z = cg * hd
    y = lax.conv_general_dilated(z, conv_w[:, None, :].astype(z.dtype), window_strides=(1,),
                                 padding=[(CONV_W - 1, 0)],
                                 dimension_numbers=('NWC', 'WIO', 'NWC'),
                                 feature_group_count=D_WIDTH)
    return bg * y

def _swiglu(h, w_gate, w_up, w_down):
    return (jax.nn.silu(h @ w_gate) * (h @ w_up)) @ w_down

def _moe_swiglu(h, w_router, b_router, w_gate, w_up, w_down):
    bsz, t, d = h.shape
    n = bsz * t
    nk = n * TOP_K
    xf = h.reshape(n, d)
    logits = (xf @ w_router).astype(jnp.float32) + b_router.astype(jnp.float32)
    top_val, top_idx = lax.top_k(logits, TOP_K)
    gates = jax.nn.softmax(top_val, axis=-1)
    e_flat = top_idx.reshape(-1)
    tok_flat = jnp.repeat(jnp.arange(n, dtype=jnp.int32), TOP_K)
    g_flat = gates.reshape(-1)
    order = jnp.argsort(e_flat)
    e_sorted = e_flat[order]
    counts = jax.ops.segment_sum(jnp.ones_like(e_flat), e_flat, num_segments=N_EXPERTS)
    padded = ((counts + MOE_BLK - 1) // MOE_BLK) * MOE_BLK
    p_end = jnp.cumsum(padded)
    p_start = p_end - padded
    u_start = jnp.cumsum(counts) - counts
    dest = p_start[e_sorted] + jnp.arange(nk) - u_start[e_sorted]
    n_blk = (nk + MOE_BLK - 1) // MOE_BLK + N_EXPERTS
    p_rows = n_blk * MOE_BLK
    row_tok = jnp.zeros((p_rows,), jnp.int32).at[dest].set(tok_flat[order])
    row_w = jnp.zeros((p_rows,), jnp.float32).at[dest].set(g_flat[order])
    blk_e = jnp.minimum(jnp.searchsorted(p_end, jnp.arange(n_blk) * MOE_BLK, side='right'), N_EXPERTS - 1)
    xs = xf[row_tok].reshape(n_blk, MOE_BLK, d)

    def expert_block(args):
        xb, e = args
        return (jax.nn.silu(xb @ w_gate[e]) * (xb @ w_up[e])) @ w_down[e]

    yb = lax.map(expert_block, (xs, blk_e)).reshape(p_rows, d)
    out = jnp.zeros((n, d), h.dtype).at[row_tok].add(yb * row_w[:, None].astype(yb.dtype))
    return out.reshape(bsz, t, d)

def second_inputs(seed: int = 0) -> dict:
    key = jax.random.key(seed)
    keys = iter(jax.random.split(key, 48))

    def nrm(shape, scale):
        return scale * jax.random.normal(next(keys), shape, jnp.float32)

    def gain(shape):
        return 1.0 + nrm(shape, 0.1)

    def unif(shape, lo, hi):
        return jax.random.uniform(next(keys), shape, jnp.float32, lo, hi)

    E, O, D = N_EVEN, N_ODD, D_MODEL
    return {
        "x": nrm((BATCH, SEQ, D), 1.0),
        "e_norm_mix": gain((E, D)),
        "e_w_in": nrm((E, D, IN0), D ** -0.5),
        "sgu_ln_g": gain((E, A_WIDTH)),
        "sgu_ln_b": nrm((E, A_WIDTH), 0.02),
        "sgu_w": nrm((E, A_GROUPS, CHUNK_2, CHUNK_2), CHUNK_2 ** -0.5),
        "sgu_b": gain((E, A_GROUPS, CHUNK_2)),
        "rwkv_mu": unif((E, B_IN), 0.0, 1.0),
        "rwkv_w0": unif((E, B_WIDTH), -2.5, 0.5),
        "rwkv_w2": nrm((E, DECAY_LORA, B_WIDTH), 0.1 * DECAY_LORA ** -0.5),
        "rwkv_a0": nrm((E, B_WIDTH), 0.5),
        "rwkv_a2": nrm((E, ICLR_LORA, B_WIDTH), 0.5 * ICLR_LORA ** -0.5),
        "rwkv_g2": nrm((E, GATE_LORA, B_WIDTH), GATE_LORA ** -0.5),
        "rwkv_k_k": 0.85 + nrm((E, B_WIDTH), 0.1),
        "rwkv_k_a": gain((E, B_WIDTH)),
        "rwkv_r_k": nrm((E, B_HEADS, B_HEAD_DIM), 0.1),
        "rwkv_gn_g": gain((E, B_WIDTH)),
        "rwkv_gn_b": nrm((E, B_WIDTH), 0.02),
        "e_w_out": nrm((E, MIX_WIDTH, D), MIX_WIDTH ** -0.5),
        "e_norm_ffn": gain((E, D)),
        "ffn_w_gate": nrm((E, D, FFN_DIM), D ** -0.5),
        "ffn_w_up": nrm((E, D, FFN_DIM), D ** -0.5),
        "ffn_w_down": nrm((E, FFN_DIM, D), FFN_DIM ** -0.5),
        "o_norm_mix": gain((O, D)),
        "o_w_in": nrm((O, D, IN1), D ** -0.5),
        "nsa_cmp_pos_k": nrm((O, CMP_LEN, C_HEAD_DIM), 0.1),
        "nsa_cmp_pos_v": nrm((O, CMP_LEN, C_HEAD_DIM), 0.1),
        "nsa_cmp_k_w1": nrm((O, CMP_LEN * C_HEAD_DIM, CMP_HIDDEN), (CMP_LEN * C_HEAD_DIM) ** -0.5),
        "nsa_cmp_k_w2": nrm((O, CMP_HIDDEN, C_HEAD_DIM), CMP_HIDDEN ** -0.5),
        "nsa_cmp_v_w1": nrm((O, CMP_LEN * C_HEAD_DIM, CMP_HIDDEN), (CMP_LEN * C_HEAD_DIM) ** -0.5),
        "nsa_cmp_v_w2": nrm((O, CMP_HIDDEN, C_HEAD_DIM), CMP_HIDDEN ** -0.5),
        "conv_w": nrm((O, CONV_W, D_WIDTH), CONV_W ** -0.5),
        "o_w_out": nrm((O, MIX_WIDTH, D), MIX_WIDTH ** -0.5),
        "o_norm_ffn": gain((O, D)),
        "moe_router": nrm((O, D, N_EXPERTS), D ** -0.5),
        "moe_router_b": nrm((O, N_EXPERTS), 0.01),
        "moe_w_gate": nrm((O, N_EXPERTS, D, EXPERT_DIM), D ** -0.5),
        "moe_w_up": nrm((O, N_EXPERTS, D, EXPERT_DIM), D ** -0.5),
        "moe_w_down": nrm((O, N_EXPERTS, EXPERT_DIM, D), EXPERT_DIM ** -0.5),
        "final_norm": gain((D,)),
    }

def second_block(x, e_norm_mix, e_w_in, sgu_ln_g, sgu_ln_b, sgu_w, sgu_b, rwkv_mu, rwkv_w0, rwkv_w2,
              rwkv_a0, rwkv_a2, rwkv_g2, rwkv_k_k, rwkv_k_a, rwkv_r_k, rwkv_gn_g, rwkv_gn_b, e_w_out,
              e_norm_ffn, ffn_w_gate, ffn_w_up, ffn_w_down, o_norm_mix, o_w_in, nsa_cmp_pos_k,
              nsa_cmp_pos_v, nsa_cmp_k_w1, nsa_cmp_k_w2, nsa_cmp_v_w1, nsa_cmp_v_w2, conv_w, o_w_out,
              o_norm_ffn, moe_router, moe_router_b, moe_w_gate, moe_w_up, moe_w_down, final_norm):
    t = x.shape[1]
    pos = jnp.arange(t, dtype=jnp.float32)
    inv_freq = ROPE_THETA ** (-jnp.arange(0, ROT_DIM, 2, dtype=jnp.float32) / ROT_DIM)
    ang = pos[:, None] * inv_freq[None, :]
    cos, sin = jnp.cos(ang), jnp.sin(ang)

    h = x
    for layer in range(DEPTH):
        i = layer // 2
        if layer % 2 == 0:
            hn = _rms_norm(h, e_norm_mix[i])
            p = hn @ e_w_in[i]
            pu, pv, pb = _split(p, [A_WIDTH, A_WIDTH, B_IN])
            ya = _chunked_sgu(jax.nn.gelu(pu), jax.nn.gelu(pv), sgu_ln_g[i], sgu_ln_b[i], sgu_w[i], sgu_b[i])
            yb = _rwkv7_time_mix(pb, rwkv_mu[i], rwkv_w0[i], rwkv_w2[i], rwkv_a0[i], rwkv_a2[i],
                                 rwkv_g2[i], rwkv_k_k[i], rwkv_k_a[i], rwkv_r_k[i],
                                 rwkv_gn_g[i], rwkv_gn_b[i])
            h = h + jnp.concatenate([ya.astype(h.dtype), yb.astype(h.dtype)], axis=-1) @ e_w_out[i]
            hn = _rms_norm(h, e_norm_ffn[i])
            h = h + _swiglu(hn, ffn_w_gate[i], ffn_w_up[i], ffn_w_down[i])
        else:
            hn = _rms_norm(h, o_norm_mix[i])
            p = hn @ o_w_in[i]
            q, kc, vc, ks, vs, kw, vw, gl, bg, cg, hd = _split(
                p, [C_WIDTH] + [KV_WIDTH] * 6 + [C_HEADS * N_BRANCH] + [D_WIDTH] * 3)
            yc = _nsa(q, kc, vc, ks, vs, kw, vw, gl, nsa_cmp_pos_k[i], nsa_cmp_pos_v[i],
                      nsa_cmp_k_w1[i], nsa_cmp_k_w2[i], nsa_cmp_v_w1[i], nsa_cmp_v_w2[i], cos, sin)
            yd = _short_conv(bg, cg, hd, conv_w[i])
            h = h + jnp.concatenate([yc.astype(h.dtype), yd.astype(h.dtype)], axis=-1) @ o_w_out[i]
            hn = _rms_norm(h, o_norm_ffn[i])
            h = h + _moe_swiglu(hn, moe_router[i], moe_router_b[i], moe_w_gate[i], moe_w_up[i], moe_w_down[i])
    return _rms_norm(h, final_norm)


def setup_inputs(seed=0):
    out = dict(first_inputs(seed))
    for name, value in second_inputs(seed + 1).items():
        if name != "x":
            out[name + "_2"] = value
    return out


def reference(
    x, w_in, w_out, pre_mix_w, post_mix_w, pre_mlp_w, post_mlp_w, w_ff1, w_ff2, conv_dw_w,
    conv_dw_b, conv_ln_w, conv_ln_b, diff_lambda_q1, diff_lambda_k1, diff_lambda_q2,
    diff_lambda_k2, diff_subln_w, delta_conv_w, delta_A_log, delta_dt_bias, delta_norm_w,
    e_norm_mix_2, e_w_in_2, sgu_ln_g_2, sgu_ln_b_2, sgu_w_2, sgu_b_2, rwkv_mu_2, rwkv_w0_2,
    rwkv_w2_2, rwkv_a0_2, rwkv_a2_2, rwkv_g2_2, rwkv_k_k_2, rwkv_k_a_2, rwkv_r_k_2, rwkv_gn_g_2,
    rwkv_gn_b_2, e_w_out_2, e_norm_ffn_2, ffn_w_gate_2, ffn_w_up_2, ffn_w_down_2, o_norm_mix_2,
    o_w_in_2, nsa_cmp_pos_k_2, nsa_cmp_pos_v_2, nsa_cmp_k_w1_2, nsa_cmp_k_w2_2, nsa_cmp_v_w1_2,
    nsa_cmp_v_w2_2, conv_w_2, o_w_out_2, o_norm_ffn_2, moe_router_2, moe_router_b_2,
    moe_w_gate_2, moe_w_up_2, moe_w_down_2, final_norm_2,
):
    x = first_block(
        x, w_in, w_out, pre_mix_w, post_mix_w, pre_mlp_w, post_mlp_w, w_ff1, w_ff2, conv_dw_w,
        conv_dw_b, conv_ln_w, conv_ln_b, diff_lambda_q1, diff_lambda_k1, diff_lambda_q2,
        diff_lambda_k2, diff_subln_w, delta_conv_w, delta_A_log, delta_dt_bias, delta_norm_w,
    )
    return second_block(
        x, e_norm_mix_2, e_w_in_2, sgu_ln_g_2, sgu_ln_b_2, sgu_w_2, sgu_b_2, rwkv_mu_2,
        rwkv_w0_2, rwkv_w2_2, rwkv_a0_2, rwkv_a2_2, rwkv_g2_2, rwkv_k_k_2, rwkv_k_a_2,
        rwkv_r_k_2, rwkv_gn_g_2, rwkv_gn_b_2, e_w_out_2, e_norm_ffn_2, ffn_w_gate_2, ffn_w_up_2,
        ffn_w_down_2, o_norm_mix_2, o_w_in_2, nsa_cmp_pos_k_2, nsa_cmp_pos_v_2, nsa_cmp_k_w1_2,
        nsa_cmp_k_w2_2, nsa_cmp_v_w1_2, nsa_cmp_v_w2_2, conv_w_2, o_w_out_2, o_norm_ffn_2,
        moe_router_2, moe_router_b_2, moe_w_gate_2, moe_w_up_2, moe_w_down_2, final_norm_2,
    )


_drawn_inputs = setup_inputs


def setup_inputs(seed=0):
    import zlib

    import numpy as np

    out = dict(_drawn_inputs(seed))
    spreads = {}
    factors = {'conv_ln_b': 3.538,
     'sgu_ln_b_2': 8.0,
     'rwkv_w2_2': 6.028,
     'rwkv_gn_b_2': 7.045,
     'nsa_cmp_pos_k_2': 8.0,
     'nsa_cmp_pos_v_2': 5.627,
     'nsa_cmp_k_w1_2': 3.498,
     'nsa_cmp_k_w2_2': 3.495,
     'moe_router_b_2': 4.997}
    for name, (base, spread) in spreads.items():
        noise = np.random.default_rng([zlib.crc32(name.encode()), seed]).standard_normal(out[name].shape)
        drawn = base * np.exp(spread * noise) if base else spread * noise
        out[name] = jnp.asarray(drawn.astype(out[name].dtype))
    for name, factor in factors.items():
        out[name] = (out[name] * factor).astype(out[name].dtype)
    return out
```

```python
from contextlib import ExitStack, contextmanager
import math

import numpy as np

import concourse.bass as bass
from concourse import mybir

F32 = mybir.dt.float32
U32 = mybir.dt.uint32
ACT = mybir.ActivationFunctionType
ALU = mybir.AluOpType
AX_X = mybir.AxisListType.X

P = 128
SEQ = 512
D_MODEL = 1024
KD = D_MODEL // P
TT = SEQ // P
DEPTH = 2
HEAD = 64
NORM_EPS = 1e-6
BIG = 1e30

DIFF_W = 384
DIFF_DIM = 32
DIFF_HEADS = DIFF_W // HEAD
DELTA_W = 384
DELTA_HEADS = DELTA_W // HEAD
CONV_CH = D_MODEL - DIFF_W - DELTA_W
CONV_T = CONV_CH // P
CONV_WIDTH = 31
SHORT_CONV = 3
D_FF = 4 * D_MODEL
PAIRS1 = DELTA_HEADS // 2
GATES1 = 4 * DELTA_HEADS
TM1 = DIFF_W + GATES1
U_CA, U_CG, U_DQ, U_DK, U_GQ, U_GK, U_GV, U_GZ = 0, 2, 4, 7, 10, 13, 16, 19
UT1 = 22

B_HEADS = 8
B_WIDTH = 512
A_WIDTH = 512
A_GROUPS = 4
RW_PAIRS = B_HEADS // 2
LORA = 64
SGU_LN_EPS = 1e-5
RWKV_GN_EPS = 64e-5
E_U, E_R, E_K, E_V, E_WA, E_G = 0, 4, 8, 12, 16, 17
UTE = 18
FFN_DIM = 2816
FFN_T = FFN_DIM // P
C_HEADS = 8
C_KV = 2
C_GROUP = C_HEADS // C_KV
KV_WIDTH = C_KV * HEAD
N_BRANCH = 3
CMP_LEN = 32
CMP_STRIDE = 16
N_CMP = (SEQ - CMP_LEN) // CMP_STRIDE + 1
CMP_HIDDEN = 256
ROT_DIM = HEAD // 4
ROPE_THETA = 500000.0
D_WIDTH = 512
TMO = 2 * KV_WIDTH + C_HEADS * N_BRANCH
O_Q, O_KC, O_VC, O_KS, O_KW, O_BG, O_CG, O_HD = 0, 4, 5, 6, 8, 10, 14, 18
UTO = 22
N_EXPERTS = 8
TOP_K = 2
EXPERT_DIM = 1408
EXP_T = EXPERT_DIM // P

LEVELS = int(math.log2(P))
SLOTS = 2
SLOT = 4096


class Columns:

    def __init__(self):
        self.at, self.size = {}, 0

    def add(self, name, n):
        self.at[name] = (self.size, n)
        self.size += n
        return self

    def __call__(self, tensor, name, i=None, n=1):
        first, size = self.at[name]
        if i is None:
            return tensor[:, first:first + size]
        return tensor[:, first + i:first + i + n]


CONST = Columns()
for _name, _n in [("ident", P), ("ones", P), ("pair_ones", P), ("rot", P),
                  ("lower_in", P), ("upper_in", P), ("upper_strict", P), ("neg_lower_strict", P),
                  ("lower_strict_max", P), ("upper_strict_max", P), ("upper_in_min", P), ("lower_in_min", P),
                  ("causal_min", P), ("neg_slopes", DIFF_HEADS),
                  ("cmp_min", TT * N_CMP), ("cmp_one", TT * N_CMP), ("not_first", SEQ),
                  ("experts", N_EXPERTS), ("eps", 4)]:
    CONST.add(_name, _n)

VEC1 = Columns()
for _name, _n in [("pre_mix", KD), ("post_mix", KD), ("pre_mlp", KD), ("post_mlp", KD),
                  ("conv_w", CONV_T * CONV_WIDTH), ("conv_b", CONV_T), ("ln_w", CONV_T), ("ln_b", CONV_T),
                  ("subln", 1), ("delta_conv", 3 * PAIRS1 * SHORT_CONV), ("delta_norm", 1)]:
    VEC1.add(_name, _n)

VECE = Columns()
for _name, _n in [("norm_mix", KD), ("norm_ffn", KD), ("mu", 14), ("w0", RW_PAIRS), ("a0", RW_PAIRS),
                  ("k_k", RW_PAIRS), ("k_a", RW_PAIRS), ("r_k", RW_PAIRS), ("gn_g", RW_PAIRS), ("gn_b", RW_PAIRS)]:
    VECE.add(_name, _n)

VECO = Columns()
for _name, _n in [("norm_mix", KD), ("norm_ffn", KD), ("final", KD), ("pos_k", CMP_LEN), ("pos_v", CMP_LEN),
                  ("conv", (D_WIDTH // P) * 3)]:
    VECO.add(_name, _n)


class Steps:

    def __init__(self, engine, sem):
        self.engine, self.sem, self.count, self.open = engine, sem, {}, set()

    def did(self, instruction, sem=None):
        sem = self.sem if sem is None else sem
        self.count[sem] = self.count.get(sem, 0) + 1
        self.open.add(sem)
        return instruction.then_inc(sem, 1)

    def settle(self):
        for sem in [s for s in self.count if s in self.open]:
            self.engine.wait_ge(sem, self.count[sem])
        self.open = set()


@contextmanager
def phase(nc, *names):
    sems = [nc.alloc_semaphore(f"{n}_{nc.next_id()}") for n in names]
    with nc.Block() as block:
        yield (block, *sems)
    nc.clear_and_free_semaphores(sems)
    nc.all_engine_barrier()


@contextmanager
def buffers(nc, **shapes):
    with ExitStack() as stack:
        yield [stack.enter_context(nc.sbuf_tensor(f"{n}_{nc.next_id()}", s, F32)) for n, s in shapes.items()]


def rms_norm(nc, mem, source, gain, out, add_to=None):
    with buffers(nc, squares=[P, KD, SEQ], scale=[P, SEQ]) as (squares, scale), phase(
            nc, "squares_ready", "sum_ready", "root_ready", "dve_steps") as (
            block, squares_ready, sum_ready, root_ready, dve_steps):
        total = mem.bank[0]

        @block.scalar
        def _(act):
            for k in range(KD):
                nc.scalar.activation(squares[:, k, :], source[:, k, :], ACT.Square).then_inc(squares_ready, 1)
            act.wait_ge(sum_ready, 1)
            nc.scalar.activation(scale[:, :], total[:, :], ACT.Sqrt, bias=mem.eps[:, 0:1],
                                 scale=1.0 / D_MODEL).then_inc(root_ready, 1)

        @block.tensor
        def _(pe):
            for k in range(KD):
                pe.wait_ge(squares_ready, k + 1)
                last = nc.tensor.matmul(total[:, :], CONST(mem.const, "ones"), squares[:, k, :],
                                        start=(k == 0), stop=(k == KD - 1))
            last.then_inc(sum_ready, 1)

        @block.vector
        def _(dve):
            steps = Steps(dve, dve_steps)
            dve.wait_ge(root_ready, 1)
            steps.did(nc.vector.reciprocal(scale[:, :], scale[:, :]))
            steps.settle()
            for k in range(KD):
                to = out if add_to is None else squares
                steps.did(nc.vector.scalar_tensor_tensor(out=to[:, k, :], in0=source[:, k, :], scalar=gain(k),
                                                         in1=scale[:, :], op0=ALU.mult, op1=ALU.mult))
            if add_to is not None:
                steps.settle()
                for k in range(KD):
                    steps.did(nc.vector.tensor_tensor(add_to[:, k, :], add_to[:, k, :], squares[:, k, :], ALU.add))
            steps.settle()


def linear(nc, mem, weights, units, tiles, kt, source, evacuate, on_vector=False, gated=None):
    size = tiles * kt * P
    loops, rest = divmod(units, SLOTS)
    n_banks = SLOTS * tiles
    names = [f"filled{s}" for s in range(SLOTS)] + [f"gate_ready{s}" for s in range(SLOTS)]
    names += [f"product{b}" for b in range(n_banks)] + [f"taken{b}" for b in range(n_banks)]
    with phase(nc, *names) as (block, *sems):
        filled, gate_ready = sems[:SLOTS], sems[SLOTS:2 * SLOTS]
        product, taken = sems[2 * SLOTS:2 * SLOTS + n_banks], sems[2 * SLOTS + n_banks:]
        bank_free = [gate_ready[b // 2] if gated is not None and b % 2 == 0 else taken[b] for b in range(n_banks)]

        def rounds(engine, body):
            if loops:
                with engine.Fori(0, loops) as i:
                    body(i, SLOTS)
            if rest:
                body(loops, rest)

        @block.sync
        def _(sp):
            def fill(i, s):
                sp.dma_start(mem.ring[:, s, 0:size], weights(i * SLOTS + s)).then_inc(filled[s], 16)

            for s in range(min(SLOTS, units)):
                fill(0, s)

            def refill(i, slots):
                for s in range(slots):
                    sp.wait_ge(product[(s + 1) * tiles - 1], i)
                    fill(i, s)

            if loops > 1:
                with sp.Fori(1, loops) as i:
                    refill(i, SLOTS)
            if rest and loops:
                refill(loops, rest)

        @block.tensor
        def _(pe):
            def multiply(i, slots):
                for s in range(slots):
                    pe.wait_ge(filled[s], i * 16 + 16)
                    for j in range(tiles):
                        b = s * tiles + j
                        pe.wait_ge(bank_free[b], i + 1)
                        for k in range(kt):
                            at = (j * kt + k) * P
                            last = nc.tensor.matmul(mem.bank[b][:, :], mem.ring[:, s, at:at + P], source[:, k, :],
                                                    start=(k == 0), stop=(k == kt - 1))
                        last.then_inc(product[b], 1)

            rounds(pe, multiply)

        if gated is not None:
            @block.scalar
            def _(act):
                for s in range(SLOTS):
                    act.sem_inc(gate_ready[s], 1)

                def activate(i, slots):
                    for s in range(slots):
                        act.wait_ge(product[2 * s], i + 1)
                        act.wait_ge(taken[2 * s + 1], i + 1)
                        nc.scalar.activation(gated[:, s, :], mem.bank[2 * s][:, :], ACT.Silu) \
                            .then_inc(gate_ready[s], 1)

                rounds(act, activate)

            @block.vector
            def _(dve):
                for s in range(SLOTS):
                    dve.sem_inc(taken[2 * s + 1], 1)

                def multiply(i, slots):
                    for s in range(slots):
                        dve.wait_ge(product[2 * s + 1], i + 1)
                        dve.wait_ge(gate_ready[s], i + 2)
                        evacuate(mem.bank[2 * s + 1], i * SLOTS + s, gated[:, s, :]).then_inc(taken[2 * s + 1], 1)

                rounds(dve, multiply)
            return

        @(block.vector if on_vector else block.scalar)
        def _(taker):
            for b in range(n_banks):
                taker.sem_inc(taken[b], 1)

            def take(i, slots):
                for b in range(slots * tiles):
                    taker.wait_ge(product[b], i + 1)
                    evacuate(mem.bank[b], i * n_banks + b).then_inc(taken[b], 1)

            rounds(taker, take)


def tile_at(tensor, index):
    return tensor[:, bass.ds(index, 1), :].rearrange("p a n -> p (a n)")


def copy_out(nc, out):
    def evacuate(bank, tile):
        return nc.scalar.activation(tile_at(out, tile), bank[:, :], ACT.Copy)
    return evacuate


def add_out(nc, target):
    def evacuate(bank, tile):
        return nc.vector.tensor_tensor(tile_at(target, tile), tile_at(target, tile), bank[:, :], ALU.add)
    return evacuate


def token_major(nc, mem, weights, cols, source, out):
    with phase(nc, "filled", "product", "taken") as (block, filled, product, taken):
        w = mem.ring[:, :, :].rearrange("p s n -> p (s n)")

        @block.sync
        def _(sp):
            sp.dma_start(w[:, 0:KD * cols], weights).then_inc(filled, 16)

        @block.tensor
        def _(pe):
            pe.wait_ge(filled, 16)
            for t in range(TT):
                for k in range(KD):
                    last = nc.tensor.matmul(mem.bank[t][:, 0:cols], source[:, k, t * P:(t + 1) * P],
                                            w[:, k * cols:(k + 1) * cols], start=(k == 0), stop=(k == KD - 1))
                last.then_inc(product, 1)

        @block.scalar
        def _(act):
            for t in range(TT):
                act.wait_ge(product, t + 1)
                nc.scalar.activation(out[:, t, 0:cols], mem.bank[t][:, 0:cols], ACT.Copy).then_inc(taken, 1)
            act.wait_ge(taken, TT)


def squared_relu_mlp(nc, mem, w_up, w_down):
    with buffers(nc, hidden=[P, D_FF // P, SEQ]) as (hidden,):
        def squared_relu(bank, tile):
            return nc.scalar.activation(tile_at(hidden, tile), bank[:, :], ACT.Relu)

        linear(nc, mem, w_up, D_FF // P // 2, 2, KD, mem.h, squared_relu)
        with phase(nc, "squared") as (block, squared):
            half = D_FF // P // 2

            @block.vector
            def _(dve):
                for q in range(half):
                    nc.vector.tensor_tensor(hidden[:, q, :], hidden[:, q, :], hidden[:, q, :], ALU.mult)

            @block.scalar
            def _(act):
                for q in range(half, 2 * half):
                    nc.scalar.activation(hidden[:, q, :], hidden[:, q, :], ACT.Square)
        linear(nc, mem, w_down, KD, 1, D_FF // P, hidden, copy_out(nc, mem.h))


def conv_module(nc, mem, vec, u, y):
    half = CONV_WIDTH // 2
    with buffers(nc, padded=[P, CONV_T, SEQ + 2 * half], acc=[P, CONV_T, SEQ], sig=[P, CONV_T, SEQ],
                 squares=[P, CONV_T, SEQ], scale=[P, SEQ]) as (padded, acc, sig, squares, scale), phase(
            nc, "gate_ready", "conv_done", "mean_ready", "centred", "squares_ready", "var_ready",
            "root_ready", "normed", "dve_steps") as (
            block, gate_ready, conv_done, mean_ready, centred, squares_ready, var_ready,
            root_ready, normed, dve_steps):
        total, spread = mem.bank[0], mem.bank[1]

        @block.scalar
        def _(act):
            for c in range(CONV_T):
                nc.scalar.activation(sig[:, c, :], u[:, U_CG + c, :], ACT.Sigmoid).then_inc(gate_ready, 1)
            for c in range(CONV_T):
                act.wait_ge(centred, c + 1)
                nc.scalar.activation(squares[:, c, :], acc[:, c, :], ACT.Square).then_inc(squares_ready, 1)
            act.wait_ge(var_ready, 1)
            nc.scalar.activation(scale[:, :], spread[:, :], ACT.Sqrt, bias=mem.eps[:, 1:2],
                                 scale=1.0 / CONV_CH).then_inc(root_ready, 1)
            for c in range(CONV_T):
                act.wait_ge(normed, c + 1)
                nc.scalar.activation(y[:, c, :], acc[:, c, :], ACT.Silu, scale=VEC1(vec, "ln_w", c),
                                     bias=VEC1(vec, "ln_b", c))

        @block.tensor
        def _(pe):
            for c in range(CONV_T):
                pe.wait_ge(conv_done, c + 1)
                last = nc.tensor.matmul(total[:, :], CONST(mem.const, "ones"), acc[:, c, :],
                                        start=(c == 0), stop=(c == CONV_T - 1))
            last.then_inc(mean_ready, 1)
            for c in range(CONV_T):
                pe.wait_ge(squares_ready, c + 1)
                last = nc.tensor.matmul(spread[:, :], CONST(mem.const, "ones"), squares[:, c, :],
                                        start=(c == 0), stop=(c == CONV_T - 1))
            last.then_inc(var_ready, 1)

        @block.vector
        def _(dve):
            steps = Steps(dve, dve_steps)
            steps.did(nc.vector.memset(padded[:, :, :], 0.0))
            steps.settle()
            for c in range(CONV_T):
                dve.wait_ge(gate_ready, c + 1)
                steps.did(nc.vector.tensor_tensor(padded[:, c, half:half + SEQ], u[:, U_CA + c, :], sig[:, c, :],
                                                  ALU.mult))
            steps.settle()
            for tap in range(CONV_WIDTH):
                for c in range(CONV_T):
                    window = padded[:, c, tap:tap + SEQ]
                    weight = VEC1(vec, "conv_w", c * CONV_WIDTH + tap)
                    if tap == 0:
                        last = nc.vector.tensor_scalar(acc[:, c, :], window, weight, VEC1(vec, "conv_b", c),
                                                       ALU.mult, ALU.add)
                    else:
                        if tap < CONV_WIDTH - 1:
                            dve.wait_ge(dve_steps, steps.count[dve_steps] - CONV_T + 1)
                        else:
                            steps.settle()
                        last = nc.vector.scalar_tensor_tensor(out=acc[:, c, :], in0=window, scalar=weight,
                                                              in1=acc[:, c, :], op0=ALU.mult, op1=ALU.add)
                    steps.did(last, conv_done if tap == CONV_WIDTH - 1 else None)
            dve.wait_ge(mean_ready, 1)
            steps.settle()
            for c in range(CONV_T):
                steps.did(nc.vector.scalar_tensor_tensor(out=acc[:, c, :], in0=total[:, :], scalar=-1.0 / CONV_CH,
                                                         in1=acc[:, c, :], op0=ALU.mult, op1=ALU.add), centred)
            dve.wait_ge(root_ready, 1)
            steps.did(nc.vector.reciprocal(scale[:, :], scale[:, :]))
            steps.settle()
            dve.wait_ge(squares_ready, CONV_T)
            for c in range(CONV_T):
                steps.did(nc.vector.tensor_tensor(acc[:, c, :], acc[:, c, :], scale[:, :], ALU.mult), normed)
            steps.settle()


def diff_lambda(nc, mem, lam_rows, coef):
    with buffers(nc, prod=[P, 2, DIFF_DIM], dots=[P, 4]) as (prod, dots), phase(
            nc, "dots_ready", "exps_ready", "dve_steps") as (block, dots_ready, exps_ready, dve_steps):
        @block.vector
        def _(dve):
            steps = Steps(dve, dve_steps)
            for m in range(2):
                steps.did(nc.vector.tensor_tensor(prod[:, m, :], lam_rows[:, 2 * m * DIFF_DIM:(2 * m + 1) * DIFF_DIM],
                                                  lam_rows[:, (2 * m + 1) * DIFF_DIM:(2 * m + 2) * DIFF_DIM], ALU.mult))
            steps.settle()
            steps.did(nc.vector.reduce_sum(dots[:, 0:2], prod[:, :, :], AX_X), dots_ready)
            steps.did(nc.vector.memset(coef[:, 0:1], 1.0))
            dve.wait_ge(exps_ready, 1)
            steps.did(nc.vector.tensor_tensor(dots[:, 0:1], dots[:, 3:4], dots[:, 2:3], ALU.subtract))
            steps.settle()
            steps.did(nc.vector.tensor_tensor(coef[:, 1:2], dots[:, 0:1], lam_rows[:, 4 * DIFF_DIM:4 * DIFF_DIM + 1],
                                              ALU.subtract))
            steps.settle()

        @block.scalar
        def _(act):
            act.wait_ge(dots_ready, 1)
            nc.scalar.activation(dots[:, 2:4], dots[:, 0:2], ACT.Exp).then_inc(exps_ready, 1)


def diff_attention(nc, mem, vec, lam_rows, distances, u, tm, y):
    first_tile = CONV_T
    units = [(h, t) for h in range(2) for t in range(TT)]
    with buffers(nc, coef=[P, 2], dist=[P, TT, SEQ]) as (coef, dist):
        load(nc, (dist[:, :, :], distances))
        diff_lambda(nc, mem, lam_rows, coef)
        with nc.Fori(0, PAIRS1) as j, buffers(
                nc, q=[P, SEQ], k=[P, SEQ], v=[P, TT, P], slope=[P, 2], scores=[P, 4, SEQ], tops=[P, 16],
                sums=[P, 16], inv=[P, 16], mixed=[P, 2, SEQ], turned=[P, 2, SEQ], heads=[P, SEQ],
                squares=[P, SEQ], scale=[P, SEQ], gain=[P, 1]) as (
                q, k, v, slope, scores, tops, sums, inv, mixed, turned, heads, squares, scale, gain), phase(
                nc, "staged", "dve_staged", "score", "topped", "exped", "mixed_ready", "turn", "turned_ready", "applied",
                "heads_taken", "squared", "summed", "rooted", "dve_steps", "act_steps") as (
                block, staged, dve_staged, score, topped, exped, mixed_ready, turn, turned_ready, applied,
                heads_taken, squared, summed, rooted, dve_steps, act_steps):
            out_bank, sum_bank = mem.bank[6], mem.bank[7]

            @block.scalar
            def _(act):
                nc.scalar.activation(q[:, :], tile_at(u, j + U_DQ), ACT.Copy, scale=DIFF_DIM ** -0.5).then_inc(staged, 1)
                nc.scalar.activation(k[:, :], tile_at(u, j + U_DK), ACT.Copy).then_inc(staged, 1)

                def turned_copy(n):
                    act.wait_ge(turn, n + 1)
                    if n >= 2:
                        act.wait_ge(applied, n - 1)
                    nc.scalar.activation(turned[:, n % 2, :], mem.bank[4 + n % 2][:, :], ACT.Copy) \
                        .then_inc(turned_ready, 1)

                for n in range(len(units)):
                    for m in range(2):
                        i = 2 * n + m
                        act.wait_ge(topped, n + 1)
                        nc.scalar.activation(scores[:, i % 4, :], scores[:, i % 4, :], ACT.Exp, bias=tops[:, i:i + 1],
                                             accum_out=sums[:, i:i + 1]).then_inc(exped, 1)
                    if n >= 1:
                        turned_copy(n - 1)
                turned_copy(len(units) - 1)
                act.wait_ge(heads_taken, 1)
                nc.scalar.activation(squares[:, :], heads[:, :], ACT.Square).then_inc(squared, 1)
                act.wait_ge(summed, 1)
                nc.scalar.activation(scale[:, :], sum_bank[:, :], ACT.Sqrt, bias=mem.eps[:, 1:2],
                                     scale=1.0 / HEAD).then_inc(rooted, 1)

            @block.tensor
            def _(pe):
                pe.wait_ge(staged, 2)
                pe.wait_ge(dve_staged, 1)

                def scored(n):
                    h, t = units[n]
                    for m in range(2):
                        i = 2 * n + m
                        if i >= 4:
                            pe.wait_ge(topped, (i - 4) // 2 + 1)
                        lanes = slice(DIFF_DIM * (2 * h + m), DIFF_DIM * (2 * h + m + 1))
                        nc.tensor.matmul(mem.bank[i % 4][:, :], q[lanes, t * P:(t + 1) * P], k[lanes, :],
                                         start=True, stop=True).then_inc(score, 1)

                def transposed(n):
                    pe.wait_ge(mixed_ready, n + 1)
                    if n >= 2:
                        pe.wait_ge(turned_ready, n - 1)
                    for b in range(TT):
                        last = nc.tensor.transpose(mem.bank[4 + n % 2][:, b * P:(b + 1) * P],
                                                   mixed[:, n % 2, b * P:(b + 1) * P], CONST(mem.const, "ident"))
                    last.then_inc(turn, 1)

                def apply(n):
                    h, t = units[n]
                    pe.wait_ge(turned_ready, n + 1)
                    for b in range(TT):
                        last = nc.tensor.matmul(out_bank[h * HEAD:(h + 1) * HEAD, t * P:(t + 1) * P],
                                                v[:, b, h * HEAD:(h + 1) * HEAD], turned[:, n % 2, b * P:(b + 1) * P],
                                                start=(b == 0), stop=(b == TT - 1))
                    last.then_inc(applied, 1)

                for n in range(len(units)):
                    scored(n)
                    if n >= 1:
                        transposed(n - 1)
                    if n >= 2:
                        apply(n - 2)
                transposed(len(units) - 1)
                for n in (len(units) - 2, len(units) - 1):
                    apply(n)
                pe.wait_ge(squared, 1)
                nc.tensor.matmul(sum_bank[:, :], CONST(mem.const, "pair_ones"), squares[:, :], start=True,
                                 stop=True).then_inc(summed, 1)

            @block.vector
            def _(dve):
                steps = Steps(dve, dve_steps)
                steps.did(nc.vector.tensor_copy(v[:, :, :], tm[:, :, bass.ds(j * P, P)]), dve_staged)
                steps.did(nc.vector.tensor_copy(slope[:, :], CONST(mem.const, "neg_slopes")[:, bass.ds(j * 2, 2)]), dve_staged)
                steps.did(nc.vector.tensor_tensor(gain[:, :], VEC1(vec, "subln"),
                                                  lam_rows[:, 4 * DIFF_DIM + 1:4 * DIFF_DIM + 2], ALU.mult), dve_staged)
                steps.settle()

                def biased(n):
                    h, t = units[n]
                    for m in range(2):
                        i = 2 * n + m
                        dve.wait_ge(score, i + 1)
                        if n >= 2:
                            dve.wait_ge(mixed_ready, n - 1)
                        steps.did(nc.vector.scalar_tensor_tensor(
                            out=scores[:, i % 4, :], in0=dist[:, t, :], scalar=slope[:, h:h + 1],
                            in1=mem.bank[i % 4][:, :], op0=ALU.mult, op1=ALU.add))
                    steps.settle()
                    for m in range(2):
                        i = 2 * n + m
                        steps.did(nc.vector.reduce_max(inv[:, i:i + 1], scores[:, i % 4, :], AX_X))
                    steps.settle()
                    i = 2 * n
                    steps.did(nc.vector.tensor_scalar(tops[:, i:i + 2], inv[:, i:i + 2], -1.0, None, ALU.mult),
                              topped)
                    steps.settle()

                def mix(n):
                    i = 2 * n
                    dve.wait_ge(exped, i + 2)
                    steps.did(nc.vector.reciprocal(inv[:, i:i + 2], sums[:, i:i + 2]))
                    steps.settle()
                    steps.did(nc.vector.tensor_tensor(inv[:, i:i + 2], inv[:, i:i + 2], coef[:, :], ALU.mult))
                    steps.settle()
                    if n >= 2:
                        dve.wait_ge(turn, n - 1)
                    steps.did(nc.vector.tensor_scalar(mixed[:, n % 2, :], scores[:, i % 4, :], inv[:, i:i + 1], None,
                                                      ALU.mult))
                    steps.settle()
                    steps.did(nc.vector.scalar_tensor_tensor(
                        out=mixed[:, n % 2, :], in0=scores[:, (i + 1) % 4, :], scalar=inv[:, i + 1:i + 2],
                        in1=mixed[:, n % 2, :], op0=ALU.mult, op1=ALU.add), mixed_ready)

                for n in range(len(units)):
                    biased(n)
                    if n >= 1:
                        mix(n - 1)
                mix(len(units) - 1)
                dve.wait_ge(applied, len(units))
                steps.did(nc.vector.tensor_copy(heads[:, :], out_bank[:, :]), heads_taken)
                dve.wait_ge(rooted, 1)
                steps.did(nc.vector.reciprocal(scale[:, :], scale[:, :]))
                steps.settle()
                steps.did(nc.vector.scalar_tensor_tensor(out=tile_at(y, j + first_tile), in0=heads[:, :],
                                                         scalar=gain[:, 0:1], in1=scale[:, :], op0=ALU.mult,
                                                         op1=ALU.mult))
                steps.settle()


G_NEG, G_NBETA, G_BETA, G_BEXP, G_KDEC, G_LAST = range(6)
KINDS = 6
GH = 2 * DELTA_HEADS


def delta_gates(nc, mem, gates, tm, cols, rows):
    with buffers(nc, beta=[P, TT, GH], pre=[P, TT, GH], soft=[P, TT, GH], g=[P, TT, GH], rate=[P, GH],
                 run=[P, TT, GH], total=[P, TT, GH]) as (beta, pre, soft, g, rate, run, total), phase(
            nc, "beta_ready", "pre_ready", "soft_ready", "g_ready", "summed", "taken", "row_ready", "row_taken",
            "shifted", "exped", "act_steps", "dve_steps") as (
            block, beta_ready, pre_ready, soft_ready, g_ready, summed, taken, row_ready, row_taken,
            shifted, exped, act_steps, dve_steps):
        @block.scalar
        def _(act):
            steps = Steps(act, act_steps)
            nc.scalar.activation(beta[:, :, :], tm[:, :, DIFF_W:DIFF_W + GH], ACT.Sigmoid).then_inc(beta_ready, 1)
            steps.did(nc.scalar.activation(rate[:, :], gates[:, 0, :], ACT.Exp))
            act.wait_ge(pre_ready, 1)
            steps.did(nc.scalar.activation(soft[:, :, :], soft[:, :, :], ACT.Exp))
            steps.settle()
            nc.scalar.activation(soft[:, :, :], soft[:, :, :], ACT.Ln, bias=1.0).then_inc(soft_ready, 1)
            act.wait_ge(summed, 1)
            steps.did(nc.scalar.activation(run[:, :, :], mem.bank[0][:, 0:TT * GH], ACT.Copy), taken)
            steps.did(nc.scalar.activation(total[:, :, :], mem.bank[1][:, 0:TT * GH], ACT.Copy), taken)
            for n in range(GH):
                act.wait_ge(row_ready, n + 1)
                nc.scalar.activation(rows[:, n, :], mem.bank[2 + n % 2][:, :], ACT.Copy).then_inc(row_taken, 1)
            act.wait_ge(shifted, 1)
            nc.scalar.activation(cols[:, G_KDEC, :, :], cols[:, G_KDEC, :, :], ACT.Exp).then_inc(exped, 1)
            nc.scalar.activation(cols[:, G_LAST, :, :], total[:, :, :], ACT.Exp).then_inc(exped, 1)
            nc.scalar.activation(cols[:, G_BEXP, :, :], run[:, :, :], ACT.Exp).then_inc(exped, 1)

        @block.vector
        def _(dve):
            steps = Steps(dve, dve_steps)
            bias = gates[:, 1, :].unsqueeze(1).broadcast_to([P, TT, GH])
            steps.did(nc.vector.tensor_tensor(pre[:, :, :], tm[:, :, DIFF_W + GH:DIFF_W + 2 * GH], bias, ALU.add))
            steps.settle()
            steps.did(nc.vector.scalar_tensor_tensor(out=soft[:, :, :], in0=pre[:, :, :], scalar=-1.0,
                                                     in1=pre[:, :, :], op0=ALU.mult, op1=ALU.min), pre_ready)
            dve.wait_ge(soft_ready, 1)
            steps.did(nc.vector.scalar_tensor_tensor(out=pre[:, :, :], in0=pre[:, :, :], scalar=0.0,
                                                     in1=soft[:, :, :], op0=ALU.max, op1=ALU.add))
            steps.settle()
            dve.wait_ge(act_steps, 1)
            steps.did(nc.vector.scalar_tensor_tensor(
                out=g[:, :, :], in0=pre[:, :, :], scalar=-1.0, in1=rate[:, :].unsqueeze(1).broadcast_to([P, TT, GH]),
                op0=ALU.mult, op1=ALU.mult), g_ready)
            dve.wait_ge(beta_ready, 1)
            steps.did(nc.vector.tensor_scalar(cols[:, G_NBETA, :, :], beta[:, :, :], -1.0, None, ALU.mult))
            steps.did(nc.vector.tensor_copy(cols[:, G_BETA, :, :], beta[:, :, :]))
            dve.wait_ge(taken, 2)
            steps.did(nc.vector.tensor_scalar(cols[:, G_NEG, :, :], run[:, :, :], -1.0, None, ALU.mult))
            steps.did(nc.vector.tensor_tensor(cols[:, G_KDEC, :, :], total[:, :, :], run[:, :, :], ALU.subtract),
                      shifted)
            dve.wait_ge(exped, 3)
            steps.did(nc.vector.tensor_tensor(cols[:, G_BEXP, :, :], cols[:, G_BEXP, :, :], beta[:, :, :], ALU.mult))
            steps.settle()

        @block.tensor
        def _(pe):
            pe.wait_ge(g_ready, 1)
            run_sum, whole = mem.bank[0], mem.bank[1]
            half = DELTA_HEADS
            triangle = [CONST(mem.const, "upper_in"), CONST(mem.const, "lower_in")]
            for t in range(TT):
                nc.tensor.matmul(whole[:, t * GH:(t + 1) * GH], CONST(mem.const, "ones"), g[:, t, :],
                                 start=True, stop=True)
                for d in range(2):
                    last = nc.tensor.matmul(run_sum[:, t * GH + d * half:t * GH + (d + 1) * half], triangle[d],
                                            g[:, t, d * half:(d + 1) * half], start=True, stop=True)
            last.then_inc(summed, 1)
            for n in range(GH):
                if n >= 2:
                    pe.wait_ge(row_taken, n - 1)
                for t in range(TT):
                    last = nc.tensor.matmul(mem.bank[2 + n % 2][:, t * P:(t + 1) * P],
                                            g[:, t, n:n + 1].broadcast_to([P, P]), triangle[n // half],
                                            start=True, stop=True)
                last.then_inc(row_ready, 1)


def delta_prepare(nc, mem, vec, u, cols, rows, hp, b):
    with buffers(nc, conv=[P, 3, SEQ], taps=[P, 3 * SHORT_CONV], squares=[P, 2, SEQ], scale=[P, 2, SEQ],
                 kk=[P, 2, SEQ], kq=[P, 2, SEQ], decay=[P, 2, SEQ]) as (
            conv, taps, squares, scale, kk, kq, decay), phase(
            nc, "conv_done", "silued", "squared", "summed", "rooted", "normed", "turned", "turned_taken",
            "product", "product_taken", "bounded", "exped", "dve_steps", "act_steps") as (
            block, conv_done, silued, squared, summed, rooted, normed, turned, turned_taken,
            product, product_taken, bounded, exped, dve_steps, act_steps):
        streams = [(d, par) for d in range(2) for par in range(2)]

        @block.vector
        def _(dve):
            steps = Steps(dve, dve_steps)
            for s in range(3):
                at = VEC1.at["delta_conv"][0] + s * PAIRS1 * SHORT_CONV
                steps.did(nc.vector.tensor_copy(taps[:, s * SHORT_CONV:(s + 1) * SHORT_CONV],
                                                vec[:, bass.ds(hp * SHORT_CONV + at, SHORT_CONV)]))
            for d in range(2):
                steps.did(nc.vector.tensor_copy(
                    b.cols[:, :, d, :],
                    cols[:, :, :, :].rearrange("p k t h -> p (k t) h")[:, :, bass.ds(hp * 2 + d * DELTA_HEADS, 2)]))
            steps.settle()
            source = [U_GQ, U_GK, U_GV]
            x = [u[:, bass.ds(hp + source[s], 1), :] for s in range(3)]
            for s in range(3):
                steps.did(nc.vector.tensor_scalar(conv[:, s:s + 1, :], x[s], taps[:, 3 * s + 1:3 * s + 2], None,
                                                  ALU.mult))
            steps.settle()
            for s in range(3):
                steps.did(nc.vector.scalar_tensor_tensor(
                    out=conv[:, s:s + 1, 1:SEQ], in0=x[s][:, :, 0:SEQ - 1], scalar=taps[:, 3 * s:3 * s + 1],
                    in1=conv[:, s:s + 1, 1:SEQ], op0=ALU.mult, op1=ALU.add))
            steps.settle()
            for s in range(3):
                steps.did(nc.vector.scalar_tensor_tensor(
                    out=conv[:, s:s + 1, 0:SEQ - 1], in0=x[s][:, :, 1:SEQ], scalar=taps[:, 3 * s + 2:3 * s + 3],
                    in1=conv[:, s:s + 1, 0:SEQ - 1], op0=ALU.mult, op1=ALU.add), conv_done)
            for s in range(2):
                dve.wait_ge(rooted, s + 1)
                steps.did(nc.vector.reciprocal(scale[:, s, :], scale[:, s, :]))
            steps.settle()
            dve.wait_ge(silued, 3)
            steps.did(nc.vector.scalar_tensor_tensor(out=b.q[:, :], in0=conv[:, 0, :], scalar=HEAD ** -0.5,
                                                     in1=scale[:, 0, :], op0=ALU.mult, op1=ALU.mult), normed)
            steps.did(nc.vector.tensor_tensor(b.k[:, :], conv[:, 1, :], scale[:, 1, :], ALU.mult), normed)

            def bound(n):
                d, par = streams[n]
                row = rows[:, bass.ds(hp * 2 + d * DELTA_HEADS + par, 1), :].rearrange("p a n -> p (a n)")
                masks = [("lower_strict_max", ALU.max), ("upper_in_min", ALU.min)] if d == 0 else \
                    [("upper_strict_max", ALU.max), ("lower_in_min", ALU.min)]
                for e in range(2):
                    for t in range(TT):
                        steps.did(nc.vector.scalar_tensor_tensor(
                            out=decay[:, e, t * P:(t + 1) * P], in0=row[:, t * P:(t + 1) * P],
                            scalar=b.cols[:, G_NEG * TT + t, d, par:par + 1], in1=CONST(mem.const, masks[e][0]),
                            op0=ALU.add, op1=masks[e][1]), bounded)

            for n, (d, par) in enumerate(streams):
                bound(n)
                dve.wait_ge(product_taken, 4)
                dve.wait_ge(exped, 2 * n + 2)
                for t in range(TT):
                    steps.did(nc.vector.scalar_tensor_tensor(
                        out=b.neg[:, n, t * P:(t + 1) * P], in0=kk[:, par, t * P:(t + 1) * P],
                        scalar=b.cols[:, G_NBETA * TT + t, d, par:par + 1], in1=decay[:, 0, t * P:(t + 1) * P],
                        op0=ALU.mult, op1=ALU.mult))
                steps.did(nc.vector.tensor_tensor(b.seen[:, n, :], kq[:, par, :], decay[:, 1, :], ALU.mult))
                steps.settle()

        @block.scalar
        def _(act):
            for s in range(3):
                act.wait_ge(conv_done, s + 1)
                nc.scalar.activation(conv[:, s, :], conv[:, s, :], ACT.Silu).then_inc(silued, 1)
            for s in range(2):
                act.wait_ge(silued, s + 1)
                nc.scalar.activation(squares[:, s, :], conv[:, s, :], ACT.Square).then_inc(squared, 1)
            for s in range(2):
                act.wait_ge(summed, s + 1)
                nc.scalar.activation(scale[:, s, :], mem.bank[s][:, :], ACT.Sqrt, bias=mem.eps[:, 0:1]) \
                    .then_inc(rooted, 1)
            for s, to in ((0, b.v_rows), (1, b.k_rows)):
                act.wait_ge(turned, s + 1)
                nc.scalar.activation(to[:, :, :].rearrange("p t n -> p (t n)"), mem.bank[2 + s][:, :], ACT.Copy) \
                    .then_inc(turned_taken, 1)
            for n in range(4):
                act.wait_ge(product, n + 1)
                to = kk if n < 2 else kq
                nc.scalar.activation(to[:, n % 2, :], mem.bank[4 + n][:, :], ACT.Copy).then_inc(product_taken, 1)
            for n in range(4):
                for e in range(2):
                    act.wait_ge(bounded, 2 * TT * n + TT * (e + 1))
                    nc.scalar.activation(decay[:, e, :], decay[:, e, :], ACT.Exp,
                                         scale=-1.0 if e == 0 else 1.0).then_inc(exped, 1)

        @block.tensor
        def _(pe):
            for s in range(2):
                pe.wait_ge(squared, s + 1)
                nc.tensor.matmul(mem.bank[s][:, :], CONST(mem.const, "pair_ones"), squares[:, s, :],
                                 start=True, stop=True).then_inc(summed, 1)
            pe.wait_ge(silued, 3)
            for t in range(TT):
                last = nc.tensor.transpose(mem.bank[2][:, t * P:(t + 1) * P], conv[:, 2, t * P:(t + 1) * P],
                                           CONST(mem.const, "ident"))
            last.then_inc(turned, 1)
            pe.wait_ge(normed, 2)
            for t in range(TT):
                last = nc.tensor.transpose(mem.bank[3][:, t * P:(t + 1) * P], b.k[:, t * P:(t + 1) * P],
                                           CONST(mem.const, "ident"))
            last.then_inc(turned, 1)
            for n in range(4):
                lanes = slice((n % 2) * HEAD, (n % 2 + 1) * HEAD)
                for t in range(TT):
                    right = (b.k if n < 2 else b.q)[lanes, t * P:(t + 1) * P]
                    last = nc.tensor.matmul(mem.bank[4 + n][:, t * P:(t + 1) * P], b.k[lanes, t * P:(t + 1) * P],
                                            right, start=True, stop=True)
                last.then_inc(product, 1)


def invert(nc, mem, neg, full, turned, upper):
    count = len(upper)
    with buffers(nc, joint=[P, count, SEQ]) as (joint,), phase(
            nc, "start", *[f"{w}{n}" for n in range(count) for w in ("through", "joined", "grown", "added")]) as (
            block, start, *sems):
        through, joined, grown, added = sems[0::4], sems[1::4], sems[2::4], sems[3::4]

        @block.vector
        def _(dve):
            ident = CONST(mem.const, "ident").unsqueeze(1).broadcast_to([P, TT, P])
            for n in range(count):
                for to in (full, turned):
                    nc.vector.tensor_copy(to[:, n, :].rearrange("p (t c) -> p t c", t=TT), ident) \
                        .then_inc(added[n], 1)
            for l in range(LEVELS):
                for n in range(count):
                    mask = mem.levels[:, upper[n], l, :].unsqueeze(1).broadcast_to([P, TT, P])
                    dve.wait_ge(through[n], l + 1)
                    if l >= 1:
                        dve.wait_ge(grown[n], 2 * l)
                    nc.vector.tensor_tensor(joint[:, n, :].rearrange("p (t c) -> p t c", t=TT),
                                            mem.bank[2 * n][:, :].rearrange("p (t c) -> p t c", t=TT), mask,
                                            ALU.mult).then_inc(joined[n], 1)
                for n in range(count):
                    last_level = l == LEVELS - 1
                    dve.wait_ge(grown[n], 2 * l + 2)
                    dve.wait_ge(added[n], 2 * l + 2)
                    if not last_level:
                        nc.vector.tensor_tensor(full[:, n, :], full[:, n, :], mem.bank[2 * n + 1][:, :], ALU.add) \
                            .then_inc(added[n], 1)
                    nc.vector.tensor_tensor(turned[:, n, :], turned[:, n, :], mem.bank[2 * n][:, :], ALU.add) \
                        .then_inc(added[n], 1)

        @block.tensor
        def _(pe):
            for l in range(LEVELS):
                for n in range(count):
                    pe.wait_ge(added[n], 2 * l + 2)
                    for t in range(TT):
                        c = slice(t * P, (t + 1) * P)
                        last = nc.tensor.matmul(mem.bank[2 * n][:, c], neg[:, n, c], turned[:, n, c],
                                                start=True, stop=True)
                    last.then_inc(through[n], 1)
                for n in range(count):
                    pe.wait_ge(joined[n], l + 1)
                    for t in range(TT):
                        c = slice(t * P, (t + 1) * P)
                        last = nc.tensor.matmul(mem.bank[2 * n + 1][:, c], joint[:, n, c], full[:, n, c],
                                                start=True, stop=True)
                    last.then_inc(grown[n], 1)
                    for t in range(TT):
                        c = slice(t * P, (t + 1) * P)
                        last = nc.tensor.matmul(mem.bank[2 * n][:, c], full[:, n, c], joint[:, n, c],
                                                start=True, stop=True)
                    last.then_inc(grown[n], 1)


def delta_scan(nc, mem, vec, u, rows, y, hp, b):
    first_tile = CONV_T + PAIRS1
    with buffers(nc, w=[P, 2, SEQ], qg=[P, 2, SEQ], last=[P, 2, TT], state=[P, 2, HEAD], fresh=[P, 2, 2, P],
                 o=[P, 2, SEQ], squares=[P, SEQ], scale=[P, SEQ], gate=[P, SEQ]) as (
            w, qg, last_decay, state, fresh, o, squares, scale, gate), phase(
            nc, "scaled", "solved", "solved_taken", "rows_exped", "queries", "passed0", "passed1", "fresh0", "fresh1",
            "out0", "out1", "grown0", "grown1", "state0", "state1", "out_taken0", "out_taken1", "summed_dirs",
            "squared", "summed", "rooted", "gate_ready", "dve_steps") as (
            block, scaled, solved, solved_taken, rows_exped, queries, passed0, passed1, fresh0, fresh1,
            out0, out1, grown0, grown1, state0, state1, out_taken0, out_taken1, summed_dirs,
            squared, summed, rooted, gate_ready, dve_steps):
        streams = [(d, par) for d in range(2) for par in range(2)]
        vb, kb, kd, u0 = b.vb, b.kb, b.kd, b.u0
        passed, fresh_ready, out_ready = (passed0, passed1), (fresh0, fresh1), (out0, out1)
        grown, state_ready, out_taken = (grown0, grown1), (state0, state1), (out_taken0, out_taken1)
        lanes = [slice(0, HEAD), slice(HEAD, 2 * HEAD)]
        chunk = [lambda s: s, lambda s: TT - 1 - s]

        @block.vector
        def _(dve):
            steps = Steps(dve, dve_steps)
            for n, (d, par) in enumerate(streams):
                for kind, to, rows_of in ((G_BETA, vb, b.v_rows), (G_BEXP, kb, b.k_rows), (G_KDEC, kd, b.k_rows)):
                    by = b.cols[:, kind * TT:(kind + 1) * TT, d, par:par + 1].broadcast_to([P, TT, HEAD])
                    steps.did(nc.vector.tensor_tensor(to[:, n, :, :], rows_of[:, :, lanes[par]], by, ALU.mult), scaled)
                steps.did(nc.vector.tensor_copy(last_decay[lanes[par], d, :],
                                                b.cols[lanes[par], G_LAST * TT:(G_LAST + 1) * TT, d, par]))
            for d in range(2):
                dve.wait_ge(rows_exped, 2 * d + 2)
                steps.did(nc.vector.tensor_tensor(qg[:, d, :], qg[:, d, :], b.q[:, :], ALU.mult), queries)
            steps.settle()
            for s in range(TT):
                for d in range(2):
                    t = chunk[d](s)
                    if s == 0:
                        dve.wait_ge(solved_taken, 2 * d + 2)
                    if s >= 2:
                        dve.wait_ge(out_ready[d], s - 1)
                    for par in range(2):
                        e = slice(par * HEAD, (par + 1) * HEAD)
                        if s == 0:
                            steps.did(nc.vector.tensor_copy(fresh[:, d, s % 2, e], u0[:, d, t, e]), fresh_ready[d])
                        else:
                            dve.wait_ge(passed[d], 2 * s - 1 + par)
                            steps.did(nc.vector.tensor_tensor(fresh[:, d, s % 2, e], u0[:, d, t, e],
                                                              mem.bank[d + 2 * par][:, 0:HEAD], ALU.subtract),
                                      fresh_ready[d])
                for d in range(2):
                    if s == TT - 1:
                        break
                    t = chunk[d](s)
                    dve.wait_ge(grown[d], s + 1)
                    if s == 0:
                        steps.did(nc.vector.tensor_copy(state[:, d, :], mem.bank[4 + d][:, 0:HEAD]), state_ready[d])
                    else:
                        dve.wait_ge(state_ready[d], s)
                        dve.wait_ge(out_ready[d], s + 1)
                        steps.did(nc.vector.scalar_tensor_tensor(
                            out=state[:, d, :], in0=state[:, d, :], scalar=last_decay[:, d, t:t + 1],
                            in1=mem.bank[4 + d][:, 0:HEAD], op0=ALU.mult, op1=ALU.add), state_ready[d])
            for d in range(2):
                dve.wait_ge(out_taken[d], TT)
            steps.did(nc.vector.tensor_tensor(o[:, 0, :], o[:, 0, :], o[:, 1, :], ALU.add), summed_dirs)
            dve.wait_ge(rooted, 1)
            steps.did(nc.vector.reciprocal(scale[:, :], scale[:, :]))
            steps.settle()
            steps.did(nc.vector.scalar_tensor_tensor(out=scale[:, :], in0=o[:, 0, :], scalar=VEC1(vec, "delta_norm"),
                                                     in1=scale[:, :], op0=ALU.mult, op1=ALU.mult))
            steps.settle()
            dve.wait_ge(gate_ready, 1)
            steps.did(nc.vector.tensor_tensor(tile_at(y, hp + first_tile), scale[:, :], gate[:, :], ALU.mult))
            steps.settle()

        @block.tensor
        def _(pe):
            for d in range(2):
                pe.wait_ge(scaled, 6 * d + 6)
                for par in range(2):
                    n = 2 * d + par
                    for t in range(TT):
                        c = slice(t * P, (t + 1) * P)
                        last = nc.tensor.matmul(mem.bank[d][:, t * P + par * HEAD:t * P + (par + 1) * HEAD],
                                                b.turned[:, n, c], vb[:, n, t, :], start=True, stop=True)
                last.then_inc(solved, 1)
                for par in range(2):
                    n = 2 * d + par
                    for t in range(TT):
                        c = slice(t * P, (t + 1) * P)
                        last = nc.tensor.matmul(mem.bank[2 + d][lanes[par], c], kb[:, n, t, :], b.turned[:, n, c],
                                                start=True, stop=True)
                last.then_inc(solved, 1)
            pe.wait_ge(solved_taken, 4)
            pe.wait_ge(queries, 2)
            for s in range(TT):
                for d in range(2):
                    if s == 0:
                        continue
                    t = chunk[d](s)
                    pe.wait_ge(state_ready[d], s)
                    pe.wait_ge(fresh_ready[d], 2 * s)
                    for par in range(2):
                        nc.tensor.matmul(mem.bank[d + 2 * par][:, 0:HEAD], w[lanes[par], d, t * P:(t + 1) * P],
                                         state[lanes[par], d, :], start=True, stop=True).then_inc(passed[d], 1)
                for d in range(2):
                    t = chunk[d](s)
                    c = slice(t * P, (t + 1) * P)
                    pe.wait_ge(fresh_ready[d], 2 * s + 2)
                    if s >= 1:
                        pe.wait_ge(state_ready[d], s)
                    for par in range(2):
                        n = 2 * d + par
                        last = nc.tensor.matmul(mem.bank[4 + d][lanes[par], 0:HEAD], kd[:, n, t, :],
                                                fresh[:, d, s % 2, par * HEAD:(par + 1) * HEAD], start=True, stop=True)
                    last.then_inc(grown[d], 1)
                    if s >= 1:
                        pe.wait_ge(out_taken[d], s)
                    for par in range(2):
                        n = 2 * d + par
                        to = mem.bank[6 + d][lanes[par], 0:P]
                        if s >= 1:
                            nc.tensor.matmul(to, state[lanes[par], d, :], qg[lanes[par], d, c], start=True, stop=False)
                        last = nc.tensor.matmul(to, fresh[:, d, s % 2, par * HEAD:(par + 1) * HEAD], b.seen[:, n, c],
                                                start=(s == 0), stop=True)
                    last.then_inc(out_ready[d], 1)
            pe.wait_ge(squared, 1)
            nc.tensor.matmul(mem.bank[0][:, :], CONST(mem.const, "pair_ones"), squares[:, :], start=True,
                             stop=True).then_inc(summed, 1)

        @block.scalar
        def _(act):
            for d, par in streams:
                row = rows[lanes[par], bass.ds(hp * 2 + d * DELTA_HEADS + par, 1), :].rearrange("p a n -> p (a n)")
                nc.scalar.activation(qg[lanes[par], d, :], row, ACT.Exp).then_inc(rows_exped, 1)
            for d in range(2):
                act.wait_ge(solved, 2 * d + 2)
                nc.scalar.activation(u0[:, d, :, :].rearrange("p t n -> p (t n)"), mem.bank[d][:, :], ACT.Copy) \
                    .then_inc(solved_taken, 1)
                nc.scalar.activation(w[:, d, :], mem.bank[2 + d][:, :], ACT.Copy).then_inc(solved_taken, 1)
            for s in range(TT):
                for d in range(2):
                    t = chunk[d](s)
                    act.wait_ge(out_ready[d], s + 1)
                    nc.scalar.activation(o[:, d, t * P:(t + 1) * P], mem.bank[6 + d][:, 0:P], ACT.Copy) \
                        .then_inc(out_taken[d], 1)
            act.wait_ge(summed_dirs, 1)
            nc.scalar.activation(squares[:, :], o[:, 0, :], ACT.Square).then_inc(squared, 1)
            nc.scalar.activation(gate[:, :], tile_at(u, hp + U_GZ), ACT.Silu).then_inc(gate_ready, 1)
            act.wait_ge(summed, 1)
            nc.scalar.activation(scale[:, :], mem.bank[0][:, :], ACT.Sqrt, bias=mem.eps[:, 0:1],
                                 scale=1.0 / HEAD).then_inc(rooted, 1)


class PairBuffers:

    def __init__(self, mem, q, k, k_rows, v_rows, cols):
        self.q, self.k, self.k_rows, self.v_rows, self.cols = q, k, k_rows, v_rows, cols
        self.full, self.turned = mem.h[:, 0:4, :], mem.h[:, 4:8, :]
        ring = mem.ring[:, :, :].rearrange("p s n -> p (s n)")
        size = 4 * SEQ
        self.neg = ring[:, 0:size].rearrange("p (n s) -> p n s", n=4)
        self.seen = ring[:, size:2 * size].rearrange("p (n s) -> p n s", n=4)
        rows = [ring[:, 2 * size + i * 2 * SEQ:2 * size + (i + 1) * 2 * SEQ] for i in range(4)]
        self.vb, self.kb, self.kd = [r.rearrange("p (n t e) -> p n t e", n=4, t=TT) for r in rows[:3]]
        self.u0 = rows[3].rearrange("p (d t e) -> p d t e", d=2, t=TT)


def delta_net(nc, mem, vec, gates, u, tm, y):
    with buffers(nc, cols=[P, KINDS, TT, GH], rows=[P, GH, SEQ]) as (cols, rows):
        delta_gates(nc, mem, gates, tm, cols, rows)
        with nc.Fori(0, PAIRS1) as hp, buffers(
                nc, q=[P, SEQ], k=[P, SEQ], k_rows=[P, TT, P], v_rows=[P, TT, P],
                pair_cols=[P, KINDS * TT, 2, 2]) as parts:
            b = PairBuffers(mem, *parts)
            delta_prepare(nc, mem, vec, u, cols, rows, hp, b)
            invert(nc, mem, b.neg, b.full, b.turned, [0, 0, 1, 1])
            delta_scan(nc, mem, vec, u, rows, y, hp, b)


def spatial_gate(nc, mem, a, u, pv, y):
    groups = [slice(g * P, (g + 1) * P) for g in range(A_GROUPS)]
    n_stats = TT * A_GROUPS
    with buffers(nc, mix=[P, A_GROUPS, P], bias=[P, A_GROUPS, P], ln=[P, 2, A_WIDTH], stats=[P, n_stats, 6],
                 moments=[P, n_stats, 2], root=[P, n_stats], shift=[P, n_stats]) as (
            mix, bias, ln, stats, moments, root, shift), phase(
            nc, "loaded", "gelued", "u_ready", "spread", "rooted", "normed", "mixed", "dve_steps") as (
            block, loaded, gelued, u_ready, spread, rooted, normed, mixed, dve_steps):
        @block.sync
        def _(sp):
            sp.dma_start(mix[:, :, :], a["sgu_w"]).then_inc(loaded, 16)
            sp.dma_start(bias[:, :, :], a["sgu_b"].partition_broadcast(P)).then_inc(loaded, 16)
            sp.dma_start(ln[:, :, :], a["sgu_ln"].partition_broadcast(P)).then_inc(loaded, 16)

        @block.scalar
        def _(act):
            for t in range(TT):
                nc.scalar.activation(pv[:, t, :], pv[:, t, :], ACT.Gelu_apprx_tanh).then_inc(gelued, 1)
            for g in range(A_GROUPS):
                nc.scalar.activation(u[:, E_U + g, :], u[:, E_U + g, :], ACT.Gelu_apprx_tanh).then_inc(u_ready, 1)
            act.wait_ge(spread, 1)
            nc.scalar.activation(root[:, :], moments[:, :, 1], ACT.Sqrt, bias=mem.eps[:, 1:2]).then_inc(rooted, 1)

        @block.vector
        def _(dve):
            steps = Steps(dve, dve_steps)
            dve.wait_ge(loaded, 48)
            steps.did(nc.vector.tensor_tensor(
                mix[:, :, :], mix[:, :, :],
                CONST(mem.const, "upper_in").unsqueeze(1).broadcast_to([P, A_GROUPS, P]), ALU.mult))
            for t in range(TT):
                dve.wait_ge(gelued, t + 1)
                for g in range(A_GROUPS):
                    steps.did(nc.vector.bn_stats(stats[:, t * A_GROUPS + g, :], pv[:, t, groups[g]]))
            steps.settle()
            for n in range(n_stats):
                steps.did(nc.vector.bn_aggr(moments[:, n, :], stats[:, n, :]), spread if n == n_stats - 1 else None)
            dve.wait_ge(rooted, 1)
            steps.did(nc.vector.reciprocal(root[:, :], root[:, :]))
            steps.settle()
            steps.did(nc.vector.scalar_tensor_tensor(out=shift[:, :], in0=moments[:, :, 0], scalar=-1.0,
                                                     in1=root[:, :], op0=ALU.mult, op1=ALU.mult))
            steps.settle()
            for t in range(TT):
                for g in range(A_GROUPS):
                    n = t * A_GROUPS + g
                    steps.did(nc.vector.tensor_scalar(pv[:, t, groups[g]], pv[:, t, groups[g]], root[:, n:n + 1],
                                                      shift[:, n:n + 1], ALU.mult, ALU.add))
            steps.settle()
            for i, op in ((0, ALU.mult), (1, ALU.add)):
                steps.did(nc.vector.tensor_tensor(pv[:, :, :], pv[:, :, :],
                                                  ln[:, i, :].unsqueeze(1).broadcast_to([P, TT, A_WIDTH]), op),
                          normed if i else None)
                steps.settle()
            dve.wait_ge(u_ready, A_GROUPS)
            for g in range(A_GROUPS):
                dve.wait_ge(mixed, g + 1)
                steps.did(nc.vector.tensor_tensor(
                    y[:, g, :].rearrange("p (c t) -> p c t", c=TT),
                    mem.bank[g][:, :].rearrange("p (c t) -> p c t", c=TT),
                    bias[:, g, :].unsqueeze(1).broadcast_to([P, TT, P]), ALU.add))
            steps.settle()
            for g in range(A_GROUPS):
                steps.did(nc.vector.tensor_tensor(y[:, g, :], y[:, g, :], u[:, E_U + g, :], ALU.mult))
            steps.settle()

        @block.tensor
        def _(pe):
            pe.wait_ge(normed, 1)
            for g in range(A_GROUPS):
                for c in range(TT):
                    last = nc.tensor.matmul(mem.bank[g][:, c * P:(c + 1) * P], pv[:, c, groups[g]], mix[:, g, :],
                                            start=True, stop=True)
                last.then_inc(mixed, 1)


def token_shift(nc, mem, vec, u):
    n_tiles, batch = UTE - E_R, 7
    with phase(nc, "dve_steps") as (block, dve_steps):
        @block.vector
        def _(dve):
            steps = Steps(dve, dve_steps)
            for first in range(0, n_tiles, batch):
                part = u[:, E_R + first:E_R + first + batch, :]
                change = mem.h[:, 0:batch, :]
                steps.did(nc.vector.tensor_tensor(change[:, :, 1:SEQ], part[:, :, 0:SEQ - 1], part[:, :, 1:SEQ],
                                                  ALU.subtract))
                steps.did(nc.vector.tensor_scalar(change[:, :, 0:1], part[:, :, 0:1], -1.0, None, ALU.mult))
                steps.settle()
                for i in range(batch):
                    steps.did(nc.vector.scalar_tensor_tensor(
                        out=part[:, i, :], in0=change[:, i, :], scalar=VECE(vec, "mu", first + i), in1=part[:, i, :],
                        op0=ALU.mult, op1=ALU.add))
                steps.settle()


def rwkv_gates(nc, mem, a, vec, u, decay, rate, gate):
    with buffers(nc, wa2=[P, B_WIDTH], g2=[P, B_WIDTH]) as (wa2, g2), phase(
            nc, "loaded", "inner", "product", "taken", "dve_steps") as (block, loaded, inner, product, taken,
                                                                        dve_steps):
        @block.sync
        def _(sp):
            sp.dma_start(wa2[:, :], a["wa2"]).then_inc(loaded, 16)
            sp.dma_start(g2[:, :], a["g2"]).then_inc(loaded, 16)

        @block.scalar
        def _(act):
            nc.scalar.activation(u[0:LORA, E_WA, :], u[0:LORA, E_WA, :], ACT.Tanh).then_inc(inner, 1)
            nc.scalar.activation(u[:, E_G, :], u[:, E_G, :], ACT.Sigmoid).then_inc(inner, 1)
            for j in range(RW_PAIRS):
                act.wait_ge(product, 3 * j + 3)
                b = 3 * (j % 2)
                nc.scalar.activation(decay[:, j, :], mem.bank[b][:, :], ACT.Sigmoid, bias=VECE(vec, "w0", j)) \
                    .then_inc(taken, 1)
                nc.scalar.activation(rate[:, j, :], mem.bank[b + 1][:, :], ACT.Sigmoid, bias=VECE(vec, "a0", j)) \
                    .then_inc(taken, 1)
                nc.scalar.activation(gate[:, j, :], mem.bank[b + 2][:, :], ACT.Copy).then_inc(taken, 1)

        @block.tensor
        def _(pe):
            pe.wait_ge(loaded, 32)
            pe.wait_ge(inner, 2)
            for j in range(RW_PAIRS):
                if j >= 2:
                    pe.wait_ge(taken, 3 * (j - 1))
                b, c = 3 * (j % 2), slice(j * P, (j + 1) * P)
                nc.tensor.matmul(mem.bank[b][:, :], wa2[0:LORA, c], u[0:LORA, E_WA, :], start=True, stop=True) \
                    .then_inc(product, 1)
                nc.tensor.matmul(mem.bank[b + 1][:, :], wa2[LORA:P, c], u[LORA:P, E_WA, :], start=True, stop=True) \
                    .then_inc(product, 1)
                nc.tensor.matmul(mem.bank[b + 2][:, :], g2[:, c], u[:, E_G, :], start=True, stop=True) \
                    .then_inc(product, 1)

        @block.vector
        def _(dve):
            dve.wait_ge(taken, 3 * RW_PAIRS)
            nc.vector.tensor_scalar(decay[:, :, :], decay[:, :, :], -math.exp(-0.5), None, ALU.mult)


class TimeMix:

    def __init__(self, mem, v, gate, bonus, factor, par):
        self.v, self.gate, self.bonus, self.factor, self.par = v, gate, bonus, factor, par
        ring = mem.ring[:, :, :].rearrange("p s n -> p (s n)")
        parts = [ring[:, i * SEQ:(i + 1) * SEQ] for i in range(SLOTS * SLOT // SEQ)]
        self.rho, self.alpha, self.beta, self.kappa = parts[0:4]
        self.alpha_rows, self.beta_rows, self.kappa_rows, self.v_rows = [
            x.rearrange("p (t n) -> p t n", t=TT) for x in parts[4:8]]
        pairs = [ring[:, (8 + 2 * i) * SEQ:(10 + 2 * i) * SEQ].rearrange("p (n s) -> p n s", n=2) for i in range(4)]
        self.neg, self.key_past, self.key_seen, self.rate_seen = pairs
        self.full, self.turned = mem.h[:, 0:2, :], mem.h[:, 2:4, :]


VEC_J = ["k_k", "k_a", "r_k", "gn_g", "gn_b"]


def rwkv_prepare(nc, mem, vec, u, decay, rate, gate, j, b):
    mid = P // 2 - 1
    with buffers(nc, r=[P, SEQ], k=[P, SEQ], kk=[P, SEQ], bk=[P, SEQ], run=[P, SEQ], about=[P, SEQ],
                 up=[P, SEQ], down=[P, SEQ], before=[P, SEQ], squares=[P, SEQ], scale=[P, SEQ]) as (
            r, k, kk, bk, run, about, up, down, before, squares, scale), phase(
            nc, "kk_ready", "squared", "summed", "rooted", "about_ready", "before_ready", "ups", "factor_ready",
            "bonus_ready", "bonus_summed", "ready", "turned", "rows_taken", "product", "dve_steps") as (
            block, kk_ready, squared, summed, rooted, about_ready, before_ready, ups, factor_ready,
            bonus_ready, bonus_summed, ready, turned, rows_taken, product, dve_steps):
        by_chunk = lambda x: x.rearrange("p (c t) -> p c t", c=TT)
        lanes = [slice(0, HEAD), slice(HEAD, 2 * HEAD)]
        sets = [("neg", "alpha", "beta"), ("key_past", "kappa", "alpha"), ("key_seen", "kappa", "rho"),
                ("rate_seen", "beta", "rho")]
        masks = ["neg_lower_strict", "upper_strict", "upper_in", "upper_in"]
        left = [b.alpha, b.kappa, b.kappa, b.beta]
        right = [b.beta, b.alpha, b.rho, b.rho]
        target = [b.neg, b.key_past, b.key_seen, b.rate_seen]

        @block.vector
        def _(dve):
            steps = Steps(dve, dve_steps)
            for i, name in enumerate(VEC_J):
                at = VECE.at[name][0]
                steps.did(nc.vector.tensor_copy(b.par[:, i:i + 1], vec[:, bass.ds(j + at, 1)]))
            steps.did(nc.vector.tensor_copy(r[:, :], tile_at(u, j + E_R)))
            steps.did(nc.vector.tensor_copy(b.v[:, :], tile_at(u, j + E_V)))
            steps.did(nc.vector.tensor_copy(b.gate[:, :], tile_at(gate, j)))
            steps.did(nc.vector.tensor_copy(before[:, :], tile_at(decay, j)))
            steps.settle()
            steps.did(nc.vector.tensor_scalar(kk[:, :], tile_at(u, j + E_K), b.par[:, 0:1], None, ALU.mult), kk_ready)
            steps.did(nc.vector.tensor_scalar(k[:, :], tile_at(rate, j), -1.0, b.par[:, 1:2], ALU.add, ALU.mult))
            steps.did(nc.vector.tensor_tensor_scan(run[:, :], CONST(mem.const, "not_first"), before[:, :], 0.0,
                                                   ALU.mult, ALU.add))
            steps.settle()
            steps.did(nc.vector.scalar_tensor_tensor(out=k[:, :], in0=k[:, :], scalar=1.0, in1=tile_at(u, j + E_K),
                                                     op0=ALU.add, op1=ALU.mult))
            middle = by_chunk(run[:, :])[:, :, mid:mid + 1].broadcast_to([P, TT, P])
            steps.did(nc.vector.tensor_tensor(by_chunk(about[:, :]), by_chunk(run[:, :]), middle, ALU.subtract),
                      about_ready)
            steps.settle()
            steps.did(nc.vector.tensor_tensor(before[:, :], about[:, :], before[:, :], ALU.subtract), before_ready)
            ends = by_chunk(about[:, :])[:, 0:TT - 1, P - 1]
            steps.did(nc.vector.tensor_tensor(b.factor[:, 0:TT - 1], ends, by_chunk(run[:, :])[:, 1:TT, mid], ALU.add),
                      factor_ready)
            steps.did(nc.vector.scalar_tensor_tensor(out=bk[:, :], in0=r[:, :], scalar=b.par[:, 2:3], in1=k[:, :],
                                                     op0=ALU.mult, op1=ALU.mult), bonus_ready)
            dve.wait_ge(rooted, 1)
            steps.did(nc.vector.tensor_scalar(scale[:, :], scale[:, :], 1e-12, None, ALU.max))
            steps.settle()
            steps.did(nc.vector.reciprocal(scale[:, :], scale[:, :]))
            steps.settle()
            steps.did(nc.vector.tensor_tensor(kk[:, :], kk[:, :], scale[:, :], ALU.mult))
            dve.wait_ge(ups, 3)
            steps.did(nc.vector.tensor_tensor(b.rho, r[:, :], up[:, :], ALU.mult), ready)
            steps.did(nc.vector.tensor_tensor(b.kappa, k[:, :], down[:, :], ALU.mult), ready)
            steps.settle()
            steps.did(nc.vector.tensor_tensor(b.alpha, kk[:, :], before[:, :], ALU.mult), ready)
            steps.did(nc.vector.tensor_tensor(kk[:, :], kk[:, :], tile_at(rate, j), ALU.mult))
            steps.settle()
            steps.did(nc.vector.tensor_tensor(b.beta, kk[:, :], down[:, :], ALU.mult), ready)
            dve.wait_ge(bonus_summed, 1)
            steps.did(nc.vector.tensor_tensor(b.bonus[:, :], mem.bank[0][:, :], b.v[:, :], ALU.mult), bonus_ready)
            for i in range(4):
                for par in range(2):
                    dve.wait_ge(product, 2 * i + par + 1)
                    mask = CONST(mem.const, masks[i]).unsqueeze(1).broadcast_to([P, TT, P])
                    steps.did(nc.vector.tensor_tensor(by_chunk(target[i][:, par, :]),
                                                      by_chunk(mem.bank[2 * i + par][:, :]), mask, ALU.mult))
            steps.settle()

        @block.scalar
        def _(act):
            act.wait_ge(kk_ready, 1)
            nc.scalar.activation(squares[:, :], kk[:, :], ACT.Square).then_inc(squared, 1)
            act.wait_ge(summed, 1)
            nc.scalar.activation(scale[:, :], mem.bank[1][:, :], ACT.Sqrt).then_inc(rooted, 1)
            act.wait_ge(about_ready, 1)
            nc.scalar.activation(up[:, :], about[:, :], ACT.Exp).then_inc(ups, 1)
            nc.scalar.activation(down[:, :], about[:, :], ACT.Exp, scale=-1.0).then_inc(ups, 1)
            act.wait_ge(before_ready, 1)
            nc.scalar.activation(before[:, :], before[:, :], ACT.Exp).then_inc(ups, 1)
            act.wait_ge(factor_ready, 1)
            nc.scalar.activation(b.factor[:, 0:TT - 1], b.factor[:, 0:TT - 1], ACT.Exp)
            for i, to in enumerate([b.v_rows, b.kappa_rows, b.alpha_rows, b.beta_rows]):
                act.wait_ge(turned, i + 1)
                nc.scalar.activation(to.rearrange("p t n -> p (t n)"), mem.bank[2 + i][:, :], ACT.Copy) \
                    .then_inc(rows_taken, 1)

        @block.tensor
        def _(pe):
            pe.wait_ge(squared, 1)
            nc.tensor.matmul(mem.bank[1][:, :], CONST(mem.const, "pair_ones"), squares[:, :], start=True,
                             stop=True).then_inc(summed, 1)
            pe.wait_ge(bonus_ready, 1)
            nc.tensor.matmul(mem.bank[0][:, :], CONST(mem.const, "pair_ones"), bk[:, :], start=True,
                             stop=True).then_inc(bonus_summed, 1)
            for i, (of, need) in enumerate([(b.v[:, :], 0), (b.kappa, 2), (b.alpha, 3), (b.beta, 4)]):
                if need:
                    pe.wait_ge(ready, need)
                for t in range(TT):
                    last = nc.tensor.transpose(mem.bank[2 + i][:, t * P:(t + 1) * P], of[:, t * P:(t + 1) * P],
                                               CONST(mem.const, "ident"))
                last.then_inc(turned, 1)
            pe.wait_ge(rows_taken, 4)
            pe.wait_ge(bonus_ready, 2)
            for i in range(4):
                for par in range(2):
                    for t in range(TT):
                        c = slice(t * P, (t + 1) * P)
                        last = nc.tensor.matmul(mem.bank[2 * i + par][:, c], left[i][lanes[par], c],
                                                right[i][lanes[par], c], start=True, stop=True)
                    last.then_inc(product, 1)


def rwkv_scan(nc, mem, y, j, b):
    first_tile = A_GROUPS
    with buffers(nc, past=[P, 2, TT, HEAD], u0=[P, 2, TT, HEAD], w=[P, SEQ], state=[P, HEAD], fresh=[P, 2, P],
                 out=[P, SEQ], squares=[P, SEQ], scale=[P, SEQ]) as (
            past, u0, w, state, fresh, out, squares, scale), phase(
            nc, "past_ready", "past_taken", "solved", "solved_taken", "passed", "fresh_ready", "out_ready", "grown",
            "added", "state_ready", "out_taken", "mean_ready", "centred", "squared", "summed", "rooted",
            "dve_steps") as (
            block, past_ready, past_taken, solved, solved_taken, passed, fresh_ready, out_ready, grown,
            added, state_ready, out_taken, mean_ready, centred, squared, summed, rooted, dve_steps):
        lanes = [slice(0, HEAD), slice(HEAD, 2 * HEAD)]

        @block.tensor
        def _(pe):
            for par in range(2):
                for t in range(TT):
                    c = slice(t * P, (t + 1) * P)
                    last = nc.tensor.matmul(mem.bank[par][:, t * HEAD:(t + 1) * HEAD], b.key_past[:, par, c],
                                            b.v_rows[:, t, lanes[par]], start=True, stop=True)
                last.then_inc(past_ready, 1)
            for par in range(2):
                for t in range(TT):
                    c = slice(t * P, (t + 1) * P)
                    last = nc.tensor.matmul(mem.bank[4][lanes[par], c], b.alpha_rows[:, t, lanes[par]],
                                            b.turned[:, par, c], start=True, stop=True)
                last.then_inc(solved, 1)
            for par in range(2):
                pe.wait_ge(past_taken, par + 1)
                for t in range(TT):
                    last = nc.tensor.matmul(mem.bank[2 + par][:, t * HEAD:(t + 1) * HEAD],
                                            b.turned[:, par, t * P:(t + 1) * P], past[:, par, t, :],
                                            start=True, stop=True)
                last.then_inc(solved, 1)
            pe.wait_ge(solved_taken, 3)
            for s in range(TT):
                c = slice(s * P, (s + 1) * P)
                if s >= 1:
                    pe.wait_ge(state_ready, s)
                    for par in range(2):
                        nc.tensor.matmul(mem.bank[par][:, 0:HEAD], w[lanes[par], c], state[lanes[par], :],
                                         start=True, stop=True).then_inc(passed, 1)
                if s < TT - 1:
                    for par in range(2):
                        nc.tensor.matmul(mem.bank[5][lanes[par], 0:HEAD], b.kappa_rows[:, s, lanes[par]],
                                         b.v_rows[:, s, lanes[par]], start=True, stop=False)
                        pe.wait_ge(fresh_ready, 2 * s + 1 + par)
                        last = nc.tensor.matmul(mem.bank[5][lanes[par], 0:HEAD], b.beta_rows[:, s, lanes[par]],
                                                fresh[:, s % 2, lanes[par]], start=False, stop=True)
                    last.then_inc(grown, 1)
                pe.wait_ge(fresh_ready, 2 * s + 2)
                if s >= 2:
                    pe.wait_ge(out_taken, s - 1)
                for par in range(2):
                    to = mem.bank[6 + s % 2][lanes[par], 0:P]
                    if s >= 1:
                        nc.tensor.matmul(to, state[lanes[par], :], b.rho[lanes[par], c], start=True, stop=False)
                    nc.tensor.matmul(to, b.v_rows[:, s, lanes[par]], b.key_seen[:, par, c], start=(s == 0), stop=False)
                    last = nc.tensor.matmul(to, fresh[:, s % 2, lanes[par]], b.rate_seen[:, par, c],
                                            start=False, stop=True)
                last.then_inc(out_ready, 1)
            pe.wait_ge(out_taken, TT)
            nc.tensor.matmul(mem.bank[0][:, :], CONST(mem.const, "pair_ones"), out[:, :], start=True,
                             stop=True).then_inc(mean_ready, 1)
            pe.wait_ge(squared, 1)
            nc.tensor.matmul(mem.bank[1][:, :], CONST(mem.const, "pair_ones"), squares[:, :], start=True,
                             stop=True).then_inc(summed, 1)

        @block.scalar
        def _(act):
            for par in range(2):
                act.wait_ge(past_ready, par + 1)
                nc.scalar.activation(past[:, par, :, :].rearrange("p t e -> p (t e)"),
                                     mem.bank[par][:, 0:TT * HEAD], ACT.Copy).then_inc(past_taken, 1)
            act.wait_ge(solved, 2)
            nc.scalar.activation(w[:, :], mem.bank[4][:, :], ACT.Copy).then_inc(solved_taken, 1)
            for par in range(2):
                act.wait_ge(solved, 3 + par)
                nc.scalar.activation(u0[:, par, :, :].rearrange("p t e -> p (t e)"),
                                     mem.bank[2 + par][:, 0:TT * HEAD], ACT.Copy).then_inc(solved_taken, 1)
            for s in range(TT):
                act.wait_ge(out_ready, s + 1)
                nc.scalar.activation(out[:, s * P:(s + 1) * P], mem.bank[6 + s % 2][:, 0:P], ACT.Copy) \
                    .then_inc(out_taken, 1)
            act.wait_ge(centred, 1)
            nc.scalar.activation(squares[:, :], out[:, :], ACT.Square).then_inc(squared, 1)
            act.wait_ge(summed, 1)
            nc.scalar.activation(scale[:, :], mem.bank[1][:, :], ACT.Sqrt, bias=mem.eps[:, 2:3],
                                 scale=1.0 / HEAD).then_inc(rooted, 1)

        @block.vector
        def _(dve):
            steps = Steps(dve, dve_steps)
            dve.wait_ge(solved_taken, 3)
            for s in range(TT):
                if s >= 2:
                    dve.wait_ge(out_ready, s - 1)
                for par in range(2):
                    if s == 0:
                        steps.did(nc.vector.tensor_scalar(fresh[:, 0, lanes[par]], u0[:, par, 0, :], -1.0, None,
                                                          ALU.mult), fresh_ready)
                    else:
                        dve.wait_ge(passed, 2 * s - 1 + par)
                        steps.did(nc.vector.scalar_tensor_tensor(
                            out=fresh[:, s % 2, lanes[par]], in0=mem.bank[par][:, 0:HEAD], scalar=-1.0,
                            in1=u0[:, par, s, :], op0=ALU.mult, op1=ALU.subtract), fresh_ready)
                if s == TT - 1:
                    break
                dve.wait_ge(grown, s + 1)
                if s == 0:
                    steps.did(nc.vector.tensor_scalar(state[:, :], mem.bank[5][:, 0:HEAD], b.factor[:, s:s + 1], None,
                                                      ALU.mult), state_ready)
                else:
                    dve.wait_ge(out_ready, s + 1)
                    steps.settle()
                    steps.did(nc.vector.tensor_tensor(state[:, :], state[:, :], mem.bank[5][:, 0:HEAD], ALU.add))
                    steps.settle()
                    steps.did(nc.vector.tensor_scalar(state[:, :], state[:, :], b.factor[:, s:s + 1], None, ALU.mult),
                              state_ready)
            dve.wait_ge(mean_ready, 1)
            steps.did(nc.vector.scalar_tensor_tensor(out=out[:, :], in0=mem.bank[0][:, :], scalar=-1.0 / HEAD,
                                                     in1=out[:, :], op0=ALU.mult, op1=ALU.add), centred)
            dve.wait_ge(rooted, 1)
            steps.did(nc.vector.reciprocal(scale[:, :], scale[:, :]))
            steps.settle()
            steps.did(nc.vector.scalar_tensor_tensor(out=out[:, :], in0=out[:, :], scalar=b.par[:, 3:4],
                                                     in1=scale[:, :], op0=ALU.mult, op1=ALU.mult))
            steps.settle()
            steps.did(nc.vector.scalar_tensor_tensor(out=out[:, :], in0=out[:, :], scalar=b.par[:, 4:5],
                                                     in1=b.bonus[:, :], op0=ALU.add, op1=ALU.add))
            steps.settle()
            steps.did(nc.vector.tensor_tensor(tile_at(y, j + first_tile), out[:, :], b.gate[:, :], ALU.mult))
            steps.settle()


def time_mix(nc, mem, a, vec, u, y):
    token_shift(nc, mem, vec, u)
    with buffers(nc, decay=[P, RW_PAIRS, SEQ], rate=[P, RW_PAIRS, SEQ], gate=[P, RW_PAIRS, SEQ]) as (
            decay, rate, gate):
        rwkv_gates(nc, mem, a, vec, u, decay, rate, gate)
        with nc.Fori(0, RW_PAIRS) as j, buffers(nc, v=[P, SEQ], pair_gate=[P, SEQ], bonus=[P, SEQ], factor=[P, TT],
                                                par=[P, len(VEC_J)]) as parts:
            b = TimeMix(mem, *parts)
            rwkv_prepare(nc, mem, vec, u, decay, rate, gate, j, b)
            invert(nc, mem, b.neg, b.full, b.turned, [0, 0])
            rwkv_scan(nc, mem, y, j, b)


def gated_tile(nc, hidden):
    def evacuate(bank, tile, silu):
        return nc.vector.tensor_tensor(tile_at(hidden, tile), silu, bank[:, :], ALU.mult)
    return evacuate


def second_even(nc, mem, a):
    with buffers(nc, vec=[P, VECE.size]) as (vec,):
        load(nc, (vec[:, :], a["vece"]))
        with buffers(nc, y=[P, KD, SEQ], u=[P, UTE, SEQ]) as (y, u):
            rms_norm(nc, mem, mem.x, lambda k: VECE(vec, "norm_mix", k), mem.h)
            with buffers(nc, pv=[P, TT, A_WIDTH]) as (pv,):
                linear(nc, mem, unit_of(a["w_ine"]), UTE // 2, 2, KD, mem.h, copy_out(nc, u))
                token_major(nc, mem, a["w_tme"], A_WIDTH, mem.h, pv)
                spatial_gate(nc, mem, a, u, pv, y)
            time_mix(nc, mem, a, vec, u, y)
            if mem.stop == "even":
                dump(nc, mem, a, y, 0, 8)
            linear(nc, mem, unit_of(a["w_oute"]), KD // 2, 2, KD, y, add_out(nc, mem.x), on_vector=True)
        rms_norm(nc, mem, mem.x, lambda k: VECE(vec, "norm_ffn", k), mem.h)
        with buffers(nc, hidden=[P, FFN_T, SEQ], gated=[P, SLOTS, SEQ]) as (hidden, gated):
            linear(nc, mem, unit_of(a["w_ffe"]), FFN_T, 2, KD, mem.h, gated_tile(nc, hidden), gated=gated)
            linear(nc, mem, unit_of(a["w_downe"]), KD, 1, FFN_T, hidden, add_out(nc, mem.x), on_vector=True)


def interleaved(gate, up):
    k, m = gate.shape
    both = np.stack([gate.reshape(k, m // P, P), up.reshape(k, m // P, P)], axis=2)
    return both.reshape(k, 2 * m)


def lay_out_even(i, a):
    w = i["e_w_in_2"][0]
    a["w_ine"] = weight_units(np.concatenate([w[:, :A_WIDTH], w[:, 2 * A_WIDTH:]], axis=1), 2)
    a["w_tme"] = moving(w[:, A_WIDTH:2 * A_WIDTH])
    a["w_oute"] = weight_units(i["e_w_out_2"][0], 2)
    a["w_ffe"] = weight_units(interleaved(i["ffn_w_gate_2"][0], i["ffn_w_up_2"][0]), 2)
    a["w_downe"] = weight_units(i["ffn_w_down_2"][0], 1)
    a["sgu_w"] = i["sgu_w_2"][0].transpose(2, 0, 1)
    a["sgu_b"] = i["sgu_b_2"][0]
    a["sgu_ln"] = np.stack([i["sgu_ln_g_2"][0], i["sgu_ln_b_2"][0]])
    a["wa2"] = np.concatenate([i["rwkv_w2_2"][0], i["rwkv_a2_2"][0]])
    a["g2"] = i["rwkv_g2_2"][0]
    vec = np.zeros((P, VECE.size), np.float32)
    for name, key in [("norm_mix", "e_norm_mix_2"), ("norm_ffn", "e_norm_ffn_2"), ("mu", "rwkv_mu_2"),
                      ("w0", "rwkv_w0_2"), ("a0", "rwkv_a0_2"), ("k_k", "rwkv_k_k_2"), ("k_a", "rwkv_k_a_2"),
                      ("r_k", "rwkv_r_k_2"), ("gn_g", "rwkv_gn_g_2"), ("gn_b", "rwkv_gn_b_2")]:
        VECE(vec, name)[...] = columns(i[key][0].reshape(-1))
    a["vece"] = vec




def short_conv(nc, mem, vec, u, y):
    n = D_WIDTH // P
    first_tile = C_HEADS * HEAD // P
    taps = 3
    with phase(nc, "dve_steps") as (block, dve_steps):
        @block.vector
        def _(dve):
            steps = Steps(dve, dve_steps)
            z, out = u[:, O_CG:O_CG + n, :], y[:, first_tile:first_tile + n, :]
            steps.did(nc.vector.tensor_tensor(z, z, u[:, O_HD:O_HD + n, :], ALU.mult))
            steps.settle()
            for lag in range(taps):
                for c in range(n):
                    weight = VECO(vec, "conv", taps * c + taps - 1 - lag)
                    if lag == 0:
                        steps.did(nc.vector.tensor_scalar(out[:, c, :], z[:, c, :], weight, None, ALU.mult))
                    else:
                        steps.did(nc.vector.scalar_tensor_tensor(
                            out=out[:, c, lag:SEQ], in0=z[:, c, 0:SEQ - lag], scalar=weight, in1=out[:, c, lag:SEQ],
                            op0=ALU.mult, op1=ALU.add))
                steps.settle()
            steps.did(nc.vector.tensor_tensor(out, out, u[:, O_BG:O_BG + n, :], ALU.mult))
            steps.settle()


def rotate_keys(nc, mem, rope, u):
    tiles = range(O_KS, O_KS + 2 * C_KV)
    with buffers(nc, turn=[P, 2 * C_KV, SEQ]) as (turn,), phase(nc, "rotated", "dve_steps") as (
            block, rotated, dve_steps):
        @block.tensor
        def _(pe):
            for i, t in enumerate(tiles):
                nc.tensor.matmul(mem.bank[i][:, :], CONST(mem.const, "rot"), u[:, t, :], start=True, stop=True) \
                    .then_inc(rotated, 1)

        @block.vector
        def _(dve):
            steps = Steps(dve, dve_steps)
            for i, t in enumerate(tiles):
                dve.wait_ge(rotated, i + 1)
                steps.did(nc.vector.tensor_tensor(turn[:, i, :], mem.bank[i][:, :], rope[:, 1, :], ALU.mult))
                steps.did(nc.vector.tensor_tensor(u[:, t, :], u[:, t, :], rope[:, 0, :], ALU.mult))
            steps.settle()
            for i, t in enumerate(tiles):
                steps.did(nc.vector.tensor_tensor(u[:, t, :], u[:, t, :], turn[:, i, :], ALU.add))
            steps.settle()


def compress(nc, mem, w1, w2, pos, z, k_out, v_out):
    halves = CMP_HIDDEN // P
    lanes = [slice(0, HEAD), slice(HEAD, 2 * HEAD)]
    with buffers(nc, blocks=[P, CMP_LEN, N_CMP], second=[P, halves, HEAD], hidden=[P, C_KV, halves, N_CMP]) as (
            blocks, second, hidden), phase(
            nc, "loaded", "blocks_ready", "inner", "inner_taken", "outer", "outer_taken") as (
            block, loaded, blocks_ready, inner, inner_taken, outer, outer_taken):
        first = mem.ring[:, :, :].rearrange("p s n -> p (s n)").rearrange("p (l h) -> p l h", l=CMP_LEN)

        @block.sync
        def _(sp):
            for c in range(C_KV):
                sp.dma_start(first[lanes[c], :, :], w1).then_inc(loaded, 16)
            sp.dma_start(second[:, :, :], w2).then_inc(loaded, 16)

        @block.vector
        def _(dve):
            by_stride = z.rearrange("p (m r) -> p r m", r=CMP_STRIDE)
            for part in range(CMP_LEN // CMP_STRIDE):
                at = pos[:, part * CMP_STRIDE:(part + 1) * CMP_STRIDE].unsqueeze(2)
                nc.vector.tensor_tensor(blocks[:, part * CMP_STRIDE:(part + 1) * CMP_STRIDE, :],
                                        by_stride[:, :, part:part + N_CMP],
                                        at.broadcast_to([P, CMP_STRIDE, N_CMP]), ALU.add).then_inc(blocks_ready, 1)

        @block.tensor
        def _(pe):
            pe.wait_ge(loaded, 48)
            pe.wait_ge(blocks_ready, 2)
            for c in range(C_KV):
                for h in range(halves):
                    for l in range(CMP_LEN):
                        last = nc.tensor.matmul(mem.bank[c * halves + h][:, 0:N_CMP],
                                                first[lanes[c], l, h * P:(h + 1) * P], blocks[lanes[c], l, :],
                                                start=(l == 0), stop=(l == CMP_LEN - 1))
                    last.then_inc(inner, 1)
            for c in range(C_KV):
                pe.wait_ge(inner_taken, (c + 1) * halves)
                if k_out is not None:
                    for side in range(2):
                        for h in range(halves):
                            last = nc.tensor.matmul(mem.bank[4 + c][lanes[side], 0:N_CMP], second[:, h, :],
                                                    hidden[:, c, h, :], start=(h == 0), stop=(h == halves - 1))
                else:
                    for h in range(halves):
                        last = nc.tensor.matmul(mem.bank[4 + c][0:N_CMP, 0:HEAD], hidden[:, c, h, :], second[:, h, :],
                                                start=(h == 0), stop=(h == halves - 1))
                last.then_inc(outer, 1)

        @block.scalar
        def _(act):
            for c in range(C_KV):
                for h in range(halves):
                    act.wait_ge(inner, c * halves + h + 1)
                    nc.scalar.activation(hidden[:, c, h, :], mem.bank[c * halves + h][:, 0:N_CMP],
                                         ACT.Gelu_apprx_tanh).then_inc(inner_taken, 1)
            for c in range(C_KV):
                act.wait_ge(outer, c + 1)
                if k_out is not None:
                    nc.scalar.activation(k_out[:, c, :], mem.bank[4 + c][:, 0:N_CMP], ACT.Copy).then_inc(outer_taken, 1)
                else:
                    nc.scalar.activation(v_out[0:N_CMP, c, :], mem.bank[4 + c][0:N_CMP, 0:HEAD], ACT.Copy) \
                        .then_inc(outer_taken, 1)


def sparse_attention(nc, mem, rope, u, tm, k_cmp, v_cmp, y):
    lanes = [slice(0, HEAD), slice(HEAD, 2 * HEAD)]
    units = [(h, t) for h in range(2) for t in range(TT)]
    n_units = len(units)
    scale = HEAD ** -0.5
    SLC, WIN = range(2)
    with nc.Fori(0, C_KV) as kv, nc.Fori(0, C_GROUP // 2) as half, buffers(
            nc, q=[P, SEQ], q_rot=[P, SEQ], turn=[P, SEQ], keys=[P, 2, SEQ], values=[P, 2, TT, HEAD],
            kc=[P, N_CMP], vc=[P, HEAD], gate=[P, TT, 2, N_BRANCH], probs=[P, 2, 2, SEQ], probs_c=[P, 2, TT, N_CMP],
            top_c=[P, 2, TT], sum_c=[P, 2, TT], tops=[P, 2 * n_units], sums=[P, 2 * n_units],
            weights=[P, 2 * n_units], turned=[P, 2, 2, SEQ], turned_c=[P, 2, SEQ]) as (
            q, q_rot, turn, keys, values, kc, vc, gate, probs, probs_c, top_c, sum_c, tops, sums, weights, turned,
            turned_c), phase(
            nc, "gate_ready", "q_ready", "rotated", "keys_staged", "staged", "scored_c", "topped_c", "exped_c",
            "weighted_c", "transposed_c", "taken_c", "scored", "topped", "exped", "weighted", "transposed",
            "taken", "applied", "dve_steps") as (
            block, gate_ready, q_ready, rotated, keys_staged, staged, scored_c, topped_c, exped_c,
            weighted_c, transposed_c, taken_c, scored, topped, exped, weighted, transposed,
            taken, applied, dve_steps):
        j = kv * (C_GROUP // 2) + half
        first_gate = 2 * KV_WIDTH
        out_bank = mem.bank[7]

        def score_bank(n, branch):
            return mem.bank[2 * (n % 2) + branch]

        @block.scalar
        def _(act):
            nc.scalar.activation(gate[:, :, :, :].rearrange("p t h b -> p t (h b)"),
                                 tm[:, :, bass.ds(j * 2 * N_BRANCH + first_gate, 2 * N_BRANCH)],
                                 ACT.Sigmoid).then_inc(gate_ready, 1)
            nc.scalar.activation(q[:, :], tile_at(u, j + O_Q), ACT.Copy, scale=scale).then_inc(q_ready, 1)
            act.wait_ge(topped_c, 1)
            nc.scalar.activation(probs_c[:, :, :, :], probs_c[:, :, :, :], ACT.Exp).then_inc(exped_c, 1)
            for h in range(2):
                act.wait_ge(transposed_c, h + 1)
                nc.scalar.activation(turned_c[0:N_CMP, h, :], mem.bank[2 + h][0:N_CMP, :], ACT.Copy) \
                    .then_inc(taken_c, 1)

            def take_turned(n):
                h, t = units[n]
                width = (t + 1) * P
                act.wait_ge(transposed, n + 1)
                if n >= 2:
                    act.wait_ge(applied, n - 1)
                for branch in (SLC, WIN):
                    nc.scalar.activation(turned[:, n % 2, branch, 0:width], mem.bank[5 + branch][:, 0:width], ACT.Copy) \
                        .then_inc(taken, 1)

            for n, (h, t) in enumerate(units):
                width = (t + 1) * P
                act.wait_ge(topped, n + 1)
                if n >= 2:
                    act.wait_ge(transposed, n - 1)
                for branch in (SLC, WIN):
                    i = 2 * n + branch
                    nc.scalar.activation(probs[:, n % 2, branch, 0:width], score_bank(n, branch)[:, 0:width], ACT.Exp,
                                         bias=tops[:, i:i + 1], accum_out=sums[:, i:i + 1]).then_inc(exped, 1)
                if n >= 1:
                    take_turned(n - 1)
            take_turned(n_units - 1)

        @block.tensor
        def _(pe):
            pe.wait_ge(q_ready, 1)
            nc.tensor.matmul(out_bank[:, :], CONST(mem.const, "rot"), q[:, :], start=True, stop=True) \
                .then_inc(rotated, 1)
            pe.wait_ge(keys_staged, 1)
            for h in range(2):
                for t in range(TT):
                    last = nc.tensor.matmul(mem.bank[h][:, t * N_CMP:(t + 1) * N_CMP], q[lanes[h], t * P:(t + 1) * P],
                                            kc[lanes[h], :], start=True, stop=True)
                last.then_inc(scored_c, 1)
            pe.wait_ge(weighted_c, 1)
            for h in range(2):
                for t in range(TT):
                    last = nc.tensor.transpose(mem.bank[2 + h][0:N_CMP, t * P:(t + 1) * P], probs_c[:, h, t, :],
                                               CONST(mem.const, "ident"))
                last.then_inc(transposed_c, 1)
            pe.wait_ge(taken_c, 2)
            pe.wait_ge(staged, 1)

            def score(n):
                h, t = units[n]
                c = slice(t * P, (t + 1) * P)
                if n >= 2:
                    pe.wait_ge(exped, 2 * n - 2)
                for branch in (SLC, WIN):
                    nc.tensor.matmul(score_bank(n, branch)[:, 0:(t + 1) * P], q_rot[lanes[h], c],
                                     keys[lanes[h], branch, 0:(t + 1) * P], start=True, stop=True) \
                        .then_inc(scored, 1)

            def transpose(n):
                h, t = units[n]
                pe.wait_ge(weighted, 2 * n + 2)
                if n >= 1:
                    pe.wait_ge(taken, 2 * n)
                for branch in (SLC, WIN):
                    for b in range(t + 1):
                        c = slice(b * P, (b + 1) * P)
                        last = nc.tensor.transpose(mem.bank[5 + branch][:, c], probs[:, n % 2, branch, c],
                                                   CONST(mem.const, "ident"))
                last.then_inc(transposed, 1)

            def apply(n):
                h, t = units[n]
                to = out_bank[lanes[h], t * P:(t + 1) * P]
                nc.tensor.matmul(to, vc[0:N_CMP, :], turned_c[0:N_CMP, h, t * P:(t + 1) * P], start=True, stop=False)
                pe.wait_ge(taken, 2 * n + 2)
                for branch in (SLC, WIN):
                    for b in range(t + 1):
                        last = nc.tensor.matmul(to, values[:, branch, b, :],
                                                turned[:, n % 2, branch, b * P:(b + 1) * P],
                                                start=False, stop=(branch == WIN and b == t))
                last.then_inc(applied, 1)

            for n in range(n_units):
                score(n)
                if n >= 1:
                    transpose(n - 1)
                if n >= 2:
                    apply(n - 2)
            transpose(n_units - 1)
            apply(n_units - 2)
            apply(n_units - 1)

        @block.vector
        def _(dve):
            steps = Steps(dve, dve_steps)
            steps.did(nc.vector.tensor_copy(vc[0:N_CMP, :],
                                            v_cmp[0:N_CMP, bass.ds(kv, 1), :].rearrange("p a n -> p (a n)")))
            steps.did(nc.vector.tensor_copy(keys[:, SLC, :], tile_at(u, kv + O_KS)))
            steps.did(nc.vector.tensor_copy(keys[:, WIN, :], tile_at(u, kv + O_KW)))
            for branch in (SLC, WIN):
                steps.did(nc.vector.tensor_copy(values[:, branch, :, :],
                                                tm[:, :, bass.ds(kv * HEAD + branch * KV_WIDTH, HEAD)]))
            steps.settle()
            steps.did(nc.vector.tensor_copy(kc[:, :], k_cmp[:, bass.ds(kv, 1), :].rearrange("p a n -> p (a n)")),
                      keys_staged)
            dve.wait_ge(q_ready, 1)
            steps.did(nc.vector.tensor_tensor(q_rot[:, :], q[:, :], rope[:, 0, :], ALU.mult))
            dve.wait_ge(rotated, 1)
            steps.did(nc.vector.tensor_tensor(turn[:, :], out_bank[:, :], rope[:, 1, :], ALU.mult))
            steps.settle()
            steps.did(nc.vector.tensor_tensor(q_rot[:, :], q_rot[:, :], turn[:, :], ALU.add), staged)
            mask = CONST(mem.const, "cmp_min").rearrange("p (t n) -> p t n", t=TT)
            seen = CONST(mem.const, "cmp_one").rearrange("p (t n) -> p t n", t=TT)
            for h in range(2):
                dve.wait_ge(scored_c, h + 1)
                steps.did(nc.vector.tensor_tensor(
                    probs_c[:, h, :, :], mem.bank[h][:, 0:TT * N_CMP].rearrange("p (t n) -> p t n", t=TT), mask,
                    ALU.min))
            steps.settle()
            steps.did(nc.vector.reduce_max(top_c[:, :, :], probs_c[:, :, :, :], AX_X))
            steps.settle()
            for h in range(2):
                steps.did(nc.vector.tensor_tensor(probs_c[:, h, :, :], probs_c[:, h, :, :],
                                                  top_c[:, h, :].unsqueeze(2).broadcast_to([P, TT, N_CMP]),
                                                  ALU.subtract), topped_c if h else None)
                steps.settle()
            dve.wait_ge(exped_c, 1)
            for h in range(2):
                steps.did(nc.vector.tensor_tensor(probs_c[:, h, :, :], probs_c[:, h, :, :], seen, ALU.mult))
            steps.settle()
            steps.did(nc.vector.reduce_sum(sum_c[:, :, :], probs_c[:, :, :, :], AX_X))
            steps.settle()
            steps.did(nc.vector.tensor_scalar(sum_c[:, :, :], sum_c[:, :, :], 1e-30, None, ALU.max))
            steps.settle()
            steps.did(nc.vector.reciprocal(sum_c[:, :, :], sum_c[:, :, :]))
            steps.settle()
            dve.wait_ge(gate_ready, 1)
            for h in range(2):
                steps.did(nc.vector.tensor_tensor(sum_c[:, h, :], sum_c[:, h, :], gate[:, :, h, 0], ALU.mult))
            steps.settle()
            for h in range(2):
                steps.did(nc.vector.tensor_tensor(probs_c[:, h, :, :], probs_c[:, h, :, :],
                                                  sum_c[:, h, :].unsqueeze(2).broadcast_to([P, TT, N_CMP]),
                                                  ALU.mult), weighted_c if h else None)
                steps.settle()

            def top(n):
                h, t = units[n]
                width, i = (t + 1) * P, 2 * n
                for branch in (SLC, WIN):
                    dve.wait_ge(scored, i + branch + 1)
                    own = score_bank(n, branch)[:, t * P:width]
                    steps.did(nc.vector.tensor_tensor(own, own, CONST(mem.const, "causal_min"), ALU.min))
                steps.settle()
                for branch in (SLC, WIN):
                    steps.did(nc.vector.reduce_max(weights[:, i + branch:i + branch + 1],
                                                   score_bank(n, branch)[:, 0:width], AX_X))
                steps.settle()
                steps.did(nc.vector.tensor_scalar(tops[:, i:i + 2], weights[:, i:i + 2], -1.0, None, ALU.mult), topped)

            def weigh(n):
                h, t = units[n]
                width, i = (t + 1) * P, 2 * n
                dve.wait_ge(exped, 2 * n + 2)
                steps.did(nc.vector.reciprocal(weights[:, i:i + 2], sums[:, i:i + 2]))
                steps.settle()
                steps.did(nc.vector.tensor_tensor(weights[:, i:i + 2], weights[:, i:i + 2], gate[:, t, h, 1:3],
                                                  ALU.mult))
                steps.settle()
                for branch in (SLC, WIN):
                    p = probs[:, n % 2, branch, 0:width]
                    steps.did(nc.vector.tensor_scalar(p, p, weights[:, i + branch:i + branch + 1], None, ALU.mult),
                              weighted)

            for n in range(n_units):
                top(n)
                if n >= 1:
                    weigh(n - 1)
            weigh(n_units - 1)
            dve.wait_ge(applied, n_units)
            steps.did(nc.vector.tensor_copy(tile_at(y, j), out_bank[:, :]))
            steps.settle()


def second_odd(nc, mem, a):
    with buffers(nc, vec=[P, VECO.size]) as (vec,):
        load(nc, (vec[:, :], a["veco"]))
        with buffers(nc, y=[P, KD, SEQ], u=[P, UTO, SEQ], tm=[P, TT, TMO], rope=[P, 2, SEQ], k_cmp=[P, C_KV, N_CMP],
                     v_cmp=[P, C_KV, HEAD]) as (y, u, tm, rope, k_cmp, v_cmp):
            load(nc, (rope[:, :, :], a["rope"]))
            rms_norm(nc, mem, mem.x, lambda k: VECO(vec, "norm_mix", k), mem.h)
            linear(nc, mem, unit_of(a["w_ino"]), UTO // 2, 2, KD, mem.h, copy_out(nc, u))
            token_major(nc, mem, a["w_tmo"], TMO, mem.h, tm)
            short_conv(nc, mem, vec, u, y)
            rotate_keys(nc, mem, rope, u)
            compress(nc, mem, a["cmp_k1"], a["cmp_k2"], VECO(vec, "pos_k"), u[:, O_KC, :], k_cmp, None)
            compress(nc, mem, a["cmp_v1"], a["cmp_v2"], VECO(vec, "pos_v"), u[:, O_VC, :], None, v_cmp)
            sparse_attention(nc, mem, rope, u, tm, k_cmp, v_cmp, y)
            if mem.stop in ("odd", "nsa"):
                dump(nc, mem, a, y, 0, 8)
            linear(nc, mem, unit_of(a["w_outo"]), KD // 2, 2, KD, y, add_out(nc, mem.x), on_vector=True)
        rms_norm(nc, mem, mem.x, lambda k: VECO(vec, "norm_ffn", k), mem.h)
        if mem.stop != "nsa":
            mixture(nc, mem, a)
        rms_norm(nc, mem, mem.x, lambda k: VECO(vec, "final", k), mem.h)


def lay_out_odd(i, a):
    w = i["o_w_in_2"][0]
    at = C_HEADS * HEAD
    q, rest = w[:, :at], w[:, at:]
    kc, vc, ks, vs, kw, vw = [rest[:, n * KV_WIDTH:(n + 1) * KV_WIDTH] for n in range(6)]
    gates, conv = rest[:, 6 * KV_WIDTH:6 * KV_WIDTH + C_HEADS * N_BRANCH], rest[:, 6 * KV_WIDTH + C_HEADS * N_BRANCH:]
    twice = lambda k: [k[:, c * HEAD:(c + 1) * HEAD] for c in (0, 0, 1, 1)]
    a["w_ino"] = weight_units(np.concatenate([q, kc, vc, *twice(ks), *twice(kw), conv], axis=1), 2)
    a["w_tmo"] = moving(np.concatenate([vs, vw, gates], axis=1))
    a["w_outo"] = weight_units(i["o_w_out_2"][0], 2)
    for n in "kv":
        a[f"cmp_{n}1"] = i[f"nsa_cmp_{n}_w1_2"][0].reshape(CMP_LEN, HEAD, CMP_HIDDEN).transpose(1, 0, 2)
        a[f"cmp_{n}2"] = i[f"nsa_cmp_{n}_w2_2"][0].reshape(CMP_HIDDEN // P, P, HEAD).transpose(1, 0, 2)
    vec = np.zeros((P, VECO.size), np.float32)
    VECO(vec, "norm_mix")[...] = columns(i["o_norm_mix_2"][0])
    VECO(vec, "norm_ffn")[...] = columns(i["o_norm_ffn_2"][0])
    VECO(vec, "final")[...] = columns(i["final_norm_2"])
    VECO(vec, "pos_k")[...] = np.tile(i["nsa_cmp_pos_k_2"][0].T, (2, 1))
    VECO(vec, "pos_v")[...] = np.tile(i["nsa_cmp_pos_v_2"][0].T, (2, 1))
    VECO(vec, "conv")[...] = i["conv_w_2"][0].reshape(3, D_WIDTH // P, P).transpose(2, 1, 0).reshape(P, -1)
    a["veco"] = vec
    a["router"] = moving(i["moe_router_2"][0])
    a["router_b"] = i["moe_router_b_2"][0]
    a["w_expert"] = np.stack([weight_units(interleaved(g, u), 2)
                              for g, u in zip(i["moe_w_gate_2"][0], i["moe_w_up_2"][0])])
    a["w_expert_down"] = np.stack([weight_units(w, 1) for w in i["moe_w_down_2"][0]])


def lay_out_second(i, a):
    lay_out_even(i, a)
    lay_out_odd(i, a)


def route(nc, mem, a, gate, rows):
    with buffers(nc, router=[P, KD * N_EXPERTS], bias=[P, N_EXPERTS], logits=[P, TT, N_EXPERTS],
                 best=[P, TT, 8], place=[P, TT, 8], part=[P, TT, 2], hot=[P, TT, 2, N_EXPERTS]) as (
            router, bias, logits, best, place, part, hot), nc.sbuf_tensor(
            f"order_{nc.next_id()}", [P, TT, 8], U32) as order, phase(
            nc, "loaded", "product", "ranked", "exped", "gated", "row", "row_taken", "dve_steps") as (
            block, loaded, product, ranked, exped, gated, row, row_taken, dve_steps):
        @block.sync
        def _(sp):
            sp.dma_start(router[:, :], a["router"]).then_inc(loaded, 16)
            sp.dma_start(bias[:, :], a["router_b"].partition_broadcast(P)).then_inc(loaded, 16)

        @block.tensor
        def _(pe):
            pe.wait_ge(loaded, 32)
            for t in range(TT):
                for k in range(KD):
                    last = nc.tensor.matmul(mem.bank[0][:, t * N_EXPERTS:(t + 1) * N_EXPERTS],
                                            mem.h[:, k, t * P:(t + 1) * P],
                                            router[:, k * N_EXPERTS:(k + 1) * N_EXPERTS],
                                            start=(k == 0), stop=(k == KD - 1))
            last.then_inc(product, 1)
            pe.wait_ge(gated, 1)
            for e in range(N_EXPERTS):
                if e >= 2:
                    pe.wait_ge(row_taken, e - 1)
                for t in range(TT):
                    last = nc.tensor.matmul(mem.bank[1 + e % 2][:, t * P:(t + 1) * P],
                                            gate[:, t, e:e + 1].broadcast_to([P, P]), CONST(mem.const, "ident"),
                                            start=True, stop=True)
                last.then_inc(row, 1)

        @block.scalar
        def _(act):
            act.wait_ge(ranked, 1)
            nc.scalar.activation(part[:, :, 1], part[:, :, 1], ACT.Exp).then_inc(exped, 1)
            for e in range(N_EXPERTS):
                act.wait_ge(row, e + 1)
                nc.scalar.activation(rows[:, e, :], mem.bank[1 + e % 2][:, :], ACT.Copy).then_inc(row_taken, 1)

        @block.vector
        def _(dve):
            steps = Steps(dve, dve_steps)
            dve.wait_ge(product, 1)
            steps.did(nc.vector.tensor_tensor(
                logits[:, :, :], mem.bank[0][:, 0:TT * N_EXPERTS].rearrange("p (t e) -> p t e", t=TT),
                bias[:, :].unsqueeze(1).broadcast_to([P, TT, N_EXPERTS]), ALU.add))
            steps.settle()
            for t in range(TT):
                steps.did(nc.vector.max(best[:, t, :], logits[:, t, :]))
            steps.settle()
            for t in range(TT):
                steps.did(nc.vector.max_index(order[:, t, :], best[:, t, :], logits[:, t, :]))
            steps.settle()
            steps.did(nc.vector.tensor_copy(place[:, :, :], order[:, :, :]))
            steps.did(nc.vector.tensor_tensor(part[:, :, 1], best[:, :, 1], best[:, :, 0], ALU.subtract), ranked)
            steps.settle()
            for t in range(TT):
                for c in range(TOP_K):
                    steps.did(nc.vector.tensor_scalar(hot[:, t, c, :], CONST(mem.const, "experts"),
                                                      place[:, t, c:c + 1], None, ALU.is_equal))
            dve.wait_ge(exped, 1)
            steps.did(nc.vector.tensor_scalar(part[:, :, 0], part[:, :, 1], 1.0, None, ALU.add))
            steps.settle()
            steps.did(nc.vector.reciprocal(part[:, :, 0], part[:, :, 0]))
            steps.settle()
            steps.did(nc.vector.tensor_tensor(part[:, :, 1], part[:, :, 1], part[:, :, 0], ALU.mult))
            steps.settle()
            for t in range(TT):
                steps.did(nc.vector.tensor_scalar(gate[:, t, :], hot[:, t, 0, :], part[:, t, 0:1], None, ALU.mult))
            steps.settle()
            for t in range(TT):
                steps.did(nc.vector.scalar_tensor_tensor(out=gate[:, t, :], in0=hot[:, t, 1, :], scalar=part[:, t, 1:2],
                                                         in1=gate[:, t, :], op0=ALU.mult, op1=ALU.add),
                          gated if t == TT - 1 else None)
            steps.settle()


def mixture(nc, mem, a):
    with buffers(nc, gate=[P, TT, N_EXPERTS], rows=[P, N_EXPERTS, SEQ]) as (gate, rows):
        route(nc, mem, a, gate, rows)
        with nc.Fori(0, N_EXPERTS) as e, buffers(nc, hidden=[P, EXP_T, SEQ], gated=[P, SLOTS, SEQ],
                                                 out=[P, KD, SEQ]) as (hidden, gated, out):
            linear(nc, mem, unit_of(a["w_expert"], e), EXP_T, 2, KD, mem.h, gated_tile(nc, hidden), gated=gated)
            linear(nc, mem, unit_of(a["w_expert_down"], e), KD, 1, EXP_T, hidden, copy_out(nc, out))
            with phase(nc, "weighted", "dve_steps") as (block, weighted, dve_steps):
                @block.vector
                def _(dve):
                    row = rows[:, bass.ds(e, 1), :].broadcast_to([P, KD, SEQ])
                    nc.vector.tensor_tensor(out[:, :, :], out[:, :, :], row, ALU.mult).then_inc(weighted, 1)
                    dve.wait_ge(weighted, 1)
                    nc.vector.tensor_tensor(mem.x[:, :, :], mem.x[:, :, :], out[:, :, :], ALU.add)


class Memory:

    def __init__(self, nc, stack):
        def sb(name, shape):
            return stack.enter_context(nc.sbuf_tensor(name, shape, F32))

        self.x = sb("x_res", [P, KD, SEQ])
        self.h = sb("h_branch", [P, KD, SEQ])
        self.ring = sb("weight_ring", [P, SLOTS, SLOT])
        self.const = sb("const_cols", [P, CONST.size])
        self.levels = sb("level_masks", [P, 2, LEVELS, P])
        self.eps = CONST(self.const, "eps")
        self.bank = [stack.enter_context(nc.psum_tensor(f"bank{b}", [P, SEQ], F32)) for b in range(8)]


def load(nc, *pairs):
    with phase(nc, "loaded") as (block, loaded):
        @block.sync
        def _(sp):
            for to, source in pairs:
                sp.dma_start(to, source).then_inc(loaded, 16)
            sp.wait_ge(loaded, 16 * len(pairs))


def layer_of(array, l):
    one = array[bass.ds(l, 1)]
    names = "abcdefg"[:len(one.shape) - 1]
    return one.rearrange(f"z {' '.join(names)} -> (z {names[0]}) {' '.join(names[1:])}")


def unit_of(array, l=None):
    def weights(u):
        if l is None:
            return array[bass.ds(u, 1)].rearrange("a p n -> (a p) n")
        return array[bass.ds(l, 1), bass.ds(u, 1)].rearrange("z a p n -> (z a p) n")
    return weights


def first_block(nc, mem, a):
    with nc.Fori(0, DEPTH) as l, buffers(nc, vec=[P, VEC1.size]) as (vec,):
        with buffers(nc, y=[P, KD, SEQ], u=[P, UT1, SEQ], tm=[P, TT, TM1], 
                     lam=[P, 4 * DIFF_DIM + 2], gates=[P, 2, 2 * DELTA_HEADS]) as (y, u, tm, lam, gates):
            load(nc, (vec[:, :], layer_of(a["vec1"], l)),
                 (lam[:, :], a["lam"][bass.ds(l, 1), :].partition_broadcast(P)),
                 (gates[:, :, :], a["gates"][bass.ds(l, 1), :, :].partition_broadcast(P)))
            rms_norm(nc, mem, mem.x, lambda k: VEC1(vec, "pre_mix", k), mem.h)
            linear(nc, mem, unit_of(a["w_in1"], l), UT1 // 2, 2, KD, mem.h, copy_out(nc, u))
            token_major(nc, mem, layer_of(a["w_tm1"], l), TM1, mem.h, tm)
            if mem.stop == "in":
                dump(nc, mem, a, u, 0, 8); dump(nc, mem, a, tm.rearrange("p a b -> p (a b)") if 0 else u, 8, 22)
            conv_module(nc, mem, vec, u, y)
            diff_attention(nc, mem, vec, lam, a["dist"], u, tm, y)
            delta_net(nc, mem, vec, gates, u, tm, y)
            if mem.stop == "mix1":
                dump(nc, mem, a, y, 0, 8)
                return
            linear(nc, mem, unit_of(a["w_out1"], l), KD // 2, 2, KD, y, copy_out(nc, mem.h))
        rms_norm(nc, mem, mem.h, lambda k: VEC1(vec, "post_mix", k), None, add_to=mem.x)
        rms_norm(nc, mem, mem.x, lambda k: VEC1(vec, "pre_mlp", k), mem.h)
        squared_relu_mlp(nc, mem, unit_of(a["w_ff1"], l), unit_of(a["w_ff2"], l))
        rms_norm(nc, mem, mem.h, lambda k: VEC1(vec, "post_mlp", k), None, add_to=mem.x)


def dump(nc, mem, a, t, first, last):
    load(nc, (a["dbg"][:, first:last, :], t[:, first:last, :]))


def build(nc, a, out, stop=None):
    with ExitStack() as stack:
        mem = Memory(nc, stack)
        mem.stop = stop
        load(nc, (mem.x[:, :, :], a["x"]), (mem.const[:, :], a["const"]), (mem.levels[:, :, :, :], a["levels"]))
        if stop in (None, "mix1", "first"):
            first_block(nc, mem, a)
        if stop == "even":
            second_even(nc, mem, a)
            dump_at = (a["dbg"][:, 8:16, :], mem.x[:, :, :])
            load(nc, dump_at)
        if stop == "first":
            dump(nc, mem, a, mem.x, 0, 8)
        if stop is None:
            second_even(nc, mem, a)
        if stop in (None, "odd", "nsa", "all"):
            second_odd(nc, mem, a)
        load(nc, (out, mem.h[:, :, :]))


def weight_units(w, tiles):
    k, m = w.shape
    w = w.reshape(k // P, P, m // (P * tiles), tiles, P).transpose(2, 1, 3, 0, 4)
    return np.ascontiguousarray(w.reshape(m // (P * tiles), P, -1))


def moving(w):
    k, m = w.shape
    return np.ascontiguousarray(w.reshape(k // P, P, m).transpose(1, 0, 2).reshape(P, -1))


def columns(v):
    return v.reshape(-1, P).T


def alibi_slopes(n):
    def pow2(m):
        start = 2.0 ** (-8.0 / m)
        return [start ** (i + 1) for i in range(m)]
    if math.log2(n).is_integer():
        return pow2(n)
    c = 2 ** int(math.floor(math.log2(n)))
    return pow2(c) + pow2(2 * c)[0::2][: n - c]


def constants():
    i, j = np.arange(P)[:, None], np.arange(P)[None, :]
    c = np.zeros((P, CONST.size), np.float32)

    def put(name, value):
        CONST(c, name)[...] = value

    put("ident", i == j)
    put("ones", 1)
    put("pair_ones", i // HEAD == j // HEAD)
    half, d = ROT_DIM // 2, np.arange(P) % HEAD
    rot = np.zeros((P, P))
    for p in range(P):
        if d[p] < half:
            rot[p + half, p] = -1
        elif d[p] < ROT_DIM:
            rot[p - half, p] = 1
    put("rot", rot)
    put("lower_in", i >= j)
    put("upper_in", i <= j)
    put("upper_strict", i < j)
    put("neg_lower_strict", -1.0 * (i > j))
    put("lower_strict_max", np.where(i > j, 0, BIG))
    put("upper_strict_max", np.where(i < j, 0, BIG))
    put("upper_in_min", np.where(i <= j, 0, -BIG))
    put("lower_in_min", np.where(i >= j, 0, -BIG))
    put("causal_min", np.where(i >= j, 3e38, -BIG))
    put("neg_slopes", -np.asarray(alibi_slopes(DIFF_HEADS), np.float32))
    t = (np.arange(TT)[None, :, None] * P + np.arange(P)[:, None, None])
    seen = (np.arange(N_CMP) * CMP_STRIDE + CMP_LEN - 1)[None, None, :] <= t
    put("cmp_min", np.where(seen, 3e38, -BIG).reshape(P, -1))
    put("cmp_one", seen.reshape(P, -1))
    put("not_first", np.arange(SEQ)[None, :] % P != 0)
    put("experts", np.arange(N_EXPERTS)[None, :])
    put("eps", np.array([NORM_EPS, 1e-5, RWKV_GN_EPS, 0.0]))
    levels = np.zeros((P, 2, LEVELS, P), np.float32)
    for n in range(LEVELS):
        b = 2 ** n
        low = (i // (2 * b) == j // (2 * b)) & (i // b % 2 == 1) & (j // b % 2 == 0)
        levels[:, 0, n, :], levels[:, 1, n, :] = low.T, low
    q = (np.arange(TT)[None, :, None] * P + np.arange(P)[:, None, None])
    dist = np.abs(q - np.arange(SEQ)[None, None, :]).astype(np.float32)
    pos = np.arange(SEQ, dtype=np.float32)
    freq = (np.float32(ROPE_THETA) ** (-np.arange(0, ROT_DIM, 2, dtype=np.float32) / np.float32(ROT_DIM))).astype(np.float32)
    angle = pos[:, None] * freq[None, :]
    rope = np.zeros((P, 2, SEQ), np.float32)
    rope[:, 0, :] = 1
    for p in range(P):
        if d[p] < ROT_DIM:
            rope[p, 0], rope[p, 1] = np.cos(angle[:, d[p] % half]), np.sin(angle[:, d[p] % half])
    return {"const": c, "levels": levels, "dist": dist, "rope": rope}


def lay_out(i):
    a = dict(constants())
    a["x"] = np.ascontiguousarray(i["x"][0].T.reshape(KD, P, SEQ).transpose(1, 0, 2))
    w_in = i["w_in"]
    o_dv, o_g, o_b = 2 * CONV_CH + 2 * DIFF_W, 2 * CONV_CH + 3 * DIFF_W, 2 * CONV_CH + 3 * DIFF_W + 4 * DELTA_W
    fm = np.concatenate([w_in[:, :, :o_dv], w_in[:, :, o_g:o_b]], axis=2)
    tm = np.concatenate([w_in[:, :, o_dv:o_g], w_in[:, :, o_b:]], axis=2)
    a["w_in1"] = np.stack([weight_units(w, 2) for w in fm])
    a["w_tm1"] = np.stack([moving(w) for w in tm])
    a["w_out1"] = np.stack([weight_units(w, 2) for w in i["w_out"]])
    a["w_ff1"] = np.stack([weight_units(w, 2) for w in i["w_ff1"]])
    a["w_ff2"] = np.stack([weight_units(w, 1) for w in i["w_ff2"]])
    vec = np.zeros((DEPTH, P, VEC1.size), np.float32)
    lam = np.zeros((DEPTH, 4 * DIFF_DIM + 2), np.float32)
    for l in range(DEPTH):
        def put(name, value):
            VEC1(vec[l], name)[...] = value
        put("pre_mix", columns(i["pre_mix_w"][l]))
        put("post_mix", columns(i["post_mix_w"][l]))
        put("pre_mlp", columns(i["pre_mlp_w"][l]))
        put("post_mlp", columns(i["post_mlp_w"][l]))
        put("conv_w", i["conv_dw_w"][l].reshape(CONV_WIDTH, CONV_T, P).transpose(2, 1, 0).reshape(P, -1))
        put("conv_b", columns(i["conv_dw_b"][l]))
        put("ln_w", columns(i["conv_ln_w"][l]))
        put("ln_b", columns(i["conv_ln_b"][l]))
        put("subln", np.tile(i["diff_subln_w"][l], 2)[:, None])
        put("delta_conv", i["delta_conv_w"][l].reshape(SHORT_CONV, 3 * PAIRS1, P).transpose(2, 1, 0).reshape(P, -1))
        put("delta_norm", np.tile(i["delta_norm_w"][l], 2)[:, None])
        init = 0.8 - 0.6 * math.exp(-0.3 * l)
        lam[l] = np.concatenate([i["diff_lambda_q1"][l], i["diff_lambda_k1"][l], i["diff_lambda_q2"][l],
                                 i["diff_lambda_k2"][l], np.array([init, 1.0 - init], np.float32)])
    a["vec1"], a["lam"] = vec, lam
    a["gates"] = np.stack([i["delta_A_log"].reshape(DEPTH, -1), i["delta_dt_bias"].reshape(DEPTH, -1)], axis=1)
    lay_out_second(i, a)
    return {n: np.ascontiguousarray(v, dtype=np.float32) for n, v in a.items()}


def kernel(**inputs):
    import concourse.bacc as bacc
    from concourse.bass_utils import run_bass_kernel_spmd

    arrays = lay_out({n: np.asarray(v) for n, v in inputs.items()})
    nc = bacc.Bacc("TRN2", target_bir_lowering=False, num_devices=1)
    handles = {n: nc.dram_tensor(f"in_{n}", v.shape, F32, kind="ExternalInput").ap() for n, v in arrays.items()}
    out = nc.dram_tensor("out", (P, KD, SEQ), F32, kind="ExternalOutput").ap()
    build(nc, handles, out)
    result = run_bass_kernel_spmd(nc, [{f"in_{n}": v for n, v in arrays.items()}], core_ids=[0])
    y = result.results[0]["out"]
    return np.ascontiguousarray(y.transpose(2, 1, 0).reshape(1, SEQ, D_MODEL))
```

```python
from contextlib import ExitStack, contextmanager
import math

import numpy as np

import concourse.bass as bass
from concourse import mybir

F32 = mybir.dt.float32
U32 = mybir.dt.uint32
I32 = mybir.dt.int32
F32R = mybir.dt.float32r
ACT = mybir.ActivationFunctionType
ALU = mybir.AluOpType
AX_X = mybir.AxisListType.X

P = 128
SEQ = 512
D_MODEL = 1024
KD = D_MODEL // P
TT = SEQ // P
DEPTH = 2
HEAD = 64
NORM_EPS = 1e-6
BIG = 1e30

DIFF_W = 384
DIFF_DIM = 32
DIFF_HEADS = DIFF_W // HEAD
DELTA_W = 384
DELTA_HEADS = DELTA_W // HEAD
CONV_CH = D_MODEL - DIFF_W - DELTA_W
CONV_T = CONV_CH // P
CONV_WIDTH = 31
SHORT_CONV = 3
D_FF = 4 * D_MODEL
PAIRS1 = DELTA_HEADS // 2
GATES1 = 4 * DELTA_HEADS
TM1 = DIFF_W + GATES1
U_CA, U_CG, U_DQ, U_DK, U_GQ, U_GK, U_GV, U_GZ = 0, 2, 4, 7, 10, 13, 16, 19
UT1 = 22

B_HEADS = 8
B_WIDTH = 512
A_WIDTH = 512
A_GROUPS = 4
RW_PAIRS = B_HEADS // 2
LORA = 64
SGU_LN_EPS = 1e-5
RWKV_GN_EPS = 64e-5
E_U, E_R, E_K, E_V, E_WA, E_G = 0, 4, 8, 12, 16, 17
UTE = 18
FFN_DIM = 2816
FFN_T = FFN_DIM // P
C_HEADS = 8
C_KV = 2
C_GROUP = C_HEADS // C_KV
KV_WIDTH = C_KV * HEAD
N_BRANCH = 3
CMP_LEN = 32
CMP_STRIDE = 16
N_CMP = (SEQ - CMP_LEN) // CMP_STRIDE + 1
CMP_COLS = N_CMP + N_CMP % 2
CMP_HIDDEN = 256
ROT_DIM = HEAD // 4
ROPE_THETA = 500000.0
D_WIDTH = 512
TMO = 2 * KV_WIDTH + C_HEADS * N_BRANCH
O_Q, O_KC, O_VC, O_KS, O_KW, O_BG, O_CG, O_HD = 0, 4, 5, 6, 8, 10, 14, 18
UTO = 22
N_EXPERTS = 8
TOP_K = 2
EXPERT_DIM = 1408
EXP_T = EXPERT_DIM // P
BLOCK = 176
BLOCK_TILES = -(-BLOCK // P)
MAX_JOBS = N_EXPERTS + (SEQ * TOP_K - N_EXPERTS) // BLOCK
UNPICKED = 2.0 ** 14
EXP_SLOTS = 4

LEVELS = int(math.log2(P))
SLOTS = 2
SLOT = 2048


class Columns:

    def __init__(self):
        self.at, self.size = {}, 0

    def add(self, name, n):
        self.at[name] = (self.size, n)
        self.size += n
        return self

    def __call__(self, tensor, name, i=None, n=1):
        first, size = self.at[name]
        if i is None:
            return tensor[:, first:first + size]
        return tensor[:, first + i:first + i + n]


CONST = Columns()
for _name, _n in [("ident", P), ("ones", P), ("pair_ones", P), ("rot", P),
                  ("lower_in", P), ("upper_in", P), ("upper_strict", P), ("neg_lower_strict", P),
                  ("lower_strict_max", P), ("upper_strict_max", P), ("upper_in_min", P), ("lower_in_min", P),
                  ("causal_min", P), ("neg_slopes", DIFF_HEADS),
                  ("cmp_min", TT * N_CMP), ("cmp_one", TT * N_CMP), ("not_first", SEQ),
                  ("eps", 4)]:
    CONST.add(_name, _n)

CONSTM = Columns()
for _name, _n in [("experts", N_EXPERTS), ("experts_upto", N_EXPERTS * N_EXPERTS), ("jobs", MAX_JOBS + 1),
                  ("job_slots", MAX_JOBS + 1), ("slots", BLOCK)]:
    CONSTM.add(_name, _n)

VEC1 = Columns()
for _name, _n in [("pre_mix", KD), ("post_mix", KD), ("pre_mlp", KD), ("post_mlp", KD),
                  ("conv_w", CONV_T * CONV_WIDTH), ("conv_b", CONV_T), ("ln_w", CONV_T), ("ln_b", CONV_T),
                  ("subln", 1), ("delta_conv", 3 * PAIRS1 * SHORT_CONV), ("delta_norm", 1)]:
    VEC1.add(_name, _n)

VECE = Columns()
for _name, _n in [("norm_mix", KD), ("norm_ffn", KD), ("mu", 14), ("w0", RW_PAIRS), ("a0", RW_PAIRS),
                  ("k_k", RW_PAIRS), ("k_a", RW_PAIRS), ("r_k", RW_PAIRS), ("gn_g", RW_PAIRS), ("gn_b", RW_PAIRS)]:
    VECE.add(_name, _n)

VECO = Columns()
for _name, _n in [("norm_mix", KD), ("norm_ffn", KD), ("final", KD), ("pos_k", CMP_LEN), ("pos_v", CMP_LEN),
                  ("conv", (D_WIDTH // P) * 3)]:
    VECO.add(_name, _n)


class Steps:

    def __init__(self, engine, sem):
        self.engine, self.sem, self.count, self.open = engine, sem, {}, set()

    def did(self, instruction, sem=None):
        sem = self.sem if sem is None else sem
        self.count[sem] = self.count.get(sem, 0) + 1
        self.open.add(sem)
        return instruction.then_inc(sem, 1)

    def settle(self):
        for sem in [s for s in self.count if s in self.open]:
            self.engine.wait_ge(sem, self.count[sem])
        self.open = set()


@contextmanager
def phase(nc, *names):
    sems = [nc.alloc_semaphore(f"{n}_{nc.next_id()}") for n in names]
    with nc.Block() as block:
        yield (block, *sems)
    nc.clear_and_free_semaphores(sems)
    nc.all_engine_barrier()


@contextmanager
def buffers(nc, **shapes):
    with ExitStack() as stack:
        yield [stack.enter_context(nc.sbuf_tensor(f"{n}_{nc.next_id()}", s, F32)) for n, s in shapes.items()]


def rms_norm(nc, mem, source, gain, out, add_to=None):
    with buffers(nc, squares=[P, KD, SEQ], scale=[P, SEQ]) as (squares, scale), phase(
            nc, "squares_ready", "sum_ready", "root_ready", "dve_steps") as (
            block, squares_ready, sum_ready, root_ready, dve_steps):
        total = mem.bank[0]

        @block.scalar
        def _(act):
            for k in range(KD):
                nc.scalar.activation(squares[:, k, :], source[:, k, :], ACT.Square).then_inc(squares_ready, 1)
            act.wait_ge(sum_ready, 1)
            nc.scalar.activation(scale[:, :], total[:, :], ACT.Sqrt, bias=mem.eps[:, 0:1],
                                 scale=1.0 / D_MODEL).then_inc(root_ready, 1)

        @block.tensor
        def _(pe):
            for k in range(KD):
                pe.wait_ge(squares_ready, k + 1)
                last = nc.tensor.matmul(total[:, :], CONST(mem.const, "ones"), squares[:, k, :],
                                        start=(k == 0), stop=(k == KD - 1))
            last.then_inc(sum_ready, 1)

        @block.vector
        def _(dve):
            steps = Steps(dve, dve_steps)
            dve.wait_ge(root_ready, 1)
            steps.did(nc.vector.reciprocal(scale[:, :], scale[:, :]))
            steps.settle()
            for k in range(KD):
                to = out if add_to is None else squares
                steps.did(nc.vector.scalar_tensor_tensor(out=to[:, k, :], in0=source[:, k, :], scalar=gain(k),
                                                         in1=scale[:, :], op0=ALU.mult, op1=ALU.mult))
            if add_to is not None:
                steps.settle()
                for k in range(KD):
                    steps.did(nc.vector.tensor_tensor(add_to[:, k, :], add_to[:, k, :], squares[:, k, :], ALU.add))
            steps.settle()


@contextmanager
def parts_of(nc, tiles, width=SEQ):
    with ExitStack() as stack:
        yield [stack.enter_context(nc.sbuf_tensor(f"{n}_{nc.next_id()}", [P, tiles, width], F32R))
               for n in ("high", "low")]


def linear(nc, mem, weights, units, tiles, kt, parts, evacuate=None, on_vector=False, source=None, gate=None,
           result=None):
    size = tiles * kt * P
    n_banks = SLOTS * tiles
    gates = {None: [], "silu": [(0, 1)], "relu": [(j, j) for j in range(tiles)]}[gate]
    per = len(gates)
    n_gates = SLOTS * per
    names = [f"{n}{s}" for n in ("filled", "high_ready", "low_ready") for s in range(SLOTS)]
    names += [f"{n}{g}" for n in ("gate_ready", "gated_high", "gated_low") for g in range(n_gates)]
    names += [f"product{b}" for b in range(n_banks)] + [f"taken{b}" for b in range(n_banks)]
    names += ["source_high", "source_low"]
    with ExitStack() as stack:
        w_high, w_low = stack.enter_context(parts_of(nc, SLOTS, size))
        if gates:
            gated, = stack.enter_context(buffers(nc, gated=[P, n_gates, SEQ]))
        block, *sems = stack.enter_context(phase(nc, *names))
        filled, high_ready, low_ready = sems[:SLOTS], sems[SLOTS:2 * SLOTS], sems[2 * SLOTS:3 * SLOTS]
        sems = sems[3 * SLOTS:]
        gate_ready, gated_high, gated_low = sems[:n_gates], sems[n_gates:2 * n_gates], sems[2 * n_gates:3 * n_gates]
        sems = sems[3 * n_gates:]
        product, taken, (source_high, source_low) = sems[:n_banks], sems[n_banks:2 * n_banks], sems[2 * n_banks:]

        def rounds(engine, take, prepare):
            loops = max(units - SLOTS, 0) // SLOTS
            if loops:
                with engine.Fori(0, loops) as i:
                    for s in range(SLOTS):
                        take(i, s)
                        prepare(i + 1, s)
            for u in range(loops * SLOTS, units):
                take(u // SLOTS, u % SLOTS)
                if u + SLOTS < units:
                    prepare(u // SLOTS + 1, u % SLOTS)

        def after(engine, sem, i):
            if not (type(i) is int and i == 0):
                engine.wait_ge(sem, i)

        @block.sync
        def _(sp):
            def fill(i, s):
                after(sp, low_ready[s], i)
                sp.dma_start(mem.ring[:, s, 0:size], weights(i * SLOTS + s)).then_inc(filled[s], 16)

            for s in range(min(SLOTS, units)):
                fill(0, s)
            rounds(sp, lambda i, s: None, fill)

        @block.tensor
        def _(pe):
            high, low = parts

            def multiply(i, s):
                pe.wait_ge(low_ready[s], i + 1)
                for j in range(tiles):
                    b = s * tiles + j
                    by_gate = [g for g, (from_tile, to_tile) in enumerate(gates) if j == from_tile != to_tile]
                    free = gate_ready[s * per + by_gate[0]] if by_gate else taken[b]
                    pe.wait_ge(free, i + 1)
                    for k in range(kt):
                        if source is not None and b == 0:
                            pe.wait_ge(source_low, k + 1)
                        at = (j * kt + k) * P
                        whole, rest = w_high[:, s, at:at + P], w_low[:, s, at:at + P]
                        nc.tensor.matmul(mem.bank[b][:, :], whole, high[:, k, :], start=(k == 0), stop=False)
                        nc.tensor.matmul(mem.bank[b][:, :], whole, low[:, k, :], start=False, stop=False)
                        last = nc.tensor.matmul(mem.bank[b][:, :], rest, high[:, k, :], start=False, stop=(k == kt - 1))
                    last.then_inc(product[b], 1)

            rounds(pe, multiply, lambda i, s: None)

        @block.scalar
        def _(act):
            def round_weights(i, s):
                act.wait_ge(filled[s], i * 16 + 16)
                after(act, product[(s + 1) * tiles - 1], i)
                nc.scalar.activation(w_high[:, s, :], mem.ring[:, s, 0:size], ACT.Copy).then_inc(high_ready[s], 1)

            def take(i, s):
                for g, (from_tile, to_tile) in enumerate(gates):
                    b = s * tiles + from_tile
                    act.wait_ge(product[b], i + 1)
                    act.wait_ge(gated_low[s * per + g], i + 1)
                    nc.scalar.activation(gated[:, s * per + g, :], mem.bank[b][:, :],
                                         ACT.Silu if gate == "silu" else ACT.Relu).then_inc(gate_ready[s * per + g], 1)
                for g, (from_tile, to_tile) in enumerate(gates):
                    act.wait_ge(taken[s * tiles + to_tile], i + 2)
                    nc.scalar.activation(tile_at(result[0], (i * SLOTS + s) * per + g), gated[:, s * per + g, :],
                                         ACT.Copy).then_inc(gated_high[s * per + g], 1)
                if not (gates or on_vector):
                    for b in range(s * tiles, (s + 1) * tiles):
                        act.wait_ge(product[b], i + 1)
                        evacuate(mem.bank[b], i * n_banks + b).then_inc(taken[b], 1)

            if gates:
                for g in range(n_gates):
                    act.sem_inc(gate_ready[g], 1)
            elif not on_vector:
                for b in range(n_banks):
                    act.sem_inc(taken[b], 1)
            for s in range(min(SLOTS, units)):
                round_weights(0, s)
                if source is not None and s == 0:
                    for k in range(kt):
                        nc.scalar.activation(parts[0][:, k, :], source[:, k, :], ACT.Copy).then_inc(source_high, 1)
            rounds(act, take, round_weights)

        @block.vector
        def _(dve):
            def rest_of_weights(i, s):
                dve.wait_ge(high_ready[s], i + 1)
                nc.vector.tensor_tensor(w_low[:, s, :], mem.ring[:, s, 0:size], w_high[:, s, :],
                                        ALU.subtract).then_inc(low_ready[s], 1)

            def take(i, s):
                for g, (from_tile, to_tile) in enumerate(gates):
                    b, whole = s * tiles + to_tile, gated[:, s * per + g, :]
                    dve.wait_ge(product[b], i + 1)
                    dve.wait_ge(gate_ready[s * per + g], i + 2)
                    nc.vector.tensor_tensor(whole, whole, mem.bank[b][:, :], ALU.mult).then_inc(taken[b], 1)
                for g in range(per):
                    dve.wait_ge(gated_high[s * per + g], i + 1)
                    tile = (i * SLOTS + s) * per + g
                    nc.vector.tensor_tensor(tile_at(result[1], tile), gated[:, s * per + g, :],
                                            tile_at(result[0], tile), ALU.subtract).then_inc(gated_low[s * per + g], 1)
                if on_vector:
                    for b in range(s * tiles, (s + 1) * tiles):
                        dve.wait_ge(product[b], i + 1)
                        evacuate(mem.bank[b], i * n_banks + b).then_inc(taken[b], 1)

            if gates or on_vector:
                for b in range(n_banks):
                    dve.sem_inc(taken[b], 1)
                for g in range(n_gates):
                    dve.sem_inc(gated_low[g], 1)
            for s in range(min(SLOTS, units)):
                rest_of_weights(0, s)
                if source is not None and s == 0:
                    for k in range(kt):
                        dve.wait_ge(source_high, k + 1)
                        nc.vector.tensor_tensor(parts[1][:, k, :], source[:, k, :], parts[0][:, k, :],
                                                ALU.subtract).then_inc(source_low, 1)
            rounds(dve, take, rest_of_weights)


def project(nc, mem, weights, units, tiles, source, evacuate, on_vector=False):
    kt = source.shape[1]
    with parts_of(nc, kt) as parts:
        linear(nc, mem, weights, units, tiles, kt, parts, evacuate, on_vector, source=source)


def later_units(weights, first, part=slice(None)):
    return lambda u: weights(u + first)[:, part]


def tile_at(tensor, index):
    return tensor[:, bass.ds(index, 1), :].rearrange("p a n -> p (a n)")


def copy_out(nc, out):
    def evacuate(bank, tile):
        return nc.scalar.activation(tile_at(out, tile), bank[:, :], ACT.Copy)
    return evacuate


def add_out(nc, target):
    def evacuate(bank, tile):
        return nc.vector.tensor_tensor(tile_at(target, tile), tile_at(target, tile), bank[:, :], ALU.add)
    return evacuate


def token_major(nc, mem, weights, cols, source, out):
    with phase(nc, "filled", "product", "taken") as (block, filled, product, taken):
        w = mem.ring[:, :, :].rearrange("p s n -> p (s n)")

        @block.sync
        def _(sp):
            sp.dma_start(w[:, 0:KD * cols], weights).then_inc(filled, 16)

        @block.tensor
        def _(pe):
            pe.wait_ge(filled, 16)
            for t in range(TT):
                for k in range(KD):
                    last = nc.tensor.matmul(mem.bank[t][:, 0:cols], source[:, k, t * P:(t + 1) * P],
                                            w[:, k * cols:(k + 1) * cols], start=(k == 0), stop=(k == KD - 1))
                last.then_inc(product, 1)

        @block.scalar
        def _(act):
            for t in range(TT):
                act.wait_ge(product, t + 1)
                nc.scalar.activation(out[:, t, 0:cols], mem.bank[t][:, 0:cols], ACT.Copy).then_inc(taken, 1)
            act.wait_ge(taken, TT)


def feed_forward(nc, mem, w_up, w_down, hidden_tiles, gate, first_out, on_vector):
    part = hidden_tiles // 2
    up_units = part // (2 if gate == "relu" else 1)
    with parts_of(nc, KD) as parts, parts_of(nc, part) as hidden:
        for half in range(2):
            linear(nc, mem, later_units(w_up, half * up_units), up_units, 2, KD, parts,
                   source=None if half else mem.h, gate=gate, result=hidden)
            linear(nc, mem, later_units(w_down, 0, slice(half * part * P, (half + 1) * part * P)), KD, 1, part, hidden,
                   first_out(half), on_vector=on_vector(half))


def conv_module(nc, mem, vec, u, y):
    half = CONV_WIDTH // 2
    with buffers(nc, padded=[P, CONV_T, SEQ + 2 * half], acc=[P, CONV_T, SEQ], sig=[P, CONV_T, SEQ],
                 squares=[P, CONV_T, SEQ], scale=[P, SEQ]) as (padded, acc, sig, squares, scale), phase(
            nc, "gate_ready", "conv_done", "mean_ready", "centred", "squares_ready", "var_ready",
            "root_ready", "normed", "dve_steps") as (
            block, gate_ready, conv_done, mean_ready, centred, squares_ready, var_ready,
            root_ready, normed, dve_steps):
        total, spread = mem.bank[0], mem.bank[1]

        @block.scalar
        def _(act):
            for c in range(CONV_T):
                nc.scalar.activation(sig[:, c, :], u[:, U_CG + c, :], ACT.Sigmoid).then_inc(gate_ready, 1)
            for c in range(CONV_T):
                act.wait_ge(centred, c + 1)
                nc.scalar.activation(squares[:, c, :], acc[:, c, :], ACT.Square).then_inc(squares_ready, 1)
            act.wait_ge(var_ready, 1)
            nc.scalar.activation(scale[:, :], spread[:, :], ACT.Sqrt, bias=mem.eps[:, 1:2],
                                 scale=1.0 / CONV_CH).then_inc(root_ready, 1)
            for c in range(CONV_T):
                act.wait_ge(normed, c + 1)
                nc.scalar.activation(y[:, c, :], acc[:, c, :], ACT.Silu, scale=VEC1(vec, "ln_w", c),
                                     bias=VEC1(vec, "ln_b", c))

        @block.tensor
        def _(pe):
            for c in range(CONV_T):
                pe.wait_ge(conv_done, c + 1)
                last = nc.tensor.matmul(total[:, :], CONST(mem.const, "ones"), acc[:, c, :],
                                        start=(c == 0), stop=(c == CONV_T - 1))
            last.then_inc(mean_ready, 1)
            for c in range(CONV_T):
                pe.wait_ge(squares_ready, c + 1)
                last = nc.tensor.matmul(spread[:, :], CONST(mem.const, "ones"), squares[:, c, :],
                                        start=(c == 0), stop=(c == CONV_T - 1))
            last.then_inc(var_ready, 1)

        @block.vector
        def _(dve):
            steps = Steps(dve, dve_steps)
            steps.did(nc.vector.memset(padded[:, :, :], 0.0))
            steps.settle()
            for c in range(CONV_T):
                dve.wait_ge(gate_ready, c + 1)
                steps.did(nc.vector.tensor_tensor(padded[:, c, half:half + SEQ], u[:, U_CA + c, :], sig[:, c, :],
                                                  ALU.mult))
            steps.settle()
            for tap in range(CONV_WIDTH):
                for c in range(CONV_T):
                    window = padded[:, c, tap:tap + SEQ]
                    weight = VEC1(vec, "conv_w", c * CONV_WIDTH + tap)
                    if tap == 0:
                        last = nc.vector.tensor_scalar(acc[:, c, :], window, weight, VEC1(vec, "conv_b", c),
                                                       ALU.mult, ALU.add)
                    else:
                        if tap < CONV_WIDTH - 1:
                            dve.wait_ge(dve_steps, steps.count[dve_steps] - CONV_T + 1)
                        else:
                            steps.settle()
                        last = nc.vector.scalar_tensor_tensor(out=acc[:, c, :], in0=window, scalar=weight,
                                                              in1=acc[:, c, :], op0=ALU.mult, op1=ALU.add)
                    steps.did(last, conv_done if tap == CONV_WIDTH - 1 else None)
            dve.wait_ge(mean_ready, 1)
            steps.settle()
            for c in range(CONV_T):
                steps.did(nc.vector.scalar_tensor_tensor(out=acc[:, c, :], in0=total[:, :], scalar=-1.0 / CONV_CH,
                                                         in1=acc[:, c, :], op0=ALU.mult, op1=ALU.add), centred)
            dve.wait_ge(root_ready, 1)
            steps.did(nc.vector.reciprocal(scale[:, :], scale[:, :]))
            steps.settle()
            dve.wait_ge(squares_ready, CONV_T)
            for c in range(CONV_T):
                steps.did(nc.vector.tensor_tensor(acc[:, c, :], acc[:, c, :], scale[:, :], ALU.mult), normed)
            steps.settle()


def diff_lambda(nc, mem, lam_rows, coef):
    with buffers(nc, prod=[P, 2, DIFF_DIM], dots=[P, 4]) as (prod, dots), phase(
            nc, "dots_ready", "exps_ready", "dve_steps") as (block, dots_ready, exps_ready, dve_steps):
        @block.vector
        def _(dve):
            steps = Steps(dve, dve_steps)
            for m in range(2):
                steps.did(nc.vector.tensor_tensor(prod[:, m, :], lam_rows[:, 2 * m * DIFF_DIM:(2 * m + 1) * DIFF_DIM],
                                                  lam_rows[:, (2 * m + 1) * DIFF_DIM:(2 * m + 2) * DIFF_DIM], ALU.mult))
            steps.settle()
            steps.did(nc.vector.reduce_sum(dots[:, 0:2], prod[:, :, :], AX_X), dots_ready)
            steps.did(nc.vector.memset(coef[:, 0:1], 1.0))
            dve.wait_ge(exps_ready, 1)
            steps.did(nc.vector.tensor_tensor(dots[:, 0:1], dots[:, 3:4], dots[:, 2:3], ALU.subtract))
            steps.settle()
            steps.did(nc.vector.tensor_tensor(coef[:, 1:2], dots[:, 0:1], lam_rows[:, 4 * DIFF_DIM:4 * DIFF_DIM + 1],
                                              ALU.subtract))
            steps.settle()

        @block.scalar
        def _(act):
            act.wait_ge(dots_ready, 1)
            nc.scalar.activation(dots[:, 2:4], dots[:, 0:2], ACT.Exp).then_inc(exps_ready, 1)


def diff_attention(nc, mem, vec, lam_rows, distances, u, tm, y):
    first_tile = CONV_T
    units = [(h, t) for h in range(2) for t in range(TT)]
    with buffers(nc, coef=[P, 2], dist=[P, TT, SEQ]) as (coef, dist):
        load(nc, (dist[:, :, :], distances))
        diff_lambda(nc, mem, lam_rows, coef)
        with nc.Fori(0, PAIRS1) as j, buffers(
                nc, q=[P, SEQ], k=[P, SEQ], v=[P, TT, P], slope=[P, 2], scores=[P, 4, SEQ], tops=[P, 16],
                sums=[P, 16], inv=[P, 16], mixed=[P, 2, SEQ], turned=[P, 2, SEQ], heads=[P, SEQ],
                squares=[P, SEQ], scale=[P, SEQ], gain=[P, 1]) as (
                q, k, v, slope, scores, tops, sums, inv, mixed, turned, heads, squares, scale, gain), phase(
                nc, "staged", "dve_staged", "score", "topped", "exped", "mixed_ready", "turn", "turned_ready", "applied",
                "heads_taken", "squared", "summed", "rooted", "dve_steps", "act_steps") as (
                block, staged, dve_staged, score, topped, exped, mixed_ready, turn, turned_ready, applied,
                heads_taken, squared, summed, rooted, dve_steps, act_steps):
            out_bank, sum_bank = mem.bank[6], mem.bank[7]

            @block.scalar
            def _(act):
                nc.scalar.activation(q[:, :], tile_at(u, j + U_DQ), ACT.Copy, scale=DIFF_DIM ** -0.5).then_inc(staged, 1)
                nc.scalar.activation(k[:, :], tile_at(u, j + U_DK), ACT.Copy).then_inc(staged, 1)

                def turned_copy(n):
                    act.wait_ge(turn, n + 1)
                    if n >= 2:
                        act.wait_ge(applied, n - 1)
                    nc.scalar.activation(turned[:, n % 2, :], mem.bank[4 + n % 2][:, :], ACT.Copy) \
                        .then_inc(turned_ready, 1)

                for n in range(len(units)):
                    for m in range(2):
                        i = 2 * n + m
                        act.wait_ge(topped, n + 1)
                        nc.scalar.activation(scores[:, i % 4, :], scores[:, i % 4, :], ACT.Exp, bias=tops[:, i:i + 1],
                                             accum_out=sums[:, i:i + 1]).then_inc(exped, 1)
                    if n >= 1:
                        turned_copy(n - 1)
                turned_copy(len(units) - 1)
                act.wait_ge(heads_taken, 1)
                nc.scalar.activation(squares[:, :], heads[:, :], ACT.Square).then_inc(squared, 1)
                act.wait_ge(summed, 1)
                nc.scalar.activation(scale[:, :], sum_bank[:, :], ACT.Sqrt, bias=mem.eps[:, 1:2],
                                     scale=1.0 / HEAD).then_inc(rooted, 1)

            @block.tensor
            def _(pe):
                pe.wait_ge(staged, 2)
                pe.wait_ge(dve_staged, 1)

                def scored(n):
                    h, t = units[n]
                    for m in range(2):
                        i = 2 * n + m
                        if i >= 4:
                            pe.wait_ge(topped, (i - 4) // 2 + 1)
                        lanes = slice(DIFF_DIM * (2 * h + m), DIFF_DIM * (2 * h + m + 1))
                        nc.tensor.matmul(mem.bank[i % 4][:, :], q[lanes, t * P:(t + 1) * P], k[lanes, :],
                                         start=True, stop=True).then_inc(score, 1)

                def transposed(n):
                    pe.wait_ge(mixed_ready, n + 1)
                    if n >= 2:
                        pe.wait_ge(turned_ready, n - 1)
                    for b in range(TT):
                        last = nc.tensor.transpose(mem.bank[4 + n % 2][:, b * P:(b + 1) * P],
                                                   mixed[:, n % 2, b * P:(b + 1) * P], CONST(mem.const, "ident"))
                    last.then_inc(turn, 1)

                def apply(n):
                    h, t = units[n]
                    pe.wait_ge(turned_ready, n + 1)
                    for b in range(TT):
                        last = nc.tensor.matmul(out_bank[h * HEAD:(h + 1) * HEAD, t * P:(t + 1) * P],
                                                v[:, b, h * HEAD:(h + 1) * HEAD], turned[:, n % 2, b * P:(b + 1) * P],
                                                start=(b == 0), stop=(b == TT - 1))
                    last.then_inc(applied, 1)

                scored(0)
                scored(1)
                for n in range(len(units)):
                    if n + 2 < len(units):
                        scored(n + 2)
                    transposed(n)
                    if n >= 1:
                        apply(n - 1)
                apply(len(units) - 1)
                pe.wait_ge(squared, 1)
                nc.tensor.matmul(sum_bank[:, :], CONST(mem.const, "pair_ones"), squares[:, :], start=True,
                                 stop=True).then_inc(summed, 1)

            @block.vector
            def _(dve):
                steps = Steps(dve, dve_steps)
                steps.did(nc.vector.tensor_copy(v[:, :, :], tm[:, :, bass.ds(j * P, P)]), dve_staged)
                steps.did(nc.vector.tensor_copy(slope[:, :], CONST(mem.const, "neg_slopes")[:, bass.ds(j * 2, 2)]), dve_staged)
                steps.did(nc.vector.tensor_tensor(gain[:, :], VEC1(vec, "subln"),
                                                  lam_rows[:, 4 * DIFF_DIM + 1:4 * DIFF_DIM + 2], ALU.mult), dve_staged)
                steps.settle()

                def biased(n):
                    h, t = units[n]
                    for m in range(2):
                        i = 2 * n + m
                        dve.wait_ge(score, i + 1)
                        if n >= 2:
                            dve.wait_ge(mixed_ready, n - 1)
                        steps.did(nc.vector.scalar_tensor_tensor(
                            out=scores[:, i % 4, :], in0=dist[:, t, :], scalar=slope[:, h:h + 1],
                            in1=mem.bank[i % 4][:, :], op0=ALU.mult, op1=ALU.add))
                    steps.settle()
                    for m in range(2):
                        i = 2 * n + m
                        steps.did(nc.vector.reduce_max(inv[:, i:i + 1], scores[:, i % 4, :], AX_X))
                    steps.settle()
                    i = 2 * n
                    steps.did(nc.vector.tensor_scalar(tops[:, i:i + 2], inv[:, i:i + 2], -1.0, None, ALU.mult),
                              topped)
                    steps.settle()

                def mix(n):
                    i = 2 * n
                    dve.wait_ge(exped, i + 2)
                    steps.did(nc.vector.reciprocal(inv[:, i:i + 2], sums[:, i:i + 2]))
                    steps.settle()
                    steps.did(nc.vector.tensor_tensor(inv[:, i:i + 2], inv[:, i:i + 2], coef[:, :], ALU.mult))
                    steps.settle()
                    if n >= 2:
                        dve.wait_ge(turn, n - 1)
                    steps.did(nc.vector.tensor_scalar(mixed[:, n % 2, :], scores[:, i % 4, :], inv[:, i:i + 1], None,
                                                      ALU.mult))
                    steps.settle()
                    steps.did(nc.vector.scalar_tensor_tensor(
                        out=mixed[:, n % 2, :], in0=scores[:, (i + 1) % 4, :], scalar=inv[:, i + 1:i + 2],
                        in1=mixed[:, n % 2, :], op0=ALU.mult, op1=ALU.add), mixed_ready)

                for n in range(len(units)):
                    biased(n)
                    if n >= 1:
                        mix(n - 1)
                mix(len(units) - 1)
                dve.wait_ge(applied, len(units))
                steps.did(nc.vector.tensor_copy(heads[:, :], out_bank[:, :]), heads_taken)
                dve.wait_ge(rooted, 1)
                steps.did(nc.vector.reciprocal(scale[:, :], scale[:, :]))
                steps.settle()
                steps.did(nc.vector.scalar_tensor_tensor(out=tile_at(y, j + first_tile), in0=heads[:, :],
                                                         scalar=gain[:, 0:1], in1=scale[:, :], op0=ALU.mult,
                                                         op1=ALU.mult))
                steps.settle()


G_NEG, G_NBETA, G_BETA, G_BEXP, G_KDEC, G_LAST = range(6)
KINDS = 6
GH = 2 * DELTA_HEADS


def delta_gates(nc, mem, gates, tm, cols, rows):
    with buffers(nc, beta=[P, TT, GH], pre=[P, TT, GH], soft=[P, TT, GH], g=[P, TT, GH], rate=[P, GH],
                 run=[P, TT, GH], total=[P, TT, GH]) as (beta, pre, soft, g, rate, run, total), phase(
            nc, "beta_ready", "pre_ready", "soft_ready", "g_ready", "summed", "taken", "row_ready", "row_taken",
            "shifted", "exped", "act_steps", "dve_steps") as (
            block, beta_ready, pre_ready, soft_ready, g_ready, summed, taken, row_ready, row_taken,
            shifted, exped, act_steps, dve_steps):
        @block.scalar
        def _(act):
            steps = Steps(act, act_steps)
            nc.scalar.activation(beta[:, :, :], tm[:, :, DIFF_W:DIFF_W + GH], ACT.Sigmoid).then_inc(beta_ready, 1)
            steps.did(nc.scalar.activation(rate[:, :], gates[:, 0, :], ACT.Exp))
            act.wait_ge(pre_ready, 1)
            steps.did(nc.scalar.activation(soft[:, :, :], soft[:, :, :], ACT.Exp))
            steps.settle()
            nc.scalar.activation(soft[:, :, :], soft[:, :, :], ACT.Ln, bias=1.0).then_inc(soft_ready, 1)
            act.wait_ge(summed, 1)
            steps.did(nc.scalar.activation(run[:, :, :], mem.bank[0][:, 0:TT * GH], ACT.Copy), taken)
            steps.did(nc.scalar.activation(total[:, :, :], mem.bank[1][:, 0:TT * GH], ACT.Copy), taken)
            for n in range(GH):
                act.wait_ge(row_ready, n + 1)
                nc.scalar.activation(rows[:, n, :], mem.bank[2 + n % 2][:, :], ACT.Copy).then_inc(row_taken, 1)
            act.wait_ge(shifted, 1)
            nc.scalar.activation(cols[:, G_KDEC, :, :], cols[:, G_KDEC, :, :], ACT.Exp).then_inc(exped, 1)
            nc.scalar.activation(cols[:, G_LAST, :, :], total[:, :, :], ACT.Exp).then_inc(exped, 1)
            nc.scalar.activation(cols[:, G_BEXP, :, :], run[:, :, :], ACT.Exp).then_inc(exped, 1)

        @block.vector
        def _(dve):
            steps = Steps(dve, dve_steps)
            bias = gates[:, 1, :].unsqueeze(1).broadcast_to([P, TT, GH])
            steps.did(nc.vector.tensor_tensor(pre[:, :, :], tm[:, :, DIFF_W + GH:DIFF_W + 2 * GH], bias, ALU.add))
            steps.settle()
            steps.did(nc.vector.scalar_tensor_tensor(out=soft[:, :, :], in0=pre[:, :, :], scalar=-1.0,
                                                     in1=pre[:, :, :], op0=ALU.mult, op1=ALU.min), pre_ready)
            dve.wait_ge(soft_ready, 1)
            steps.did(nc.vector.scalar_tensor_tensor(out=pre[:, :, :], in0=pre[:, :, :], scalar=0.0,
                                                     in1=soft[:, :, :], op0=ALU.max, op1=ALU.add))
            steps.settle()
            dve.wait_ge(act_steps, 1)
            steps.did(nc.vector.scalar_tensor_tensor(
                out=g[:, :, :], in0=pre[:, :, :], scalar=-1.0, in1=rate[:, :].unsqueeze(1).broadcast_to([P, TT, GH]),
                op0=ALU.mult, op1=ALU.mult), g_ready)
            dve.wait_ge(beta_ready, 1)
            steps.did(nc.vector.tensor_scalar(cols[:, G_NBETA, :, :], beta[:, :, :], -1.0, None, ALU.mult))
            steps.did(nc.vector.tensor_copy(cols[:, G_BETA, :, :], beta[:, :, :]))
            dve.wait_ge(taken, 2)
            steps.did(nc.vector.tensor_scalar(cols[:, G_NEG, :, :], run[:, :, :], -1.0, None, ALU.mult))
            steps.did(nc.vector.tensor_tensor(cols[:, G_KDEC, :, :], total[:, :, :], run[:, :, :], ALU.subtract),
                      shifted)
            dve.wait_ge(exped, 3)
            steps.did(nc.vector.tensor_tensor(cols[:, G_BEXP, :, :], cols[:, G_BEXP, :, :], beta[:, :, :], ALU.mult))
            steps.settle()

        @block.tensor
        def _(pe):
            pe.wait_ge(g_ready, 1)
            run_sum, whole = mem.bank[0], mem.bank[1]
            half = DELTA_HEADS
            triangle = [CONST(mem.const, "upper_in"), CONST(mem.const, "lower_in")]
            for t in range(TT):
                nc.tensor.matmul(whole[:, t * GH:(t + 1) * GH], CONST(mem.const, "ones"), g[:, t, :],
                                 start=True, stop=True)
                for d in range(2):
                    last = nc.tensor.matmul(run_sum[:, t * GH + d * half:t * GH + (d + 1) * half], triangle[d],
                                            g[:, t, d * half:(d + 1) * half], start=True, stop=True)
            last.then_inc(summed, 1)
            for n in range(GH):
                if n >= 2:
                    pe.wait_ge(row_taken, n - 1)
                for t in range(TT):
                    last = nc.tensor.matmul(mem.bank[2 + n % 2][:, t * P:(t + 1) * P],
                                            g[:, t, n:n + 1].broadcast_to([P, P]), triangle[n // half],
                                            start=True, stop=True)
                last.then_inc(row_ready, 1)


def delta_prepare(nc, mem, vec, u, cols, rows, hp, b):
    with buffers(nc, conv=[P, 3, SEQ], taps=[P, 3 * SHORT_CONV], squares=[P, 2, SEQ], scale=[P, 2, SEQ],
                 kk=[P, 2, SEQ], kq=[P, 2, SEQ], decay=[P, 2, SEQ]) as (
            conv, taps, squares, scale, kk, kq, decay), phase(
            nc, "conv_done", "silued", "squared", "summed", "rooted", "normed", "turned", "turned_taken",
            "product", "product_taken", "bounded", "exped", "dve_steps", "act_steps") as (
            block, conv_done, silued, squared, summed, rooted, normed, turned, turned_taken,
            product, product_taken, bounded, exped, dve_steps, act_steps):
        streams = [(d, par) for d in range(2) for par in range(2)]

        @block.vector
        def _(dve):
            steps = Steps(dve, dve_steps)
            for s in range(3):
                at = VEC1.at["delta_conv"][0] + s * PAIRS1 * SHORT_CONV
                steps.did(nc.vector.tensor_copy(taps[:, s * SHORT_CONV:(s + 1) * SHORT_CONV],
                                                vec[:, bass.ds(hp * SHORT_CONV + at, SHORT_CONV)]))
            for d in range(2):
                steps.did(nc.vector.tensor_copy(
                    b.cols[:, :, d, :],
                    cols[:, :, :, :].rearrange("p k t h -> p (k t) h")[:, :, bass.ds(hp * 2 + d * DELTA_HEADS, 2)]))
            steps.settle()
            source = [U_GQ, U_GK, U_GV]
            x = [u[:, bass.ds(hp + source[s], 1), :] for s in range(3)]
            for s in range(3):
                steps.did(nc.vector.tensor_scalar(conv[:, s:s + 1, :], x[s], taps[:, 3 * s + 1:3 * s + 2], None,
                                                  ALU.mult))
            steps.settle()
            for s in range(3):
                steps.did(nc.vector.scalar_tensor_tensor(
                    out=conv[:, s:s + 1, 1:SEQ], in0=x[s][:, :, 0:SEQ - 1], scalar=taps[:, 3 * s:3 * s + 1],
                    in1=conv[:, s:s + 1, 1:SEQ], op0=ALU.mult, op1=ALU.add))
            steps.settle()
            for s in range(3):
                steps.did(nc.vector.scalar_tensor_tensor(
                    out=conv[:, s:s + 1, 0:SEQ - 1], in0=x[s][:, :, 1:SEQ], scalar=taps[:, 3 * s + 2:3 * s + 3],
                    in1=conv[:, s:s + 1, 0:SEQ - 1], op0=ALU.mult, op1=ALU.add), conv_done)
            for s in range(2):
                dve.wait_ge(rooted, s + 1)
                steps.did(nc.vector.reciprocal(scale[:, s, :], scale[:, s, :]))
            steps.settle()
            dve.wait_ge(silued, 3)
            steps.did(nc.vector.scalar_tensor_tensor(out=b.q[:, :], in0=conv[:, 0, :], scalar=HEAD ** -0.5,
                                                     in1=scale[:, 0, :], op0=ALU.mult, op1=ALU.mult), normed)
            steps.did(nc.vector.tensor_tensor(b.k[:, :], conv[:, 1, :], scale[:, 1, :], ALU.mult), normed)

            def bound(n):
                d, par = streams[n]
                row = rows[:, bass.ds(hp * 2 + d * DELTA_HEADS + par, 1), :].rearrange("p a n -> p (a n)")
                masks = [("lower_strict_max", ALU.max), ("upper_in_min", ALU.min)] if d == 0 else \
                    [("upper_strict_max", ALU.max), ("lower_in_min", ALU.min)]
                for e in range(2):
                    for t in range(TT):
                        steps.did(nc.vector.scalar_tensor_tensor(
                            out=decay[:, e, t * P:(t + 1) * P], in0=row[:, t * P:(t + 1) * P],
                            scalar=b.cols[:, G_NEG * TT + t, d, par:par + 1], in1=CONST(mem.const, masks[e][0]),
                            op0=ALU.add, op1=masks[e][1]), bounded)

            for n, (d, par) in enumerate(streams):
                bound(n)
                dve.wait_ge(product_taken, 4)
                dve.wait_ge(exped, 2 * n + 2)
                for t in range(TT):
                    steps.did(nc.vector.scalar_tensor_tensor(
                        out=b.neg[:, n, t * P:(t + 1) * P], in0=kk[:, par, t * P:(t + 1) * P],
                        scalar=b.cols[:, G_NBETA * TT + t, d, par:par + 1], in1=decay[:, 0, t * P:(t + 1) * P],
                        op0=ALU.mult, op1=ALU.mult))
                steps.did(nc.vector.tensor_tensor(b.seen[:, n, :], kq[:, par, :], decay[:, 1, :], ALU.mult))
                steps.settle()

        @block.scalar
        def _(act):
            for s in range(3):
                act.wait_ge(conv_done, s + 1)
                nc.scalar.activation(conv[:, s, :], conv[:, s, :], ACT.Silu).then_inc(silued, 1)
            for s in range(2):
                act.wait_ge(silued, s + 1)
                nc.scalar.activation(squares[:, s, :], conv[:, s, :], ACT.Square).then_inc(squared, 1)
            for s in range(2):
                act.wait_ge(summed, s + 1)
                nc.scalar.activation(scale[:, s, :], mem.bank[s][:, :], ACT.Sqrt, bias=mem.eps[:, 0:1]) \
                    .then_inc(rooted, 1)
            for s, to in ((0, b.v_rows), (1, b.k_rows)):
                act.wait_ge(turned, s + 1)
                nc.scalar.activation(to[:, :, :].rearrange("p t n -> p (t n)"), mem.bank[2 + s][:, :], ACT.Copy) \
                    .then_inc(turned_taken, 1)
            for n in range(4):
                act.wait_ge(product, n + 1)
                to = kk if n < 2 else kq
                nc.scalar.activation(to[:, n % 2, :], mem.bank[4 + n][:, :], ACT.Copy).then_inc(product_taken, 1)
            for n in range(4):
                for e in range(2):
                    act.wait_ge(bounded, 2 * TT * n + TT * (e + 1))
                    nc.scalar.activation(decay[:, e, :], decay[:, e, :], ACT.Exp,
                                         scale=-1.0 if e == 0 else 1.0).then_inc(exped, 1)

        @block.tensor
        def _(pe):
            for s in range(2):
                pe.wait_ge(squared, s + 1)
                nc.tensor.matmul(mem.bank[s][:, :], CONST(mem.const, "pair_ones"), squares[:, s, :],
                                 start=True, stop=True).then_inc(summed, 1)
            pe.wait_ge(silued, 3)
            for t in range(TT):
                last = nc.tensor.transpose(mem.bank[2][:, t * P:(t + 1) * P], conv[:, 2, t * P:(t + 1) * P],
                                           CONST(mem.const, "ident"))
            last.then_inc(turned, 1)
            pe.wait_ge(normed, 2)
            for t in range(TT):
                last = nc.tensor.transpose(mem.bank[3][:, t * P:(t + 1) * P], b.k[:, t * P:(t + 1) * P],
                                           CONST(mem.const, "ident"))
            last.then_inc(turned, 1)
            for n in range(4):
                lanes = slice((n % 2) * HEAD, (n % 2 + 1) * HEAD)
                for t in range(TT):
                    right = (b.k if n < 2 else b.q)[lanes, t * P:(t + 1) * P]
                    last = nc.tensor.matmul(mem.bank[4 + n][:, t * P:(t + 1) * P], b.k[lanes, t * P:(t + 1) * P],
                                            right, start=True, stop=True)
                last.then_inc(product, 1)


def invert(nc, mem, neg, turned, upper):
    count = len(upper)

    def of_side(columns, level, n):
        return columns.rearrange("p (g h b) -> p g h b", h=2, b=2 ** level)[:, :, 0 if upper[n] else 1, :]

    def chunks(x):
        return x.rearrange("p (t c) -> p t c", t=TT)

    with buffers(nc, joint=[P, count, SEQ]) as (joint,), phase(
            nc, *[f"{w}{n}" for n in range(count) for w in ("flipped", "joined", "grown", "added")]) as (block, *sems):
        flipped, joined, grown, added = sems[0::4], sems[1::4], sems[2::4], sems[3::4]
        slices = [slice(t * P, (t + 1) * P) for t in range(TT)]

        @block.vector
        def _(dve):
            def join(n, l):
                mask = mem.levels[:, upper[n], l, :].unsqueeze(1).broadcast_to([P, TT, P])
                nc.vector.tensor_tensor(chunks(joint[:, n, :]), chunks(turned[:, n, :]), mask, ALU.mult) \
                    .then_inc(joined[n], 1)

            for n in range(count):
                dve.wait_ge(flipped[n], 1)
                nc.vector.tensor_tensor(chunks(turned[:, n, :]), chunks(mem.bank[2 * n][:, :]),
                                        CONST(mem.const, "ident").unsqueeze(1).broadcast_to([P, TT, P]), ALU.add) \
                    .then_inc(added[n], 1)
            for n in range(count):
                dve.wait_ge(added[n], 1)
                join(n, 0)
            for l in range(LEVELS):
                for n in range(count):
                    last_level = l == LEVELS - 1
                    dve.wait_ge(grown[n], l + 1)
                    dve.wait_ge(joined[n], l + 1)
                    at = of_side(turned[:, n, :], l, n)
                    nc.vector.tensor_tensor(at, at, of_side(mem.bank[2 * n][:, :], l, n), ALU.add).then_inc(added[n], 1)
                    if not last_level:
                        nc.vector.tensor_tensor(neg[:, n, :], neg[:, n, :], mem.bank[2 * n + 1][:, :], ALU.add) \
                            .then_inc(added[n], 1)
                        dve.wait_ge(added[n], 2 * l + 2)
                        join(n, l + 1)

        @block.tensor
        def _(pe):
            for n in range(count):
                for c in slices:
                    last = nc.tensor.matmul(mem.bank[2 * n][:, c], neg[:, n, c], CONST(mem.const, "ident"),
                                            start=True, stop=True)
                last.then_inc(flipped[n], 1)
            for l in range(LEVELS):
                for n in range(count):
                    pe.wait_ge(joined[n], l + 1)
                    pe.wait_ge(added[n], 2 * l + 1)
                    if l < LEVELS - 1:
                        for c in slices:
                            nc.tensor.matmul(mem.bank[2 * n + 1][:, c], joint[:, n, c], neg[:, n, c],
                                             start=True, stop=True)
                    for c in slices:
                        last = nc.tensor.matmul(of_side(mem.bank[2 * n][:, c], l, n), neg[:, n, c],
                                                of_side(joint[:, n, c], l, n), start=True, stop=True)
                    last.then_inc(grown[n], 1)


def delta_scan(nc, mem, vec, u, rows, y, hp, b):
    first_tile = CONV_T + PAIRS1
    with buffers(nc, w=[P, 2, SEQ], qg=[P, 2, SEQ], last=[P, 2, TT], state=[P, 2, HEAD], fresh=[P, 2, 2, P],
                 o=[P, 2, SEQ], squares=[P, SEQ], scale=[P, SEQ], gate=[P, SEQ]) as (
            w, qg, last_decay, state, fresh, o, squares, scale, gate), phase(
            nc, "scaled", "solved", "solved_taken", "rows_exped", "queries", "passed0", "passed1", "fresh0", "fresh1",
            "out0", "out1", "grown0", "grown1", "state0", "state1", "out_taken0", "out_taken1", "summed_dirs",
            "squared", "summed", "rooted", "gate_ready", "dve_steps") as (
            block, scaled, solved, solved_taken, rows_exped, queries, passed0, passed1, fresh0, fresh1,
            out0, out1, grown0, grown1, state0, state1, out_taken0, out_taken1, summed_dirs,
            squared, summed, rooted, gate_ready, dve_steps):
        streams = [(d, par) for d in range(2) for par in range(2)]
        vb, kb, kd, u0 = b.vb, b.kb, b.kd, b.u0
        passed, fresh_ready, out_ready = (passed0, passed1), (fresh0, fresh1), (out0, out1)
        grown, state_ready, out_taken = (grown0, grown1), (state0, state1), (out_taken0, out_taken1)
        lanes = [slice(0, HEAD), slice(HEAD, 2 * HEAD)]
        chunk = [lambda s: s, lambda s: TT - 1 - s]

        @block.vector
        def _(dve):
            steps = Steps(dve, dve_steps)
            for n, (d, par) in enumerate(streams):
                for kind, to, rows_of in ((G_BETA, vb, b.v_rows), (G_BEXP, kb, b.k_rows), (G_KDEC, kd, b.k_rows)):
                    by = b.cols[:, kind * TT:(kind + 1) * TT, d, par:par + 1].broadcast_to([P, TT, HEAD])
                    steps.did(nc.vector.tensor_tensor(to[:, n, :, :], rows_of[:, :, lanes[par]], by, ALU.mult), scaled)
                steps.did(nc.vector.tensor_copy(last_decay[lanes[par], d, :],
                                                b.cols[lanes[par], G_LAST * TT:(G_LAST + 1) * TT, d, par]))
            for d in range(2):
                dve.wait_ge(rows_exped, 2 * d + 2)
                steps.did(nc.vector.tensor_tensor(qg[:, d, :], qg[:, d, :], b.q[:, :], ALU.mult), queries)
            steps.settle()
            for s in range(TT):
                for d in range(2):
                    t = chunk[d](s)
                    if s == 0:
                        dve.wait_ge(solved_taken, 2 * d + 2)
                    if s >= 2:
                        dve.wait_ge(out_ready[d], s - 1)
                    for par in range(2):
                        e = slice(par * HEAD, (par + 1) * HEAD)
                        if s == 0:
                            steps.did(nc.vector.tensor_copy(fresh[:, d, s % 2, e], u0[:, d, t, e]), fresh_ready[d])
                        else:
                            dve.wait_ge(passed[d], 2 * s - 1 + par)
                            steps.did(nc.vector.tensor_tensor(fresh[:, d, s % 2, e], u0[:, d, t, e],
                                                              mem.bank[d + 2 * par][:, 0:HEAD], ALU.subtract),
                                      fresh_ready[d])
                for d in range(2):
                    if s == TT - 1:
                        break
                    t = chunk[d](s)
                    dve.wait_ge(grown[d], s + 1)
                    if s == 0:
                        steps.did(nc.vector.tensor_copy(state[:, d, :], mem.bank[4 + d][:, 0:HEAD]), state_ready[d])
                    else:
                        dve.wait_ge(state_ready[d], s)
                        dve.wait_ge(out_ready[d], s + 1)
                        steps.did(nc.vector.scalar_tensor_tensor(
                            out=state[:, d, :], in0=state[:, d, :], scalar=last_decay[:, d, t:t + 1],
                            in1=mem.bank[4 + d][:, 0:HEAD], op0=ALU.mult, op1=ALU.add), state_ready[d])
            for d in range(2):
                dve.wait_ge(out_taken[d], TT)
            steps.did(nc.vector.tensor_tensor(o[:, 0, :], o[:, 0, :], o[:, 1, :], ALU.add), summed_dirs)
            dve.wait_ge(rooted, 1)
            steps.did(nc.vector.reciprocal(scale[:, :], scale[:, :]))
            steps.settle()
            steps.did(nc.vector.scalar_tensor_tensor(out=scale[:, :], in0=o[:, 0, :], scalar=VEC1(vec, "delta_norm"),
                                                     in1=scale[:, :], op0=ALU.mult, op1=ALU.mult))
            steps.settle()
            dve.wait_ge(gate_ready, 1)
            steps.did(nc.vector.tensor_tensor(tile_at(y, hp + first_tile), scale[:, :], gate[:, :], ALU.mult))
            steps.settle()

        @block.tensor
        def _(pe):
            for d in range(2):
                pe.wait_ge(scaled, 6 * d + 6)
                for par in range(2):
                    n = 2 * d + par
                    for t in range(TT):
                        c = slice(t * P, (t + 1) * P)
                        last = nc.tensor.matmul(mem.bank[d][:, t * P + par * HEAD:t * P + (par + 1) * HEAD],
                                                b.turned[:, n, c], vb[:, n, t, :], start=True, stop=True)
                last.then_inc(solved, 1)
                for par in range(2):
                    n = 2 * d + par
                    for t in range(TT):
                        c = slice(t * P, (t + 1) * P)
                        last = nc.tensor.matmul(mem.bank[2 + d][lanes[par], c], kb[:, n, t, :], b.turned[:, n, c],
                                                start=True, stop=True)
                last.then_inc(solved, 1)
            pe.wait_ge(solved_taken, 4)
            pe.wait_ge(queries, 2)
            for s in range(TT):
                for d in range(2):
                    if s == 0:
                        continue
                    t = chunk[d](s)
                    pe.wait_ge(state_ready[d], s)
                    pe.wait_ge(fresh_ready[d], 2 * s)
                    for par in range(2):
                        nc.tensor.matmul(mem.bank[d + 2 * par][:, 0:HEAD], w[lanes[par], d, t * P:(t + 1) * P],
                                         state[lanes[par], d, :], start=True, stop=True).then_inc(passed[d], 1)
                for d in range(2):
                    t = chunk[d](s)
                    c = slice(t * P, (t + 1) * P)
                    pe.wait_ge(fresh_ready[d], 2 * s + 2)
                    if s >= 1:
                        pe.wait_ge(state_ready[d], s)
                    for par in range(2):
                        n = 2 * d + par
                        last = nc.tensor.matmul(mem.bank[4 + d][lanes[par], 0:HEAD], kd[:, n, t, :],
                                                fresh[:, d, s % 2, par * HEAD:(par + 1) * HEAD], start=True, stop=True)
                    last.then_inc(grown[d], 1)
                    if s >= 1:
                        pe.wait_ge(out_taken[d], s)
                    for par in range(2):
                        n = 2 * d + par
                        to = mem.bank[6 + d][lanes[par], 0:P]
                        if s >= 1:
                            nc.tensor.matmul(to, state[lanes[par], d, :], qg[lanes[par], d, c], start=True, stop=False)
                        last = nc.tensor.matmul(to, fresh[:, d, s % 2, par * HEAD:(par + 1) * HEAD], b.seen[:, n, c],
                                                start=(s == 0), stop=True)
                    last.then_inc(out_ready[d], 1)
            pe.wait_ge(squared, 1)
            nc.tensor.matmul(mem.bank[0][:, :], CONST(mem.const, "pair_ones"), squares[:, :], start=True,
                             stop=True).then_inc(summed, 1)

        @block.scalar
        def _(act):
            for d, par in streams:
                row = rows[lanes[par], bass.ds(hp * 2 + d * DELTA_HEADS + par, 1), :].rearrange("p a n -> p (a n)")
                nc.scalar.activation(qg[lanes[par], d, :], row, ACT.Exp).then_inc(rows_exped, 1)
            for d in range(2):
                act.wait_ge(solved, 2 * d + 2)
                nc.scalar.activation(u0[:, d, :, :].rearrange("p t n -> p (t n)"), mem.bank[d][:, :], ACT.Copy) \
                    .then_inc(solved_taken, 1)
                nc.scalar.activation(w[:, d, :], mem.bank[2 + d][:, :], ACT.Copy).then_inc(solved_taken, 1)
            for s in range(TT):
                for d in range(2):
                    t = chunk[d](s)
                    act.wait_ge(out_ready[d], s + 1)
                    nc.scalar.activation(o[:, d, t * P:(t + 1) * P], mem.bank[6 + d][:, 0:P], ACT.Copy) \
                        .then_inc(out_taken[d], 1)
            act.wait_ge(summed_dirs, 1)
            nc.scalar.activation(squares[:, :], o[:, 0, :], ACT.Square).then_inc(squared, 1)
            nc.scalar.activation(gate[:, :], tile_at(u, hp + U_GZ), ACT.Silu).then_inc(gate_ready, 1)
            act.wait_ge(summed, 1)
            nc.scalar.activation(scale[:, :], mem.bank[0][:, :], ACT.Sqrt, bias=mem.eps[:, 0:1],
                                 scale=1.0 / HEAD).then_inc(rooted, 1)


class PairBuffers:

    def __init__(self, mem, q, k, k_rows, v_rows, cols, more):
        self.q, self.k, self.k_rows, self.v_rows, self.cols = q, k, k_rows, v_rows, cols
        self.turned = mem.h[:, 4:8, :]
        ring = mem.ring[:, :, :].rearrange("p s n -> p (s n)")
        size = 4 * SEQ
        self.neg = ring[:, 0:size].rearrange("p (n s) -> p n s", n=4)
        self.seen = ring[:, size:2 * size].rearrange("p (n s) -> p n s", n=4)
        rows = [more[:, i * 2 * SEQ:(i + 1) * 2 * SEQ] for i in range(4)]
        self.vb, self.kb, self.kd = [r.rearrange("p (n t e) -> p n t e", n=4, t=TT) for r in rows[:3]]
        self.u0 = rows[3].rearrange("p (d t e) -> p d t e", d=2, t=TT)


def delta_net(nc, mem, vec, gates, u, tm, y):
    with buffers(nc, cols=[P, KINDS, TT, GH], rows=[P, GH, SEQ]) as (cols, rows):
        delta_gates(nc, mem, gates, tm, cols, rows)
        with nc.Fori(0, PAIRS1) as hp, buffers(
                nc, q=[P, SEQ], k=[P, SEQ], k_rows=[P, TT, P], v_rows=[P, TT, P],
                pair_cols=[P, KINDS * TT, 2, 2], more=[P, 8 * SEQ]) as parts:
            b = PairBuffers(mem, *parts)
            delta_prepare(nc, mem, vec, u, cols, rows, hp, b)
            invert(nc, mem, b.neg, b.turned, [0, 0, 1, 1])
            delta_scan(nc, mem, vec, u, rows, y, hp, b)


def spatial_gate(nc, mem, a, u, pv, y):
    groups = [slice(g * P, (g + 1) * P) for g in range(A_GROUPS)]
    n_stats = TT * A_GROUPS
    with buffers(nc, mix=[P, A_GROUPS, P], bias=[P, A_GROUPS, P], ln=[P, 2, A_WIDTH], stats=[P, n_stats, 6],
                 moments=[P, n_stats, 2], root=[P, n_stats], shift=[P, n_stats]) as (
            mix, bias, ln, stats, moments, root, shift), phase(
            nc, "loaded", "gelued", "u_ready", "spread", "rooted", "normed", "mixed", "dve_steps") as (
            block, loaded, gelued, u_ready, spread, rooted, normed, mixed, dve_steps):
        @block.sync
        def _(sp):
            sp.dma_start(mix[:, :, :], a["sgu_w"]).then_inc(loaded, 16)
            sp.dma_start(bias[:, :, :], a["sgu_b"].partition_broadcast(P)).then_inc(loaded, 16)
            sp.dma_start(ln[:, :, :], a["sgu_ln"].partition_broadcast(P)).then_inc(loaded, 16)

        @block.scalar
        def _(act):
            for t in range(TT):
                nc.scalar.activation(pv[:, t, :], pv[:, t, :], ACT.Gelu_apprx_tanh).then_inc(gelued, 1)
            for g in range(A_GROUPS):
                nc.scalar.activation(u[:, E_U + g, :], u[:, E_U + g, :], ACT.Gelu_apprx_tanh).then_inc(u_ready, 1)
            act.wait_ge(spread, 1)
            nc.scalar.activation(root[:, :], moments[:, :, 1], ACT.Sqrt, bias=mem.eps[:, 1:2]).then_inc(rooted, 1)

        @block.vector
        def _(dve):
            steps = Steps(dve, dve_steps)
            dve.wait_ge(loaded, 48)
            steps.did(nc.vector.tensor_tensor(
                mix[:, :, :], mix[:, :, :],
                CONST(mem.const, "upper_in").unsqueeze(1).broadcast_to([P, A_GROUPS, P]), ALU.mult))
            for t in range(TT):
                dve.wait_ge(gelued, t + 1)
                for g in range(A_GROUPS):
                    steps.did(nc.vector.bn_stats(stats[:, t * A_GROUPS + g, :], pv[:, t, groups[g]]))
            steps.settle()
            for n in range(n_stats):
                steps.did(nc.vector.bn_aggr(moments[:, n, :], stats[:, n, :]), spread if n == n_stats - 1 else None)
            dve.wait_ge(rooted, 1)
            steps.did(nc.vector.reciprocal(root[:, :], root[:, :]))
            steps.settle()
            steps.did(nc.vector.scalar_tensor_tensor(out=shift[:, :], in0=moments[:, :, 0], scalar=-1.0,
                                                     in1=root[:, :], op0=ALU.mult, op1=ALU.mult))
            steps.settle()
            for t in range(TT):
                for g in range(A_GROUPS):
                    n = t * A_GROUPS + g
                    steps.did(nc.vector.tensor_scalar(pv[:, t, groups[g]], pv[:, t, groups[g]], root[:, n:n + 1],
                                                      shift[:, n:n + 1], ALU.mult, ALU.add))
            steps.settle()
            for i, op in ((0, ALU.mult), (1, ALU.add)):
                steps.did(nc.vector.tensor_tensor(pv[:, :, :], pv[:, :, :],
                                                  ln[:, i, :].unsqueeze(1).broadcast_to([P, TT, A_WIDTH]), op),
                          normed if i else None)
                steps.settle()
            dve.wait_ge(u_ready, A_GROUPS)
            for g in range(A_GROUPS):
                dve.wait_ge(mixed, g + 1)
                steps.did(nc.vector.tensor_tensor(
                    y[:, g, :].rearrange("p (c t) -> p c t", c=TT),
                    mem.bank[g][:, :].rearrange("p (c t) -> p c t", c=TT),
                    bias[:, g, :].unsqueeze(1).broadcast_to([P, TT, P]), ALU.add))
            steps.settle()
            for g in range(A_GROUPS):
                steps.did(nc.vector.tensor_tensor(y[:, g, :], y[:, g, :], u[:, E_U + g, :], ALU.mult))
            steps.settle()

        @block.tensor
        def _(pe):
            pe.wait_ge(normed, 1)
            for g in range(A_GROUPS):
                for c in range(TT):
                    last = nc.tensor.matmul(mem.bank[g][:, c * P:(c + 1) * P], pv[:, c, groups[g]], mix[:, g, :],
                                            start=True, stop=True)
                last.then_inc(mixed, 1)


def token_shift(nc, mem, vec, u):
    n_tiles, batch = UTE - E_R, 7
    with phase(nc, "dve_steps") as (block, dve_steps):
        @block.vector
        def _(dve):
            steps = Steps(dve, dve_steps)
            for first in range(0, n_tiles, batch):
                part = u[:, E_R + first:E_R + first + batch, :]
                change = mem.h[:, 0:batch, :]
                steps.did(nc.vector.tensor_tensor(change[:, :, 1:SEQ], part[:, :, 0:SEQ - 1], part[:, :, 1:SEQ],
                                                  ALU.subtract))
                steps.did(nc.vector.tensor_scalar(change[:, :, 0:1], part[:, :, 0:1], -1.0, None, ALU.mult))
                steps.settle()
                for i in range(batch):
                    steps.did(nc.vector.scalar_tensor_tensor(
                        out=part[:, i, :], in0=change[:, i, :], scalar=VECE(vec, "mu", first + i), in1=part[:, i, :],
                        op0=ALU.mult, op1=ALU.add))
                steps.settle()


def rwkv_gates(nc, mem, a, vec, u, decay, rate, gate):
    with buffers(nc, wa2=[P, B_WIDTH], g2=[P, B_WIDTH]) as (wa2, g2), phase(
            nc, "loaded", "inner", "product", "taken", "dve_steps") as (block, loaded, inner, product, taken,
                                                                        dve_steps):
        @block.sync
        def _(sp):
            sp.dma_start(wa2[:, :], a["wa2"]).then_inc(loaded, 16)
            sp.dma_start(g2[:, :], a["g2"]).then_inc(loaded, 16)

        @block.scalar
        def _(act):
            nc.scalar.activation(u[0:LORA, E_WA, :], u[0:LORA, E_WA, :], ACT.Tanh).then_inc(inner, 1)
            nc.scalar.activation(u[:, E_G, :], u[:, E_G, :], ACT.Sigmoid).then_inc(inner, 1)
            for j in range(RW_PAIRS):
                act.wait_ge(product, 3 * j + 3)
                b = 3 * (j % 2)
                nc.scalar.activation(decay[:, j, :], mem.bank[b][:, :], ACT.Sigmoid, bias=VECE(vec, "w0", j)) \
                    .then_inc(taken, 1)
                nc.scalar.activation(rate[:, j, :], mem.bank[b + 1][:, :], ACT.Sigmoid, bias=VECE(vec, "a0", j)) \
                    .then_inc(taken, 1)
                nc.scalar.activation(gate[:, j, :], mem.bank[b + 2][:, :], ACT.Copy).then_inc(taken, 1)

        @block.tensor
        def _(pe):
            pe.wait_ge(loaded, 32)
            pe.wait_ge(inner, 2)
            for j in range(RW_PAIRS):
                if j >= 2:
                    pe.wait_ge(taken, 3 * (j - 1))
                b, c = 3 * (j % 2), slice(j * P, (j + 1) * P)
                nc.tensor.matmul(mem.bank[b][:, :], wa2[0:LORA, c], u[0:LORA, E_WA, :], start=True, stop=True) \
                    .then_inc(product, 1)
                nc.tensor.matmul(mem.bank[b + 1][:, :], wa2[LORA:P, c], u[LORA:P, E_WA, :], start=True, stop=True) \
                    .then_inc(product, 1)
                nc.tensor.matmul(mem.bank[b + 2][:, :], g2[:, c], u[:, E_G, :], start=True, stop=True) \
                    .then_inc(product, 1)

        @block.vector
        def _(dve):
            dve.wait_ge(taken, 3 * RW_PAIRS)
            nc.vector.tensor_scalar(decay[:, :, :], decay[:, :, :], -math.exp(-0.5), None, ALU.mult)


class TimeMix:

    def __init__(self, mem, v, gate, bonus, factor, par, more):
        self.v, self.gate, self.bonus, self.factor, self.par = v, gate, bonus, factor, par
        ring = mem.ring[:, :, :].rearrange("p s n -> p (s n)")
        parts = [ring[:, i * SEQ:(i + 1) * SEQ] for i in range(8)]
        self.rho, self.alpha, self.beta, self.kappa = parts[0:4]
        self.alpha_rows, self.beta_rows, self.kappa_rows, self.v_rows = [
            x.rearrange("p (t n) -> p t n", t=TT) for x in parts[4:8]]
        pairs = [more[:, 2 * i:2 * i + 2, :] for i in range(4)]
        self.neg, self.key_past, self.key_seen, self.rate_seen = pairs
        self.turned = mem.h[:, 2:4, :]


VEC_J = ["k_k", "k_a", "r_k", "gn_g", "gn_b"]


def rwkv_prepare(nc, mem, vec, u, decay, rate, gate, j, b):
    mid = P // 2 - 1
    with buffers(nc, r=[P, SEQ], k=[P, SEQ], kk=[P, SEQ], bk=[P, SEQ], run=[P, SEQ], about=[P, SEQ],
                 up=[P, SEQ], down=[P, SEQ], before=[P, SEQ], squares=[P, SEQ], scale=[P, SEQ]) as (
            r, k, kk, bk, run, about, up, down, before, squares, scale), phase(
            nc, "kk_ready", "squared", "summed", "rooted", "about_ready", "before_ready", "ups", "factor_ready",
            "bonus_ready", "bonus_summed", "ready", "turned", "rows_taken", "product", "dve_steps") as (
            block, kk_ready, squared, summed, rooted, about_ready, before_ready, ups, factor_ready,
            bonus_ready, bonus_summed, ready, turned, rows_taken, product, dve_steps):
        by_chunk = lambda x: x.rearrange("p (c t) -> p c t", c=TT)
        lanes = [slice(0, HEAD), slice(HEAD, 2 * HEAD)]
        sets = [("neg", "alpha", "beta"), ("key_past", "kappa", "alpha"), ("key_seen", "kappa", "rho"),
                ("rate_seen", "beta", "rho")]
        masks = ["neg_lower_strict", "upper_strict", "upper_in", "upper_in"]
        left = [b.alpha, b.kappa, b.kappa, b.beta]
        right = [b.beta, b.alpha, b.rho, b.rho]
        target = [b.neg, b.key_past, b.key_seen, b.rate_seen]

        @block.vector
        def _(dve):
            steps = Steps(dve, dve_steps)
            for i, name in enumerate(VEC_J):
                at = VECE.at[name][0]
                steps.did(nc.vector.tensor_copy(b.par[:, i:i + 1], vec[:, bass.ds(j + at, 1)]))
            steps.did(nc.vector.tensor_copy(r[:, :], tile_at(u, j + E_R)))
            steps.did(nc.vector.tensor_copy(b.v[:, :], tile_at(u, j + E_V)))
            steps.did(nc.vector.tensor_copy(b.gate[:, :], tile_at(gate, j)))
            steps.did(nc.vector.tensor_copy(before[:, :], tile_at(decay, j)))
            steps.settle()
            steps.did(nc.vector.tensor_scalar(kk[:, :], tile_at(u, j + E_K), b.par[:, 0:1], None, ALU.mult), kk_ready)
            steps.did(nc.vector.tensor_scalar(k[:, :], tile_at(rate, j), -1.0, b.par[:, 1:2], ALU.add, ALU.mult))
            steps.did(nc.vector.tensor_tensor_scan(run[:, :], CONST(mem.const, "not_first"), before[:, :], 0.0,
                                                   ALU.mult, ALU.add))
            steps.settle()
            steps.did(nc.vector.scalar_tensor_tensor(out=k[:, :], in0=k[:, :], scalar=1.0, in1=tile_at(u, j + E_K),
                                                     op0=ALU.add, op1=ALU.mult))
            middle = by_chunk(run[:, :])[:, :, mid:mid + 1].broadcast_to([P, TT, P])
            steps.did(nc.vector.tensor_tensor(by_chunk(about[:, :]), by_chunk(run[:, :]), middle, ALU.subtract),
                      about_ready)
            steps.settle()
            steps.did(nc.vector.tensor_tensor(before[:, :], about[:, :], before[:, :], ALU.subtract), before_ready)
            ends = by_chunk(about[:, :])[:, 0:TT - 1, P - 1]
            steps.did(nc.vector.tensor_tensor(b.factor[:, 0:TT - 1], ends, by_chunk(run[:, :])[:, 1:TT, mid], ALU.add),
                      factor_ready)
            steps.did(nc.vector.scalar_tensor_tensor(out=bk[:, :], in0=r[:, :], scalar=b.par[:, 2:3], in1=k[:, :],
                                                     op0=ALU.mult, op1=ALU.mult), bonus_ready)
            dve.wait_ge(rooted, 1)
            steps.did(nc.vector.tensor_scalar(scale[:, :], scale[:, :], 1e-12, None, ALU.max))
            steps.settle()
            steps.did(nc.vector.reciprocal(scale[:, :], scale[:, :]))
            steps.settle()
            steps.did(nc.vector.tensor_tensor(kk[:, :], kk[:, :], scale[:, :], ALU.mult))
            dve.wait_ge(ups, 3)
            steps.did(nc.vector.tensor_tensor(b.rho, r[:, :], up[:, :], ALU.mult), ready)
            steps.did(nc.vector.tensor_tensor(b.kappa, k[:, :], down[:, :], ALU.mult), ready)
            steps.settle()
            steps.did(nc.vector.tensor_tensor(b.alpha, kk[:, :], before[:, :], ALU.mult), ready)
            steps.did(nc.vector.tensor_tensor(kk[:, :], kk[:, :], tile_at(rate, j), ALU.mult))
            steps.settle()
            steps.did(nc.vector.tensor_tensor(b.beta, kk[:, :], down[:, :], ALU.mult), ready)
            dve.wait_ge(bonus_summed, 1)
            steps.did(nc.vector.tensor_tensor(b.bonus[:, :], mem.bank[0][:, :], b.v[:, :], ALU.mult), bonus_ready)
            for i in range(4):
                for par in range(2):
                    dve.wait_ge(product, 2 * i + par + 1)
                    mask = CONST(mem.const, masks[i]).unsqueeze(1).broadcast_to([P, TT, P])
                    steps.did(nc.vector.tensor_tensor(by_chunk(target[i][:, par, :]),
                                                      by_chunk(mem.bank[2 * i + par][:, :]), mask, ALU.mult))
            steps.settle()

        @block.scalar
        def _(act):
            act.wait_ge(kk_ready, 1)
            nc.scalar.activation(squares[:, :], kk[:, :], ACT.Square).then_inc(squared, 1)
            act.wait_ge(summed, 1)
            nc.scalar.activation(scale[:, :], mem.bank[1][:, :], ACT.Sqrt).then_inc(rooted, 1)
            act.wait_ge(about_ready, 1)
            nc.scalar.activation(up[:, :], about[:, :], ACT.Exp).then_inc(ups, 1)
            nc.scalar.activation(down[:, :], about[:, :], ACT.Exp, scale=-1.0).then_inc(ups, 1)
            act.wait_ge(before_ready, 1)
            nc.scalar.activation(before[:, :], before[:, :], ACT.Exp).then_inc(ups, 1)
            act.wait_ge(factor_ready, 1)
            nc.scalar.activation(b.factor[:, 0:TT - 1], b.factor[:, 0:TT - 1], ACT.Exp)
            for i, to in enumerate([b.v_rows, b.kappa_rows, b.alpha_rows, b.beta_rows]):
                act.wait_ge(turned, i + 1)
                nc.scalar.activation(to.rearrange("p t n -> p (t n)"), mem.bank[2 + i][:, :], ACT.Copy) \
                    .then_inc(rows_taken, 1)

        @block.tensor
        def _(pe):
            pe.wait_ge(squared, 1)
            nc.tensor.matmul(mem.bank[1][:, :], CONST(mem.const, "pair_ones"), squares[:, :], start=True,
                             stop=True).then_inc(summed, 1)
            pe.wait_ge(bonus_ready, 1)
            nc.tensor.matmul(mem.bank[0][:, :], CONST(mem.const, "pair_ones"), bk[:, :], start=True,
                             stop=True).then_inc(bonus_summed, 1)
            for i, (of, need) in enumerate([(b.v[:, :], 0), (b.kappa, 2), (b.alpha, 3), (b.beta, 4)]):
                if need:
                    pe.wait_ge(ready, need)
                for t in range(TT):
                    last = nc.tensor.transpose(mem.bank[2 + i][:, t * P:(t + 1) * P], of[:, t * P:(t + 1) * P],
                                               CONST(mem.const, "ident"))
                last.then_inc(turned, 1)
            pe.wait_ge(rows_taken, 4)
            pe.wait_ge(bonus_ready, 2)
            for i in range(4):
                for par in range(2):
                    for t in range(TT):
                        c = slice(t * P, (t + 1) * P)
                        last = nc.tensor.matmul(mem.bank[2 * i + par][:, c], left[i][lanes[par], c],
                                                right[i][lanes[par], c], start=True, stop=True)
                    last.then_inc(product, 1)


def rwkv_scan(nc, mem, y, j, b):
    first_tile = A_GROUPS
    with buffers(nc, past=[P, 2, TT, HEAD], u0=[P, 2, TT, HEAD], w=[P, SEQ], state=[P, HEAD], fresh=[P, 2, P],
                 out=[P, SEQ], squares=[P, SEQ], scale=[P, SEQ]) as (
            past, u0, w, state, fresh, out, squares, scale), phase(
            nc, "past_ready", "past_taken", "solved", "solved_taken", "passed", "fresh_ready", "out_ready", "grown",
            "added", "state_ready", "out_taken", "mean_ready", "centred", "squared", "summed", "rooted",
            "dve_steps") as (
            block, past_ready, past_taken, solved, solved_taken, passed, fresh_ready, out_ready, grown,
            added, state_ready, out_taken, mean_ready, centred, squared, summed, rooted, dve_steps):
        lanes = [slice(0, HEAD), slice(HEAD, 2 * HEAD)]

        @block.tensor
        def _(pe):
            for par in range(2):
                for t in range(TT):
                    c = slice(t * P, (t + 1) * P)
                    last = nc.tensor.matmul(mem.bank[par][:, t * HEAD:(t + 1) * HEAD], b.key_past[:, par, c],
                                            b.v_rows[:, t, lanes[par]], start=True, stop=True)
                last.then_inc(past_ready, 1)
            for par in range(2):
                for t in range(TT):
                    c = slice(t * P, (t + 1) * P)
                    last = nc.tensor.matmul(mem.bank[4][lanes[par], c], b.alpha_rows[:, t, lanes[par]],
                                            b.turned[:, par, c], start=True, stop=True)
                last.then_inc(solved, 1)
            for par in range(2):
                pe.wait_ge(past_taken, par + 1)
                for t in range(TT):
                    last = nc.tensor.matmul(mem.bank[2 + par][:, t * HEAD:(t + 1) * HEAD],
                                            b.turned[:, par, t * P:(t + 1) * P], past[:, par, t, :],
                                            start=True, stop=True)
                last.then_inc(solved, 1)
            pe.wait_ge(solved_taken, 3)
            for s in range(TT):
                c = slice(s * P, (s + 1) * P)
                if s >= 1:
                    pe.wait_ge(state_ready, s)
                    for par in range(2):
                        nc.tensor.matmul(mem.bank[par][:, 0:HEAD], w[lanes[par], c], state[lanes[par], :],
                                         start=True, stop=True).then_inc(passed, 1)
                if s < TT - 1:
                    for par in range(2):
                        nc.tensor.matmul(mem.bank[5][lanes[par], 0:HEAD], b.kappa_rows[:, s, lanes[par]],
                                         b.v_rows[:, s, lanes[par]], start=True, stop=False)
                        pe.wait_ge(fresh_ready, 2 * s + 1 + par)
                        last = nc.tensor.matmul(mem.bank[5][lanes[par], 0:HEAD], b.beta_rows[:, s, lanes[par]],
                                                fresh[:, s % 2, lanes[par]], start=False, stop=True)
                    last.then_inc(grown, 1)
                pe.wait_ge(fresh_ready, 2 * s + 2)
                if s >= 2:
                    pe.wait_ge(out_taken, s - 1)
                for par in range(2):
                    to = mem.bank[6 + s % 2][lanes[par], 0:P]
                    if s >= 1:
                        nc.tensor.matmul(to, state[lanes[par], :], b.rho[lanes[par], c], start=True, stop=False)
                    nc.tensor.matmul(to, b.v_rows[:, s, lanes[par]], b.key_seen[:, par, c], start=(s == 0), stop=False)
                    last = nc.tensor.matmul(to, fresh[:, s % 2, lanes[par]], b.rate_seen[:, par, c],
                                            start=False, stop=True)
                last.then_inc(out_ready, 1)
            pe.wait_ge(out_taken, TT)
            nc.tensor.matmul(mem.bank[0][:, :], CONST(mem.const, "pair_ones"), out[:, :], start=True,
                             stop=True).then_inc(mean_ready, 1)
            pe.wait_ge(squared, 1)
            nc.tensor.matmul(mem.bank[1][:, :], CONST(mem.const, "pair_ones"), squares[:, :], start=True,
                             stop=True).then_inc(summed, 1)

        @block.scalar
        def _(act):
            for par in range(2):
                act.wait_ge(past_ready, par + 1)
                nc.scalar.activation(past[:, par, :, :].rearrange("p t e -> p (t e)"),
                                     mem.bank[par][:, 0:TT * HEAD], ACT.Copy).then_inc(past_taken, 1)
            act.wait_ge(solved, 2)
            nc.scalar.activation(w[:, :], mem.bank[4][:, :], ACT.Copy).then_inc(solved_taken, 1)
            for par in range(2):
                act.wait_ge(solved, 3 + par)
                nc.scalar.activation(u0[:, par, :, :].rearrange("p t e -> p (t e)"),
                                     mem.bank[2 + par][:, 0:TT * HEAD], ACT.Copy).then_inc(solved_taken, 1)
            for s in range(TT):
                act.wait_ge(out_ready, s + 1)
                nc.scalar.activation(out[:, s * P:(s + 1) * P], mem.bank[6 + s % 2][:, 0:P], ACT.Copy) \
                    .then_inc(out_taken, 1)
            act.wait_ge(centred, 1)
            nc.scalar.activation(squares[:, :], out[:, :], ACT.Square).then_inc(squared, 1)
            act.wait_ge(summed, 1)
            nc.scalar.activation(scale[:, :], mem.bank[1][:, :], ACT.Sqrt, bias=mem.eps[:, 2:3],
                                 scale=1.0 / HEAD).then_inc(rooted, 1)

        @block.vector
        def _(dve):
            steps = Steps(dve, dve_steps)
            dve.wait_ge(solved_taken, 3)
            for s in range(TT):
                if s >= 2:
                    dve.wait_ge(out_ready, s - 1)
                for par in range(2):
                    if s == 0:
                        steps.did(nc.vector.tensor_scalar(fresh[:, 0, lanes[par]], u0[:, par, 0, :], -1.0, None,
                                                          ALU.mult), fresh_ready)
                    else:
                        dve.wait_ge(passed, 2 * s - 1 + par)
                        steps.did(nc.vector.scalar_tensor_tensor(
                            out=fresh[:, s % 2, lanes[par]], in0=mem.bank[par][:, 0:HEAD], scalar=-1.0,
                            in1=u0[:, par, s, :], op0=ALU.mult, op1=ALU.subtract), fresh_ready)
                if s == TT - 1:
                    break
                dve.wait_ge(grown, s + 1)
                if s == 0:
                    steps.did(nc.vector.tensor_scalar(state[:, :], mem.bank[5][:, 0:HEAD], b.factor[:, s:s + 1], None,
                                                      ALU.mult), state_ready)
                else:
                    dve.wait_ge(out_ready, s + 1)
                    steps.settle()
                    steps.did(nc.vector.tensor_tensor(state[:, :], state[:, :], mem.bank[5][:, 0:HEAD], ALU.add))
                    steps.settle()
                    steps.did(nc.vector.tensor_scalar(state[:, :], state[:, :], b.factor[:, s:s + 1], None, ALU.mult),
                              state_ready)
            dve.wait_ge(mean_ready, 1)
            steps.did(nc.vector.scalar_tensor_tensor(out=out[:, :], in0=mem.bank[0][:, :], scalar=-1.0 / HEAD,
                                                     in1=out[:, :], op0=ALU.mult, op1=ALU.add), centred)
            dve.wait_ge(rooted, 1)
            steps.did(nc.vector.reciprocal(scale[:, :], scale[:, :]))
            steps.settle()
            steps.did(nc.vector.scalar_tensor_tensor(out=out[:, :], in0=out[:, :], scalar=b.par[:, 3:4],
                                                     in1=scale[:, :], op0=ALU.mult, op1=ALU.mult))
            steps.settle()
            steps.did(nc.vector.scalar_tensor_tensor(out=out[:, :], in0=out[:, :], scalar=b.par[:, 4:5],
                                                     in1=b.bonus[:, :], op0=ALU.add, op1=ALU.add))
            steps.settle()
            steps.did(nc.vector.tensor_tensor(tile_at(y, j + first_tile), out[:, :], b.gate[:, :], ALU.mult))
            steps.settle()


def time_mix(nc, mem, a, vec, u, y):
    token_shift(nc, mem, vec, u)
    with buffers(nc, decay=[P, RW_PAIRS, SEQ], rate=[P, RW_PAIRS, SEQ], gate=[P, RW_PAIRS, SEQ]) as (
            decay, rate, gate):
        rwkv_gates(nc, mem, a, vec, u, decay, rate, gate)
        with nc.Fori(0, RW_PAIRS) as j, buffers(nc, v=[P, SEQ], pair_gate=[P, SEQ], bonus=[P, SEQ], factor=[P, TT],
                                                par=[P, len(VEC_J)], more=[P, 8, SEQ]) as parts:
            b = TimeMix(mem, *parts)
            rwkv_prepare(nc, mem, vec, u, decay, rate, gate, j, b)
            invert(nc, mem, b.neg, b.turned, [0, 0])
            rwkv_scan(nc, mem, y, j, b)


def second_even(nc, mem, a):
    with buffers(nc, vec=[P, VECE.size]) as (vec,):
        load(nc, (vec[:, :], a["vece"]))
        with buffers(nc, y=[P, KD, SEQ], u=[P, UTE, SEQ]) as (y, u):
            rms_norm(nc, mem, mem.x, lambda k: VECE(vec, "norm_mix", k), mem.h)
            with buffers(nc, pv=[P, TT, A_WIDTH]) as (pv,):
                token_major(nc, mem, a["w_tme"], A_WIDTH, mem.h, pv)
                project(nc, mem, unit_of(a["w_ine"]), UTE // 2, 2, mem.h, copy_out(nc, u))
                spatial_gate(nc, mem, a, u, pv, y)
            time_mix(nc, mem, a, vec, u, y)
            if mem.stop == "even":
                dump(nc, mem, a, y, 0, 8)
            project(nc, mem, unit_of(a["w_oute"]), KD // 2, 2, y, add_out(nc, mem.x), on_vector=True)
        rms_norm(nc, mem, mem.x, lambda k: VECE(vec, "norm_ffn", k), mem.h)
        feed_forward(nc, mem, unit_of(a["w_ffe"]), unit_of(a["w_downe"]), FFN_T, "silu",
                     lambda half: add_out(nc, mem.x), lambda half: True)


def interleaved(gate, up):
    k, m = gate.shape
    both = np.stack([gate.reshape(k, m // P, P), up.reshape(k, m // P, P)], axis=2)
    return both.reshape(k, 2 * m)


def lay_out_even(i, a):
    w = i["e_w_in_2"][0]
    a["w_ine"] = weight_units(np.concatenate([w[:, :A_WIDTH], w[:, 2 * A_WIDTH:]], axis=1), 2)
    a["w_tme"] = moving(w[:, A_WIDTH:2 * A_WIDTH])
    a["w_oute"] = weight_units(i["e_w_out_2"][0], 2)
    a["w_ffe"] = weight_units(interleaved(i["ffn_w_gate_2"][0], i["ffn_w_up_2"][0]), 2)
    a["w_downe"] = weight_units(i["ffn_w_down_2"][0], 1)
    a["sgu_w"] = i["sgu_w_2"][0].transpose(2, 0, 1)
    a["sgu_b"] = i["sgu_b_2"][0]
    a["sgu_ln"] = np.stack([i["sgu_ln_g_2"][0], i["sgu_ln_b_2"][0]])
    a["wa2"] = np.concatenate([i["rwkv_w2_2"][0], i["rwkv_a2_2"][0]])
    a["g2"] = i["rwkv_g2_2"][0]
    vec = np.zeros((P, VECE.size), np.float32)
    for name, key in [("norm_mix", "e_norm_mix_2"), ("norm_ffn", "e_norm_ffn_2"), ("mu", "rwkv_mu_2"),
                      ("w0", "rwkv_w0_2"), ("a0", "rwkv_a0_2"), ("k_k", "rwkv_k_k_2"), ("k_a", "rwkv_k_a_2"),
                      ("r_k", "rwkv_r_k_2"), ("gn_g", "rwkv_gn_g_2"), ("gn_b", "rwkv_gn_b_2")]:
        VECE(vec, name)[...] = columns(i[key][0].reshape(-1))
    a["vece"] = vec




def short_conv(nc, mem, vec, u, y):
    n = D_WIDTH // P
    first_tile = C_HEADS * HEAD // P
    taps = 3
    with phase(nc, "dve_steps") as (block, dve_steps):
        @block.vector
        def _(dve):
            steps = Steps(dve, dve_steps)
            z, out = u[:, O_CG:O_CG + n, :], y[:, first_tile:first_tile + n, :]
            steps.did(nc.vector.tensor_tensor(z, z, u[:, O_HD:O_HD + n, :], ALU.mult))
            steps.settle()
            for lag in range(taps):
                for c in range(n):
                    weight = VECO(vec, "conv", taps * c + taps - 1 - lag)
                    if lag == 0:
                        steps.did(nc.vector.tensor_scalar(out[:, c, :], z[:, c, :], weight, None, ALU.mult))
                    else:
                        steps.did(nc.vector.scalar_tensor_tensor(
                            out=out[:, c, lag:SEQ], in0=z[:, c, 0:SEQ - lag], scalar=weight, in1=out[:, c, lag:SEQ],
                            op0=ALU.mult, op1=ALU.add))
                steps.settle()
            steps.did(nc.vector.tensor_tensor(out, out, u[:, O_BG:O_BG + n, :], ALU.mult))
            steps.settle()


def rotate_keys(nc, mem, rope, u):
    tiles = range(O_KS, O_KS + 2 * C_KV)
    with buffers(nc, turn=[P, 2 * C_KV, SEQ]) as (turn,), phase(nc, "rotated", "dve_steps") as (
            block, rotated, dve_steps):
        @block.tensor
        def _(pe):
            for i, t in enumerate(tiles):
                nc.tensor.matmul(mem.bank[i][:, :], CONST(mem.const, "rot"), u[:, t, :], start=True, stop=True) \
                    .then_inc(rotated, 1)

        @block.vector
        def _(dve):
            steps = Steps(dve, dve_steps)
            for i, t in enumerate(tiles):
                dve.wait_ge(rotated, i + 1)
                steps.did(nc.vector.tensor_tensor(turn[:, i, :], mem.bank[i][:, :], rope[:, 1, :], ALU.mult))
                steps.did(nc.vector.tensor_tensor(u[:, t, :], u[:, t, :], rope[:, 0, :], ALU.mult))
            steps.settle()
            for i, t in enumerate(tiles):
                steps.did(nc.vector.tensor_tensor(u[:, t, :], u[:, t, :], turn[:, i, :], ALU.add))
            steps.settle()


def compress(nc, mem, w1, w2, pos, z, k_out, v_out):
    halves = CMP_HIDDEN // P
    lanes = [slice(0, HEAD), slice(HEAD, 2 * HEAD)]
    parts = 4
    per = CMP_LEN // parts
    with buffers(nc, first=[P, CMP_LEN, CMP_HIDDEN], blocks=[P, CMP_LEN, CMP_COLS], second=[P, halves, HEAD],
                 hidden=[P, C_KV, halves, CMP_COLS]) as (first, blocks, second, hidden), phase(
            nc, *[f"loaded{p}" for p in range(parts)], "second_loaded", "blocks_ready", "inner", "inner_taken", "outer",
            "outer_taken") as (
            block, *loaded, second_loaded, blocks_ready, inner, inner_taken, outer, outer_taken):
        @block.sync
        def _(sp):
            for p in range(parts):
                for c in range(C_KV):
                    sp.dma_start(first[lanes[c], p * per:(p + 1) * per, :], w1[:, p * per:(p + 1) * per, :]) \
                        .then_inc(loaded[p], 16)
            sp.dma_start(second[:, :, :], w2).then_inc(second_loaded, 16)

        @block.vector
        def _(dve):
            if CMP_COLS > N_CMP:
                nc.vector.memset(blocks[:, :, N_CMP:CMP_COLS], 0.0).then_inc(blocks_ready, 1)
            by_stride = z.rearrange("p (m r) -> p r m", r=CMP_STRIDE)
            for part in range(CMP_LEN // CMP_STRIDE):
                at = pos[:, part * CMP_STRIDE:(part + 1) * CMP_STRIDE].unsqueeze(2)
                last = nc.vector.tensor_tensor(blocks[:, part * CMP_STRIDE:(part + 1) * CMP_STRIDE, 0:N_CMP],
                                               by_stride[:, :, part:part + N_CMP],
                                               at.broadcast_to([P, CMP_STRIDE, N_CMP]), ALU.add)
                last.then_inc(blocks_ready, 1)

        @block.tensor
        def _(pe):
            pe.wait_ge(blocks_ready, CMP_LEN // CMP_STRIDE + (CMP_COLS > N_CMP))
            for p in range(parts):
                pe.wait_ge(loaded[p], 32)
                for c in range(C_KV):
                    for h in range(halves):
                        for l in range(p * per, (p + 1) * per):
                            last = nc.tensor.matmul(mem.bank[c * halves + h][:, 0:CMP_COLS],
                                                    first[lanes[c], l, h * P:(h + 1) * P], blocks[lanes[c], l, :],
                                                    start=(l == 0), stop=(l == CMP_LEN - 1))
                        if p == parts - 1:
                            last.then_inc(inner, 1)
            pe.wait_ge(second_loaded, 16)
            for c in range(C_KV):
                pe.wait_ge(inner_taken, (c + 1) * halves)
                if k_out is not None:
                    for side in range(2):
                        for h in range(halves):
                            last = nc.tensor.matmul(mem.bank[4 + c][lanes[side], 0:CMP_COLS], second[:, h, :],
                                                    hidden[:, c, h, :], start=(h == 0), stop=(h == halves - 1))
                else:
                    for h in range(halves):
                        last = nc.tensor.matmul(mem.bank[4 + c][0:CMP_COLS, 0:HEAD], hidden[:, c, h, :],
                                                second[:, h, :], start=(h == 0), stop=(h == halves - 1))
                last.then_inc(outer, 1)

        @block.scalar
        def _(act):
            for c in range(C_KV):
                for h in range(halves):
                    act.wait_ge(inner, c * halves + h + 1)
                    nc.scalar.activation(hidden[:, c, h, :], mem.bank[c * halves + h][:, 0:CMP_COLS],
                                         ACT.Gelu_apprx_tanh).then_inc(inner_taken, 1)
            for c in range(C_KV):
                act.wait_ge(outer, c + 1)
                if k_out is not None:
                    nc.scalar.activation(k_out[:, c, :], mem.bank[4 + c][:, 0:N_CMP], ACT.Copy).then_inc(outer_taken, 1)
                else:
                    nc.scalar.activation(v_out[0:N_CMP, c, :], mem.bank[4 + c][0:N_CMP, 0:HEAD], ACT.Copy) \
                        .then_inc(outer_taken, 1)


def sparse_attention(nc, mem, rope, u, tm, k_cmp, v_cmp, y):
    lanes = [slice(0, HEAD), slice(HEAD, 2 * HEAD)]
    units = [(h, t) for h in range(2) for t in range(TT)]
    n_units = len(units)
    scale = HEAD ** -0.5
    SLC, WIN = range(2)
    with nc.Fori(0, C_KV) as kv, nc.Fori(0, C_GROUP // 2) as half, buffers(
            nc, q=[P, SEQ], q_rot=[P, SEQ], turn=[P, SEQ], keys=[P, 2, SEQ], values=[P, 2, TT, HEAD],
            kc=[P, N_CMP], vc=[P, HEAD], gate=[P, TT, 2, N_BRANCH], probs=[P, 2, 2, SEQ], probs_c=[P, 2, TT, N_CMP],
            top_c=[P, 2, TT], sum_c=[P, 2, TT], tops=[P, 2 * n_units], sums=[P, 2 * n_units],
            weights=[P, 2 * n_units], turned=[P, 2, 2, SEQ], turned_c=[P, 2, SEQ]) as (
            q, q_rot, turn, keys, values, kc, vc, gate, probs, probs_c, top_c, sum_c, tops, sums, weights, turned,
            turned_c), phase(
            nc, "gate_ready", "q_ready", "rotated", "keys_staged", "staged", "scored_c", "topped_c", "exped_c",
            "weighted_c", "transposed_c", "taken_c", "scored", "topped", "exped", "weighted", "transposed",
            "taken", "applied", "dve_steps") as (
            block, gate_ready, q_ready, rotated, keys_staged, staged, scored_c, topped_c, exped_c,
            weighted_c, transposed_c, taken_c, scored, topped, exped, weighted, transposed,
            taken, applied, dve_steps):
        j = kv * (C_GROUP // 2) + half
        first_gate = 2 * KV_WIDTH
        out_bank = mem.bank[7]

        def score_bank(n, branch):
            return mem.bank[2 * (n % 2) + branch]

        @block.scalar
        def _(act):
            nc.scalar.activation(gate[:, :, :, :].rearrange("p t h b -> p t (h b)"),
                                 tm[:, :, bass.ds(j * 2 * N_BRANCH + first_gate, 2 * N_BRANCH)],
                                 ACT.Sigmoid).then_inc(gate_ready, 1)
            nc.scalar.activation(q[:, :], tile_at(u, j + O_Q), ACT.Copy, scale=scale).then_inc(q_ready, 1)
            act.wait_ge(topped_c, 1)
            nc.scalar.activation(probs_c[:, :, :, :], probs_c[:, :, :, :], ACT.Exp).then_inc(exped_c, 1)
            for h in range(2):
                act.wait_ge(transposed_c, h + 1)
                nc.scalar.activation(turned_c[0:N_CMP, h, :], mem.bank[2 + h][0:N_CMP, :], ACT.Copy) \
                    .then_inc(taken_c, 1)

            def take_turned(n):
                h, t = units[n]
                width = (t + 1) * P
                act.wait_ge(transposed, n + 1)
                if n >= 2:
                    act.wait_ge(applied, n - 1)
                for branch in (SLC, WIN):
                    nc.scalar.activation(turned[:, n % 2, branch, 0:width], mem.bank[5 + branch][:, 0:width], ACT.Copy) \
                        .then_inc(taken, 1)

            for n, (h, t) in enumerate(units):
                width = (t + 1) * P
                act.wait_ge(topped, n + 1)
                if n >= 2:
                    act.wait_ge(transposed, n - 1)
                for branch in (SLC, WIN):
                    i = 2 * n + branch
                    nc.scalar.activation(probs[:, n % 2, branch, 0:width], score_bank(n, branch)[:, 0:width], ACT.Exp,
                                         bias=tops[:, i:i + 1], accum_out=sums[:, i:i + 1]).then_inc(exped, 1)
                if n >= 1:
                    take_turned(n - 1)
            take_turned(n_units - 1)

        @block.tensor
        def _(pe):
            pe.wait_ge(q_ready, 1)
            nc.tensor.matmul(out_bank[:, :], CONST(mem.const, "rot"), q[:, :], start=True, stop=True) \
                .then_inc(rotated, 1)
            pe.wait_ge(keys_staged, 1)
            for h in range(2):
                for t in range(TT):
                    last = nc.tensor.matmul(mem.bank[h][:, t * N_CMP:(t + 1) * N_CMP], q[lanes[h], t * P:(t + 1) * P],
                                            kc[lanes[h], :], start=True, stop=True)
                last.then_inc(scored_c, 1)
            pe.wait_ge(weighted_c, 1)
            for h in range(2):
                for t in range(TT):
                    last = nc.tensor.transpose(mem.bank[2 + h][0:N_CMP, t * P:(t + 1) * P], probs_c[:, h, t, :],
                                               CONST(mem.const, "ident"))
                last.then_inc(transposed_c, 1)
            pe.wait_ge(taken_c, 2)
            pe.wait_ge(staged, 1)

            def score(n):
                h, t = units[n]
                c = slice(t * P, (t + 1) * P)
                if n >= 2:
                    pe.wait_ge(exped, 2 * n - 2)
                for branch in (SLC, WIN):
                    nc.tensor.matmul(score_bank(n, branch)[:, 0:(t + 1) * P], q_rot[lanes[h], c],
                                     keys[lanes[h], branch, 0:(t + 1) * P], start=True, stop=True) \
                        .then_inc(scored, 1)

            def transpose(n):
                h, t = units[n]
                pe.wait_ge(weighted, 2 * n + 2)
                if n >= 1:
                    pe.wait_ge(taken, 2 * n)
                for branch in (SLC, WIN):
                    for b in range(t + 1):
                        c = slice(b * P, (b + 1) * P)
                        last = nc.tensor.transpose(mem.bank[5 + branch][:, c], probs[:, n % 2, branch, c],
                                                   CONST(mem.const, "ident"))
                last.then_inc(transposed, 1)

            def apply(n):
                h, t = units[n]
                to = out_bank[lanes[h], t * P:(t + 1) * P]
                nc.tensor.matmul(to, vc[0:N_CMP, :], turned_c[0:N_CMP, h, t * P:(t + 1) * P], start=True, stop=False)
                pe.wait_ge(taken, 2 * n + 2)
                for branch in (SLC, WIN):
                    for b in range(t + 1):
                        last = nc.tensor.matmul(to, values[:, branch, b, :],
                                                turned[:, n % 2, branch, b * P:(b + 1) * P],
                                                start=False, stop=(branch == WIN and b == t))
                last.then_inc(applied, 1)

            score(0)
            score(1)
            for n in range(n_units):
                if n + 2 < n_units:
                    score(n + 2)
                transpose(n)
                if n >= 1:
                    apply(n - 1)
            apply(n_units - 1)

        @block.vector
        def _(dve):
            steps = Steps(dve, dve_steps)
            steps.did(nc.vector.tensor_copy(vc[0:N_CMP, :],
                                            v_cmp[0:N_CMP, bass.ds(kv, 1), :].rearrange("p a n -> p (a n)")))
            steps.did(nc.vector.tensor_copy(keys[:, SLC, :], tile_at(u, kv + O_KS)))
            steps.did(nc.vector.tensor_copy(keys[:, WIN, :], tile_at(u, kv + O_KW)))
            for branch in (SLC, WIN):
                steps.did(nc.vector.tensor_copy(values[:, branch, :, :],
                                                tm[:, :, bass.ds(kv * HEAD + branch * KV_WIDTH, HEAD)]))
            steps.settle()
            steps.did(nc.vector.tensor_copy(kc[:, :], k_cmp[:, bass.ds(kv, 1), :].rearrange("p a n -> p (a n)")),
                      keys_staged)
            dve.wait_ge(q_ready, 1)
            steps.did(nc.vector.tensor_tensor(q_rot[:, :], q[:, :], rope[:, 0, :], ALU.mult))
            dve.wait_ge(rotated, 1)
            steps.did(nc.vector.tensor_tensor(turn[:, :], out_bank[:, :], rope[:, 1, :], ALU.mult))
            steps.settle()
            steps.did(nc.vector.tensor_tensor(q_rot[:, :], q_rot[:, :], turn[:, :], ALU.add), staged)
            mask = CONST(mem.const, "cmp_min").rearrange("p (t n) -> p t n", t=TT)
            seen = CONST(mem.const, "cmp_one").rearrange("p (t n) -> p t n", t=TT)
            for h in range(2):
                dve.wait_ge(scored_c, h + 1)
                steps.did(nc.vector.tensor_tensor(
                    probs_c[:, h, :, :], mem.bank[h][:, 0:TT * N_CMP].rearrange("p (t n) -> p t n", t=TT), mask,
                    ALU.min))
            steps.settle()
            steps.did(nc.vector.reduce_max(top_c[:, :, :], probs_c[:, :, :, :], AX_X))
            steps.settle()
            for h in range(2):
                steps.did(nc.vector.tensor_tensor(probs_c[:, h, :, :], probs_c[:, h, :, :],
                                                  top_c[:, h, :].unsqueeze(2).broadcast_to([P, TT, N_CMP]),
                                                  ALU.subtract), topped_c if h else None)
                steps.settle()
            dve.wait_ge(exped_c, 1)
            for h in range(2):
                steps.did(nc.vector.tensor_tensor(probs_c[:, h, :, :], probs_c[:, h, :, :], seen, ALU.mult))
            steps.settle()
            steps.did(nc.vector.reduce_sum(sum_c[:, :, :], probs_c[:, :, :, :], AX_X))
            steps.settle()
            steps.did(nc.vector.tensor_scalar(sum_c[:, :, :], sum_c[:, :, :], 1e-30, None, ALU.max))
            steps.settle()
            steps.did(nc.vector.reciprocal(sum_c[:, :, :], sum_c[:, :, :]))
            steps.settle()
            dve.wait_ge(gate_ready, 1)
            for h in range(2):
                steps.did(nc.vector.tensor_tensor(sum_c[:, h, :], sum_c[:, h, :], gate[:, :, h, 0], ALU.mult))
            steps.settle()
            for h in range(2):
                steps.did(nc.vector.tensor_tensor(probs_c[:, h, :, :], probs_c[:, h, :, :],
                                                  sum_c[:, h, :].unsqueeze(2).broadcast_to([P, TT, N_CMP]),
                                                  ALU.mult), weighted_c if h else None)
                steps.settle()

            def top(n):
                h, t = units[n]
                width, i = (t + 1) * P, 2 * n
                for branch in (SLC, WIN):
                    dve.wait_ge(scored, i + branch + 1)
                    own = score_bank(n, branch)[:, t * P:width]
                    steps.did(nc.vector.tensor_tensor(own, own, CONST(mem.const, "causal_min"), ALU.min))
                steps.settle()
                for branch in (SLC, WIN):
                    steps.did(nc.vector.reduce_max(weights[:, i + branch:i + branch + 1],
                                                   score_bank(n, branch)[:, 0:width], AX_X))
                steps.settle()
                steps.did(nc.vector.tensor_scalar(tops[:, i:i + 2], weights[:, i:i + 2], -1.0, None, ALU.mult), topped)

            def weigh(n):
                h, t = units[n]
                width, i = (t + 1) * P, 2 * n
                dve.wait_ge(exped, 2 * n + 2)
                steps.did(nc.vector.reciprocal(weights[:, i:i + 2], sums[:, i:i + 2]))
                steps.settle()
                steps.did(nc.vector.tensor_tensor(weights[:, i:i + 2], weights[:, i:i + 2], gate[:, t, h, 1:3],
                                                  ALU.mult))
                steps.settle()
                for branch in (SLC, WIN):
                    p = probs[:, n % 2, branch, 0:width]
                    steps.did(nc.vector.tensor_scalar(p, p, weights[:, i + branch:i + branch + 1], None, ALU.mult),
                              weighted)

            for n in range(n_units):
                top(n)
                if n >= 1:
                    weigh(n - 1)
            weigh(n_units - 1)
            dve.wait_ge(applied, n_units)
            steps.did(nc.vector.tensor_copy(tile_at(y, j), out_bank[:, :]))
            steps.settle()


def second_odd(nc, mem, a):
    with buffers(nc, vec=[P, VECO.size]) as (vec,):
        load(nc, (vec[:, :], a["veco"]))
        with buffers(nc, y=[P, KD, SEQ], u=[P, UTO, SEQ], tm=[P, TT, TMO], rope=[P, 2, SEQ], k_cmp=[P, C_KV, N_CMP],
                     v_cmp=[P, C_KV, HEAD]) as (y, u, tm, rope, k_cmp, v_cmp):
            load(nc, (rope[:, :, :], a["rope"]))
            rms_norm(nc, mem, mem.x, lambda k: VECO(vec, "norm_mix", k), mem.h)
            token_major(nc, mem, a["w_tmo"], TMO, mem.h, tm)
            project(nc, mem, unit_of(a["w_ino"]), UTO // 2, 2, mem.h, copy_out(nc, u))
            short_conv(nc, mem, vec, u, y)
            rotate_keys(nc, mem, rope, u)
            compress(nc, mem, a["cmp_k1"], a["cmp_k2"], VECO(vec, "pos_k"), u[:, O_KC, :], k_cmp, None)
            compress(nc, mem, a["cmp_v1"], a["cmp_v2"], VECO(vec, "pos_v"), u[:, O_VC, :], None, v_cmp)
            sparse_attention(nc, mem, rope, u, tm, k_cmp, v_cmp, y)
            if mem.stop in ("odd", "nsa"):
                dump(nc, mem, a, y, 0, 8)
            project(nc, mem, unit_of(a["w_outo"]), KD // 2, 2, y, add_out(nc, mem.x), on_vector=True)
        rms_norm(nc, mem, mem.x, lambda k: VECO(vec, "norm_ffn", k), mem.h)
        if mem.stop != "nsa":
            mixture(nc, mem, a)
        rms_norm(nc, mem, mem.x, lambda k: VECO(vec, "final", k), mem.h)


def lay_out_odd(i, a):
    w = i["o_w_in_2"][0]
    at = C_HEADS * HEAD
    q, rest = w[:, :at], w[:, at:]
    kc, vc, ks, vs, kw, vw = [rest[:, n * KV_WIDTH:(n + 1) * KV_WIDTH] for n in range(6)]
    gates, conv = rest[:, 6 * KV_WIDTH:6 * KV_WIDTH + C_HEADS * N_BRANCH], rest[:, 6 * KV_WIDTH + C_HEADS * N_BRANCH:]
    twice = lambda k: [k[:, c * HEAD:(c + 1) * HEAD] for c in (0, 0, 1, 1)]
    a["w_ino"] = weight_units(np.concatenate([q, kc, vc, *twice(ks), *twice(kw), conv], axis=1), 2)
    a["w_tmo"] = moving(np.concatenate([vs, vw, gates], axis=1))
    a["w_outo"] = weight_units(i["o_w_out_2"][0], 2)
    for n in "kv":
        a[f"cmp_{n}1"] = i[f"nsa_cmp_{n}_w1_2"][0].reshape(CMP_LEN, HEAD, CMP_HIDDEN).transpose(1, 0, 2)
        a[f"cmp_{n}2"] = i[f"nsa_cmp_{n}_w2_2"][0].reshape(CMP_HIDDEN // P, P, HEAD).transpose(1, 0, 2)
    vec = np.zeros((P, VECO.size), np.float32)
    VECO(vec, "norm_mix")[...] = columns(i["o_norm_mix_2"][0])
    VECO(vec, "norm_ffn")[...] = columns(i["o_norm_ffn_2"][0])
    VECO(vec, "final")[...] = columns(i["final_norm_2"])
    VECO(vec, "pos_k")[...] = np.tile(i["nsa_cmp_pos_k_2"][0].T, (2, 1))
    VECO(vec, "pos_v")[...] = np.tile(i["nsa_cmp_pos_v_2"][0].T, (2, 1))
    VECO(vec, "conv")[...] = i["conv_w_2"][0].reshape(3, D_WIDTH // P, P).transpose(2, 1, 0).reshape(P, -1)
    a["veco"] = vec
    a["router"] = moving(i["moe_router_2"][0])
    a["router_b"] = i["moe_router_b_2"][0]
    a["w_expert"] = np.stack([weight_units(interleaved(g, u), 2)
                              for g, u in zip(i["moe_w_gate_2"][0], i["moe_w_up_2"][0])])
    a["w_expert_down"] = np.stack([weight_units(w, 1) for w in i["moe_w_down_2"][0]])


def lay_out_second(i, a):
    lay_out_even(i, a)
    lay_out_odd(i, a)


def route(nc, mem, a, tokens, job_key, job_gate, job_expert, job_count):
    with buffers(nc, router=[P, KD * N_EXPERTS], bias=[P, N_EXPERTS], logits=[P, TT, N_EXPERTS],
                 best=[P, TT, 8], place=[P, TT, 8], part=[P, TT, 2], hot=[P, TT, 2, N_EXPERTS],
                 gate=[P, TT, N_EXPERTS], mask=[P, TT, N_EXPERTS], key=[P, TT, N_EXPERTS],
                 blocks=[P, N_EXPERTS], upto=[P, N_EXPERTS], first=[P, N_EXPERTS],
                 table=[P, N_EXPERTS * N_EXPERTS], member=[P, MAX_JOBS + 1, N_EXPERTS],
                 ended=[P, MAX_JOBS + 1, N_EXPERTS], wide=[P, TT, MAX_JOBS + 1, N_EXPERTS],
                 wide_gate=[P, TT, MAX_JOBS + 1, N_EXPERTS], expert=[P, MAX_JOBS + 1]) as (
            router, bias, logits, best, place, part, hot, gate, mask, key, blocks, upto, first, table, member,
            ended, wide, wide_gate, expert), nc.sbuf_tensor(
            f"order_{nc.next_id()}", [P, TT, 8], U32) as order, phase(
            nc, "loaded", "product", "ranked", "exped", "masked", "turned", "turned_taken", "counted",
            "dve_steps") as (
            block, loaded, product, ranked, exped, masked, turned, turned_taken, counted, dve_steps):
        n_rank = TT * N_EXPERTS
        rank_of = mem.bank[1][:, 0:n_rank].rearrange("p (t e) -> p t e", t=TT)
        count_of = mem.bank[1][:, n_rank:n_rank + N_EXPERTS]
        halves = D_MODEL // SEQ
        turn_banks = 4

        @block.sync
        def _(sp):
            sp.dma_start(router[:, :], a["router"]).then_inc(loaded, 16)
            sp.dma_start(bias[:, :], a["router_b"].partition_broadcast(P)).then_inc(loaded, 16)

        @block.tensor
        def _(pe):
            pe.wait_ge(loaded, 32)
            for t in range(TT):
                for k in range(KD):
                    last = nc.tensor.matmul(mem.bank[0][:, t * N_EXPERTS:(t + 1) * N_EXPERTS],
                                            mem.h[:, k, t * P:(t + 1) * P],
                                            router[:, k * N_EXPERTS:(k + 1) * N_EXPERTS],
                                            start=(k == 0), stop=(k == KD - 1))
            last.then_inc(product, 1)
            for t in range(TT):
                for half in range(halves):
                    n = t * halves + half
                    if n >= turn_banks:
                        pe.wait_ge(turned_taken, n - turn_banks + 1)
                    for c in range(SEQ // P):
                        last = nc.tensor.matmul(mem.bank[2 + n % turn_banks][:, c * P:(c + 1) * P],
                                                mem.h[:, half * (SEQ // P) + c, t * P:(t + 1) * P],
                                                CONST(mem.const, "ident"), start=True, stop=True)
                    last.then_inc(turned, 1)
            pe.wait_ge(masked, 1)
            for t in range(TT):
                for s in range(t + 1):
                    nc.tensor.matmul(mem.bank[1][:, t * N_EXPERTS:(t + 1) * N_EXPERTS],
                                     CONST(mem.const, "upper_strict" if s == t else "ones"), mask[:, s, :],
                                     start=(s == 0), stop=(s == t))
            for s in range(TT):
                last = nc.tensor.matmul(count_of, CONST(mem.const, "ones"), mask[:, s, :],
                                        start=(s == 0), stop=(s == TT - 1))
            last.then_inc(counted, 1)

        @block.scalar
        def _(act):
            for n in range(TT * halves):
                t, half = divmod(n, halves)
                act.wait_ge(turned, n + 1)
                nc.scalar.activation(tokens[:, t, half * SEQ:(half + 1) * SEQ], mem.bank[2 + n % turn_banks][:, :],
                                     ACT.Copy).then_inc(turned_taken, 1)
            act.wait_ge(ranked, 1)
            nc.scalar.activation(part[:, :, 1], part[:, :, 1], ACT.Exp).then_inc(exped, 1)

        @block.vector
        def _(dve):
            steps = Steps(dve, dve_steps)
            v = nc.vector
            dve.wait_ge(product, 1)
            steps.did(v.tensor_tensor(
                logits[:, :, :], mem.bank[0][:, 0:n_rank].rearrange("p (t e) -> p t e", t=TT),
                bias[:, :].unsqueeze(1).broadcast_to([P, TT, N_EXPERTS]), ALU.add))
            steps.settle()
            for t in range(TT):
                steps.did(v.max(best[:, t, :], logits[:, t, :]))
            steps.settle()
            for t in range(TT):
                steps.did(v.max_index(order[:, t, :], best[:, t, :], logits[:, t, :]))
            steps.did(v.tensor_tensor(part[:, :, 1], best[:, :, 1], best[:, :, 0], ALU.subtract), ranked)
            steps.settle()
            steps.did(v.tensor_copy(place[:, :, :], order[:, :, :]))
            steps.settle()
            for t in range(TT):
                for c in range(TOP_K):
                    steps.did(v.tensor_scalar(hot[:, t, c, :], CONSTM(mem.moe_const, "experts"),
                                              place[:, t, c:c + 1], None, ALU.is_equal))
            steps.settle()
            steps.did(v.tensor_tensor(mask[:, :, :], hot[:, :, 0, :], hot[:, :, 1, :], ALU.add), masked)
            dve.wait_ge(exped, 1)
            steps.did(v.tensor_scalar(part[:, :, 0], part[:, :, 1], 1.0, None, ALU.add))
            steps.settle()
            steps.did(v.reciprocal(part[:, :, 0], part[:, :, 0]))
            steps.settle()
            steps.did(v.tensor_tensor(part[:, :, 1], part[:, :, 1], part[:, :, 0], ALU.mult))
            steps.settle()
            for t in range(TT):
                steps.did(v.tensor_scalar(gate[:, t, :], hot[:, t, 0, :], part[:, t, 0:1], None, ALU.mult))
            steps.settle()
            for t in range(TT):
                steps.did(v.scalar_tensor_tensor(out=gate[:, t, :], in0=hot[:, t, 1, :], scalar=part[:, t, 1:2],
                                                 in1=gate[:, t, :], op0=ALU.mult, op1=ALU.add))
            dve.wait_ge(counted, 1)
            steps.did(v.tensor_scalar(blocks[:, :], count_of, 0.0, None, ALU.is_gt))
            for more in range(BLOCK, SEQ, BLOCK):
                steps.settle()
                steps.did(v.scalar_tensor_tensor(out=blocks[:, :], in0=count_of, scalar=float(more),
                                                 in1=blocks[:, :], op0=ALU.is_gt, op1=ALU.add))
            steps.did(v.scalar_tensor_tensor(out=key[:, :, :], in0=rank_of, scalar=UNPICKED, in1=mask[:, :, :],
                                             op0=ALU.add, op1=ALU.mult))
            steps.settle()
            square = table[:, :].rearrange("p (e f) -> p e f", e=N_EXPERTS)
            steps.did(v.tensor_tensor(square, blocks[:, :].unsqueeze(1).broadcast_to([P, N_EXPERTS, N_EXPERTS]),
                                      CONSTM(mem.moe_const, "experts_upto").rearrange("p (e f) -> p e f", e=N_EXPERTS),
                                      ALU.mult))
            steps.settle()
            steps.did(v.tensor_reduce(upto[:, :], square, AX_X, ALU.add))
            steps.settle()
            steps.did(v.tensor_tensor(first[:, :], upto[:, :], blocks[:, :], ALU.subtract))
            steps.did(v.tensor_copy(job_count[:, :], upto[:, N_EXPERTS - 1:N_EXPERTS]))
            by_job = [P, MAX_JOBS + 1, N_EXPERTS]
            job = CONSTM(mem.moe_const, "jobs").unsqueeze(2).broadcast_to(by_job)
            steps.did(v.tensor_tensor(ended[:, :, :], job, upto[:, :].unsqueeze(1).broadcast_to(by_job), ALU.is_ge))
            steps.settle()
            steps.did(v.tensor_tensor(member[:, :, :], job, first[:, :].unsqueeze(1).broadcast_to(by_job), ALU.is_ge))
            steps.did(v.tensor_scalar(upto[:, :], first[:, :], float(BLOCK), -UNPICKED, ALU.mult, ALU.add))
            steps.settle()
            steps.did(v.tensor_tensor(member[:, :, :], member[:, :, :], ended[:, :, :], ALU.subtract))
            steps.did(v.tensor_tensor(key[:, :, :], key[:, :, :],
                                      upto[:, :].unsqueeze(1).broadcast_to([P, TT, N_EXPERTS]), ALU.add))
            steps.settle()
            steps.did(v.tensor_tensor(ended[:, :, :], member[:, :, :],
                                      CONSTM(mem.moe_const, "experts").unsqueeze(1).broadcast_to(by_job), ALU.mult))
            for t in range(TT):
                steps.did(v.tensor_tensor(wide[:, t, :, :], member[:, :, :],
                                          key[:, t, :].unsqueeze(1).broadcast_to(by_job), ALU.mult))
                steps.did(v.tensor_tensor(wide_gate[:, t, :, :], member[:, :, :],
                                          gate[:, t, :].unsqueeze(1).broadcast_to(by_job), ALU.mult))
            steps.settle()
            steps.did(v.tensor_reduce(expert[:, :], ended[:, :, :], AX_X, ALU.add))
            steps.did(v.tensor_reduce(job_key[:, :, :], wide[:, :, :, :], AX_X, ALU.add))
            steps.did(v.tensor_reduce(job_gate[:, :, :], wide_gate[:, :, :, :], AX_X, ALU.add))
            steps.settle()
            steps.did(v.tensor_copy(job_expert[:, :], expert[:, :]))
            steps.did(v.tensor_tensor(job_key[:, :, :], job_key[:, :, :], CONSTM(mem.moe_const, "job_slots").unsqueeze(1)
                                      .broadcast_to([P, TT, MAX_JOBS + 1]), ALU.subtract))
            steps.settle()


def mixture(nc, mem, a):
    j1 = MAX_JOBS + 1
    with buffers(nc, tokens=[P, TT, D_MODEL], job_key=[P, TT, j1], job_gate=[P, TT, j1],
                 moe_const=[P, CONSTM.size]) as (tokens, job_key, job_gate, mem.moe_const), \
            nc.sbuf_tensor(f"job_expert_{nc.next_id()}", [P, j1], I32) as job_expert, \
            nc.sbuf_tensor(f"job_count_{nc.next_id()}", [P, 1], I32) as job_count:
        load(nc, (mem.moe_const[:, :], a["moe_const"]))
        route(nc, mem, a, tokens, job_key, job_gate, job_expert, job_count)
        run_jobs(nc, mem, a, tokens, job_key, job_gate, job_expert, job_count)


def run_jobs(nc, mem, a, tokens, job_key, job_gate, job_expert, job_count):
    pairs, turns = KD // 2, 3 * BLOCK_TILES
    heights = [min(P, BLOCK - s * P) for s in range(BLOCK_TILES)]
    names = [f"glu_filled{s}" for s in range(EXP_SLOTS)] + [f"down_filled{s}" for s in range(EXP_SLOTS)]
    names += ["picks_ready", "weights_ready", "picked", "picked_out", "glu_product", "silu_ready", "hidden_ready",
              "down_product", "down_out", "turned", "turned_out", "spread", "added"]
    glu_size = 2 * KD * P
    with buffers(nc, glu_ring=[P, EXP_SLOTS, glu_size], down_ring=[P, EXP_SLOTS, EXP_T * P], picks=[P, TT, BLOCK], weights=[P, TT, BLOCK],
                 chosen=[P, KD, BLOCK], silu=[P, EXP_SLOTS, BLOCK], hidden=[P, EXP_T, BLOCK],
                 result=[P, KD, BLOCK], result_rows=[P, BLOCK_TILES, D_MODEL],
                 spreader=[P, BLOCK_TILES, SEQ]) as (
            glu_ring, down_ring, picks, weights, chosen, silu, hidden, result, result_rows, spreader), \
            phase(nc, *names) as (block, *sems):
        glu_filled, down_filled = sems[:EXP_SLOTS], sems[EXP_SLOTS:2 * EXP_SLOTS]
        (picks_ready, weights_ready, picked, picked_out, glu_product, silu_ready, hidden_ready, down_product,
         down_out, turned, turned_out, spread, added) = sems[2 * EXP_SLOTS:]
        glu_uses = [len(range(s, EXP_T, EXP_SLOTS)) for s in range(EXP_SLOTS)]
        down_uses = KD // EXP_SLOTS
        low, high = mem.bank[:EXP_SLOTS], mem.bank[EXP_SLOTS:]

        def two(bank):
            return bank[:, 0:2 * BLOCK].rearrange("p (a n) -> p a n", a=2)

        def job_loop(engine, body):
            jobs = engine.value_load(job_count[0:1, 0:1], min_val=1, max_val=MAX_JOBS)
            with engine.Fori(0, jobs) as j:
                body(j)


        @block.sync
        def _(sp):
            def job(j):
                e = sp.value_load(job_expert[0:1, bass.ds(j, 1)], min_val=0, max_val=N_EXPERTS - 1)
                for u in range(EXP_T):
                    s = u % EXP_SLOTS
                    before = u - EXP_SLOTS if u >= EXP_SLOTS else s + (glu_uses[s] - 1) * EXP_SLOTS - EXP_T
                    sp.wait_ge(glu_product, j * EXP_T + (EXP_T + before + 1))
                    sp.dma_start(glu_ring[:, s, :], unit_of(a["w_expert"], e)(u)).then_inc(glu_filled[s], 16)
                for m in range(KD):
                    s = m % EXP_SLOTS
                    sp.wait_ge(down_product, j * KD + (KD + m - EXP_SLOTS + 1))
                    sp.dma_start(down_ring[:, s, :], unit_of(a["w_expert_down"], e)(m)).then_inc(down_filled[s], 16)

            job_loop(sp, job)

        @block.tensor
        def _(pe):
            pe.sem_inc(glu_product, EXP_T)
            pe.sem_inc(down_product, KD)
            pe.sem_inc(turned, turns)

            def pick():
                for p in range(pairs):
                    for k in (2 * p, 2 * p + 1):
                        for t in range(TT):
                            last = nc.tensor.matmul(two(low[p])[:, k % 2, :], tokens[:, t, k * P:(k + 1) * P],
                                                    picks[:, t, :], start=(t == 0), stop=(t == TT - 1))
                    last.then_inc(picked, 1)

            pe.wait_ge(picks_ready, 1)
            pick()

            def job(j):
                pe.wait_ge(picked_out, j * pairs + pairs)
                for u in range(EXP_T):
                    s = u % EXP_SLOTS
                    if u < EXP_SLOTS:
                        pe.wait_ge(added, j * KD + (KD - EXP_SLOTS + u + 1))
                    else:
                        pe.wait_ge(hidden_ready, j * EXP_T + (u - EXP_SLOTS + 1))
                    pe.wait_ge(glu_filled[s], j * (16 * glu_uses[s]) + 16 * (u // EXP_SLOTS + 1))
                    for half in range(2):
                        for k in range(KD):
                            at = (half * KD + k) * P
                            last = nc.tensor.matmul(two(low[s])[:, half, :], glu_ring[:, s, at:at + P],
                                                    chosen[:, k, :], start=(k == 0), stop=(k == KD - 1))
                    last.then_inc(glu_product, 1)
                for m in range(KD):
                    s = m % EXP_SLOTS
                    if m % 2 == 0:
                        pe.wait_ge(turned_out, j * turns + (BLOCK_TILES + m // 2 + 1))
                    pe.wait_ge(down_filled[s], j * (16 * down_uses) + 16 * (m // EXP_SLOTS + 1))
                    for k in range(EXP_T):
                        if m == 0:
                            pe.wait_ge(hidden_ready, j * EXP_T + (k + 1))
                        last = nc.tensor.matmul(two(high[m // 2])[:, m % 2, :], down_ring[:, s, k * P:(k + 1) * P],
                                                hidden[:, k, :], start=(k == 0), stop=(k == EXP_T - 1))
                    last.then_inc(down_product, 1)
                pe.wait_ge(picks_ready, j + 2)
                pick()
                pe.wait_ge(weights_ready, j + 1)
                pe.wait_ge(picked_out, j * pairs + (pairs + BLOCK_TILES))
                for s in range(BLOCK_TILES):
                    for t in range(TT):
                        last = nc.tensor.matmul(low[s][0:heights[s], t * P:(t + 1) * P],
                                                weights[:, t, s * P:s * P + heights[s]], CONST(mem.const, "ident"),
                                                start=True, stop=True)
                    last.then_inc(turned, 1)
                for half in range(2):
                    pe.wait_ge(down_out, j * pairs + (half + 1) * pairs // 2)
                    for s in range(BLOCK_TILES):
                        for c in range(KD // 2):
                            last = nc.tensor.matmul(high[half * BLOCK_TILES + s][0:heights[s], c * P:(c + 1) * P],
                                                    result[:, half * KD // 2 + c, s * P:s * P + heights[s]],
                                                    CONST(mem.const, "ident"), start=True, stop=True)
                        last.then_inc(turned, 1)
                pe.wait_ge(picked_out, j * pairs + 2 * pairs)
                for k in range(KD):
                    if k % (KD // 2) == 0:
                        pe.wait_ge(turned_out, j * turns + (turns + BLOCK_TILES * (2 + k // (KD // 2))))
                    if k >= EXP_SLOTS:
                        pe.wait_ge(added, j * KD + (KD + k - EXP_SLOTS + 1))
                    for s in range(BLOCK_TILES):
                        last = nc.tensor.matmul(low[k % EXP_SLOTS][:, :],
                                                result_rows[0:heights[s], s, k * P:(k + 1) * P],
                                                spreader[0:heights[s], s, :], start=(s == 0), stop=(s == BLOCK_TILES - 1))
                    last.then_inc(spread, 1)

            job_loop(pe, job)

        @block.scalar
        def _(act):
            def take_picked(done):
                for p in range(pairs):
                    act.wait_ge(picked, done + (p + 1))
                    nc.scalar.activation(chosen[:, 2 * p:2 * p + 2, :], two(low[p]), ACT.Copy).then_inc(picked_out, 1)

            take_picked(0)

            def job(j):
                for u in range(EXP_T):
                    s = u % EXP_SLOTS
                    act.wait_ge(glu_product, j * EXP_T + (EXP_T + u + 1))
                    nc.scalar.activation(silu[:, s, :], two(low[s])[:, 0, :], ACT.Silu).then_inc(silu_ready, 1)
                for p in range(pairs):
                    act.wait_ge(down_product, j * KD + (KD + 2 * p + 2))
                    nc.scalar.activation(result[:, 2 * p:2 * p + 2, :], two(high[p]), ACT.Copy).then_inc(down_out, 1)
                take_picked(j * pairs + pairs)

            job_loop(act, job)

        @block.vector
        def _(dve):
            dve.sem_inc(turned_out, turns)
            dve.sem_inc(added, KD)
            one = CONSTM(mem.moe_const, "slots")

            def choose(j):
                for t in range(TT):
                    last = nc.vector.tensor_scalar(picks[:, t, :], one, job_key[:, t, bass.ds(j, 1)], None, ALU.is_equal)
                last.then_inc(picks_ready, 1)

            choose(0)

            def job(j):
                for u in range(EXP_T):
                    s = u % EXP_SLOTS
                    dve.wait_ge(silu_ready, j * EXP_T + (u + 1))
                    nc.vector.tensor_tensor(hidden[:, u, :], silu[:, s, :], two(low[s])[:, 1, :], ALU.mult) \
                        .then_inc(hidden_ready, 1)
                dve.wait_ge(turned, j * turns + BLOCK_TILES)
                for t in range(TT):
                    last = nc.vector.tensor_scalar(weights[:, t, :], one, job_key[:, t, bass.ds(j, 1)],
                                                   job_gate[:, t, bass.ds(j, 1)], ALU.is_equal, ALU.mult)
                last.then_inc(weights_ready, 1)
                dve.wait_ge(picked, j * pairs + pairs)
                choose(j + 1)
                for s in range(BLOCK_TILES):
                    dve.wait_ge(turned, j * turns + (turns + s + 1))
                    nc.vector.tensor_copy(spreader[0:heights[s], s, :], low[s][0:heights[s], :]).then_inc(turned_out, 1)
                for half in range(2):
                    for s in range(BLOCK_TILES):
                        n = half * BLOCK_TILES + s
                        dve.wait_ge(turned, j * turns + (turns + BLOCK_TILES + n + 1))
                        nc.vector.tensor_copy(result_rows[0:heights[s], s, half * SEQ:(half + 1) * SEQ],
                                              high[n][0:heights[s], :]).then_inc(turned_out, 1)
                for k in range(KD):
                    dve.wait_ge(spread, j * KD + (k + 1))
                    dve.wait_ge(added, j * KD + (k + 1))
                    nc.vector.tensor_tensor(mem.x[:, k, :], mem.x[:, k, :], low[k % EXP_SLOTS][:, :], ALU.add) \
                        .then_inc(added, 1)

            job_loop(dve, job)


class Memory:

    def __init__(self, nc, stack):
        def sb(name, shape):
            return stack.enter_context(nc.sbuf_tensor(name, shape, F32))

        self.x = sb("x_res", [P, KD, SEQ])
        self.h = sb("h_branch", [P, KD, SEQ])
        self.ring = sb("weight_ring", [P, SLOTS, SLOT])
        self.const = sb("const_cols", [P, CONST.size])
        self.levels = sb("level_masks", [P, 2, LEVELS, P])
        self.eps = CONST(self.const, "eps")
        self.bank = [stack.enter_context(nc.psum_tensor(f"bank{b}", [P, SEQ], F32)) for b in range(8)]


def load(nc, *pairs):
    with phase(nc, "loaded") as (block, loaded):
        @block.sync
        def _(sp):
            for to, source in pairs:
                sp.dma_start(to, source).then_inc(loaded, 16)
            sp.wait_ge(loaded, 16 * len(pairs))


def layer_of(array, l):
    one = array[bass.ds(l, 1)]
    names = "abcdefg"[:len(one.shape) - 1]
    return one.rearrange(f"z {' '.join(names)} -> (z {names[0]}) {' '.join(names[1:])}")


def unit_of(array, l=None):
    def weights(u):
        if l is None:
            return array[bass.ds(u, 1)].rearrange("a p n -> (a p) n")
        return array[bass.ds(l, 1), bass.ds(u, 1)].rearrange("z a p n -> (z a p) n")
    return weights


def first_block(nc, mem, a):
    with nc.Fori(0, DEPTH) as l, buffers(nc, vec=[P, VEC1.size]) as (vec,):
        with buffers(nc, y=[P, KD, SEQ], u=[P, UT1, SEQ], tm=[P, TT, TM1], 
                     lam=[P, 4 * DIFF_DIM + 2], gates=[P, 2, 2 * DELTA_HEADS]) as (y, u, tm, lam, gates):
            load(nc, (vec[:, :], layer_of(a["vec1"], l)),
                 (lam[:, :], a["lam"][bass.ds(l, 1), :].partition_broadcast(P)),
                 (gates[:, :, :], a["gates"][bass.ds(l, 1), :, :].partition_broadcast(P)))
            rms_norm(nc, mem, mem.x, lambda k: VEC1(vec, "pre_mix", k), mem.h)
            token_major(nc, mem, layer_of(a["w_tm1"], l), TM1, mem.h, tm)
            project(nc, mem, unit_of(a["w_in1"], l), UT1 // 2, 2, mem.h, copy_out(nc, u))
            conv_module(nc, mem, vec, u, y)
            diff_attention(nc, mem, vec, lam, a["dist"], u, tm, y)
            delta_net(nc, mem, vec, gates, u, tm, y)
            if mem.stop == "mix1":
                dump(nc, mem, a, y, 0, 8)
                return
            project(nc, mem, unit_of(a["w_out1"], l), KD // 2, 2, y, copy_out(nc, mem.h))
        rms_norm(nc, mem, mem.h, lambda k: VEC1(vec, "post_mix", k), None, add_to=mem.x)
        rms_norm(nc, mem, mem.x, lambda k: VEC1(vec, "pre_mlp", k), mem.h)
        feed_forward(nc, mem, unit_of(a["w_ff1"], l), unit_of(a["w_ff2"], l), D_FF // P, "relu",
                     lambda half: add_out(nc, mem.h) if half else copy_out(nc, mem.h), bool)
        rms_norm(nc, mem, mem.h, lambda k: VEC1(vec, "post_mlp", k), None, add_to=mem.x)


def dump(nc, mem, a, t, first, last):
    load(nc, (a["dbg"][:, first:last, :], t[:, first:last, :]))


def build(nc, a, out, stop=None):
    with ExitStack() as stack:
        mem = Memory(nc, stack)
        mem.stop = stop
        load(nc, (mem.x[:, :, :], a["x"]), (mem.const[:, :], a["const"]), (mem.levels[:, :, :, :], a["levels"]))
        if stop in (None, "mix1", "first"):
            first_block(nc, mem, a)
        if stop == "even":
            second_even(nc, mem, a)
            dump_at = (a["dbg"][:, 8:16, :], mem.x[:, :, :])
            load(nc, dump_at)
        if stop == "first":
            dump(nc, mem, a, mem.x, 0, 8)
        if stop is None:
            second_even(nc, mem, a)
        if stop in (None, "odd", "nsa", "all"):
            second_odd(nc, mem, a)
        load(nc, (out, mem.h[:, :, :]))


def weight_units(w, tiles):
    k, m = w.shape
    w = w.reshape(k // P, P, m // (P * tiles), tiles, P).transpose(2, 1, 3, 0, 4)
    return np.ascontiguousarray(w.reshape(m // (P * tiles), P, -1))


def moving(w):
    k, m = w.shape
    return np.ascontiguousarray(w.reshape(k // P, P, m).transpose(1, 0, 2).reshape(P, -1))


def columns(v):
    return v.reshape(-1, P).T


def alibi_slopes(n):
    def pow2(m):
        start = 2.0 ** (-8.0 / m)
        return [start ** (i + 1) for i in range(m)]
    if math.log2(n).is_integer():
        return pow2(n)
    c = 2 ** int(math.floor(math.log2(n)))
    return pow2(c) + pow2(2 * c)[0::2][: n - c]


def constants():
    i, j = np.arange(P)[:, None], np.arange(P)[None, :]
    c = np.zeros((P, CONST.size), np.float32)

    def put(name, value):
        CONST(c, name)[...] = value

    put("ident", i == j)
    put("ones", 1)
    put("pair_ones", i // HEAD == j // HEAD)
    half, d = ROT_DIM // 2, np.arange(P) % HEAD
    rot = np.zeros((P, P))
    for p in range(P):
        if d[p] < half:
            rot[p + half, p] = -1
        elif d[p] < ROT_DIM:
            rot[p - half, p] = 1
    put("rot", rot)
    put("lower_in", i >= j)
    put("upper_in", i <= j)
    put("upper_strict", i < j)
    put("neg_lower_strict", -1.0 * (i > j))
    put("lower_strict_max", np.where(i > j, 0, BIG))
    put("upper_strict_max", np.where(i < j, 0, BIG))
    put("upper_in_min", np.where(i <= j, 0, -BIG))
    put("lower_in_min", np.where(i >= j, 0, -BIG))
    put("causal_min", np.where(i >= j, 3e38, -BIG))
    put("neg_slopes", -np.asarray(alibi_slopes(DIFF_HEADS), np.float32))
    t = (np.arange(TT)[None, :, None] * P + np.arange(P)[:, None, None])
    seen = (np.arange(N_CMP) * CMP_STRIDE + CMP_LEN - 1)[None, None, :] <= t
    put("cmp_min", np.where(seen, 3e38, -BIG).reshape(P, -1))
    put("cmp_one", seen.reshape(P, -1))
    put("not_first", np.arange(SEQ)[None, :] % P != 0)
    put("eps", np.array([NORM_EPS, 1e-5, RWKV_GN_EPS, 0.0]))
    m = np.zeros((P, CONSTM.size), np.float32)
    CONSTM(m, "experts")[...] = np.arange(N_EXPERTS)
    CONSTM(m, "experts_upto")[...] = np.tril(np.ones((N_EXPERTS, N_EXPERTS))).reshape(-1)
    CONSTM(m, "jobs")[...] = np.arange(MAX_JOBS + 1)
    CONSTM(m, "job_slots")[...] = BLOCK * np.arange(MAX_JOBS + 1)
    CONSTM(m, "slots")[...] = np.arange(BLOCK)
    levels = np.zeros((P, 2, LEVELS, P), np.float32)
    for n in range(LEVELS):
        b = 2 ** n
        low = (i // (2 * b) == j // (2 * b)) & (i // b % 2 == 1) & (j // b % 2 == 0)
        levels[:, 0, n, :], levels[:, 1, n, :] = low.T, low
    q = (np.arange(TT)[None, :, None] * P + np.arange(P)[:, None, None])
    dist = np.abs(q - np.arange(SEQ)[None, None, :]).astype(np.float32)
    pos = np.arange(SEQ, dtype=np.float32)
    freq = (np.float32(ROPE_THETA) ** (-np.arange(0, ROT_DIM, 2, dtype=np.float32) / np.float32(ROT_DIM))).astype(np.float32)
    angle = pos[:, None] * freq[None, :]
    rope = np.zeros((P, 2, SEQ), np.float32)
    rope[:, 0, :] = 1
    for p in range(P):
        if d[p] < ROT_DIM:
            rope[p, 0], rope[p, 1] = np.cos(angle[:, d[p] % half]), np.sin(angle[:, d[p] % half])
    return {"const": c, "moe_const": m, "levels": levels, "dist": dist, "rope": rope}


def lay_out(i):
    a = dict(constants())
    a["x"] = np.ascontiguousarray(i["x"][0].T.reshape(KD, P, SEQ).transpose(1, 0, 2))
    w_in = i["w_in"]
    o_dv, o_g, o_b = 2 * CONV_CH + 2 * DIFF_W, 2 * CONV_CH + 3 * DIFF_W, 2 * CONV_CH + 3 * DIFF_W + 4 * DELTA_W
    fm = np.concatenate([w_in[:, :, :o_dv], w_in[:, :, o_g:o_b]], axis=2)
    tm = np.concatenate([w_in[:, :, o_dv:o_g], w_in[:, :, o_b:]], axis=2)
    a["w_in1"] = np.stack([weight_units(w, 2) for w in fm])
    a["w_tm1"] = np.stack([moving(w) for w in tm])
    a["w_out1"] = np.stack([weight_units(w, 2) for w in i["w_out"]])
    a["w_ff1"] = np.stack([weight_units(w, 2) for w in i["w_ff1"]])
    a["w_ff2"] = np.stack([weight_units(w, 1) for w in i["w_ff2"]])
    vec = np.zeros((DEPTH, P, VEC1.size), np.float32)
    lam = np.zeros((DEPTH, 4 * DIFF_DIM + 2), np.float32)
    for l in range(DEPTH):
        def put(name, value):
            VEC1(vec[l], name)[...] = value
        put("pre_mix", columns(i["pre_mix_w"][l]))
        put("post_mix", columns(i["post_mix_w"][l]))
        put("pre_mlp", columns(i["pre_mlp_w"][l]))
        put("post_mlp", columns(i["post_mlp_w"][l]))
        put("conv_w", i["conv_dw_w"][l].reshape(CONV_WIDTH, CONV_T, P).transpose(2, 1, 0).reshape(P, -1))
        put("conv_b", columns(i["conv_dw_b"][l]))
        put("ln_w", columns(i["conv_ln_w"][l]))
        put("ln_b", columns(i["conv_ln_b"][l]))
        put("subln", np.tile(i["diff_subln_w"][l], 2)[:, None])
        put("delta_conv", i["delta_conv_w"][l].reshape(SHORT_CONV, 3 * PAIRS1, P).transpose(2, 1, 0).reshape(P, -1))
        put("delta_norm", np.tile(i["delta_norm_w"][l], 2)[:, None])
        init = 0.8 - 0.6 * math.exp(-0.3 * l)
        lam[l] = np.concatenate([i["diff_lambda_q1"][l], i["diff_lambda_k1"][l], i["diff_lambda_q2"][l],
                                 i["diff_lambda_k2"][l], np.array([init, 1.0 - init], np.float32)])
    a["vec1"], a["lam"] = vec, lam
    a["gates"] = np.stack([i["delta_A_log"].reshape(DEPTH, -1), i["delta_dt_bias"].reshape(DEPTH, -1)], axis=1)
    lay_out_second(i, a)
    return {n: np.ascontiguousarray(v, dtype=np.float32) for n, v in a.items()}


def kernel(**inputs):
    import concourse.bacc as bacc
    from concourse.bass_utils import run_bass_kernel_spmd

    arrays = lay_out({n: np.asarray(v) for n, v in inputs.items()})
    nc = bacc.Bacc("TRN2", target_bir_lowering=False, num_devices=1)
    handles = {n: nc.dram_tensor(f"in_{n}", v.shape, F32, kind="ExternalInput").ap() for n, v in arrays.items()}
    out = nc.dram_tensor("out", (P, KD, SEQ), F32, kind="ExternalOutput").ap()
    build(nc, handles, out)
    result = run_bass_kernel_spmd(nc, [{f"in_{n}": v for n, v in arrays.items()}], core_ids=[0])
    y = result.results[0]["out"]
    return np.ascontiguousarray(y.transpose(2, 1, 0).reshape(1, SEQ, D_MODEL))
```

```python
from contextlib import ExitStack, contextmanager
import math

import numpy as np

import concourse.bass as bass
from concourse import mybir

F32 = mybir.dt.float32
U32 = mybir.dt.uint32
I32 = mybir.dt.int32
F32R = mybir.dt.float32r
ACT = mybir.ActivationFunctionType
ALU = mybir.AluOpType
AX_X = mybir.AxisListType.X

P = 128
SEQ = 512
D_MODEL = 1024
KD = D_MODEL // P
TT = SEQ // P
DEPTH = 2
HEAD = 64
NORM_EPS = 1e-6
BIG = 1e30

DIFF_W = 384
DIFF_DIM = 32
DIFF_HEADS = DIFF_W // HEAD
DELTA_W = 384
DELTA_HEADS = DELTA_W // HEAD
CONV_CH = D_MODEL - DIFF_W - DELTA_W
CONV_T = CONV_CH // P
CONV_WIDTH = 31
SHORT_CONV = 3
D_FF = 4 * D_MODEL
assert (CONV_WIDTH - 1) % (DELTA_HEADS // 2) == 0 and DELTA_HEADS == DIFF_HEADS
PAIRS1 = DELTA_HEADS // 2
GATES1 = 4 * DELTA_HEADS
TM1 = DIFF_W + GATES1
U_CA, U_CG, U_DQ, U_DK, U_GQ, U_GK, U_GV, U_GZ = 0, 2, 4, 7, 10, 13, 16, 19
UT1 = 22

B_HEADS = 8
B_WIDTH = 512
A_WIDTH = 512
A_GROUPS = 4
RW_PAIRS = B_HEADS // 2
LORA = 64
SGU_LN_EPS = 1e-5
RWKV_GN_EPS = 64e-5
E_U, E_R, E_K, E_V, E_WA, E_G = 0, 4, 8, 12, 16, 17
UTE = 18
FFN_DIM = 2816
FFN_T = FFN_DIM // P
C_HEADS = 8
C_KV = 2
C_GROUP = C_HEADS // C_KV
KV_WIDTH = C_KV * HEAD
N_BRANCH = 3
CMP_LEN = 32
CMP_STRIDE = 16
N_CMP = (SEQ - CMP_LEN) // CMP_STRIDE + 1
CMP_COLS = N_CMP + N_CMP % 2
CMP_HIDDEN = 256
ROT_DIM = HEAD // 4
ROPE_THETA = 500000.0
D_WIDTH = 512
TMO = 2 * KV_WIDTH + C_HEADS * N_BRANCH
O_Q, O_KC, O_VC, O_KS, O_KW, O_BG, O_CG, O_HD = 0, 4, 5, 6, 8, 10, 14, 18
UTO = 22
N_EXPERTS = 8
TOP_K = 2
EXPERT_DIM = 1408
EXP_T = EXPERT_DIM // P
BLOCK = 176
BLOCK_TILES = -(-BLOCK // P)
MAX_JOBS = N_EXPERTS + (SEQ * TOP_K - N_EXPERTS) // BLOCK
UNPICKED = 2.0 ** 14
EXP_SLOTS = 4

LEVELS = int(math.log2(P))
SLOTS = 2
SLOT = 2048


class Columns:

    def __init__(self):
        self.at, self.size = {}, 0

    def add(self, name, n):
        self.at[name] = (self.size, n)
        self.size += n
        return self

    def __call__(self, tensor, name, i=None, n=1):
        first, size = self.at[name]
        if i is None:
            return tensor[:, first:first + size]
        return tensor[:, first + i:first + i + n]


CONST = Columns()
for _name, _n in [("ident", P), ("ones", P), ("pair_ones", P), ("rot", P),
                  ("lower_in", P), ("upper_in", P), ("upper_strict", P), ("neg_lower_strict", P),
                  ("lower_strict_max", P), ("upper_strict_max", P), ("upper_in_min", P), ("lower_in_min", P),
                  ("causal_min", P), ("slopes", DIFF_HEADS),
                  ("cmp_min", TT * N_CMP), ("cmp_one", TT * N_CMP), ("not_first", SEQ),
                  ("eps", 4)]:
    CONST.add(_name, _n)

CONSTM = Columns()
for _name, _n in [("experts", N_EXPERTS), ("experts_upto", N_EXPERTS * N_EXPERTS), ("jobs", MAX_JOBS + 1),
                  ("job_slots", MAX_JOBS + 1), ("slots", BLOCK)]:
    CONSTM.add(_name, _n)

VEC1 = Columns()
for _name, _n in [("pre_mix", KD), ("post_mix", KD), ("pre_mlp", KD), ("post_mlp", KD),
                  ("conv_w", CONV_T * CONV_WIDTH), ("conv_b", CONV_T), ("ln_w", CONV_T), ("ln_b", CONV_T),
                  ("subln", 1), ("delta_conv", 3 * PAIRS1 * SHORT_CONV), ("delta_norm", 1)]:
    VEC1.add(_name, _n)

VECE = Columns()
for _name, _n in [("norm_mix", KD), ("norm_ffn", KD), ("mu", 14), ("w0", RW_PAIRS), ("a0", RW_PAIRS),
                  ("k_k", RW_PAIRS), ("k_a", RW_PAIRS), ("r_k", RW_PAIRS), ("gn_g", RW_PAIRS), ("gn_b", RW_PAIRS)]:
    VECE.add(_name, _n)

VECO = Columns()
for _name, _n in [("norm_mix", KD), ("norm_ffn", KD), ("final", KD), ("pos_k", CMP_LEN), ("pos_v", CMP_LEN),
                  ("conv", (D_WIDTH // P) * 3)]:
    VECO.add(_name, _n)


class Steps:

    def __init__(self, engine, sem):
        self.engine, self.sem, self.count, self.open = engine, sem, {}, set()

    def did(self, instruction, sem=None):
        sem = self.sem if sem is None else sem
        self.count[sem] = self.count.get(sem, 0) + 1
        self.open.add(sem)
        return instruction.then_inc(sem, 1)

    def settle(self):
        for sem in [s for s in self.count if s in self.open]:
            self.engine.wait_ge(sem, self.count[sem])
        self.open = set()


@contextmanager
def phase(nc, *names):
    sems = [nc.alloc_semaphore(f"{n}_{nc.next_id()}") for n in names]
    with nc.Block() as block:
        yield (block, *sems)
    nc.clear_and_free_semaphores(sems)
    nc.all_engine_barrier()


@contextmanager
def buffers(nc, **shapes):
    with ExitStack() as stack:
        yield [stack.enter_context(nc.sbuf_tensor(f"{n}_{nc.next_id()}", s, F32)) for n, s in shapes.items()]


class Weights:

    def __init__(self, of_unit, units, tiles, kt):
        self.of_unit, self.units, self.tiles, self.kt = of_unit, units, tiles, kt
        self.size = tiles * kt * P


@contextmanager
def split_ring(nc, mem):
    with parts_of(nc, SLOTS, SLOT) as (mem.w_high, mem.w_low):
        yield


class Primer:

    SEMS = [f"next_loaded{s}" for s in range(SLOTS)] + ["next_high"]

    def __init__(self, nc, mem, weights, sems):
        self.nc, self.mem, self.weights, self.loaded, self.high_ready = nc, mem, weights, sems[:SLOTS], sems[SLOTS]

    def load_slot(self, sp, s):
        self.nc.sync.dma_start(self.mem.ring[:, s, 0:self.weights.size], self.weights.of_unit(s)) \
            .then_inc(self.loaded[s], 16)

    def load(self, sp):
        if self.weights is not None:
            for s in range(SLOTS):
                self.load_slot(sp, s)
            self.loads_done(sp)

    def loads_done(self, sp):
        for s in range(SLOTS):
            sp.wait_ge(self.loaded[s], 16)

    def high(self, act):
        if self.weights is not None:
            act.wait_ge(self.loaded[0], 16)
            n = self.weights.size
            self.nc.scalar.activation(self.mem.w_high[:, 0, 0:n], self.mem.ring[:, 0, 0:n], ACT.Copy) \
                .then_inc(self.high_ready, 1)

    def low(self, dve):
        if self.weights is not None:
            dve.wait_ge(self.high_ready, 1)
            n = self.weights.size
            self.nc.vector.tensor_tensor(self.mem.w_low[:, 0, 0:n], self.mem.ring[:, 0, 0:n],
                                         self.mem.w_high[:, 0, 0:n], ALU.subtract)


def rms_norm(nc, mem, source, gain, out, add_to=None, following=None, vectors=(), ahead=(),
             store=None):
    with buffers(nc, squares=[P, KD, SEQ], scale=[P, SEQ]) as (squares, scale), phase(
            nc, "vectors_loaded", "ahead_loaded", "act_squares", "dve_squares", "sum_ready", "root_ready", "made",
            "stored", "dve_steps", *Primer.SEMS) as (
            block, vectors_loaded, ahead_loaded, act_squares, dve_squares, sum_ready, root_ready, made, stored,
            dve_steps, *primer_sems):
        total = mem.bank[0]
        primer = Primer(nc, mem, following, primer_sems)

        @block.sync
        def _(sp):
            for to, data in vectors:
                sp.dma_start(to, data).then_inc(vectors_loaded, 16)
            for to, data in ahead:
                sp.dma_start(to, data).then_inc(ahead_loaded, 16)
            primer.load(sp)
            if ahead:
                sp.wait_ge(ahead_loaded, 16 * len(ahead))
            if store is not None:
                for k in range(KD):
                    sp.wait_ge(made, k + 1)
                    sp.dma_start(store[:, k, :], out[:, k, :]).then_inc(stored, 16)
                sp.wait_ge(stored, 16 * KD)

        @block.scalar
        def _(act):
            for k in range(1, KD, 2):
                nc.scalar.activation(squares[:, k, :], source[:, k, :], ACT.Square).then_inc(act_squares, 1)
            primer.high(act)
            act.wait_ge(sum_ready, 1)
            nc.scalar.activation(scale[:, :], total[:, :], ACT.Sqrt, bias=mem.eps[:, 0:1],
                                 scale=1.0 / D_MODEL).then_inc(root_ready, 1)

        @block.tensor
        def _(pe):
            for k in range(KD):
                pe.wait_ge(act_squares if k % 2 else dve_squares, k // 2 + 1)
                last = nc.tensor.matmul(total[:, :], CONST(mem.const, "ones"), squares[:, k, :],
                                        start=(k == 0), stop=(k == KD - 1))
            last.then_inc(sum_ready, 1)

        @block.vector
        def _(dve):
            steps = Steps(dve, dve_steps)
            for k in range(0, KD, 2):
                steps.did(nc.vector.tensor_tensor(squares[:, k, :], source[:, k, :], source[:, k, :], ALU.mult),
                          dve_squares)
            primer.low(dve)
            dve.wait_ge(root_ready, 1)
            steps.did(nc.vector.reciprocal(scale[:, :], scale[:, :]))
            steps.settle()
            if vectors:
                dve.wait_ge(vectors_loaded, 16 * len(vectors))
            for k in range(KD):
                to = out if add_to is None else squares
                steps.did(nc.vector.scalar_tensor_tensor(out=to[:, k, :], in0=source[:, k, :], scalar=gain(k),
                                                         in1=scale[:, :], op0=ALU.mult, op1=ALU.mult), made)
            if add_to is not None:
                steps.settle()
                for k in range(KD):
                    steps.did(nc.vector.tensor_tensor(add_to[:, k, :], add_to[:, k, :], squares[:, k, :], ALU.add))
            steps.settle()


def add_norm(nc, mem, branch, branch_gain, x, gain, out, following):
    with buffers(nc, squares=[P, KD, SEQ], x_squares=[P, KD, SEQ], scale=[P, SEQ], x_scale=[P, SEQ]) as (
            squares, x_squares, scale, x_scale), phase(
            nc, "act_squares", "dve_squares", "sum_ready", "root_ready", "normed", "added", "added_squares",
            "x_sum_ready", "x_root_ready", "dve_steps", *Primer.SEMS) as (
            block, act_squares, dve_squares, sum_ready, root_ready, normed, added, added_squares,
            x_sum_ready, x_root_ready, dve_steps, *primer_sems):
        total, x_total = mem.bank[0], mem.bank[1]
        primer = Primer(nc, mem, following, primer_sems)

        @block.sync
        def _(sp):
            primer.load(sp)

        @block.scalar
        def _(act):
            for k in range(1, KD, 2):
                nc.scalar.activation(squares[:, k, :], branch[:, k, :], ACT.Square).then_inc(act_squares, 1)
            primer.high(act)
            act.wait_ge(sum_ready, 1)
            nc.scalar.activation(scale[:, :], total[:, :], ACT.Sqrt, bias=mem.eps[:, 0:1],
                                 scale=1.0 / D_MODEL).then_inc(root_ready, 1)
            for k in range(KD):
                act.wait_ge(added, k + 1)
                nc.scalar.activation(x_squares[:, k, :], x[:, k, :], ACT.Square).then_inc(added_squares, 1)
            act.wait_ge(x_sum_ready, 1)
            nc.scalar.activation(x_scale[:, :], x_total[:, :], ACT.Sqrt, bias=mem.eps[:, 0:1],
                                 scale=1.0 / D_MODEL).then_inc(x_root_ready, 1)

        @block.tensor
        def _(pe):
            for k in range(KD):
                pe.wait_ge(act_squares if k % 2 else dve_squares, k // 2 + 1)
                last = nc.tensor.matmul(total[:, :], CONST(mem.const, "ones"), squares[:, k, :],
                                        start=(k == 0), stop=(k == KD - 1))
            last.then_inc(sum_ready, 1)
            for k in range(KD):
                pe.wait_ge(added_squares, k + 1)
                last = nc.tensor.matmul(x_total[:, :], CONST(mem.const, "ones"), x_squares[:, k, :],
                                        start=(k == 0), stop=(k == KD - 1))
            last.then_inc(x_sum_ready, 1)

        @block.vector
        def _(dve):
            steps = Steps(dve, dve_steps)
            for k in range(0, KD, 2):
                steps.did(nc.vector.tensor_tensor(squares[:, k, :], branch[:, k, :], branch[:, k, :], ALU.mult),
                          dve_squares)
            primer.low(dve)
            dve.wait_ge(root_ready, 1)
            steps.did(nc.vector.reciprocal(scale[:, :], scale[:, :]))
            steps.settle()

            def add(k):
                dve.wait_ge(normed, k + 1)
                steps.did(nc.vector.tensor_tensor(x[:, k, :], x[:, k, :], branch[:, k, :], ALU.add), added)

            for k in range(KD):
                steps.did(nc.vector.scalar_tensor_tensor(out=branch[:, k, :], in0=branch[:, k, :],
                                                         scalar=branch_gain(k), in1=scale[:, :], op0=ALU.mult,
                                                         op1=ALU.mult), normed)
                if k >= 1:
                    add(k - 1)
            add(KD - 1)
            dve.wait_ge(x_root_ready, 1)
            steps.did(nc.vector.reciprocal(x_scale[:, :], x_scale[:, :]))
            steps.settle()
            for k in range(KD):
                steps.did(nc.vector.scalar_tensor_tensor(out=out[:, k, :], in0=x[:, k, :], scalar=gain(k),
                                                         in1=x_scale[:, :], op0=ALU.mult, op1=ALU.mult))
            steps.settle()


@contextmanager
def parts_of(nc, tiles, width=SEQ):
    with ExitStack() as stack:
        yield [stack.enter_context(nc.sbuf_tensor(f"{n}_{nc.next_id()}", [P, tiles, width], F32R))
               for n in ("high", "low")]


LOADED, SPLIT = 1, 2


def linear(nc, mem, w, parts, evacuate=None, on_vector=False, source=None, gate=None, result=None, primed=0,
           following=None):
    units, tiles, kt, size = w.units, w.tiles, w.kt, w.size
    n_banks = SLOTS * tiles
    split_following = following is not None and units % SLOTS == 0
    gates = {None: [], "silu": [(0, 1)], "relu": [(j, j) for j in range(tiles)]}[gate]
    per = len(gates)
    n_gates = SLOTS * per
    names = [f"{n}{s}" for n in ("filled", "high_ready", "low_ready") for s in range(SLOTS)]
    names += [f"{n}{g}" for n in ("gate_ready", "gated_high", "gated_low") for g in range(n_gates)]
    names += [f"product{b}" for b in range(n_banks)] + [f"taken{b}" for b in range(n_banks)]
    names += ["source_high", "source_low", *Primer.SEMS]
    with ExitStack() as stack:
        w_high, w_low = mem.w_high[:, :, 0:size], mem.w_low[:, :, 0:size]
        if gates:
            gated, = stack.enter_context(buffers(nc, gated=[P, n_gates, SEQ]))
        block, *sems = stack.enter_context(phase(nc, *names))
        filled, high_ready, low_ready = sems[:SLOTS], sems[SLOTS:2 * SLOTS], sems[2 * SLOTS:3 * SLOTS]
        sems = sems[3 * SLOTS:]
        gate_ready, gated_high, gated_low = sems[:n_gates], sems[n_gates:2 * n_gates], sems[2 * n_gates:3 * n_gates]
        sems = sems[3 * n_gates:]
        product, taken = sems[:n_banks], sems[n_banks:2 * n_banks]
        source_high, source_low, *primer_sems = sems[2 * n_banks:]
        primer = Primer(nc, mem, following, primer_sems)
        of_slot = [len(range(s, units, SLOTS)) for s in range(SLOTS)]

        def rounds(engine, take, prepare, prepare_following):
            loops = max(units - SLOTS, 0) // SLOTS
            if loops:
                with engine.Fori(0, loops) as i:
                    for s in range(SLOTS):
                        take(i, s)
                        prepare(i + 1, s)
            for u in range(loops * SLOTS, units):
                take(u // SLOTS, u % SLOTS)
                if u + SLOTS < units:
                    prepare(u // SLOTS + 1, u % SLOTS)
                elif following is not None:
                    prepare_following(u % SLOTS)

        def after(engine, sem, i, count=1):
            if not (type(i) is int and i == 0):
                engine.wait_ge(sem, i * count)

        @block.sync
        def _(sp):
            def fill(i, s):
                after(sp, low_ready[s], i)
                sp.dma_start(mem.ring[:, s, 0:size], w.of_unit(i * SLOTS + s)).then_inc(filled[s], 16)

            def fill_following(s):
                sp.wait_ge(low_ready[s], of_slot[s])
                primer.load_slot(sp, s)

            if not primed:
                for s in range(min(SLOTS, units)):
                    fill(0, s)
            rounds(sp, lambda i, s: None, fill, fill_following)
            if following is not None:
                primer.loads_done(sp)

        @block.tensor
        def _(pe):
            high, low = parts

            def multiply(i, s):
                pe.wait_ge(low_ready[s], i + 1)
                for j in range(tiles):
                    b = s * tiles + j
                    by_gate = [g for g, (from_tile, to_tile) in enumerate(gates) if j == from_tile != to_tile]
                    free = gate_ready[s * per + by_gate[0]] if by_gate else taken[b]
                    pe.wait_ge(free, i + 1)
                    for k in range(kt):
                        if source is not None and b == 0:
                            pe.wait_ge(source_low, k + 1)
                        at = (j * kt + k) * P
                        whole, rest = w_high[:, s, at:at + P], w_low[:, s, at:at + P]
                        nc.tensor.matmul(mem.bank[b][:, :], whole, high[:, k, :], start=(k == 0), stop=False)
                        nc.tensor.matmul(mem.bank[b][:, :], whole, low[:, k, :], start=False, stop=False)
                        last = nc.tensor.matmul(mem.bank[b][:, :], rest, high[:, k, :], start=False, stop=(k == kt - 1))
                    last.then_inc(product[b], 1)

            rounds(pe, multiply, lambda i, s: None, lambda s: None)

        @block.scalar
        def _(act):
            def round_weights(i, s):
                if primed:
                    after(act, filled[s], i, 16)
                else:
                    act.wait_ge(filled[s], i * 16 + 16)
                after(act, product[(s + 1) * tiles - 1], i)
                nc.scalar.activation(w_high[:, s, :], mem.ring[:, s, 0:size], ACT.Copy).then_inc(high_ready[s], 1)

            def take(i, s):
                for g, (from_tile, to_tile) in enumerate(gates):
                    b = s * tiles + from_tile
                    act.wait_ge(product[b], i + 1)
                    act.wait_ge(gated_low[s * per + g], i + 1)
                    nc.scalar.activation(gated[:, s * per + g, :], mem.bank[b][:, :],
                                         ACT.Silu if gate == "silu" else ACT.Relu).then_inc(gate_ready[s * per + g], 1)
                for g, (from_tile, to_tile) in enumerate(gates):
                    act.wait_ge(taken[s * tiles + to_tile], i + 2)
                    nc.scalar.activation(tile_at(result[0], (i * SLOTS + s) * per + g), gated[:, s * per + g, :],
                                         ACT.Copy).then_inc(gated_high[s * per + g], 1)
                if not (gates or on_vector):
                    for b in range(s * tiles, (s + 1) * tiles):
                        act.wait_ge(product[b], i + 1)
                        evacuate(mem.bank[b], i * n_banks + b).then_inc(taken[b], 1)

            if gates:
                for g in range(n_gates):
                    act.sem_inc(gate_ready[g], 1)
            elif not on_vector:
                for b in range(n_banks):
                    act.sem_inc(taken[b], 1)
            def round_following(s):
                if s == 0 and split_following:
                    act.wait_ge(product[tiles - 1], of_slot[0])
                    primer.high(act)

            for s in range(min(SLOTS, units)):
                if s == 0 and primed == SPLIT:
                    act.sem_inc(high_ready[0], 1)
                else:
                    round_weights(0, s)
                if source is not None and s == 0:
                    for k in range(kt):
                        nc.scalar.activation(parts[0][:, k, :], source[:, k, :], ACT.Copy).then_inc(source_high, 1)
            rounds(act, take, round_weights, round_following)

        @block.vector
        def _(dve):
            def rest_of_weights(i, s):
                dve.wait_ge(high_ready[s], i + 1)
                nc.vector.tensor_tensor(w_low[:, s, :], mem.ring[:, s, 0:size], w_high[:, s, :],
                                        ALU.subtract).then_inc(low_ready[s], 1)

            def take(i, s):
                for g, (from_tile, to_tile) in enumerate(gates):
                    b, whole = s * tiles + to_tile, gated[:, s * per + g, :]
                    dve.wait_ge(product[b], i + 1)
                    dve.wait_ge(gate_ready[s * per + g], i + 2)
                    nc.vector.tensor_tensor(whole, whole, mem.bank[b][:, :], ALU.mult).then_inc(taken[b], 1)
                for g in range(per):
                    dve.wait_ge(gated_high[s * per + g], i + 1)
                    tile = (i * SLOTS + s) * per + g
                    nc.vector.tensor_tensor(tile_at(result[1], tile), gated[:, s * per + g, :],
                                            tile_at(result[0], tile), ALU.subtract).then_inc(gated_low[s * per + g], 1)
                if on_vector:
                    for b in range(s * tiles, (s + 1) * tiles):
                        dve.wait_ge(product[b], i + 1)
                        evacuate(mem.bank[b], i * n_banks + b).then_inc(taken[b], 1)

            if gates or on_vector:
                for b in range(n_banks):
                    dve.sem_inc(taken[b], 1)
                for g in range(n_gates):
                    dve.sem_inc(gated_low[g], 1)
            def rest_of_following(s):
                if s == 0 and split_following:
                    primer.low(dve)

            for s in range(min(SLOTS, units)):
                if s == 0 and primed == SPLIT:
                    dve.sem_inc(low_ready[0], 1)
                else:
                    rest_of_weights(0, s)
                if source is not None and s == 0:
                    for k in range(kt):
                        dve.wait_ge(source_high, k + 1)
                        nc.vector.tensor_tensor(parts[1][:, k, :], source[:, k, :], parts[0][:, k, :],
                                                ALU.subtract).then_inc(source_low, 1)
            rounds(dve, take, rest_of_weights, rest_of_following)
    return SPLIT if split_following else LOADED


def project(nc, mem, w, source, evacuate, on_vector=False, primed=0):
    with parts_of(nc, w.kt) as parts:
        linear(nc, mem, w, parts, evacuate, on_vector, source=source, primed=primed)


def later_units(weights, first, part=slice(None)):
    return lambda u: weights(u + first)[:, part]


def tile_at(tensor, index):
    return tensor[:, bass.ds(index, 1), :].rearrange("p a n -> p (a n)")


def copy_out(nc, out):
    def evacuate(bank, tile):
        return nc.scalar.activation(tile_at(out, tile), bank[:, :], ACT.Copy)
    return evacuate


def add_out(nc, target):
    def evacuate(bank, tile):
        return nc.vector.tensor_tensor(tile_at(target, tile), tile_at(target, tile), bank[:, :], ALU.add)
    return evacuate


def token_major(nc, mem, w, cols, source, out, following):
    with phase(nc, "product", "taken", *Primer.SEMS) as (block, product, taken, *primer_sems):
        primer = Primer(nc, mem, following, primer_sems)

        @block.sync
        def _(sp):
            primer.load(sp)

        @block.tensor
        def _(pe):
            for t in range(TT):
                for k in range(KD):
                    last = nc.tensor.matmul(mem.bank[t][:, 0:cols], source[:, k, t * P:(t + 1) * P],
                                            w[:, k * cols:(k + 1) * cols], start=(k == 0), stop=(k == KD - 1))
                last.then_inc(product, 1)

        @block.vector
        def _(dve):
            primer.low(dve)

        @block.scalar
        def _(act):
            primer.high(act)
            for t in range(TT):
                act.wait_ge(product, t + 1)
                nc.scalar.activation(out[:, t, 0:cols], mem.bank[t][:, 0:cols], ACT.Copy).then_inc(taken, 1)
            act.wait_ge(taken, TT)


class FeedForward:

    def __init__(self, w_up, w_down, hidden_tiles, gate):
        self.gate, self.part = gate, hidden_tiles // 2
        units = self.part // (2 if gate == "relu" else 1)
        width = self.part * P
        self.up = [Weights(later_units(w_up, half * units), units, 2, KD) for half in range(2)]
        self.down = [Weights(later_units(w_down, 0, slice(half * width, (half + 1) * width)), KD, 1, self.part)
                     for half in range(2)]


def feed_forward(nc, mem, ff, first_out, on_vector):
    with parts_of(nc, KD) as parts, parts_of(nc, ff.part) as hidden:
        primed = SPLIT
        for half in range(2):
            primed = linear(nc, mem, ff.up[half], parts, source=None if half else mem.h, gate=ff.gate, result=hidden,
                            primed=primed, following=ff.down[half])
            primed = linear(nc, mem, ff.down[half], hidden, first_out(half), on_vector=on_vector(half), primed=primed,
                            following=None if half else ff.up[1])


def conv_gate(nc, mem, vec, u, padded, y, dist, distances):
    half = CONV_WIDTH // 2
    with buffers(nc, sig=[P, CONV_T, SEQ]) as (sig,), phase(nc, "gate_ready", "loaded", "dve_steps") as (
            block, gate_ready, loaded, dve_steps):
        @block.sync
        def _(sp):
            sp.dma_start(dist[:, :, :], distances).then_inc(loaded, 16)
            sp.wait_ge(loaded, 16)

        @block.scalar
        def _(act):
            for c in range(CONV_T):
                nc.scalar.activation(sig[:, c, :], u[:, U_CG + c, :], ACT.Sigmoid).then_inc(gate_ready, 1)

        @block.vector
        def _(dve):
            steps = Steps(dve, dve_steps)
            steps.did(nc.vector.memset(padded[:, :, 0:half], 0.0))
            steps.did(nc.vector.memset(padded[:, :, half + SEQ:], 0.0))
            for c in range(CONV_T):
                dve.wait_ge(gate_ready, c + 1)
                steps.did(nc.vector.tensor_tensor(padded[:, c, half:half + SEQ], u[:, U_CA + c, :], sig[:, c, :],
                                                  ALU.mult))
            steps.settle()
            for c in range(CONV_T):
                steps.did(nc.vector.tensor_scalar(y[:, c, :], padded[:, c, 0:SEQ],
                                                  VEC1(vec, "conv_w", c * CONV_WIDTH), VEC1(vec, "conv_b", c),
                                                  ALU.mult, ALU.add))
            steps.settle()


CONV_PART = (CONV_WIDTH - 1) // PAIRS1


CONV_STEPS = CONV_PART * CONV_T
CONV_SLOTS = 4


class ConvTaps:

    def __init__(self, nc, vec, padded, y, window, taps, scaled, copied, scaled_ready, added):
        self.nc, self.vec, self.padded, self.y = nc, vec, padded, y
        self.window, self.taps, self.scaled = window, taps, scaled
        self.copied, self.scaled_ready, self.added = copied, scaled_ready, added

    def scale(self, act, first, last):
        for n in range(first, last):
            i, c = divmod(n, CONV_T)
            act.wait_ge(self.copied, 1 + CONV_T)
            if n >= CONV_SLOTS:
                act.wait_ge(self.added, n - CONV_SLOTS + 1)
            self.nc.scalar.activation(self.scaled[:, n % CONV_SLOTS, :], self.window[:, c, i:i + SEQ], ACT.Identity,
                                      scale=self.taps[:, c, i:i + 1]).then_inc(self.scaled_ready, 1)

    def add(self, pool, part):
        first = VEC1.at["conv_w"][0] + 1
        self.nc.gpsimd.tensor_copy(self.window[:, :, :],
                                   self.padded[:, :, bass.ds(part * CONV_PART + 1, SEQ + CONV_PART - 1)]) \
            .then_inc(self.copied, 1)
        for c in range(CONV_T):
            self.nc.gpsimd.tensor_copy(self.taps[:, c, :],
                                       self.vec[:, bass.ds(part * CONV_PART + (first + c * CONV_WIDTH), CONV_PART)]) \
                .then_inc(self.copied, 1)
        for n in range(CONV_STEPS):
            c = n % CONV_T
            pool.wait_ge(self.scaled_ready, n + 1)
            if n >= CONV_T:
                pool.wait_ge(self.added, n - CONV_T + 1)
            self.nc.gpsimd.tensor_tensor(self.y[:, c, :], self.y[:, c, :], self.scaled[:, n % CONV_SLOTS, :],
                                         ALU.add).then_inc(self.added, 1)


def diff_lambda(nc, mem, lam_rows, coef):
    with buffers(nc, prod=[P, 2, DIFF_DIM], dots=[P, 4]) as (prod, dots), phase(
            nc, "dots_ready", "exps_ready", "dve_steps") as (block, dots_ready, exps_ready, dve_steps):
        @block.vector
        def _(dve):
            steps = Steps(dve, dve_steps)
            for m in range(2):
                steps.did(nc.vector.tensor_tensor(prod[:, m, :], lam_rows[:, 2 * m * DIFF_DIM:(2 * m + 1) * DIFF_DIM],
                                                  lam_rows[:, (2 * m + 1) * DIFF_DIM:(2 * m + 2) * DIFF_DIM], ALU.mult))
            steps.settle()
            steps.did(nc.vector.reduce_sum(dots[:, 0:2], prod[:, :, :], AX_X), dots_ready)
            steps.did(nc.vector.memset(coef[:, 0:1], 1.0))
            dve.wait_ge(exps_ready, 1)
            steps.did(nc.vector.tensor_tensor(dots[:, 0:1], dots[:, 3:4], dots[:, 2:3], ALU.subtract))
            steps.settle()
            steps.did(nc.vector.tensor_tensor(coef[:, 1:2], dots[:, 0:1], lam_rows[:, 4 * DIFF_DIM:4 * DIFF_DIM + 1],
                                              ALU.subtract))
            steps.settle()

        @block.scalar
        def _(act):
            act.wait_ge(dots_ready, 1)
            nc.scalar.activation(dots[:, 2:4], dots[:, 0:2], ACT.Exp).then_inc(exps_ready, 1)


def diff_attention(nc, mem, vec, lam_rows, dist, u, tm, y, padded):
    first_tile = CONV_T
    units = [(h, t) for h in range(2) for t in range(TT)]
    with buffers(nc, coef=[P, 2]) as (coef,):
        diff_lambda(nc, mem, lam_rows, coef)
        with nc.Fori(0, PAIRS1) as j, buffers(
                nc, q=[P, SEQ], k=[P, SEQ], v=[P, TT, P], slope=[P, 2], scores=[P, 4, SEQ], tops=[P, 16],
                sums=[P, 16], inv=[P, 16], mixed=[P, 2, SEQ], turned=[P, 2, SEQ], window=[P, CONV_T, SEQ + CONV_PART - 1],
                taps=[P, CONV_T, CONV_PART], scaled=[P, CONV_SLOTS, SEQ]) as (
                q, k, v, slope, scores, tops, sums, inv, mixed, turned, window, taps, scaled), phase(
                nc, "staged", "dve_staged", "score", "topped", "exped", "mixed_ready", "turn", "turned_ready", "applied",
                "conv_copied", "conv_scaled", "conv_added", "dve_steps") as (
                block, staged, dve_staged, score, topped, exped, mixed_ready, turn, turned_ready, applied,
                conv_copied, conv_scaled, conv_added, dve_steps):
            out_bank = mem.bank[6]

            convolution = ConvTaps(nc, vec, padded, y, window, taps, scaled, conv_copied, conv_scaled, conv_added)

            @block.gpsimd
            def _(pool):
                convolution.add(pool, j)

            @block.scalar
            def _(act):
                nc.scalar.activation(q[:, :], tile_at(u, j + U_DQ), ACT.Copy, scale=DIFF_DIM ** -0.5).then_inc(staged, 1)
                nc.scalar.activation(k[:, :], tile_at(u, j + U_DK), ACT.Copy).then_inc(staged, 1)

                def turned_copy(n):
                    act.wait_ge(turn, n + 1)
                    if n >= 2:
                        act.wait_ge(applied, n - 1)
                    nc.scalar.activation(turned[:, n % 2, :], mem.bank[4 + n % 2][:, :], ACT.Copy) \
                        .then_inc(turned_ready, 1)

                for n in range(len(units)):
                    for m in range(2):
                        i = 2 * n + m
                        act.wait_ge(topped, n + 1)
                        nc.scalar.activation(scores[:, i % 4, :], scores[:, i % 4, :], ACT.Exp, bias=tops[:, i:i + 1],
                                             scale=-1.0, accum_out=sums[:, i:i + 1]).then_inc(exped, 1)
                    if n >= 1:
                        turned_copy(n - 1)
                    convolution.scale(act, n * CONV_STEPS // len(units), (n + 1) * CONV_STEPS // len(units))
                turned_copy(len(units) - 1)

            @block.tensor
            def _(pe):
                pe.wait_ge(staged, 2)
                pe.wait_ge(dve_staged, 1)

                def scored(n):
                    h, t = units[n]
                    for m in range(2):
                        i = 2 * n + m
                        if i >= 4:
                            pe.wait_ge(topped, (i - 4) // 2 + 1)
                        lanes = slice(DIFF_DIM * (2 * h + m), DIFF_DIM * (2 * h + m + 1))
                        nc.tensor.matmul(mem.bank[i % 4][:, :], q[lanes, t * P:(t + 1) * P], k[lanes, :],
                                         start=True, stop=True).then_inc(score, 1)

                def transposed(n):
                    pe.wait_ge(mixed_ready, n + 1)
                    if n >= 2:
                        pe.wait_ge(turned_ready, n - 1)
                    for b in range(TT):
                        last = nc.tensor.transpose(mem.bank[4 + n % 2][:, b * P:(b + 1) * P],
                                                   mixed[:, n % 2, b * P:(b + 1) * P], CONST(mem.const, "ident"))
                    last.then_inc(turn, 1)

                def apply(n):
                    h, t = units[n]
                    pe.wait_ge(turned_ready, n + 1)
                    for b in range(TT):
                        last = nc.tensor.matmul(out_bank[h * HEAD:(h + 1) * HEAD, t * P:(t + 1) * P],
                                                v[:, b, h * HEAD:(h + 1) * HEAD], turned[:, n % 2, b * P:(b + 1) * P],
                                                start=(b == 0), stop=(b == TT - 1))
                    last.then_inc(applied, 1)

                scored(0)
                scored(1)
                for n in range(len(units)):
                    if n + 2 < len(units):
                        scored(n + 2)
                    transposed(n)
                    if n >= 1:
                        apply(n - 1)
                apply(len(units) - 1)

            @block.vector
            def _(dve):
                steps = Steps(dve, dve_steps)
                steps.did(nc.vector.tensor_copy(v[:, :, :], tm[:, :, bass.ds(j * P, P)]), dve_staged)
                steps.did(nc.vector.tensor_copy(slope[:, :], CONST(mem.const, "slopes")[:, bass.ds(j * 2, 2)]), dve_staged)
                steps.settle()

                def biased(n):
                    h, t = units[n]
                    for m in range(2):
                        i = 2 * n + m
                        dve.wait_ge(score, i + 1)
                        if n >= 2:
                            dve.wait_ge(mixed_ready, n - 1)
                        steps.did(nc.vector.scalar_tensor_tensor(
                            out=scores[:, i % 4, :], in0=dist[:, t, :], scalar=slope[:, h:h + 1],
                            in1=mem.bank[i % 4][:, :], op0=ALU.mult, op1=ALU.subtract))
                    steps.settle()
                    i = 2 * n
                    steps.did(nc.vector.tensor_reduce(tops[:, i:i + 2], scores[:, i % 4:i % 4 + 2, :], AX_X, ALU.min),
                              topped)

                def mix(n):
                    i = 2 * n
                    dve.wait_ge(exped, i + 2)
                    steps.did(nc.vector.reciprocal(inv[:, i:i + 2], sums[:, i:i + 2]))
                    steps.settle()
                    steps.did(nc.vector.tensor_tensor(inv[:, i + 1:i + 2], inv[:, i + 1:i + 2], coef[:, 1:2], ALU.mult))
                    if n >= 2:
                        dve.wait_ge(turn, n - 1)
                    steps.did(nc.vector.tensor_scalar(mixed[:, n % 2, :], scores[:, i % 4, :], inv[:, i:i + 1], None,
                                                      ALU.mult))
                    steps.settle()
                    steps.did(nc.vector.scalar_tensor_tensor(
                        out=mixed[:, n % 2, :], in0=scores[:, (i + 1) % 4, :], scalar=inv[:, i + 1:i + 2],
                        in1=mixed[:, n % 2, :], op0=ALU.mult, op1=ALU.add), mixed_ready)

                for n in range(len(units)):
                    biased(n)
                    if n >= 1:
                        mix(n - 1)
                mix(len(units) - 1)
                dve.wait_ge(applied, len(units))
                steps.did(nc.vector.tensor_copy(tile_at(y, j + first_tile), out_bank[:, :]))
                steps.settle()


def mixer_norms(nc, mem, vec, lam_rows, u, y, following):
    first, heads_tiles = CONV_T, 2 * PAIRS1
    tiles = heads_tiles + 1
    per = TT * 2
    with buffers(nc, squares=[P, CONV_T + heads_tiles, SEQ], root=[P, tiles, TT, 2], wide=[P, tiles, TT, P],
                 gate=[P, PAIRS1, SEQ], gain=[P, 2]) as (squares, root, wide, gate, gain), phase(
            nc, "mean_ready", "centred", "squared", "summed", "rooted", "widened", "gated", "spread", "conv_normed",
            "normed", "dve_steps", *Primer.SEMS) as (
            block, mean_ready, centred, squared, summed, rooted, widened, gated, spread, conv_normed,
            normed, dve_steps, *primer_sems):
        primer = Primer(nc, mem, following, primer_sems)
        sums, spread_banks = mem.bank[0], mem.bank[1:]
        mean = spread_banks[heads_tiles]

        @block.sync
        def _(sp):
            primer.load(sp)

        @block.scalar
        def _(act):
            for i in range(heads_tiles):
                nc.scalar.activation(squares[:, first + i, :], y[:, first + i, :], ACT.Square).then_inc(squared, 1)
            for c in range(CONV_T):
                act.wait_ge(centred, c + 1)
                nc.scalar.activation(squares[:, c, :], y[:, c, :], ACT.Square).then_inc(squared, 1)
            for i in range(PAIRS1):
                nc.scalar.activation(gate[:, i, :], u[:, U_GZ + i, :], ACT.Silu).then_inc(gated, 1)
            primer.high(act)
            act.wait_ge(summed, 1)
            for part, (at, eps, width) in enumerate([(slice(0, PAIRS1), 1, HEAD), (slice(PAIRS1, heads_tiles), 0, HEAD),
                                                     (slice(heads_tiles, tiles), 1, CONV_CH)]):
                nc.scalar.activation(root[:, at, :, :].rearrange("p i t h -> p (i t h)"),
                                     sums[:, at.start * per:at.stop * per], ACT.Sqrt,
                                     bias=mem.eps[:, eps:eps + 1], scale=1.0 / width).then_inc(rooted, 1)
            for c in range(CONV_T):
                act.wait_ge(conv_normed, c + 1)
                nc.scalar.activation(y[:, c, :], y[:, c, :], ACT.Silu, scale=VEC1(vec, "ln_w", c),
                                     bias=VEC1(vec, "ln_b", c))

        @block.tensor
        def _(pe):
            for c in range(CONV_T):
                last = nc.tensor.matmul(mean[:, :], CONST(mem.const, "ones"), y[:, c, :],
                                        start=(c == 0), stop=(c == CONV_T - 1))
            last.then_inc(mean_ready, 1)
            heads = CONST(mem.const, "pair_ones").rearrange("p (h d) -> p d h", d=HEAD)[:, 0, :]
            for i in range(heads_tiles):
                pe.wait_ge(squared, i + 1)
                for t in range(TT):
                    nc.tensor.matmul(sums[:, i * per + 2 * t:i * per + 2 * t + 2],
                                     squares[:, first + i, t * P:(t + 1) * P], heads, start=True, stop=True)
            pe.wait_ge(squared, heads_tiles + CONV_T)
            for t in range(TT):
                at = heads_tiles * per + 2 * t
                for c in range(CONV_T):
                    last = nc.tensor.matmul(sums[:, at:at + 2], squares[:, c, t * P:(t + 1) * P],
                                            CONST(mem.const, "ones")[:, 0:2], start=(c == 0), stop=(c == CONV_T - 1))
            last.then_inc(summed, 1)
            pe.wait_ge(centred, CONV_T)
            for i in range(tiles):
                pe.wait_ge(widened, i + 1)
                for t in range(TT):
                    last = nc.tensor.matmul(spread_banks[i][:, t * P:(t + 1) * P], wide[:, i, t, :],
                                            CONST(mem.const, "ident"), start=True, stop=True)
                last.then_inc(spread, 1)

        @block.vector
        def _(dve):
            steps = Steps(dve, dve_steps)
            steps.did(nc.vector.tensor_tensor(gain[:, 0:1], VEC1(vec, "subln"),
                                              lam_rows[:, 4 * DIFF_DIM + 1:4 * DIFF_DIM + 2], ALU.mult))
            steps.did(nc.vector.tensor_copy(gain[:, 1:2], VEC1(vec, "delta_norm")))
            dve.wait_ge(mean_ready, 1)
            for c in range(CONV_T):
                steps.did(nc.vector.scalar_tensor_tensor(out=y[:, c, :], in0=mean[:, :], scalar=-1.0 / CONV_CH,
                                                         in1=y[:, c, :], op0=ALU.mult, op1=ALU.add), centred)
            primer.low(dve)
            dve.wait_ge(rooted, 3)
            steps.did(nc.vector.reciprocal(root[:, :, :, :], root[:, :, :, :]))
            steps.settle()
            for i in range(tiles):
                steps.did(nc.vector.tensor_copy(
                    wide[:, i, :, :].rearrange("p t (h d) -> p (t h) d", h=2),
                    root[:, i, :, :].rearrange("p t h -> p (t h)").unsqueeze(2).broadcast_to([P, per, HEAD])), widened)
            for i in range(heads_tiles):
                dve.wait_ge(spread, i + 1)
                to = y[:, first + i, :]
                steps.did(nc.vector.scalar_tensor_tensor(out=to, in0=to, scalar=gain[:, i // PAIRS1:i // PAIRS1 + 1],
                                                         in1=spread_banks[i][:, :], op0=ALU.mult, op1=ALU.mult), normed)
            dve.wait_ge(spread, tiles)
            for c in range(CONV_T):
                steps.did(nc.vector.tensor_tensor(y[:, c, :], y[:, c, :], spread_banks[heads_tiles][:, :], ALU.mult),
                          conv_normed)
            dve.wait_ge(gated, PAIRS1)
            for i in range(PAIRS1):
                dve.wait_ge(normed, PAIRS1 + i + 1)
                to = y[:, first + PAIRS1 + i, :]
                steps.did(nc.vector.tensor_tensor(to, to, gate[:, i, :], ALU.mult))
            steps.settle()


G_NEG, G_NBETA, G_BETA, G_BEXP, G_KDEC, G_LAST = range(6)
KINDS = 6
GH = 2 * DELTA_HEADS


def delta_inputs(nc, mem, vec, gates, tm, u, cols, rows):
    n_conv, n_norm = 3 * PAIRS1, 2 * PAIRS1
    per = TT * 2
    early_rows = 4
    with buffers(nc, conv=[P, n_conv, SEQ], squares=[P, n_norm, SEQ], root=[P, n_norm, TT, 2],
                 wide=[P, n_norm, TT, P], beta=[P, TT, GH], pre=[P, TT, GH], soft=[P, TT, GH], g=[P, TT, GH],
                 rate=[P, GH],
                 run=[P, TT, GH], total=[P, TT, GH]) as (
            conv, squares, root, wide, beta, pre, soft, g, rate, run, total), phase(
            nc, "conv_done", "silued", "squared", "norms_summed", "rooted", "widened", "norms_spread", "normed",
            "beta_ready", "pre_ready", "soft_ready", "g_ready", "summed", "taken", "row_ready", "row_taken",
            "shifted", "exped", "act_steps", "dve_steps") as (
            block, conv_done, silued, squared, norms_summed, rooted, widened, norms_spread, normed, beta_ready,
            pre_ready, soft_ready, g_ready, summed, taken, row_ready, row_taken,
            shifted, exped, act_steps, dve_steps):
        run_sum, whole, norm_sums = mem.bank[0], mem.bank[1], mem.bank[4]
        row_banks = [mem.bank[b] for b in (2, 3, 6, 7)]
        spread_banks = [mem.bank[b] for b in (5, 0, 1)]

        @block.scalar
        def _(act):
            steps = Steps(act, act_steps)

            def take_rows(first, last):
                for n in range(first, last):
                    act.wait_ge(row_ready, n + 1)
                    nc.scalar.activation(rows[:, n, :], row_banks[n % len(row_banks)][:, :], ACT.Copy) \
                        .then_inc(row_taken, 1)

            def finish_conv(part):
                tiles = range(part * PAIRS1, (part + 1) * PAIRS1)
                for i in tiles:
                    act.wait_ge(conv_done, i + 1)
                    nc.scalar.activation(conv[:, i, :], conv[:, i, :], ACT.Silu).then_inc(silued, 1)
                for i in tiles:
                    act.wait_ge(silued, i + 1)
                    nc.scalar.activation(squares[:, i, :], conv[:, i, :], ACT.Square).then_inc(squared, 1)

            nc.scalar.activation(beta[:, :, :], tm[:, :, DIFF_W:DIFF_W + GH], ACT.Sigmoid).then_inc(beta_ready, 1)
            steps.did(nc.scalar.activation(rate[:, :], gates[:, 0, :], ACT.Exp))
            act.wait_ge(pre_ready, 1)
            steps.did(nc.scalar.activation(soft[:, :, :], soft[:, :, :], ACT.Exp))
            steps.settle()
            nc.scalar.activation(soft[:, :, :], soft[:, :, :], ACT.Ln, bias=1.0).then_inc(soft_ready, 1)
            finish_conv(0)
            act.wait_ge(summed, 1)
            steps.did(nc.scalar.activation(run[:, :, :], run_sum[:, 0:TT * GH], ACT.Copy), taken)
            steps.did(nc.scalar.activation(total[:, :, :], whole[:, 0:TT * GH], ACT.Copy), taken)
            finish_conv(1)
            take_rows(0, early_rows)
            for i in range(n_norm, n_conv):
                act.wait_ge(conv_done, i + 1)
                nc.scalar.activation(u[:, U_GQ + i, :], conv[:, i, :], ACT.Silu)
            act.wait_ge(norms_summed, 2)
            nc.scalar.activation(root[:, :, :, :].rearrange("p i t h -> p (i t h)"), norm_sums[:, 0:n_norm * per],
                                 ACT.Sqrt, bias=mem.eps[:, 0:1]).then_inc(rooted, 1)
            take_rows(early_rows, GH)
            act.wait_ge(shifted, 1)
            nc.scalar.activation(cols[:, G_KDEC, :, :], cols[:, G_KDEC, :, :], ACT.Exp).then_inc(exped, 1)
            nc.scalar.activation(cols[:, G_LAST, :, :], total[:, :, :], ACT.Exp).then_inc(exped, 1)
            nc.scalar.activation(cols[:, G_BEXP, :, :], run[:, :, :], ACT.Exp).then_inc(exped, 1)

        @block.vector
        def _(dve):
            steps = Steps(dve, dve_steps)

            def convolve(part):
                tiles = range(part * PAIRS1, (part + 1) * PAIRS1)
                tap = lambda i, n: VEC1(vec, "delta_conv", SHORT_CONV * i + n)
                for i in tiles:
                    steps.did(nc.vector.tensor_scalar(conv[:, i, :], u[:, U_GQ + i, :], tap(i, 1), None, ALU.mult))
                steps.settle()
                for i in tiles:
                    steps.did(nc.vector.scalar_tensor_tensor(
                        out=conv[:, i, 1:SEQ], in0=u[:, U_GQ + i, 0:SEQ - 1], scalar=tap(i, 0),
                        in1=conv[:, i, 1:SEQ], op0=ALU.mult, op1=ALU.add))
                steps.settle()
                for i in tiles:
                    steps.did(nc.vector.scalar_tensor_tensor(
                        out=conv[:, i, 0:SEQ - 1], in0=u[:, U_GQ + i, 1:SEQ], scalar=tap(i, 2),
                        in1=conv[:, i, 0:SEQ - 1], op0=ALU.mult, op1=ALU.add), conv_done)

            bias = gates[:, 1, :].unsqueeze(1).broadcast_to([P, TT, GH])
            steps.did(nc.vector.tensor_tensor(pre[:, :, :], tm[:, :, DIFF_W + GH:DIFF_W + 2 * GH], bias, ALU.add))
            steps.settle()
            steps.did(nc.vector.scalar_tensor_tensor(out=soft[:, :, :], in0=pre[:, :, :], scalar=-1.0,
                                                     in1=pre[:, :, :], op0=ALU.mult, op1=ALU.min), pre_ready)
            convolve(0)
            dve.wait_ge(soft_ready, 1)
            steps.did(nc.vector.scalar_tensor_tensor(out=pre[:, :, :], in0=pre[:, :, :], scalar=0.0,
                                                     in1=soft[:, :, :], op0=ALU.max, op1=ALU.add))
            steps.settle()
            dve.wait_ge(act_steps, 1)
            steps.did(nc.vector.scalar_tensor_tensor(
                out=g[:, :, :], in0=pre[:, :, :], scalar=-1.0, in1=rate[:, :].unsqueeze(1).broadcast_to([P, TT, GH]),
                op0=ALU.mult, op1=ALU.mult), g_ready)
            dve.wait_ge(beta_ready, 1)
            steps.did(nc.vector.tensor_scalar(cols[:, G_NBETA, :, :], beta[:, :, :], -1.0, None, ALU.mult))
            steps.did(nc.vector.tensor_copy(cols[:, G_BETA, :, :], beta[:, :, :]))
            convolve(1)
            dve.wait_ge(taken, 2)
            steps.did(nc.vector.tensor_scalar(cols[:, G_NEG, :, :], run[:, :, :], -1.0, None, ALU.mult))
            steps.did(nc.vector.tensor_tensor(cols[:, G_KDEC, :, :], total[:, :, :], run[:, :, :], ALU.subtract),
                      shifted)
            convolve(2)
            dve.wait_ge(rooted, 1)
            steps.did(nc.vector.reciprocal(root[:, :, :, :], root[:, :, :, :]))
            steps.settle()
            for i in range(n_norm):
                steps.did(nc.vector.tensor_copy(
                    wide[:, i, :, :].rearrange("p t (h d) -> p (t h) d", h=2),
                    root[:, i, :, :].rearrange("p t h -> p (t h)").unsqueeze(2).broadcast_to([P, per, HEAD])), widened)
            dve.wait_ge(silued, n_norm)
            for i in range(n_norm):
                dve.wait_ge(norms_spread, i + 1)
                scale = HEAD ** -0.5 if i < PAIRS1 else 1.0
                steps.did(nc.vector.scalar_tensor_tensor(
                    out=u[:, U_GQ + i, :], in0=conv[:, i, :], scalar=scale, in1=spread_banks[i % len(spread_banks)][:, :],
                    op0=ALU.mult, op1=ALU.mult), normed)
            dve.wait_ge(exped, 3)
            steps.did(nc.vector.tensor_tensor(cols[:, G_BEXP, :, :], cols[:, G_BEXP, :, :], beta[:, :, :], ALU.mult))
            steps.settle()

        @block.tensor
        def _(pe):
            pe.wait_ge(g_ready, 1)
            half = DELTA_HEADS
            triangle = [CONST(mem.const, "upper_in"), CONST(mem.const, "lower_in")]
            for t in range(TT):
                nc.tensor.matmul(whole[:, t * GH:(t + 1) * GH], CONST(mem.const, "ones"), g[:, t, :],
                                 start=True, stop=True)
                for d in range(2):
                    last = nc.tensor.matmul(run_sum[:, t * GH + d * half:t * GH + (d + 1) * half], triangle[d],
                                            g[:, t, d * half:(d + 1) * half], start=True, stop=True)
            last.then_inc(summed, 1)

            def make_rows(first, last):
                for n in range(first, last):
                    if n >= len(row_banks):
                        pe.wait_ge(row_taken, n - len(row_banks) + 1)
                    for t in range(TT):
                        product = nc.tensor.matmul(row_banks[n % len(row_banks)][:, t * P:(t + 1) * P],
                                                   g[:, t, n:n + 1].broadcast_to([P, P]), triangle[n // half],
                                                   start=True, stop=True)
                    product.then_inc(row_ready, 1)

            def sum_squares(part):
                for i in range(part * PAIRS1, (part + 1) * PAIRS1):
                    pe.wait_ge(squared, i + 1)
                    for t in range(TT):
                        product = nc.tensor.matmul(norm_sums[:, i * per + 2 * t:i * per + 2 * t + 2],
                                                   squares[:, i, t * P:(t + 1) * P], heads, start=True, stop=True)
                product.then_inc(norms_summed, 1)

            heads = CONST(mem.const, "pair_ones").rearrange("p (h d) -> p d h", d=HEAD)[:, 0, :]
            sum_squares(0)
            make_rows(0, early_rows)
            sum_squares(1)
            make_rows(early_rows, GH)
            pe.wait_ge(taken, 2)
            for i in range(n_norm):
                pe.wait_ge(widened, i + 1)
                if i >= len(spread_banks):
                    pe.wait_ge(normed, i - len(spread_banks) + 1)
                for t in range(TT):
                    last = nc.tensor.matmul(spread_banks[i % len(spread_banks)][:, t * P:(t + 1) * P], wide[:, i, t, :],
                                            CONST(mem.const, "ident"), start=True, stop=True)
                last.then_inc(norms_spread, 1)


def delta_prepare(nc, mem, u, cols, rows, hp, b):
    with buffers(nc, v=[P, SEQ]) as (v,), phase(
            nc, "staged", "turned", "turned_taken", "product", "bounded", "exped", "dve_steps") as (
            block, staged, turned, turned_taken, product, bounded, exped, dve_steps):
        streams = [(d, par) for d in range(2) for par in range(2)]

        @block.vector
        def _(dve):
            steps = Steps(dve, dve_steps)
            for d in range(2):
                steps.did(nc.vector.tensor_copy(
                    b.cols[:, :, d, :],
                    cols[:, :, :, :].rearrange("p k t h -> p (k t) h")[:, :, bass.ds(hp * 2 + d * DELTA_HEADS, 2)]))
            steps.settle()

            def bound(n):
                d, par = streams[n]
                row = rows[:, bass.ds(hp * 2 + d * DELTA_HEADS + par, 1), :].rearrange("p a n -> p (a n)")
                masks = [("lower_strict_max", ALU.max), ("upper_in_min", ALU.min)] if d == 0 else \
                    [("upper_strict_max", ALU.max), ("lower_in_min", ALU.min)]
                for to, (mask, op) in zip((b.neg, b.seen), masks):
                    for t in range(TT):
                        steps.did(nc.vector.scalar_tensor_tensor(
                            out=to[:, n, t * P:(t + 1) * P], in0=row[:, t * P:(t + 1) * P],
                            scalar=b.cols[:, G_NEG * TT + t, d, par:par + 1], in1=CONST(mem.const, mask),
                            op0=ALU.add, op1=op), bounded)

            for n in range(len(streams)):
                bound(n)
            for n, (d, par) in enumerate(streams):
                dve.wait_ge(exped, 2 * n + 2)
                dve.wait_ge(product, par + 1)
                for t in range(TT):
                    at = b.neg[:, n, t * P:(t + 1) * P]
                    steps.did(nc.vector.scalar_tensor_tensor(
                        out=at, in0=mem.bank[4 + par][:, t * P:(t + 1) * P],
                        scalar=b.cols[:, G_NBETA * TT + t, d, par:par + 1], in1=at, op0=ALU.mult, op1=ALU.mult))
            for n, (d, par) in enumerate(streams):
                dve.wait_ge(product, 2 + par + 1)
                steps.did(nc.vector.tensor_tensor(b.seen[:, n, :], mem.bank[6 + par][:, :], b.seen[:, n, :], ALU.mult))
            steps.settle()

        @block.scalar
        def _(act):
            for to, first in ((b.k, U_GK), (b.q, U_GQ), (v, U_GV)):
                nc.scalar.activation(to[:, :], tile_at(u, hp + first), ACT.Copy).then_inc(staged, 1)
            for n in range(4):
                for e, to in enumerate((b.neg, b.seen)):
                    act.wait_ge(bounded, 2 * TT * n + TT * (e + 1))
                    nc.scalar.activation(to[:, n, :], to[:, n, :], ACT.Exp, scale=-1.0 if e == 0 else 1.0) \
                        .then_inc(exped, 1)
                if n < 2:
                    act.wait_ge(turned, n + 1)
                    nc.scalar.activation((b.k_rows, b.v_rows)[n][:, :, :].rearrange("p t n -> p (t n)"),
                                         mem.bank[2 + n][:, :], ACT.Copy).then_inc(turned_taken, 1)

        @block.tensor
        def _(pe):
            pe.wait_ge(staged, 1)
            for n in range(4):
                if n == 2:
                    pe.wait_ge(staged, 2)
                lanes = slice((n % 2) * HEAD, (n % 2 + 1) * HEAD)
                for t in range(TT):
                    right = (b.k if n < 2 else b.q)[lanes, t * P:(t + 1) * P]
                    last = nc.tensor.matmul(mem.bank[4 + n][:, t * P:(t + 1) * P], b.k[lanes, t * P:(t + 1) * P],
                                            right, start=True, stop=True)
                last.then_inc(product, 1)
                if n < 2:
                    pe.wait_ge(staged, 2 * n + 1)
                    for t in range(TT):
                        last = nc.tensor.transpose(mem.bank[2 + n][:, t * P:(t + 1) * P],
                                                   (b.k, v)[n][:, t * P:(t + 1) * P], CONST(mem.const, "ident"))
                    last.then_inc(turned, 1)


class ScanInputs:

    def __init__(self, nc, rows, hp, b):
        self.nc, self.rows, self.hp, self.b = nc, rows, hp, b
        self.lanes = [slice(0, HEAD), slice(HEAD, 2 * HEAD)]
        self.streams = [(d, par) for d in range(2) for par in range(2)]

    def scalar(self, rows_exped):
        nc, b = self.nc, self.b
        for d, par in self.streams:
            row = self.rows[self.lanes[par], bass.ds(self.hp * 2 + d * DELTA_HEADS + par, 1), :]
            nc.scalar.activation(b.qg[self.lanes[par], d, :], row.rearrange("p a n -> p (a n)"), ACT.Exp) \
                .then_inc(rows_exped, 1)
        for n, (d, par) in enumerate(self.streams):
            for kind, to, rows_of in ((G_BETA, b.vb, b.v_rows), (G_BEXP, b.kb, b.k_rows), (G_KDEC, b.kd, b.k_rows)):
                for t in range(TT):
                    nc.scalar.activation(to[:, n, t, :], rows_of[:, t, self.lanes[par]], ACT.Copy,
                                         scale=b.cols[:, kind * TT + t, d, par:par + 1])
            nc.scalar.activation(b.last_decay[self.lanes[par], d, :],
                                 b.cols[self.lanes[par], G_LAST * TT:(G_LAST + 1) * TT, d, par], ACT.Copy)

    def gpsimd(self, pool, rows_exped):
        for d in range(2):
            pool.wait_ge(rows_exped, 2 * d + 2)
            self.nc.gpsimd.tensor_tensor(self.b.qg[:, d, :], self.b.qg[:, d, :], self.b.q[:, :], ALU.mult)


def invert(nc, mem, neg, turned, upper, late=None, beside=None):
    count = len(upper)

    def of_side(columns, level, n):
        return columns.rearrange("p (g h b) -> p g h b", h=2, b=2 ** level)[:, :, 0 if upper[n] else 1, :]

    def chunks(x):
        return x.rearrange("p (t c) -> p t c", t=TT)

    with buffers(nc, joint=[P, count, SEQ]) as (joint,), phase(
            nc, *[f"{w}{n}" for n in range(count) for w in ("flipped", "joined", "grown", "added")],
            "late_product", "late_taken", "rows_exped") as (block, *sems):
        *sems, late_product, late_taken, rows_exped = sems
        flipped, joined, grown, added = sems[0::4], sems[1::4], sems[2::4], sems[3::4]
        slices = [slice(t * P, (t + 1) * P) for t in range(TT)]

        if beside is not None:
            @block.scalar
            def _(act):
                beside.scalar(rows_exped)

            @block.gpsimd
            def _(pool):
                beside.gpsimd(pool, rows_exped)

        @block.vector
        def _(dve):
            def join(n, l):
                mask = mem.levels[:, upper[n], l, :].unsqueeze(1).broadcast_to([P, TT, P])
                nc.vector.tensor_tensor(chunks(joint[:, n, :]), chunks(turned[:, n, :]), mask, ALU.mult) \
                    .then_inc(joined[n], 1)

            for n in range(count):
                dve.wait_ge(flipped[n], 1)
                nc.vector.tensor_tensor(chunks(turned[:, n, :]), chunks(mem.bank[2 * n][:, :]),
                                        CONST(mem.const, "ident").unsqueeze(1).broadcast_to([P, TT, P]), ALU.add) \
                    .then_inc(added[n], 1)
            for n in range(count):
                dve.wait_ge(added[n], 1)
                join(n, 0)
            for l in range(LEVELS):
                for n in range(count):
                    last_level = l == LEVELS - 1
                    dve.wait_ge(grown[n], l + 1)
                    dve.wait_ge(joined[n], l + 1)
                    at = of_side(turned[:, n, :], l, n)
                    nc.vector.tensor_tensor(at, at, of_side(mem.bank[2 * n][:, :], l, n), ALU.add).then_inc(added[n], 1)
                    if not last_level:
                        nc.vector.tensor_tensor(neg[:, n, :], neg[:, n, :], mem.bank[2 * n + 1][:, :], ALU.add) \
                            .then_inc(added[n], 1)
                        dve.wait_ge(added[n], 2 * l + 2)
                        join(n, l + 1)
                if late is not None and l < late.groups:
                    dve.wait_ge(late_product, l + 1)
                    late.take(l).then_inc(late_taken, 1)

        @block.tensor
        def _(pe):
            for n in range(count):
                for c in slices:
                    last = nc.tensor.matmul(mem.bank[2 * n][:, c], neg[:, n, c], CONST(mem.const, "ident"),
                                            start=True, stop=True)
                last.then_inc(flipped[n], 1)
            for l in range(LEVELS):
                for n in range(count):
                    pe.wait_ge(joined[n], l + 1)
                    pe.wait_ge(added[n], 2 * l + 1)
                    if l < LEVELS - 1:
                        for c in slices:
                            nc.tensor.matmul(mem.bank[2 * n + 1][:, c], joint[:, n, c], neg[:, n, c],
                                             start=True, stop=True)
                    for c in slices:
                        last = nc.tensor.matmul(of_side(mem.bank[2 * n][:, c], l, n), neg[:, n, c],
                                                of_side(joint[:, n, c], l, n), start=True, stop=True)
                    last.then_inc(grown[n], 1)
                if late is not None and l < late.groups:
                    if l >= late.banks:
                        pe.wait_ge(late_taken, l - late.banks + 1)
                    late.multiply(l).then_inc(late_product, 1)


def delta_scan(nc, mem, y, hp, b):
    first_tile = CONV_T + PAIRS1
    with buffers(nc, w=[P, 2, SEQ], state=[P, 2, HEAD], fresh=[P, 2, 2, P], o=[P, 2, SEQ]) as (
            w, state, fresh, o), phase(
            nc, "solved", "solved_taken", "passed0", "passed1", "fresh0", "fresh1",
            "out0", "out1", "grown0", "grown1", "state0", "state1", "out_taken0", "out_taken1",
            "dve_steps") as (
            block, solved, solved_taken, passed0, passed1, fresh0, fresh1,
            out0, out1, grown0, grown1, state0, state1, out_taken0, out_taken1, dve_steps):
        vb, kb, kd, u0, qg, last_decay = b.vb, b.kb, b.kd, b.u0, b.qg, b.last_decay
        passed, fresh_ready, out_ready = (passed0, passed1), (fresh0, fresh1), (out0, out1)
        grown, state_ready, out_taken = (grown0, grown1), (state0, state1), (out_taken0, out_taken1)
        lanes = [slice(0, HEAD), slice(HEAD, 2 * HEAD)]
        chunk = [lambda s: s, lambda s: TT - 1 - s]

        @block.vector
        def _(dve):
            steps = Steps(dve, dve_steps)
            for s in range(TT):
                for d in range(2):
                    t = chunk[d](s)
                    if s == 0:
                        dve.wait_ge(solved_taken, 2 * d + 2)
                    if s >= 2:
                        dve.wait_ge(out_ready[d], s - 1)
                    for par in range(2):
                        e = slice(par * HEAD, (par + 1) * HEAD)
                        if s == 0:
                            steps.did(nc.vector.tensor_copy(fresh[:, d, s % 2, e], u0[:, d, t, e]), fresh_ready[d])
                        else:
                            dve.wait_ge(passed[d], 2 * s - 1 + par)
                            steps.did(nc.vector.tensor_tensor(fresh[:, d, s % 2, e], u0[:, d, t, e],
                                                              mem.bank[d + 2 * par][:, 0:HEAD], ALU.subtract),
                                      fresh_ready[d])
                for d in range(2):
                    if s == TT - 1:
                        break
                    t = chunk[d](s)
                    dve.wait_ge(grown[d], s + 1)
                    if s == 0:
                        steps.did(nc.vector.tensor_copy(state[:, d, :], mem.bank[4 + d][:, 0:HEAD]), state_ready[d])
                    else:
                        dve.wait_ge(state_ready[d], s)
                        dve.wait_ge(out_ready[d], s + 1)
                        steps.did(nc.vector.scalar_tensor_tensor(
                            out=state[:, d, :], in0=state[:, d, :], scalar=last_decay[:, d, t:t + 1],
                            in1=mem.bank[4 + d][:, 0:HEAD], op0=ALU.mult, op1=ALU.add), state_ready[d])
            for d in range(2):
                dve.wait_ge(out_taken[d], TT)
            steps.did(nc.vector.tensor_tensor(tile_at(y, hp + first_tile), o[:, 0, :], o[:, 1, :], ALU.add))
            steps.settle()

        @block.tensor
        def _(pe):
            for d in range(2):
                for par in range(2):
                    n = 2 * d + par
                    for t in range(TT):
                        c = slice(t * P, (t + 1) * P)
                        last = nc.tensor.matmul(mem.bank[d][:, t * P + par * HEAD:t * P + (par + 1) * HEAD],
                                                b.turned[:, n, c], vb[:, n, t, :], start=True, stop=True)
                last.then_inc(solved, 1)
                for par in range(2):
                    n = 2 * d + par
                    for t in range(TT):
                        c = slice(t * P, (t + 1) * P)
                        last = nc.tensor.matmul(mem.bank[2 + d][lanes[par], c], kb[:, n, t, :], b.turned[:, n, c],
                                                start=True, stop=True)
                last.then_inc(solved, 1)
            pe.wait_ge(solved_taken, 4)
            for s in range(TT):
                for d in range(2):
                    if s == 0:
                        continue
                    t = chunk[d](s)
                    pe.wait_ge(state_ready[d], s)
                    pe.wait_ge(fresh_ready[d], 2 * s)
                    for par in range(2):
                        nc.tensor.matmul(mem.bank[d + 2 * par][:, 0:HEAD], w[lanes[par], d, t * P:(t + 1) * P],
                                         state[lanes[par], d, :], start=True, stop=True).then_inc(passed[d], 1)
                for d in range(2):
                    t = chunk[d](s)
                    c = slice(t * P, (t + 1) * P)
                    pe.wait_ge(fresh_ready[d], 2 * s + 2)
                    if s >= 1:
                        pe.wait_ge(state_ready[d], s)
                    for par in range(2):
                        n = 2 * d + par
                        last = nc.tensor.matmul(mem.bank[4 + d][lanes[par], 0:HEAD], kd[:, n, t, :],
                                                fresh[:, d, s % 2, par * HEAD:(par + 1) * HEAD], start=True, stop=True)
                    last.then_inc(grown[d], 1)
                    if s >= 1:
                        pe.wait_ge(out_taken[d], s)
                    for par in range(2):
                        n = 2 * d + par
                        to = mem.bank[6 + d][lanes[par], 0:P]
                        if s >= 1:
                            nc.tensor.matmul(to, state[lanes[par], d, :], qg[lanes[par], d, c], start=True, stop=False)
                        last = nc.tensor.matmul(to, fresh[:, d, s % 2, par * HEAD:(par + 1) * HEAD], b.seen[:, n, c],
                                                start=(s == 0), stop=True)
                    last.then_inc(out_ready[d], 1)

        @block.scalar
        def _(act):
            for d in range(2):
                act.wait_ge(solved, 2 * d + 2)
                nc.scalar.activation(u0[:, d, :, :].rearrange("p t n -> p (t n)"), mem.bank[d][:, :], ACT.Copy) \
                    .then_inc(solved_taken, 1)
                nc.scalar.activation(w[:, d, :], mem.bank[2 + d][:, :], ACT.Copy).then_inc(solved_taken, 1)
            for s in range(TT):
                for d in range(2):
                    t = chunk[d](s)
                    act.wait_ge(out_ready[d], s + 1)
                    nc.scalar.activation(o[:, d, t * P:(t + 1) * P], mem.bank[6 + d][:, 0:P], ACT.Copy) \
                        .then_inc(out_taken[d], 1)


class PairBuffers:

    def __init__(self, mem, q, k, k_rows, v_rows, cols, qg, last_decay, more):
        self.q, self.k, self.k_rows, self.v_rows, self.cols = q, k, k_rows, v_rows, cols
        self.qg, self.last_decay = qg, last_decay
        self.turned = mem.h[:, 4:8, :]
        ring = mem.ring[:, :, :].rearrange("p s n -> p (s n)")
        size = 4 * SEQ
        self.neg = ring[:, 0:size].rearrange("p (n s) -> p n s", n=4)
        self.seen = ring[:, size:2 * size].rearrange("p (n s) -> p n s", n=4)
        rows = [more[:, i * 2 * SEQ:(i + 1) * 2 * SEQ] for i in range(4)]
        self.vb, self.kb, self.kd = [r.rearrange("p (n t e) -> p n t e", n=4, t=TT) for r in rows[:3]]
        self.u0 = rows[3].rearrange("p (d t e) -> p d t e", d=2, t=TT)


def delta_net(nc, mem, vec, gates, u, tm, y):
    with buffers(nc, cols=[P, KINDS, TT, GH], rows=[P, GH, SEQ]) as (cols, rows):
        delta_inputs(nc, mem, vec, gates, tm, u, cols, rows)
        with nc.Fori(0, PAIRS1) as hp, buffers(
                nc, q=[P, SEQ], k=[P, SEQ], k_rows=[P, TT, P], v_rows=[P, TT, P],
                pair_cols=[P, KINDS * TT, 2, 2], qg=[P, 2, SEQ], last_decay=[P, 2, TT], more=[P, 8 * SEQ]) as parts:
            b = PairBuffers(mem, *parts)
            delta_prepare(nc, mem, u, cols, rows, hp, b)
            invert(nc, mem, b.neg, b.turned, [0, 0, 1, 1], beside=ScanInputs(nc, rows, hp, b))
            delta_scan(nc, mem, y, hp, b)


def spatial_gate(nc, mem, a, vec, u, pv, y, decay, rate, gate):
    groups = [slice(g * P, (g + 1) * P) for g in range(A_GROUPS)]
    n_stats = TT * A_GROUPS
    with buffers(nc, mix=[P, A_GROUPS, P], bias=[P, A_GROUPS, P], ln=[P, 2, A_WIDTH], stats=[P, n_stats, 6],
                 moments=[P, n_stats, 2], root=[P, n_stats], shift=[P, n_stats], wa2=[P, B_WIDTH], g2=[P, B_WIDTH]) as (
            mix, bias, ln, stats, moments, root, shift, wa2, g2), phase(
            nc, "loaded", "gelued", "u_ready", "spread", "rooted", "normed", "mixed", "low_rank_loaded", "shifted",
            "inner", "product", "taken", "dve_steps") as (
            block, loaded, gelued, u_ready, spread, rooted, normed, mixed, low_rank_loaded, shifted,
            inner, product, taken, dve_steps):
        gate_banks = mem.bank[A_GROUPS:]
        change = mem.h
        gate_tiles, others = range(E_WA, UTE), range(E_R, E_WA)

        @block.sync
        def _(sp):
            sp.dma_start(mix[:, :, :], a["sgu_w"]).then_inc(loaded, 16)
            sp.dma_start(bias[:, :, :], a["sgu_b"].partition_broadcast(P)).then_inc(loaded, 16)
            sp.dma_start(ln[:, :, :], a["sgu_ln"].partition_broadcast(P)).then_inc(loaded, 16)
            sp.dma_start(wa2[:, :], a["wa2"]).then_inc(low_rank_loaded, 16)
            sp.dma_start(g2[:, :], a["g2"]).then_inc(low_rank_loaded, 16)

        @block.scalar
        def _(act):
            for t in range(TT):
                nc.scalar.activation(pv[:, t, :], pv[:, t, :], ACT.Gelu_apprx_tanh).then_inc(gelued, 1)
            for g in range(A_GROUPS):
                nc.scalar.activation(u[:, E_U + g, :], u[:, E_U + g, :], ACT.Gelu_apprx_tanh).then_inc(u_ready, 1)
            act.wait_ge(shifted, len(gate_tiles))
            nc.scalar.activation(u[0:LORA, E_WA, :], u[0:LORA, E_WA, :], ACT.Tanh).then_inc(inner, 1)
            nc.scalar.activation(u[:, E_G, :], u[:, E_G, :], ACT.Sigmoid).then_inc(inner, 1)
            act.wait_ge(spread, 1)
            nc.scalar.activation(root[:, :], moments[:, :, 1], ACT.Sqrt, bias=mem.eps[:, 1:2]).then_inc(rooted, 1)
            for j in range(RW_PAIRS):
                for i, (to, func, shift_by) in enumerate(((decay, ACT.Sigmoid, VECE(vec, "w0", j)),
                                                          (rate, ACT.Sigmoid, VECE(vec, "a0", j)), (gate, ACT.Copy, None))):
                    n = 3 * j + i
                    act.wait_ge(product, n + 1)
                    bank = gate_banks[n % len(gate_banks)]
                    if shift_by is None:
                        nc.scalar.activation(to[:, j, :], bank[:, :], func).then_inc(taken, 1)
                    else:
                        nc.scalar.activation(to[:, j, :], bank[:, :], func, bias=shift_by).then_inc(taken, 1)

        @block.vector
        def _(dve):
            steps = Steps(dve, dve_steps)
            token_shift(nc, steps, vec, u, change, gate_tiles, shifted)
            dve.wait_ge(loaded, 48)
            steps.did(nc.vector.tensor_tensor(
                mix[:, :, :], mix[:, :, :],
                CONST(mem.const, "upper_in").unsqueeze(1).broadcast_to([P, A_GROUPS, P]), ALU.mult))
            for t in range(TT):
                dve.wait_ge(gelued, t + 1)
                for g in range(A_GROUPS):
                    steps.did(nc.vector.bn_stats(stats[:, t * A_GROUPS + g, :], pv[:, t, groups[g]]))
            steps.settle()
            for n in range(n_stats):
                steps.did(nc.vector.bn_aggr(moments[:, n, :], stats[:, n, :]), spread if n == n_stats - 1 else None)
            token_shift(nc, steps, vec, u, change, others[:4])
            dve.wait_ge(rooted, 1)
            steps.did(nc.vector.reciprocal(root[:, :], root[:, :]))
            steps.settle()
            steps.did(nc.vector.scalar_tensor_tensor(out=shift[:, :], in0=moments[:, :, 0], scalar=-1.0,
                                                     in1=root[:, :], op0=ALU.mult, op1=ALU.mult))
            steps.settle()
            for t in range(TT):
                for g in range(A_GROUPS):
                    n = t * A_GROUPS + g
                    steps.did(nc.vector.tensor_scalar(pv[:, t, groups[g]], pv[:, t, groups[g]], root[:, n:n + 1],
                                                      shift[:, n:n + 1], ALU.mult, ALU.add))
            steps.settle()
            for i, op in ((0, ALU.mult), (1, ALU.add)):
                steps.did(nc.vector.tensor_tensor(pv[:, :, :], pv[:, :, :],
                                                  ln[:, i, :].unsqueeze(1).broadcast_to([P, TT, A_WIDTH]), op),
                          normed if i else None)
                steps.settle()
            token_shift(nc, steps, vec, u, change, others[4:])
            dve.wait_ge(u_ready, A_GROUPS)
            for g in range(A_GROUPS):
                dve.wait_ge(mixed, g + 1)
                steps.did(nc.vector.tensor_tensor(
                    y[:, g, :].rearrange("p (c t) -> p c t", c=TT),
                    mem.bank[g][:, :].rearrange("p (c t) -> p c t", c=TT),
                    bias[:, g, :].unsqueeze(1).broadcast_to([P, TT, P]), ALU.add))
            steps.settle()
            for g in range(A_GROUPS):
                steps.did(nc.vector.tensor_tensor(y[:, g, :], y[:, g, :], u[:, E_U + g, :], ALU.mult))
            dve.wait_ge(taken, 3 * RW_PAIRS)
            steps.did(nc.vector.tensor_scalar(decay[:, :, :], decay[:, :, :], -math.exp(-0.5), None, ALU.mult))
            steps.settle()

        @block.tensor
        def _(pe):
            pe.wait_ge(low_rank_loaded, 32)
            pe.wait_ge(inner, 2)
            for j in range(RW_PAIRS):
                c = slice(j * P, (j + 1) * P)
                for i, (left, right) in enumerate(((wa2[0:LORA, c], u[0:LORA, E_WA, :]),
                                                   (wa2[LORA:P, c], u[LORA:P, E_WA, :]), (g2[:, c], u[:, E_G, :]))):
                    n = 3 * j + i
                    if n >= len(gate_banks):
                        pe.wait_ge(taken, n - len(gate_banks) + 1)
                    nc.tensor.matmul(gate_banks[n % len(gate_banks)][:, :], left, right, start=True, stop=True) \
                        .then_inc(product, 1)
            pe.wait_ge(normed, 1)
            for g in range(A_GROUPS):
                for c in range(TT):
                    last = nc.tensor.matmul(mem.bank[g][:, c * P:(c + 1) * P], pv[:, c, groups[g]], mix[:, g, :],
                                            start=True, stop=True)
                last.then_inc(mixed, 1)


def token_shift(nc, steps, vec, u, change, tiles, signal=None):
    first, n = tiles[0], len(tiles)
    part = u[:, first:first + n, :]
    steps.did(nc.vector.tensor_tensor(change[:, 0:n, 1:SEQ], part[:, :, 0:SEQ - 1], part[:, :, 1:SEQ], ALU.subtract))
    steps.did(nc.vector.tensor_scalar(change[:, 0:n, 0:1], part[:, :, 0:1], -1.0, None, ALU.mult))
    steps.settle()
    for i in range(n):
        steps.did(nc.vector.scalar_tensor_tensor(
            out=part[:, i, :], in0=change[:, i, :], scalar=VECE(vec, "mu", first + i - E_R), in1=part[:, i, :],
            op0=ALU.mult, op1=ALU.add), signal)
    steps.settle()


class TimeMix:

    def __init__(self, mem, v, factor, par, more):
        self.v, self.factor, self.par = v, factor, par
        self.past = v[:, :].rearrange("p (h t e) -> p h t e", h=2, t=TT)
        ring = mem.ring[:, :, :].rearrange("p s n -> p (s n)")
        parts = [ring[:, i * SEQ:(i + 1) * SEQ] for i in range(8)]
        self.rho, self.alpha, self.beta, self.kappa = parts[0:4]
        self.alpha_rows, self.beta_rows, self.kappa_rows, self.v_rows = [
            x.rearrange("p (t n) -> p t n", t=TT) for x in parts[4:8]]
        pairs = [more[:, 2 * i:2 * i + 2, :] for i in range(4)]
        self.neg, self.key_past, self.key_seen, self.rate_seen = pairs
        self.turned = mem.h[:, 2:4, :]


class MaskedProducts:

    def __init__(self, nc, mem, b):
        self.nc, self.mem = nc, mem
        self.sets = [(b.alpha, b.beta, "neg_lower_strict", b.neg), (b.kappa, b.alpha, "upper_strict", b.key_past),
                     (b.kappa, b.rho, "upper_in", b.key_seen), (b.beta, b.rho, "upper_in", b.rate_seen)]
        self.masked_groups, self.banks = 2 * (len(self.sets) - 1), 4
        self.groups = self.masked_groups + 1
        assert self.banks + 2 <= self.groups <= LEVELS
        self.key_past, self.v_rows, self.past = b.key_past, b.v_rows, b.past

    def multiply_group(self, bank, i, par):
        left, right, _, _ = self.sets[i]
        lanes = slice(par * HEAD, (par + 1) * HEAD)
        for t in range(TT):
            c = slice(t * P, (t + 1) * P)
            last = self.nc.tensor.matmul(bank[:, c], left[lanes, c], right[lanes, c], start=True, stop=True)
        return last

    def take_group(self, bank, i, par):
        _, _, mask, to = self.sets[i]
        chunks = lambda x: x.rearrange("p (t c) -> p t c", t=TT)
        return self.nc.vector.tensor_tensor(chunks(to[:, par, :]), chunks(bank[:, :]),
                                            CONST(self.mem.const, mask).unsqueeze(1).broadcast_to([P, TT, P]), ALU.mult)

    def multiply(self, g):
        if g == self.masked_groups:
            for par in range(2):
                for t in range(TT):
                    at = (par * TT + t) * HEAD
                    last = self.nc.tensor.matmul(
                        self.mem.bank[4 + g % self.banks][:, at:at + HEAD], self.key_past[:, par, t * P:(t + 1) * P],
                        self.v_rows[:, t, par * HEAD:(par + 1) * HEAD], start=True, stop=True)
            return last
        return self.multiply_group(self.mem.bank[4 + g % self.banks], 1 + g // 2, g % 2)

    def take(self, g):
        if g == self.masked_groups:
            return self.nc.vector.tensor_copy(self.past[:, :, :, :].rearrange("p h t e -> p (h t e)"),
                                              self.mem.bank[4 + g % self.banks][:, :])
        return self.take_group(self.mem.bank[4 + g % self.banks], 1 + g // 2, g % 2)


VEC_J = ["k_k", "k_a", "r_k"]


def rwkv_prepare(nc, mem, vec, u, decay, rate, j, b, products):
    mid = P // 2 - 1
    with buffers(nc, r=[P, SEQ], k=[P, SEQ], kk=[P, SEQ], bk=[P, SEQ], run=[P, SEQ], about=[P, SEQ],
                 up=[P, SEQ], down=[P, SEQ], before=[P, SEQ], squares=[P, SEQ], scale=[P, SEQ]) as (
            r, k, kk, bk, run, about, up, down, before, squares, scale), phase(
            nc, "staged", "kk_ready", "squared", "summed", "rooted", "about_ready", "before_ready", "ups", "factor_ready",
            "bonus_ready", "bonus_summed", "ready", "turned", "rows_taken", "product", "dve_steps") as (
            block, staged, kk_ready, squared, summed, rooted, about_ready, before_ready, ups, factor_ready,
            bonus_ready, bonus_summed, ready, turned, rows_taken, product, dve_steps):
        by_chunk = lambda x: x.rearrange("p (c t) -> p c t", c=TT)

        @block.vector
        def _(dve):
            steps = Steps(dve, dve_steps)
            for i, name in enumerate(VEC_J):
                at = VECE.at[name][0]
                steps.did(nc.vector.tensor_copy(b.par[:, i:i + 1], vec[:, bass.ds(j + at, 1)]))
            steps.settle()
            steps.did(nc.vector.tensor_scalar(kk[:, :], tile_at(u, j + E_K), b.par[:, 0:1], None, ALU.mult), kk_ready)
            steps.did(nc.vector.tensor_copy(before[:, :], tile_at(decay, j)))
            steps.did(nc.vector.tensor_scalar(k[:, :], tile_at(rate, j), -1.0, b.par[:, 1:2], ALU.add, ALU.mult))
            steps.settle()
            steps.did(nc.vector.tensor_tensor_scan(run[:, :], CONST(mem.const, "not_first"), before[:, :], 0.0,
                                                   ALU.mult, ALU.add))
            steps.settle()
            steps.did(nc.vector.scalar_tensor_tensor(out=k[:, :], in0=k[:, :], scalar=1.0, in1=tile_at(u, j + E_K),
                                                     op0=ALU.add, op1=ALU.mult))
            middle = by_chunk(run[:, :])[:, :, mid:mid + 1].broadcast_to([P, TT, P])
            steps.did(nc.vector.tensor_tensor(by_chunk(about[:, :]), by_chunk(run[:, :]), middle, ALU.subtract),
                      about_ready)
            steps.settle()
            steps.did(nc.vector.tensor_tensor(before[:, :], about[:, :], before[:, :], ALU.subtract), before_ready)
            ends = by_chunk(about[:, :])[:, 0:TT - 1, P - 1]
            steps.did(nc.vector.tensor_tensor(b.factor[:, 0:TT - 1], ends, by_chunk(run[:, :])[:, 1:TT, mid], ALU.add),
                      factor_ready)
            dve.wait_ge(staged, 2)
            steps.did(nc.vector.scalar_tensor_tensor(out=bk[:, :], in0=r[:, :], scalar=b.par[:, 2:3], in1=k[:, :],
                                                     op0=ALU.mult, op1=ALU.mult), bonus_ready)
            dve.wait_ge(rooted, 1)
            steps.did(nc.vector.tensor_scalar(scale[:, :], scale[:, :], 1e-12, None, ALU.max))
            steps.settle()
            steps.did(nc.vector.reciprocal(scale[:, :], scale[:, :]))
            steps.settle()
            steps.did(nc.vector.tensor_tensor(kk[:, :], kk[:, :], scale[:, :], ALU.mult))
            steps.settle()
            dve.wait_ge(ups, 3)
            steps.did(nc.vector.tensor_tensor(b.alpha, kk[:, :], before[:, :], ALU.mult), ready)
            steps.did(nc.vector.tensor_tensor(kk[:, :], kk[:, :], tile_at(rate, j), ALU.mult))
            steps.settle()
            steps.did(nc.vector.tensor_tensor(b.beta, kk[:, :], down[:, :], ALU.mult), ready)
            steps.did(nc.vector.tensor_tensor(b.kappa, k[:, :], down[:, :], ALU.mult), ready)
            steps.did(nc.vector.tensor_tensor(b.rho, r[:, :], up[:, :], ALU.mult), ready)
            dve.wait_ge(bonus_summed, 1)
            steps.did(nc.vector.tensor_tensor(tile_at(u, j + E_V), mem.bank[0][:, :], b.v[:, :], ALU.mult))
            for par in range(2):
                dve.wait_ge(product, par + 1)
                steps.did(products.take_group(mem.bank[6 + par], 0, par))
            steps.settle()

        @block.scalar
        def _(act):
            act.wait_ge(kk_ready, 1)
            nc.scalar.activation(squares[:, :], kk[:, :], ACT.Square).then_inc(squared, 1)
            for to, first in ((r, E_R), (b.v, E_V)):
                nc.scalar.activation(to[:, :], tile_at(u, j + first), ACT.Copy).then_inc(staged, 1)
            act.wait_ge(summed, 1)
            nc.scalar.activation(scale[:, :], mem.bank[1][:, :], ACT.Sqrt).then_inc(rooted, 1)
            act.wait_ge(about_ready, 1)
            nc.scalar.activation(up[:, :], about[:, :], ACT.Exp).then_inc(ups, 1)
            nc.scalar.activation(down[:, :], about[:, :], ACT.Exp, scale=-1.0).then_inc(ups, 1)
            act.wait_ge(before_ready, 1)
            nc.scalar.activation(before[:, :], before[:, :], ACT.Exp).then_inc(ups, 1)
            act.wait_ge(factor_ready, 1)
            nc.scalar.activation(b.factor[:, 0:TT - 1], b.factor[:, 0:TT - 1], ACT.Exp)
            for i, to in enumerate([b.v_rows, b.alpha_rows, b.beta_rows, b.kappa_rows]):
                act.wait_ge(turned, i + 1)
                nc.scalar.activation(to.rearrange("p t n -> p (t n)"), mem.bank[2 + i][:, :], ACT.Copy) \
                    .then_inc(rows_taken, 1)

        @block.tensor
        def _(pe):
            pe.wait_ge(squared, 1)
            nc.tensor.matmul(mem.bank[1][:, :], CONST(mem.const, "pair_ones"), squares[:, :], start=True,
                             stop=True).then_inc(summed, 1)
            pe.wait_ge(staged, 2)
            pe.wait_ge(bonus_ready, 1)
            nc.tensor.matmul(mem.bank[0][:, :], CONST(mem.const, "pair_ones"), bk[:, :], start=True,
                             stop=True).then_inc(bonus_summed, 1)
            for i, (of, need) in enumerate([(b.v[:, :], 0), (b.alpha, 1), (b.beta, 2), (b.kappa, 3)]):
                if need:
                    pe.wait_ge(ready, need)
                if need == 3:
                    for par in range(2):
                        products.multiply_group(mem.bank[6 + par], 0, par).then_inc(product, 1)
                for t in range(TT):
                    last = nc.tensor.transpose(mem.bank[2 + i][:, t * P:(t + 1) * P], of[:, t * P:(t + 1) * P],
                                               CONST(mem.const, "ident"))
                last.then_inc(turned, 1)


def rwkv_scan(nc, mem, y, j, b):
    first_tile = A_GROUPS
    with buffers(nc, u0=[P, 2, TT, HEAD], w=[P, SEQ], state=[P, HEAD], fresh=[P, 2, P],
                 out=[P, SEQ]) as (u0, w, state, fresh, out), phase(
            nc, "solved", "solved_taken", "passed", "fresh_ready", "out_ready", "grown",
            "state_ready", "out_taken", "dve_steps") as (
            block, solved, solved_taken, passed, fresh_ready, out_ready, grown,
            state_ready, out_taken, dve_steps):
        lanes = [slice(0, HEAD), slice(HEAD, 2 * HEAD)]

        @block.tensor
        def _(pe):
            for par in range(2):
                for t in range(TT):
                    c = slice(t * P, (t + 1) * P)
                    last = nc.tensor.matmul(mem.bank[4][lanes[par], c], b.alpha_rows[:, t, lanes[par]],
                                            b.turned[:, par, c], start=True, stop=True)
                last.then_inc(solved, 1)
            for par in range(2):
                for t in range(TT):
                    last = nc.tensor.matmul(mem.bank[2 + par][:, t * HEAD:(t + 1) * HEAD],
                                            b.turned[:, par, t * P:(t + 1) * P], b.past[:, par, t, :],
                                            start=True, stop=True)
                last.then_inc(solved, 1)
            pe.wait_ge(solved_taken, 3)
            for s in range(TT):
                c = slice(s * P, (s + 1) * P)
                if s >= 1:
                    pe.wait_ge(state_ready, s)
                    for par in range(2):
                        nc.tensor.matmul(mem.bank[par][:, 0:HEAD], w[lanes[par], c], state[lanes[par], :],
                                         start=True, stop=True).then_inc(passed, 1)
                if s < TT - 1:
                    for par in range(2):
                        nc.tensor.matmul(mem.bank[5][lanes[par], 0:HEAD], b.kappa_rows[:, s, lanes[par]],
                                         b.v_rows[:, s, lanes[par]], start=True, stop=False)
                        pe.wait_ge(fresh_ready, 2 * s + 1 + par)
                        last = nc.tensor.matmul(mem.bank[5][lanes[par], 0:HEAD], b.beta_rows[:, s, lanes[par]],
                                                fresh[:, s % 2, lanes[par]], start=False, stop=True)
                    last.then_inc(grown, 1)
                pe.wait_ge(fresh_ready, 2 * s + 2)
                if s >= 2:
                    pe.wait_ge(out_taken, s - 1)
                for par in range(2):
                    to = mem.bank[6 + s % 2][lanes[par], 0:P]
                    if s >= 1:
                        nc.tensor.matmul(to, state[lanes[par], :], b.rho[lanes[par], c], start=True, stop=False)
                    nc.tensor.matmul(to, b.v_rows[:, s, lanes[par]], b.key_seen[:, par, c], start=(s == 0), stop=False)
                    last = nc.tensor.matmul(to, fresh[:, s % 2, lanes[par]], b.rate_seen[:, par, c],
                                            start=False, stop=True)
                last.then_inc(out_ready, 1)

        @block.scalar
        def _(act):
            act.wait_ge(solved, 2)
            nc.scalar.activation(w[:, :], mem.bank[4][:, :], ACT.Copy).then_inc(solved_taken, 1)
            for par in range(2):
                act.wait_ge(solved, 3 + par)
                nc.scalar.activation(u0[:, par, :, :].rearrange("p t e -> p (t e)"),
                                     mem.bank[2 + par][:, 0:TT * HEAD], ACT.Copy).then_inc(solved_taken, 1)
            for s in range(TT):
                act.wait_ge(out_ready, s + 1)
                nc.scalar.activation(out[:, s * P:(s + 1) * P], mem.bank[6 + s % 2][:, 0:P], ACT.Copy) \
                    .then_inc(out_taken, 1)

        @block.vector
        def _(dve):
            steps = Steps(dve, dve_steps)
            dve.wait_ge(solved_taken, 3)
            for s in range(TT):
                if s >= 2:
                    dve.wait_ge(out_ready, s - 1)
                for par in range(2):
                    if s == 0:
                        steps.did(nc.vector.tensor_scalar(fresh[:, 0, lanes[par]], u0[:, par, 0, :], -1.0, None,
                                                          ALU.mult), fresh_ready)
                    else:
                        dve.wait_ge(passed, 2 * s - 1 + par)
                        steps.did(nc.vector.scalar_tensor_tensor(
                            out=fresh[:, s % 2, lanes[par]], in0=mem.bank[par][:, 0:HEAD], scalar=-1.0,
                            in1=u0[:, par, s, :], op0=ALU.mult, op1=ALU.subtract), fresh_ready)
                if s == TT - 1:
                    break
                dve.wait_ge(grown, s + 1)
                if s == 0:
                    steps.did(nc.vector.tensor_scalar(state[:, :], mem.bank[5][:, 0:HEAD], b.factor[:, s:s + 1], None,
                                                      ALU.mult), state_ready)
                else:
                    dve.wait_ge(out_ready, s + 1)
                    steps.settle()
                    steps.did(nc.vector.tensor_tensor(state[:, :], state[:, :], mem.bank[5][:, 0:HEAD], ALU.add))
                    steps.settle()
                    steps.did(nc.vector.tensor_scalar(state[:, :], state[:, :], b.factor[:, s:s + 1], None, ALU.mult),
                              state_ready)
            dve.wait_ge(out_taken, TT)
            steps.did(nc.vector.tensor_copy(tile_at(y, j + first_tile), out[:, :]))
            steps.settle()


def group_norm(nc, mem, vec, u, gate, y, following):
    first = A_GROUPS
    per = TT * 2
    with buffers(nc, squares=[P, RW_PAIRS, SEQ], root=[P, RW_PAIRS, TT, 2], wide=[P, RW_PAIRS, TT, P]) as (
            squares, root, wide), phase(
            nc, "mean_ready", "centred", "squared", "summed", "rooted", "widened", "spread", "normed", "dve_steps",
            *Primer.SEMS) as (
            block, mean_ready, centred, squared, summed, rooted, widened, spread, normed, dve_steps, *primer_sems):
        primer = Primer(nc, mem, following, primer_sems)
        sums, means = mem.bank[0], mem.bank[1:1 + RW_PAIRS]
        spread_banks = mem.bank[1 + RW_PAIRS:] + means
        heads = CONST(mem.const, "pair_ones").rearrange("p (h d) -> p d h", d=HEAD)[:, 0, :]

        @block.sync
        def _(sp):
            primer.load(sp)

        @block.tensor
        def _(pe):
            for i in range(RW_PAIRS):
                nc.tensor.matmul(means[i][:, :], CONST(mem.const, "pair_ones"), y[:, first + i, :], start=True,
                                 stop=True).then_inc(mean_ready, 1)
            for i in range(RW_PAIRS):
                pe.wait_ge(squared, i + 1)
                for t in range(TT):
                    last = nc.tensor.matmul(sums[:, i * per + 2 * t:i * per + 2 * t + 2],
                                            squares[:, i, t * P:(t + 1) * P], heads, start=True, stop=True)
            last.then_inc(summed, 1)
            pe.wait_ge(centred, RW_PAIRS)
            for i in range(RW_PAIRS):
                pe.wait_ge(widened, i + 1)
                for t in range(TT):
                    last = nc.tensor.matmul(spread_banks[i][:, t * P:(t + 1) * P], wide[:, i, t, :],
                                            CONST(mem.const, "ident"), start=True, stop=True)
                last.then_inc(spread, 1)

        @block.scalar
        def _(act):
            for i in range(RW_PAIRS):
                act.wait_ge(centred, i + 1)
                nc.scalar.activation(squares[:, i, :], y[:, first + i, :], ACT.Square).then_inc(squared, 1)
            act.wait_ge(summed, 1)
            nc.scalar.activation(root[:, :, :, :].rearrange("p i t h -> p (i t h)"), sums[:, 0:RW_PAIRS * per],
                                 ACT.Sqrt, bias=mem.eps[:, 2:3], scale=1.0 / HEAD).then_inc(rooted, 1)

        @block.vector
        def _(dve):
            steps = Steps(dve, dve_steps)
            tiles = [y[:, first + i, :] for i in range(RW_PAIRS)]
            for i, to in enumerate(tiles):
                dve.wait_ge(mean_ready, i + 1)
                steps.did(nc.vector.scalar_tensor_tensor(out=to, in0=means[i][:, :], scalar=-1.0 / HEAD, in1=to,
                                                         op0=ALU.mult, op1=ALU.add), centred)
            dve.wait_ge(rooted, 1)
            steps.did(nc.vector.reciprocal(root[:, :, :, :], root[:, :, :, :]))
            steps.settle()
            for i in range(RW_PAIRS):
                steps.did(nc.vector.tensor_copy(
                    wide[:, i, :, :].rearrange("p t (h d) -> p (t h) d", h=2),
                    root[:, i, :, :].rearrange("p t h -> p (t h)").unsqueeze(2).broadcast_to([P, per, HEAD])), widened)
            for i, to in enumerate(tiles):
                dve.wait_ge(spread, i + 1)
                dve.wait_ge(squared, i + 1)
                steps.did(nc.vector.scalar_tensor_tensor(out=to, in0=to, scalar=VECE(vec, "gn_g", i),
                                                         in1=spread_banks[i][:, :], op0=ALU.mult, op1=ALU.mult), normed)
            for i, to in enumerate(tiles):
                dve.wait_ge(normed, i + 1)
                steps.did(nc.vector.scalar_tensor_tensor(out=to, in0=to, scalar=VECE(vec, "gn_b", i),
                                                         in1=u[:, E_V + i, :], op0=ALU.add, op1=ALU.add), normed)
            for i, to in enumerate(tiles):
                dve.wait_ge(normed, RW_PAIRS + i + 1)
                steps.did(nc.vector.tensor_tensor(to, to, gate[:, i, :], ALU.mult))
            steps.settle()


def time_mix(nc, mem, vec, u, y, decay, rate, gate, w_out):
    with nc.Fori(0, RW_PAIRS) as j, buffers(nc, v=[P, SEQ], factor=[P, TT], par=[P, len(VEC_J)],
                                            more=[P, 8, SEQ]) as parts:
        b = TimeMix(mem, *parts)
        products = MaskedProducts(nc, mem, b)
        rwkv_prepare(nc, mem, vec, u, decay, rate, j, b, products)
        invert(nc, mem, b.neg, b.turned, [0, 0], products)
        rwkv_scan(nc, mem, y, j, b)
    group_norm(nc, mem, vec, u, gate, y, w_out)


def second_even(nc, mem, a):
    with buffers(nc, vec=[P, VECE.size]) as (vec,):
        with buffers(nc, y=[P, KD, SEQ], u=[P, UTE, SEQ], gates=[P, 3, RW_PAIRS, SEQ]) as (y, u, gates):
            decay, rate, gate = [gates[:, i, :, :] for i in range(3)]
            w_tm = gates[:, :, :, :].rearrange("p i j s -> p (i j s)")[:, 0:KD * A_WIDTH]
            pv = y[:, A_GROUPS:KD, :].rearrange("p t n -> p (t n)").rearrange("p (t n) -> p t n", n=A_WIDTH)
            with split_ring(nc, mem):
                w_in = Weights(unit_of(a["w_ine"]), UTE // 2, 2, KD)
                rms_norm(nc, mem, mem.x, lambda k: VECE(vec, "norm_mix", k), mem.h,
                         vectors=[(vec[:, :], a["vece"])], ahead=[(w_tm, a["w_tme"])])
                token_major(nc, mem, w_tm, A_WIDTH, mem.h, pv, w_in)
                project(nc, mem, w_in, mem.h, copy_out(nc, u), primed=SPLIT)
            spatial_gate(nc, mem, a, vec, u, pv, y, decay, rate, gate)
            w_out = Weights(unit_of(a["w_oute"]), KD // 2, 2, KD)
            time_mix(nc, mem, vec, u, y, decay, rate, gate, w_out)
            with split_ring(nc, mem):
                project(nc, mem, w_out, y, add_out(nc, mem.x), on_vector=True, primed=LOADED)
        ff = FeedForward(unit_of(a["w_ffe"]), unit_of(a["w_downe"]), FFN_T, "silu")
        with split_ring(nc, mem):
            rms_norm(nc, mem, mem.x, lambda k: VECE(vec, "norm_ffn", k), mem.h, following=ff.up[0])
            feed_forward(nc, mem, ff, lambda half: add_out(nc, mem.x), lambda half: True)


def interleaved(gate, up):
    k, m = gate.shape
    both = np.stack([gate.reshape(k, m // P, P), up.reshape(k, m // P, P)], axis=2)
    return both.reshape(k, 2 * m)


def lay_out_even(i, a):
    w = i["e_w_in_2"][0]
    a["w_ine"] = weight_units(np.concatenate([w[:, :A_WIDTH], w[:, 2 * A_WIDTH:]], axis=1), 2)
    a["w_tme"] = moving(w[:, A_WIDTH:2 * A_WIDTH])
    a["w_oute"] = weight_units(i["e_w_out_2"][0], 2)
    a["w_ffe"] = weight_units(interleaved(i["ffn_w_gate_2"][0], i["ffn_w_up_2"][0]), 2)
    a["w_downe"] = weight_units(i["ffn_w_down_2"][0], 1)
    a["sgu_w"] = i["sgu_w_2"][0].transpose(2, 0, 1)
    a["sgu_b"] = i["sgu_b_2"][0]
    a["sgu_ln"] = np.stack([i["sgu_ln_g_2"][0], i["sgu_ln_b_2"][0]])
    a["wa2"] = np.concatenate([i["rwkv_w2_2"][0], i["rwkv_a2_2"][0]])
    a["g2"] = i["rwkv_g2_2"][0]
    vec = np.zeros((P, VECE.size), np.float32)
    for name, key in [("norm_mix", "e_norm_mix_2"), ("norm_ffn", "e_norm_ffn_2"), ("mu", "rwkv_mu_2"),
                      ("w0", "rwkv_w0_2"), ("a0", "rwkv_a0_2"), ("k_k", "rwkv_k_k_2"), ("k_a", "rwkv_k_a_2"),
                      ("r_k", "rwkv_r_k_2"), ("gn_g", "rwkv_gn_g_2"), ("gn_b", "rwkv_gn_b_2")]:
        VECE(vec, name)[...] = columns(i[key][0].reshape(-1))
    a["vece"] = vec




def short_conv(nc, steps, vec, u, y):
    n = D_WIDTH // P
    first_tile = C_HEADS * HEAD // P
    taps = 3
    z, out = u[:, O_CG:O_CG + n, :], y[:, first_tile:first_tile + n, :]
    steps.did(nc.vector.tensor_tensor(z, z, u[:, O_HD:O_HD + n, :], ALU.mult))
    steps.settle()
    for lag in range(taps):
        for c in range(n):
            weight = VECO(vec, "conv", taps * c + taps - 1 - lag)
            if lag == 0:
                steps.did(nc.vector.tensor_scalar(out[:, c, :], z[:, c, :], weight, None, ALU.mult))
            else:
                steps.did(nc.vector.scalar_tensor_tensor(
                    out=out[:, c, lag:SEQ], in0=z[:, c, 0:SEQ - lag], scalar=weight, in1=out[:, c, lag:SEQ],
                    op0=ALU.mult, op1=ALU.add))
        steps.settle()
    steps.did(nc.vector.tensor_tensor(out, out, u[:, O_BG:O_BG + n, :], ALU.mult))
    steps.settle()


def compress(nc, mem, a, vec, rope, u, y, k_out, v_out, following):
    halves = CMP_HIDDEN // P
    lanes = [slice(0, HEAD), slice(HEAD, 2 * HEAD)]
    spans = CMP_LEN // CMP_STRIDE
    pairs, span_pairs = CMP_LEN // 2, CMP_STRIDE // 2
    KEYS, VALUES = range(2)
    tiles, positions = (O_KC, O_VC), (VECO(vec, "pos_k"), VECO(vec, "pos_v"))
    weights = ((a["cmp_k1"], a["cmp_k2"]), (a["cmp_v1"], a["cmp_v2"]))
    turned_keys = range(O_KS, O_KS + 2 * C_KV)
    padding = CMP_COLS > N_CMP
    both = C_KV * CMP_COLS
    with buffers(nc, first=[P, 2, pairs, CMP_HIDDEN], twice=[P, 2, C_KV, SEQ], blocks=[P, 2, pairs, both],
                 second=[P, 2, halves, HEAD], rows=[P, 2, CMP_HIDDEN], hidden=[P, 2, halves, both],
                 turn=[P, 2 * C_KV, SEQ]) as (first, twice, blocks, second, rows, hidden, turn), phase(
            nc, "keys_twice", "values_twice", *[f"loaded{n}" for n in range(2 * spans)], "keys_second",
            "values_second", "blocks_ready", "inner", "rows_ready", "hidden_turned", "hidden_ready", "outer",
            "outer_taken", "rotated", "turns",
            "dve_steps", *Primer.SEMS) as (
            block, *sems):
        twice_ready, loaded, second_loaded = sems[:2], sems[2:2 + 2 * spans], sems[2 + 2 * spans:4 + 2 * spans]
        (blocks_ready, inner, rows_ready, hidden_turned, hidden_ready, outer, outer_taken, rotated, turns, dve_steps,
         *primer_sems) = sems[4 + 2 * spans:]
        primer = Primer(nc, mem, following, primer_sems)
        inner_banks, turn_banks, outer_banks, rotated_banks = mem.bank[0:2], mem.bank[2:4], mem.bank[4:8], mem.bank[4:8]

        @block.sync
        def _(sp):
            for i in (KEYS, VALUES):
                for c in range(C_KV):
                    for half in range(2):
                        sp.dma_start(twice[lanes[half], i, c, :], u[lanes[c], tiles[i], :]).then_inc(twice_ready[i], 16)
                for p in range(spans):
                    at = slice(p * span_pairs, (p + 1) * span_pairs)
                    sp.dma_start(first[:, i, at, :], weights[i][0][:, at, :]).then_inc(loaded[i * spans + p], 16)
                sp.dma_start(second[:, i, :, :], weights[i][1]).then_inc(second_loaded[i], 16)
            primer.load(sp)

        @block.vector
        def _(dve):
            steps = Steps(dve, dve_steps)
            if padding:
                for c in range(C_KV):
                    nc.vector.memset(blocks[:, :, :, c * CMP_COLS + N_CMP:(c + 1) * CMP_COLS], 0.0).then_inc(blocks_ready, 1)
            for i in (KEYS, VALUES):
                dve.wait_ge(twice_ready[i], 16 * 2 * C_KV)
                for p in range(spans):
                    at = slice(p * span_pairs, (p + 1) * span_pairs)
                    for c in range(C_KV):
                        for side in range(2):
                            tokens = twice[lanes[side], i, c, :].rearrange("p (m q s) -> p s q m", s=2, q=span_pairs)
                            place = positions[i][lanes[side], :].rearrange("p (q s) -> p s q", s=2)[:, side, at]
                            nc.vector.tensor_tensor(
                                blocks[lanes[side], i, at, c * CMP_COLS:c * CMP_COLS + N_CMP], tokens[:, side, :, p:p + N_CMP],
                                place.unsqueeze(2).broadcast_to([HEAD, span_pairs, N_CMP]), ALU.add) \
                                .then_inc(blocks_ready, 1)
            for n, t in enumerate(turned_keys):
                dve.wait_ge(rotated, n + 1)
                steps.did(nc.vector.tensor_tensor(turn[:, n, :], rotated_banks[n][:, :], rope[:, 1, :], ALU.mult), turns)
                steps.did(nc.vector.tensor_tensor(u[:, t, :], u[:, t, :], rope[:, 0, :], ALU.mult))
            steps.settle()
            for n, t in enumerate(turned_keys):
                steps.did(nc.vector.tensor_tensor(u[:, t, :], u[:, t, :], turn[:, n, :], ALU.add))
            short_conv(nc, steps, vec, u, y)

        @block.tensor
        def _(pe):
            for n, t in enumerate(turned_keys):
                nc.tensor.matmul(rotated_banks[n][:, :], CONST(mem.const, "rot"), u[:, t, :], start=True, stop=True) \
                    .then_inc(rotated, 1)
            for i in (KEYS, VALUES):
                for p in range(spans):
                    pe.wait_ge(loaded[i * spans + p], 16)
                    pe.wait_ge(blocks_ready, 2 * C_KV * (i * spans + p + 1) + padding * C_KV)
                    for q in range(p * span_pairs, (p + 1) * span_pairs):
                        last = nc.tensor.matmul(inner_banks[i][0:both, 0:CMP_HIDDEN], blocks[:, i, q, :],
                                                first[:, i, q, :], start=(q == 0), stop=(q == pairs - 1))
                last.then_inc(inner, 1)
            for i in (KEYS, VALUES):
                pe.wait_ge(rows_ready, i + 1)
                for h in range(halves):
                    last = nc.tensor.transpose(turn_banks[i][:, h * both:(h + 1) * both],
                                               rows[0:both, i, h * P:(h + 1) * P],
                                               CONST(mem.const, "ident")[0:both, 0:both])
                last.then_inc(hidden_turned, 1)
            pe.wait_ge(turns, 2 * C_KV)
            for i in (KEYS, VALUES):
                pe.wait_ge(second_loaded[i], 16)
                pe.wait_ge(hidden_ready, i + 1)
                for c in range(C_KV):
                    head = slice(c * CMP_COLS, (c + 1) * CMP_COLS)
                    to = outer_banks[i * C_KV + c]
                    if i == KEYS:
                        for side in range(2):
                            for h in range(halves):
                                last = nc.tensor.matmul(to[lanes[side], 0:CMP_COLS], second[:, i, h, :],
                                                        hidden[:, i, h, head], start=(h == 0), stop=(h == halves - 1))
                    else:
                        for h in range(halves):
                            last = nc.tensor.matmul(to[0:CMP_COLS, 0:HEAD], hidden[:, i, h, head], second[:, i, h, :],
                                                    start=(h == 0), stop=(h == halves - 1))
                    last.then_inc(outer, 1)

        @block.scalar
        def _(act):
            for i in (KEYS, VALUES):
                act.wait_ge(inner, i + 1)
                nc.scalar.activation(rows[0:both, i, :], inner_banks[i][0:both, 0:CMP_HIDDEN], ACT.Gelu_apprx_tanh) \
                    .then_inc(rows_ready, 1)
            for i in (KEYS, VALUES):
                act.wait_ge(hidden_turned, i + 1)
                nc.scalar.activation(hidden[:, i, :, :].rearrange("p h n -> p (h n)"), turn_banks[i][:, 0:halves * both],
                                     ACT.Copy).then_inc(hidden_ready, 1)
            for c in range(C_KV):
                act.wait_ge(outer, c + 1)
                nc.scalar.activation(k_out[:, c, :], outer_banks[c][:, 0:N_CMP], ACT.Copy).then_inc(outer_taken, 1)
            for c in range(C_KV):
                act.wait_ge(outer, C_KV + c + 1)
                nc.scalar.activation(v_out[0:N_CMP, c, :], outer_banks[C_KV + c][0:N_CMP, 0:HEAD], ACT.Copy) \
                    .then_inc(outer_taken, 1)


def sparse_attention(nc, mem, rope, u, tm, k_cmp, v_cmp, y):
    lanes = [slice(0, HEAD), slice(HEAD, 2 * HEAD)]
    units = [(h, t) for h in range(2) for t in range(TT)]
    n_units = len(units)
    scale = HEAD ** -0.5
    SLC, WIN = range(2)
    with nc.Fori(0, C_KV) as kv, nc.Fori(0, C_GROUP // 2) as half, buffers(
            nc, q=[P, SEQ], q_rot=[P, SEQ], turn=[P, SEQ], keys=[P, 2, SEQ], values=[P, 2, TT, HEAD],
            kc=[P, N_CMP], vc=[P, HEAD], gate=[P, TT, 2, N_BRANCH], probs=[P, 2, 2, SEQ], probs_c=[P, 2, TT, N_CMP],
            top_c=[P, 2, TT], sum_c=[P, 2, TT], tops=[P, 2 * n_units], sums=[P, 2 * n_units],
            weights=[P, 2 * n_units], turned=[P, 2, 2, SEQ], turned_c=[P, 2, SEQ]) as (
            q, q_rot, turn, keys, values, kc, vc, gate, probs, probs_c, top_c, sum_c, tops, sums, weights, turned,
            turned_c), phase(
            nc, "gate_ready", "q_ready", "rotated", "keys_staged", "staged", "scored_c", "topped_c", "exped_c",
            "weighted_c", "transposed_c", "taken_c", "scored", "topped", "exped", "weighted", "transposed",
            "taken", "applied", "dve_steps") as (
            block, gate_ready, q_ready, rotated, keys_staged, staged, scored_c, topped_c, exped_c,
            weighted_c, transposed_c, taken_c, scored, topped, exped, weighted, transposed,
            taken, applied, dve_steps):
        j = kv * (C_GROUP // 2) + half
        first_gate = 2 * KV_WIDTH
        out_bank = mem.bank[7]
        score_c_bank = [mem.bank[4], mem.bank[5]]

        def score_bank(n, branch):
            return mem.bank[2 * (n % 2) + branch]

        @block.scalar
        def _(act):
            nc.scalar.activation(q[:, :], tile_at(u, j + O_Q), ACT.Copy, scale=scale).then_inc(q_ready, 1)
            nc.scalar.activation(gate[:, :, :, :].rearrange("p t h b -> p t (h b)"),
                                 tm[:, :, bass.ds(j * 2 * N_BRANCH + first_gate, 2 * N_BRANCH)],
                                 ACT.Sigmoid).then_inc(gate_ready, 1)
            act.wait_ge(topped_c, 1)
            nc.scalar.activation(probs_c[:, :, :, :], probs_c[:, :, :, :], ACT.Exp).then_inc(exped_c, 1)

            def take_turned(n):
                h, t = units[n]
                width = (t + 1) * P
                act.wait_ge(transposed, n + 1)
                if n >= 2:
                    act.wait_ge(applied, n - 1)
                for branch in (SLC, WIN):
                    nc.scalar.activation(turned[:, n % 2, branch, 0:width], mem.bank[5 + branch][:, 0:width], ACT.Copy) \
                        .then_inc(taken, 1)

            for n, (h, t) in enumerate(units):
                width = (t + 1) * P
                act.wait_ge(topped, n + 1)
                if n >= 2:
                    act.wait_ge(transposed, n - 1)
                for branch in (SLC, WIN):
                    i = 2 * n + branch
                    nc.scalar.activation(probs[:, n % 2, branch, 0:width], score_bank(n, branch)[:, 0:width], ACT.Exp,
                                         bias=tops[:, i:i + 1], accum_out=sums[:, i:i + 1]).then_inc(exped, 1)
                if n == 0:
                    for side in range(2):
                        act.wait_ge(transposed_c, side + 1)
                        nc.scalar.activation(turned_c[0:N_CMP, side, :], mem.bank[5 + side][0:N_CMP, :], ACT.Copy) \
                            .then_inc(taken_c, 1)
                if n >= 1:
                    take_turned(n - 1)
            take_turned(n_units - 1)

        @block.tensor
        def _(pe):
            pe.wait_ge(q_ready, 1)
            nc.tensor.matmul(out_bank[:, :], CONST(mem.const, "rot"), q[:, :], start=True, stop=True) \
                .then_inc(rotated, 1)
            pe.wait_ge(keys_staged, 1)
            for h in range(2):
                for t in range(TT):
                    last = nc.tensor.matmul(score_c_bank[h][:, t * N_CMP:(t + 1) * N_CMP],
                                            q[lanes[h], t * P:(t + 1) * P], kc[lanes[h], :], start=True, stop=True)
                last.then_inc(scored_c, 1)

            def score(n):
                h, t = units[n]
                c = slice(t * P, (t + 1) * P)
                if n >= 2:
                    pe.wait_ge(exped, 2 * n - 2)
                for branch in (SLC, WIN):
                    nc.tensor.matmul(score_bank(n, branch)[:, 0:(t + 1) * P], q_rot[lanes[h], c],
                                     keys[lanes[h], branch, 0:(t + 1) * P], start=True, stop=True) \
                        .then_inc(scored, 1)

            def transpose(n):
                h, t = units[n]
                pe.wait_ge(weighted, 2 * n + 2)
                if n >= 1:
                    pe.wait_ge(taken, 2 * n)
                for branch in (SLC, WIN):
                    for b in range(t + 1):
                        c = slice(b * P, (b + 1) * P)
                        last = nc.tensor.transpose(mem.bank[5 + branch][:, c], probs[:, n % 2, branch, c],
                                                   CONST(mem.const, "ident"))
                last.then_inc(transposed, 1)

            def apply(n):
                h, t = units[n]
                to = out_bank[lanes[h], t * P:(t + 1) * P]
                nc.tensor.matmul(to, vc[0:N_CMP, :], turned_c[0:N_CMP, h, t * P:(t + 1) * P], start=True, stop=False)
                pe.wait_ge(taken, 2 * n + 2)
                for branch in (SLC, WIN):
                    for b in range(t + 1):
                        last = nc.tensor.matmul(to, values[:, branch, b, :],
                                                turned[:, n % 2, branch, b * P:(b + 1) * P],
                                                start=False, stop=(branch == WIN and b == t))
                last.then_inc(applied, 1)

            pe.wait_ge(staged, 1)
            score(0)
            score(1)
            pe.wait_ge(weighted_c, 1)
            for h in range(2):
                for t in range(TT):
                    last = nc.tensor.transpose(mem.bank[5 + h][0:N_CMP, t * P:(t + 1) * P], probs_c[:, h, t, :],
                                               CONST(mem.const, "ident"))
                last.then_inc(transposed_c, 1)
            for n in range(n_units):
                if n + 2 < n_units:
                    score(n + 2)
                if n == 0:
                    pe.wait_ge(taken_c, 2)
                transpose(n)
                if n >= 1:
                    apply(n - 1)
            apply(n_units - 1)

        @block.vector
        def _(dve):
            steps = Steps(dve, dve_steps)
            steps.did(nc.vector.tensor_copy(kc[:, :], k_cmp[:, bass.ds(kv, 1), :].rearrange("p a n -> p (a n)")),
                      keys_staged)
            steps.did(nc.vector.tensor_copy(vc[0:N_CMP, :],
                                            v_cmp[0:N_CMP, bass.ds(kv, 1), :].rearrange("p a n -> p (a n)")))
            steps.did(nc.vector.tensor_copy(keys[:, SLC, :], tile_at(u, kv + O_KS)))
            steps.did(nc.vector.tensor_copy(keys[:, WIN, :], tile_at(u, kv + O_KW)))
            for branch in (SLC, WIN):
                steps.did(nc.vector.tensor_copy(values[:, branch, :, :],
                                                tm[:, :, bass.ds(kv * HEAD + branch * KV_WIDTH, HEAD)]))
            dve.wait_ge(q_ready, 1)
            steps.did(nc.vector.tensor_tensor(q_rot[:, :], q[:, :], rope[:, 0, :], ALU.mult))
            dve.wait_ge(rotated, 1)
            steps.did(nc.vector.tensor_tensor(turn[:, :], out_bank[:, :], rope[:, 1, :], ALU.mult))
            steps.settle()
            steps.did(nc.vector.tensor_tensor(q_rot[:, :], q_rot[:, :], turn[:, :], ALU.add), staged)

            def top(n):
                h, t = units[n]
                width, i = (t + 1) * P, 2 * n
                for branch in (SLC, WIN):
                    dve.wait_ge(scored, i + branch + 1)
                    own = score_bank(n, branch)[:, t * P:width]
                    steps.did(nc.vector.tensor_tensor(own, own, CONST(mem.const, "causal_min"), ALU.min))
                steps.settle()
                for branch in (SLC, WIN):
                    steps.did(nc.vector.reduce_max(weights[:, i + branch:i + branch + 1],
                                                   score_bank(n, branch)[:, 0:width], AX_X))
                steps.settle()
                steps.did(nc.vector.tensor_scalar(tops[:, i:i + 2], weights[:, i:i + 2], -1.0, None, ALU.mult), topped)

            def weigh(n):
                h, t = units[n]
                width, i = (t + 1) * P, 2 * n
                dve.wait_ge(exped, 2 * n + 2)
                steps.did(nc.vector.reciprocal(weights[:, i:i + 2], sums[:, i:i + 2]))
                steps.settle()
                steps.did(nc.vector.tensor_tensor(weights[:, i:i + 2], weights[:, i:i + 2], gate[:, t, h, 1:3],
                                                  ALU.mult))
                steps.settle()
                for branch in (SLC, WIN):
                    p = probs[:, n % 2, branch, 0:width]
                    steps.did(nc.vector.tensor_scalar(p, p, weights[:, i + branch:i + branch + 1], None, ALU.mult),
                              weighted)

            mask = CONST(mem.const, "cmp_min").rearrange("p (t n) -> p t n", t=TT)
            seen = CONST(mem.const, "cmp_one").rearrange("p (t n) -> p t n", t=TT)
            for h in range(2):
                dve.wait_ge(scored_c, h + 1)
                steps.did(nc.vector.tensor_tensor(
                    probs_c[:, h, :, :], score_c_bank[h][:, 0:TT * N_CMP].rearrange("p (t n) -> p t n", t=TT), mask,
                    ALU.min))
            steps.settle()
            steps.did(nc.vector.reduce_max(top_c[:, :, :], probs_c[:, :, :, :], AX_X))
            steps.settle()
            for h in range(2):
                steps.did(nc.vector.tensor_tensor(probs_c[:, h, :, :], probs_c[:, h, :, :],
                                                  top_c[:, h, :].unsqueeze(2).broadcast_to([P, TT, N_CMP]),
                                                  ALU.subtract), topped_c if h else None)
                steps.settle()
            top(0)
            dve.wait_ge(exped_c, 1)
            for h in range(2):
                steps.did(nc.vector.tensor_tensor(probs_c[:, h, :, :], probs_c[:, h, :, :], seen, ALU.mult))
            steps.settle()
            steps.did(nc.vector.reduce_sum(sum_c[:, :, :], probs_c[:, :, :, :], AX_X))
            steps.settle()
            steps.did(nc.vector.tensor_scalar(sum_c[:, :, :], sum_c[:, :, :], 1e-30, None, ALU.max))
            steps.settle()
            steps.did(nc.vector.reciprocal(sum_c[:, :, :], sum_c[:, :, :]))
            steps.settle()
            dve.wait_ge(gate_ready, 1)
            for h in range(2):
                steps.did(nc.vector.tensor_tensor(sum_c[:, h, :], sum_c[:, h, :], gate[:, :, h, 0], ALU.mult))
            steps.settle()
            for h in range(2):
                steps.did(nc.vector.tensor_tensor(probs_c[:, h, :, :], probs_c[:, h, :, :],
                                                  sum_c[:, h, :].unsqueeze(2).broadcast_to([P, TT, N_CMP]),
                                                  ALU.mult), weighted_c if h else None)
                steps.settle()
            for n in range(1, n_units):
                top(n)
                weigh(n - 1)
            weigh(n_units - 1)
            dve.wait_ge(applied, n_units)
            steps.did(nc.vector.tensor_copy(tile_at(y, j), out_bank[:, :]))
            steps.settle()


def second_odd(nc, mem, a, out):
    with buffers(nc, vec=[P, VECO.size]) as (vec,):
        with buffers(nc, y=[P, KD, SEQ], u=[P, UTO, SEQ], tm=[P, TT, TMO], rope=[P, 2, SEQ], k_cmp=[P, C_KV, N_CMP],
                     v_cmp=[P, C_KV, HEAD]) as (y, u, tm, rope, k_cmp, v_cmp):
            with split_ring(nc, mem):
                w_in = Weights(unit_of(a["w_ino"]), UTO // 2, 2, KD)
                with buffers(nc, w_tm=[P, KD * TMO]) as (w_tm,):
                    rms_norm(nc, mem, mem.x, lambda k: VECO(vec, "norm_mix", k), mem.h,
                             vectors=[(vec[:, :], a["veco"])],
                             ahead=[(w_tm[:, :], a["w_tmo"]), (rope[:, :, :], a["rope"])])
                    token_major(nc, mem, w_tm, TMO, mem.h, tm, w_in)
                project(nc, mem, w_in, mem.h, copy_out(nc, u), primed=SPLIT)
            w_out = Weights(unit_of(a["w_outo"]), KD // 2, 2, KD)
            compress(nc, mem, a, vec, rope, u, y, k_cmp, v_cmp, w_out)
            sparse_attention(nc, mem, rope, u, tm, k_cmp, v_cmp, y)
            with split_ring(nc, mem):
                project(nc, mem, w_out, y, add_out(nc, mem.x), on_vector=True, primed=LOADED)
        mixture(nc, mem, a, lambda k: VECO(vec, "norm_ffn", k))
        rms_norm(nc, mem, mem.x, lambda k: VECO(vec, "final", k), mem.h, store=out)


def lay_out_odd(i, a):
    w = i["o_w_in_2"][0]
    at = C_HEADS * HEAD
    q, rest = w[:, :at], w[:, at:]
    kc, vc, ks, vs, kw, vw = [rest[:, n * KV_WIDTH:(n + 1) * KV_WIDTH] for n in range(6)]
    gates, conv = rest[:, 6 * KV_WIDTH:6 * KV_WIDTH + C_HEADS * N_BRANCH], rest[:, 6 * KV_WIDTH + C_HEADS * N_BRANCH:]
    twice = lambda k: [k[:, c * HEAD:(c + 1) * HEAD] for c in (0, 0, 1, 1)]
    a["w_ino"] = weight_units(np.concatenate([q, kc, vc, *twice(ks), *twice(kw), conv], axis=1), 2)
    a["w_tmo"] = moving(np.concatenate([vs, vw, gates], axis=1))
    a["w_outo"] = weight_units(i["o_w_out_2"][0], 2)
    for n in "kv":
        a[f"cmp_{n}1"] = i[f"nsa_cmp_{n}_w1_2"][0].reshape(CMP_LEN // 2, P, CMP_HIDDEN).transpose(1, 0, 2)
        a[f"cmp_{n}2"] = i[f"nsa_cmp_{n}_w2_2"][0].reshape(CMP_HIDDEN // P, P, HEAD).transpose(1, 0, 2)
    vec = np.zeros((P, VECO.size), np.float32)
    VECO(vec, "norm_mix")[...] = columns(i["o_norm_mix_2"][0])
    VECO(vec, "norm_ffn")[...] = columns(i["o_norm_ffn_2"][0])
    VECO(vec, "final")[...] = columns(i["final_norm_2"])
    VECO(vec, "pos_k")[...] = np.tile(i["nsa_cmp_pos_k_2"][0].T, (2, 1))
    VECO(vec, "pos_v")[...] = np.tile(i["nsa_cmp_pos_v_2"][0].T, (2, 1))
    VECO(vec, "conv")[...] = i["conv_w_2"][0].reshape(3, D_WIDTH // P, P).transpose(2, 1, 0).reshape(P, -1)
    a["veco"] = vec
    a["router"] = moving(i["moe_router_2"][0])
    a["router_b"] = i["moe_router_b_2"][0]
    a["w_expert"] = np.stack([weight_units(interleaved(g, u), 2)
                              for g, u in zip(i["moe_w_gate_2"][0], i["moe_w_up_2"][0])])
    a["w_expert_down"] = np.stack([weight_units(w, 1) for w in i["moe_w_down_2"][0]])


def lay_out_second(i, a):
    lay_out_even(i, a)
    lay_out_odd(i, a)


def route(nc, mem, a, tokens, job_key, job_gate, job_expert, job_count):
    with buffers(nc, router=[P, KD * N_EXPERTS], bias=[P, N_EXPERTS], logits=[P, TT, N_EXPERTS],
                 best=[P, TT, 8], place=[P, TT, 8], part=[P, TT, 2], hot=[P, TT, 2, N_EXPERTS],
                 gate=[P, TT, N_EXPERTS], mask=[P, TT, N_EXPERTS], key=[P, TT, N_EXPERTS],
                 blocks=[P, N_EXPERTS], upto=[P, N_EXPERTS], first=[P, N_EXPERTS],
                 table=[P, N_EXPERTS * N_EXPERTS], member=[P, MAX_JOBS + 1, N_EXPERTS],
                 ended=[P, MAX_JOBS + 1, N_EXPERTS], wide=[P, TT, MAX_JOBS + 1, N_EXPERTS],
                 wide_gate=[P, TT, MAX_JOBS + 1, N_EXPERTS], expert=[P, MAX_JOBS + 1]) as (
            router, bias, logits, best, place, part, hot, gate, mask, key, blocks, upto, first, table, member,
            ended, wide, wide_gate, expert), nc.sbuf_tensor(
            f"order_{nc.next_id()}", [P, TT, 8], U32) as order, phase(
            nc, "loaded", "product", "ranked", "exped", "masked", "turned", "turned_taken", "counted",
            "dve_steps") as (
            block, loaded, product, ranked, exped, masked, turned, turned_taken, counted, dve_steps):
        n_rank = TT * N_EXPERTS
        rank_of = mem.bank[1][:, 0:n_rank].rearrange("p (t e) -> p t e", t=TT)
        count_of = mem.bank[1][:, n_rank:n_rank + N_EXPERTS]
        halves = D_MODEL // SEQ
        turn_banks = 4

        @block.sync
        def _(sp):
            sp.dma_start(router[:, :], a["router"]).then_inc(loaded, 16)
            sp.dma_start(bias[:, :], a["router_b"].partition_broadcast(P)).then_inc(loaded, 16)

        @block.tensor
        def _(pe):
            pe.wait_ge(loaded, 32)
            for t in range(TT):
                for k in range(KD):
                    last = nc.tensor.matmul(mem.bank[0][:, t * N_EXPERTS:(t + 1) * N_EXPERTS],
                                            mem.h[:, k, t * P:(t + 1) * P],
                                            router[:, k * N_EXPERTS:(k + 1) * N_EXPERTS],
                                            start=(k == 0), stop=(k == KD - 1))
            last.then_inc(product, 1)
            for t in range(TT):
                for half in range(halves):
                    n = t * halves + half
                    if n >= turn_banks:
                        pe.wait_ge(turned_taken, n - turn_banks + 1)
                    for c in range(SEQ // P):
                        last = nc.tensor.matmul(mem.bank[2 + n % turn_banks][:, c * P:(c + 1) * P],
                                                mem.h[:, half * (SEQ // P) + c, t * P:(t + 1) * P],
                                                CONST(mem.const, "ident"), start=True, stop=True)
                    last.then_inc(turned, 1)
            pe.wait_ge(masked, 1)
            for t in range(TT):
                for s in range(t + 1):
                    nc.tensor.matmul(mem.bank[1][:, t * N_EXPERTS:(t + 1) * N_EXPERTS],
                                     CONST(mem.const, "upper_strict" if s == t else "ones"), mask[:, s, :],
                                     start=(s == 0), stop=(s == t))
            for s in range(TT):
                last = nc.tensor.matmul(count_of, CONST(mem.const, "ones"), mask[:, s, :],
                                        start=(s == 0), stop=(s == TT - 1))
            last.then_inc(counted, 1)

        @block.scalar
        def _(act):
            for n in range(TT * halves):
                t, half = divmod(n, halves)
                act.wait_ge(turned, n + 1)
                nc.scalar.activation(tokens[:, t, half * SEQ:(half + 1) * SEQ], mem.bank[2 + n % turn_banks][:, :],
                                     ACT.Copy).then_inc(turned_taken, 1)
            act.wait_ge(ranked, 1)
            nc.scalar.activation(part[:, :, 1], part[:, :, 1], ACT.Exp).then_inc(exped, 1)

        @block.vector
        def _(dve):
            steps = Steps(dve, dve_steps)
            v = nc.vector
            dve.wait_ge(product, 1)
            steps.did(v.tensor_tensor(
                logits[:, :, :], mem.bank[0][:, 0:n_rank].rearrange("p (t e) -> p t e", t=TT),
                bias[:, :].unsqueeze(1).broadcast_to([P, TT, N_EXPERTS]), ALU.add))
            steps.settle()
            for t in range(TT):
                steps.did(v.max(best[:, t, :], logits[:, t, :]))
            steps.settle()
            for t in range(TT):
                steps.did(v.max_index(order[:, t, :], best[:, t, :], logits[:, t, :]))
            steps.did(v.tensor_tensor(part[:, :, 1], best[:, :, 1], best[:, :, 0], ALU.subtract), ranked)
            steps.settle()
            steps.did(v.tensor_copy(place[:, :, :], order[:, :, :]))
            steps.settle()
            for t in range(TT):
                for c in range(TOP_K):
                    steps.did(v.tensor_scalar(hot[:, t, c, :], CONSTM(mem.moe_const, "experts"),
                                              place[:, t, c:c + 1], None, ALU.is_equal))
            steps.settle()
            steps.did(v.tensor_tensor(mask[:, :, :], hot[:, :, 0, :], hot[:, :, 1, :], ALU.add), masked)
            dve.wait_ge(exped, 1)
            steps.did(v.tensor_scalar(part[:, :, 0], part[:, :, 1], 1.0, None, ALU.add))
            steps.settle()
            steps.did(v.reciprocal(part[:, :, 0], part[:, :, 0]))
            steps.settle()
            steps.did(v.tensor_tensor(part[:, :, 1], part[:, :, 1], part[:, :, 0], ALU.mult))
            steps.settle()
            for t in range(TT):
                steps.did(v.tensor_scalar(gate[:, t, :], hot[:, t, 0, :], part[:, t, 0:1], None, ALU.mult))
            steps.settle()
            for t in range(TT):
                steps.did(v.scalar_tensor_tensor(out=gate[:, t, :], in0=hot[:, t, 1, :], scalar=part[:, t, 1:2],
                                                 in1=gate[:, t, :], op0=ALU.mult, op1=ALU.add))
            dve.wait_ge(counted, 1)
            steps.did(v.tensor_scalar(blocks[:, :], count_of, 0.0, None, ALU.is_gt))
            for more in range(BLOCK, SEQ, BLOCK):
                steps.settle()
                steps.did(v.scalar_tensor_tensor(out=blocks[:, :], in0=count_of, scalar=float(more),
                                                 in1=blocks[:, :], op0=ALU.is_gt, op1=ALU.add))
            steps.did(v.scalar_tensor_tensor(out=key[:, :, :], in0=rank_of, scalar=UNPICKED, in1=mask[:, :, :],
                                             op0=ALU.add, op1=ALU.mult))
            steps.settle()
            square = table[:, :].rearrange("p (e f) -> p e f", e=N_EXPERTS)
            steps.did(v.tensor_tensor(square, blocks[:, :].unsqueeze(1).broadcast_to([P, N_EXPERTS, N_EXPERTS]),
                                      CONSTM(mem.moe_const, "experts_upto").rearrange("p (e f) -> p e f", e=N_EXPERTS),
                                      ALU.mult))
            steps.settle()
            steps.did(v.tensor_reduce(upto[:, :], square, AX_X, ALU.add))
            steps.settle()
            steps.did(v.tensor_tensor(first[:, :], upto[:, :], blocks[:, :], ALU.subtract))
            steps.did(v.tensor_copy(job_count[:, :], upto[:, N_EXPERTS - 1:N_EXPERTS]))
            by_job = [P, MAX_JOBS + 1, N_EXPERTS]
            job = CONSTM(mem.moe_const, "jobs").unsqueeze(2).broadcast_to(by_job)
            steps.did(v.tensor_tensor(ended[:, :, :], job, upto[:, :].unsqueeze(1).broadcast_to(by_job), ALU.is_ge))
            steps.settle()
            steps.did(v.tensor_tensor(member[:, :, :], job, first[:, :].unsqueeze(1).broadcast_to(by_job), ALU.is_ge))
            steps.did(v.tensor_scalar(upto[:, :], first[:, :], float(BLOCK), -UNPICKED, ALU.mult, ALU.add))
            steps.settle()
            steps.did(v.tensor_tensor(member[:, :, :], member[:, :, :], ended[:, :, :], ALU.subtract))
            steps.did(v.tensor_tensor(key[:, :, :], key[:, :, :],
                                      upto[:, :].unsqueeze(1).broadcast_to([P, TT, N_EXPERTS]), ALU.add))
            steps.settle()
            steps.did(v.tensor_tensor(ended[:, :, :], member[:, :, :],
                                      CONSTM(mem.moe_const, "experts").unsqueeze(1).broadcast_to(by_job), ALU.mult))
            for t in range(TT):
                steps.did(v.tensor_tensor(wide[:, t, :, :], member[:, :, :],
                                          key[:, t, :].unsqueeze(1).broadcast_to(by_job), ALU.mult))
                steps.did(v.tensor_tensor(wide_gate[:, t, :, :], member[:, :, :],
                                          gate[:, t, :].unsqueeze(1).broadcast_to(by_job), ALU.mult))
            steps.settle()
            steps.did(v.tensor_reduce(expert[:, :], ended[:, :, :], AX_X, ALU.add))
            steps.did(v.tensor_reduce(job_key[:, :, :], wide[:, :, :, :], AX_X, ALU.add))
            steps.did(v.tensor_reduce(job_gate[:, :, :], wide_gate[:, :, :, :], AX_X, ALU.add))
            steps.settle()
            steps.did(v.tensor_copy(job_expert[:, :], expert[:, :]))
            steps.did(v.tensor_tensor(job_key[:, :, :], job_key[:, :, :], CONSTM(mem.moe_const, "job_slots").unsqueeze(1)
                                      .broadcast_to([P, TT, MAX_JOBS + 1]), ALU.subtract))
            steps.settle()


def mixture(nc, mem, a, gain):
    j1 = MAX_JOBS + 1
    with buffers(nc, tokens=[P, TT, D_MODEL], job_key=[P, TT, j1], job_gate=[P, TT, j1],
                 moe_const=[P, CONSTM.size]) as (tokens, job_key, job_gate, mem.moe_const), \
            nc.sbuf_tensor(f"job_expert_{nc.next_id()}", [P, j1], I32) as job_expert, \
            nc.sbuf_tensor(f"job_count_{nc.next_id()}", [P, 1], I32) as job_count:
        rms_norm(nc, mem, mem.x, gain, mem.h, ahead=[(mem.moe_const[:, :], a["moe_const"])])
        route(nc, mem, a, tokens, job_key, job_gate, job_expert, job_count)
        run_jobs(nc, mem, a, tokens, job_key, job_gate, job_expert, job_count)


def run_jobs(nc, mem, a, tokens, job_key, job_gate, job_expert, job_count):
    pairs, turns = KD // 2, 3 * BLOCK_TILES
    heights = [min(P, BLOCK - s * P) for s in range(BLOCK_TILES)]
    names = [f"glu_filled{s}" for s in range(EXP_SLOTS)] + [f"down_filled{s}" for s in range(EXP_SLOTS)]
    names += ["picks_ready", "picked", "picked_out", "glu_product", "silu_ready", "hidden_ready", "down_product",
              "down_out", "turned", "high_rows", "turned_out", "spread", "added"]
    glu_size = 2 * KD * P
    with buffers(nc, glu_ring=[P, EXP_SLOTS, glu_size], down_ring=[P, EXP_SLOTS, EXP_T * P], picks=[P, TT, BLOCK],
                 gates=[P, TT], chosen=[P, KD, BLOCK], silu=[P, EXP_SLOTS, BLOCK], hidden=[P, EXP_T, BLOCK],
                 result=[P, KD, BLOCK], slot_gate=[P, BLOCK_TILES]) as (
            glu_ring, down_ring, picks, gates, chosen, silu, hidden, result, slot_gate), \
            parts_of(nc, BLOCK_TILES, D_MODEL) as (rows_high, rows_low), \
            nc.sbuf_tensor(f"spreader_{nc.next_id()}", [P, BLOCK_TILES, SEQ], F32R) as spreader, \
            phase(nc, *names) as (block, *sems):
        glu_filled, down_filled = sems[:EXP_SLOTS], sems[EXP_SLOTS:2 * EXP_SLOTS]
        (picks_ready, picked, picked_out, glu_product, silu_ready, hidden_ready, down_product, down_out, turned,
         high_rows, turned_out, spread, added) = sems[2 * EXP_SLOTS:]
        halves = [slice(h * SEQ, (h + 1) * SEQ) for h in range(2)]
        glu_uses = [len(range(s, EXP_T, EXP_SLOTS)) for s in range(EXP_SLOTS)]
        down_uses = KD // EXP_SLOTS
        low, high = mem.bank[:EXP_SLOTS], mem.bank[EXP_SLOTS:]

        def two(bank):
            return bank[:, 0:2 * BLOCK].rearrange("p (a n) -> p a n", a=2)

        def job_loop(engine, body):
            jobs = engine.value_load(job_count[0:1, 0:1], min_val=1, max_val=MAX_JOBS)
            with engine.Fori(0, jobs) as j:
                body(j)


        @block.sync
        def _(sp):
            def job(j):
                e = sp.value_load(job_expert[0:1, bass.ds(j, 1)], min_val=0, max_val=N_EXPERTS - 1)
                for u in range(EXP_T):
                    s = u % EXP_SLOTS
                    before = u - EXP_SLOTS if u >= EXP_SLOTS else s + (glu_uses[s] - 1) * EXP_SLOTS - EXP_T
                    sp.wait_ge(glu_product, j * EXP_T + (EXP_T + before + 1))
                    sp.dma_start(glu_ring[:, s, :], unit_of(a["w_expert"], e)(u)).then_inc(glu_filled[s], 16)
                for m in range(KD):
                    s = m % EXP_SLOTS
                    sp.wait_ge(down_product, j * KD + (KD + m - EXP_SLOTS + 1))
                    sp.dma_start(down_ring[:, s, :], unit_of(a["w_expert_down"], e)(m)).then_inc(down_filled[s], 16)

            job_loop(sp, job)

        @block.tensor
        def _(pe):
            pe.sem_inc(glu_product, EXP_T)
            pe.sem_inc(down_product, KD)

            def pick():
                for p in range(pairs):
                    for k in (2 * p, 2 * p + 1):
                        for t in range(TT):
                            last = nc.tensor.matmul(two(low[p])[:, k % 2, :], tokens[:, t, k * P:(k + 1) * P],
                                                    picks[:, t, :], start=(t == 0), stop=(t == TT - 1))
                    last.then_inc(picked, 1)

            pe.wait_ge(picks_ready, 1)
            pick()

            def turn_results(j, half):
                pe.wait_ge(down_out, j * pairs + (half + 1) * pairs // 2)
                for s in range(BLOCK_TILES):
                    for c in range(KD // 2):
                        last = nc.tensor.matmul(high[half * BLOCK_TILES + s][0:heights[s], c * P:(c + 1) * P],
                                                result[:, half * KD // 2 + c, s * P:s * P + heights[s]],
                                                CONST(mem.const, "ident"), start=True, stop=True)
                    last.then_inc(turned, 1)

            def job(j):
                for s in range(BLOCK_TILES):
                    slots = slice(s * P, s * P + heights[s])
                    for t in range(TT):
                        nc.tensor.matmul(high[s][0:heights[s], t * P:(t + 1) * P], picks[:, t, slots],
                                         CONST(mem.const, "ident"), start=True, stop=True)
                    for t in range(TT):
                        last = nc.tensor.matmul(high[BLOCK_TILES + s][0:heights[s], 0:1], picks[:, t, slots],
                                                gates[:, t:t + 1], start=(t == 0), stop=(t == TT - 1))
                    last.then_inc(turned, 1)
                pe.wait_ge(picked_out, j * pairs + pairs)
                for u in range(EXP_T):
                    s = u % EXP_SLOTS
                    if u < EXP_SLOTS:
                        pe.wait_ge(added, j * KD + (KD - EXP_SLOTS + u + 1))
                    else:
                        pe.wait_ge(hidden_ready, j * EXP_T + (u - EXP_SLOTS + 1))
                    pe.wait_ge(glu_filled[s], j * (16 * glu_uses[s]) + 16 * (u // EXP_SLOTS + 1))
                    for half in range(2):
                        for k in range(KD):
                            at = (half * KD + k) * P
                            last = nc.tensor.matmul(two(low[s])[:, half, :], glu_ring[:, s, at:at + P],
                                                    chosen[:, k, :], start=(k == 0), stop=(k == KD - 1))
                    last.then_inc(glu_product, 1)
                pe.wait_ge(turned_out, j * turns + BLOCK_TILES)
                for m in range(KD):
                    s = m % EXP_SLOTS
                    pe.wait_ge(down_filled[s], j * (16 * down_uses) + 16 * (m // EXP_SLOTS + 1))
                    for k in range(EXP_T):
                        if m == 0:
                            pe.wait_ge(hidden_ready, j * EXP_T + (k + 1))
                        last = nc.tensor.matmul(two(high[m // 2])[:, m % 2, :], down_ring[:, s, k * P:(k + 1) * P],
                                                hidden[:, k, :], start=(k == 0), stop=(k == EXP_T - 1))
                    last.then_inc(down_product, 1)
                turn_results(j, 0)
                pe.wait_ge(picks_ready, j + 2)
                pick()
                turn_results(j, 1)
                pe.wait_ge(picked_out, j * pairs + 2 * pairs)
                for k in range(KD):
                    if k % (KD // 2) == 0:
                        pe.wait_ge(turned_out, j * turns + BLOCK_TILES * (2 + k // (KD // 2)))
                    if k >= EXP_SLOTS:
                        pe.wait_ge(added, j * KD + (KD + k - EXP_SLOTS + 1))
                    for s in range(BLOCK_TILES):
                        for part, rows in enumerate((rows_high, rows_low)):
                            last = nc.tensor.matmul(low[k % EXP_SLOTS][:, :], rows[0:heights[s], s, k * P:(k + 1) * P],
                                                    spreader[0:heights[s], s, :], start=(s == 0 and part == 0),
                                                    stop=(s == BLOCK_TILES - 1 and part == 1))
                    last.then_inc(spread, 1)

            job_loop(pe, job)

        @block.scalar
        def _(act):
            def take_picked(done):
                for p in range(pairs):
                    act.wait_ge(picked, done + (p + 1))
                    nc.scalar.activation(chosen[:, 2 * p:2 * p + 2, :], two(low[p]), ACT.Copy).then_inc(picked_out, 1)

            def gated_rows(j, half):
                for s in range(BLOCK_TILES):
                    n = half * BLOCK_TILES + s
                    act.wait_ge(turned, j * turns + (BLOCK_TILES + n + 1))
                    nc.scalar.activation(rows_high[0:heights[s], s, halves[half]], high[n][0:heights[s], :], ACT.Copy,
                                         scale=slot_gate[0:heights[s], s:s + 1]).then_inc(high_rows, 1)

            take_picked(0)

            def job(j):
                for u in range(EXP_T):
                    s = u % EXP_SLOTS
                    act.wait_ge(glu_product, j * EXP_T + (EXP_T + u + 1))
                    nc.scalar.activation(silu[:, s, :], two(low[s])[:, 0, :], ACT.Silu).then_inc(silu_ready, 1)
                for p in range(pairs):
                    act.wait_ge(down_product, j * KD + (KD + 2 * p + 2))
                    nc.scalar.activation(result[:, 2 * p:2 * p + 2, :], two(high[p]), ACT.Copy).then_inc(down_out, 1)
                act.wait_ge(turned_out, j * turns + BLOCK_TILES)
                gated_rows(j, 0)
                take_picked(j * pairs + pairs)
                gated_rows(j, 1)

            job_loop(act, job)

        @block.vector
        def _(dve):
            dve.sem_inc(added, KD)
            one = CONSTM(mem.moe_const, "slots")

            def choose(j):
                nc.vector.tensor_copy(gates[:, :], job_gate[:, :, bass.ds(j, 1)].rearrange("p t n -> p (t n)"))
                for t in range(TT):
                    last = nc.vector.tensor_scalar(picks[:, t, :], one, job_key[:, t, bass.ds(j, 1)], None, ALU.is_equal)
                last.then_inc(picks_ready, 1)

            choose(0)

            def job(j):
                for s in range(BLOCK_TILES):
                    dve.wait_ge(turned, j * turns + (s + 1))
                    nc.vector.tensor_copy(slot_gate[0:heights[s], s:s + 1], high[BLOCK_TILES + s][0:heights[s], 0:1])
                    nc.vector.tensor_copy(spreader[0:heights[s], s, :], high[s][0:heights[s], :]).then_inc(turned_out, 1)
                for u in range(EXP_T):
                    s = u % EXP_SLOTS
                    dve.wait_ge(silu_ready, j * EXP_T + (u + 1))
                    nc.vector.tensor_tensor(hidden[:, u, :], silu[:, s, :], two(low[s])[:, 1, :], ALU.mult) \
                        .then_inc(hidden_ready, 1)
                dve.wait_ge(picked, j * pairs + pairs)
                choose(j + 1)
                for half in range(2):
                    for s in range(BLOCK_TILES):
                        n = half * BLOCK_TILES + s
                        dve.wait_ge(high_rows, j * (2 * BLOCK_TILES) + (n + 1))
                        nc.vector.scalar_tensor_tensor(
                            out=rows_low[0:heights[s], s, halves[half]], in0=high[n][0:heights[s], :],
                            scalar=slot_gate[0:heights[s], s:s + 1], in1=rows_high[0:heights[s], s, halves[half]],
                            op0=ALU.mult, op1=ALU.subtract).then_inc(turned_out, 1)
                for k in range(KD):
                    dve.wait_ge(spread, j * KD + (k + 1))
                    dve.wait_ge(added, j * KD + (k + 1))
                    nc.vector.tensor_tensor(mem.x[:, k, :], mem.x[:, k, :], low[k % EXP_SLOTS][:, :], ALU.add) \
                        .then_inc(added, 1)

            job_loop(dve, job)


class Memory:

    def __init__(self, nc, stack):
        def sb(name, shape):
            return stack.enter_context(nc.sbuf_tensor(name, shape, F32))

        self.x = sb("x_res", [P, KD, SEQ])
        self.h = sb("h_branch", [P, KD, SEQ])
        self.ring = sb("weight_ring", [P, SLOTS, SLOT])
        self.const = sb("const_cols", [P, CONST.size])
        self.levels = sb("level_masks", [P, 2, LEVELS, P])
        self.eps = CONST(self.const, "eps")
        self.bank = [stack.enter_context(nc.psum_tensor(f"bank{b}", [P, SEQ], F32)) for b in range(8)]


def load(nc, *pairs):
    with phase(nc, "loaded") as (block, loaded):
        @block.sync
        def _(sp):
            for to, source in pairs:
                sp.dma_start(to, source).then_inc(loaded, 16)
            sp.wait_ge(loaded, 16 * len(pairs))


def layer_of(array, l):
    one = array[bass.ds(l, 1)]
    names = "abcdefg"[:len(one.shape) - 1]
    return one.rearrange(f"z {' '.join(names)} -> (z {names[0]}) {' '.join(names[1:])}")


def unit_of(array, l=None):
    def weights(u):
        if l is None:
            return array[bass.ds(u, 1)].rearrange("a p n -> (a p) n")
        return array[bass.ds(l, 1), bass.ds(u, 1)].rearrange("z a p n -> (z a p) n")
    return weights


def first_block(nc, mem, a):
    with nc.Fori(0, DEPTH) as l, buffers(nc, vec=[P, VEC1.size]) as (vec,):
        with buffers(nc, y=[P, KD, SEQ], u=[P, UT1, SEQ], tm=[P, TT, TM1],
                     lam=[P, 4 * DIFF_DIM + 2], gates=[P, 2, 2 * DELTA_HEADS]) as (y, u, tm, lam, gates):
            with split_ring(nc, mem):
                w_in = Weights(unit_of(a["w_in1"], l), UT1 // 2, 2, KD)
                with buffers(nc, w_tm=[P, KD * TM1]) as (w_tm,):
                    rms_norm(nc, mem, mem.x, lambda k: VEC1(vec, "pre_mix", k), mem.h,
                             vectors=[(vec[:, :], layer_of(a["vec1"], l))],
                             ahead=[(w_tm[:, :], layer_of(a["w_tm1"], l)),
                                    (lam[:, :], a["lam"][bass.ds(l, 1), :].partition_broadcast(P)),
                                    (gates[:, :, :], a["gates"][bass.ds(l, 1), :, :].partition_broadcast(P))])
                    token_major(nc, mem, w_tm, TM1, mem.h, tm, w_in)
                project(nc, mem, w_in, mem.h, copy_out(nc, u), primed=SPLIT)
            with buffers(nc, padded=[P, CONV_T, SEQ + CONV_WIDTH - 1], dist=[P, TT, SEQ]) as (padded, dist):
                conv_gate(nc, mem, vec, u, padded, y, dist, a["dist"])
                diff_attention(nc, mem, vec, lam, dist, u, tm, y, padded)
            delta_net(nc, mem, vec, gates, u, tm, y)
            with split_ring(nc, mem):
                w_out = Weights(unit_of(a["w_out1"], l), KD // 2, 2, KD)
                mixer_norms(nc, mem, vec, lam, u, y, w_out)
                project(nc, mem, w_out, y, copy_out(nc, mem.h), primed=SPLIT)
        ff = FeedForward(unit_of(a["w_ff1"], l), unit_of(a["w_ff2"], l), D_FF // P, "relu")
        with split_ring(nc, mem):
            add_norm(nc, mem, mem.h, lambda k: VEC1(vec, "post_mix", k), mem.x, lambda k: VEC1(vec, "pre_mlp", k), mem.h,
                     following=ff.up[0])
            feed_forward(nc, mem, ff, lambda half: add_out(nc, mem.h) if half else copy_out(nc, mem.h), bool)
        rms_norm(nc, mem, mem.h, lambda k: VEC1(vec, "post_mlp", k), None, add_to=mem.x)


def build(nc, a, out):
    with ExitStack() as stack:
        mem = Memory(nc, stack)
        load(nc, (mem.x[:, :, :], a["x"]), (mem.const[:, :], a["const"]), (mem.levels[:, :, :, :], a["levels"]))
        first_block(nc, mem, a)
        second_even(nc, mem, a)
        second_odd(nc, mem, a, out)


def weight_units(w, tiles):
    k, m = w.shape
    w = w.reshape(k // P, P, m // (P * tiles), tiles, P).transpose(2, 1, 3, 0, 4)
    return np.ascontiguousarray(w.reshape(m // (P * tiles), P, -1))


def moving(w):
    k, m = w.shape
    return np.ascontiguousarray(w.reshape(k // P, P, m).transpose(1, 0, 2).reshape(P, -1))


def columns(v):
    return v.reshape(-1, P).T


def alibi_slopes(n):
    def pow2(m):
        start = 2.0 ** (-8.0 / m)
        return [start ** (i + 1) for i in range(m)]
    if math.log2(n).is_integer():
        return pow2(n)
    c = 2 ** int(math.floor(math.log2(n)))
    return pow2(c) + pow2(2 * c)[0::2][: n - c]


def constants():
    i, j = np.arange(P)[:, None], np.arange(P)[None, :]
    c = np.zeros((P, CONST.size), np.float32)

    def put(name, value):
        CONST(c, name)[...] = value

    put("ident", i == j)
    put("ones", 1)
    put("pair_ones", i // HEAD == j // HEAD)
    half, d = ROT_DIM // 2, np.arange(P) % HEAD
    rot = np.zeros((P, P))
    for p in range(P):
        if d[p] < half:
            rot[p + half, p] = -1
        elif d[p] < ROT_DIM:
            rot[p - half, p] = 1
    put("rot", rot)
    put("lower_in", i >= j)
    put("upper_in", i <= j)
    put("upper_strict", i < j)
    put("neg_lower_strict", -1.0 * (i > j))
    put("lower_strict_max", np.where(i > j, 0, BIG))
    put("upper_strict_max", np.where(i < j, 0, BIG))
    put("upper_in_min", np.where(i <= j, 0, -BIG))
    put("lower_in_min", np.where(i >= j, 0, -BIG))
    put("causal_min", np.where(i >= j, 3e38, -BIG))
    put("slopes", np.asarray(alibi_slopes(DIFF_HEADS), np.float32))
    t = (np.arange(TT)[None, :, None] * P + np.arange(P)[:, None, None])
    seen = (np.arange(N_CMP) * CMP_STRIDE + CMP_LEN - 1)[None, None, :] <= t
    put("cmp_min", np.where(seen, 3e38, -BIG).reshape(P, -1))
    put("cmp_one", seen.reshape(P, -1))
    put("not_first", np.arange(SEQ)[None, :] % P != 0)
    put("eps", np.array([NORM_EPS, 1e-5, RWKV_GN_EPS, 0.0]))
    m = np.zeros((P, CONSTM.size), np.float32)
    CONSTM(m, "experts")[...] = np.arange(N_EXPERTS)
    CONSTM(m, "experts_upto")[...] = np.tril(np.ones((N_EXPERTS, N_EXPERTS))).reshape(-1)
    CONSTM(m, "jobs")[...] = np.arange(MAX_JOBS + 1)
    CONSTM(m, "job_slots")[...] = BLOCK * np.arange(MAX_JOBS + 1)
    CONSTM(m, "slots")[...] = np.arange(BLOCK)
    levels = np.zeros((P, 2, LEVELS, P), np.float32)
    for n in range(LEVELS):
        b = 2 ** n
        low = (i // (2 * b) == j // (2 * b)) & (i // b % 2 == 1) & (j // b % 2 == 0)
        levels[:, 0, n, :], levels[:, 1, n, :] = low.T, low
    q = (np.arange(TT)[None, :, None] * P + np.arange(P)[:, None, None])
    dist = np.abs(q - np.arange(SEQ)[None, None, :]).astype(np.float32)
    pos = np.arange(SEQ, dtype=np.float32)
    freq = (np.float32(ROPE_THETA) ** (-np.arange(0, ROT_DIM, 2, dtype=np.float32) / np.float32(ROT_DIM))).astype(np.float32)
    angle = pos[:, None] * freq[None, :]
    rope = np.zeros((P, 2, SEQ), np.float32)
    rope[:, 0, :] = 1
    for p in range(P):
        if d[p] < ROT_DIM:
            rope[p, 0], rope[p, 1] = np.cos(angle[:, d[p] % half]), np.sin(angle[:, d[p] % half])
    return {"const": c, "moe_const": m, "levels": levels, "dist": dist, "rope": rope}


def lay_out(i):
    a = dict(constants())
    a["x"] = np.ascontiguousarray(i["x"][0].T.reshape(KD, P, SEQ).transpose(1, 0, 2))
    w_in = i["w_in"]
    o_dv, o_g, o_b = 2 * CONV_CH + 2 * DIFF_W, 2 * CONV_CH + 3 * DIFF_W, 2 * CONV_CH + 3 * DIFF_W + 4 * DELTA_W
    fm = np.concatenate([w_in[:, :, :o_dv], w_in[:, :, o_g:o_b]], axis=2)
    tm = np.concatenate([w_in[:, :, o_dv:o_g], w_in[:, :, o_b:]], axis=2)
    a["w_in1"] = np.stack([weight_units(w, 2) for w in fm])
    a["w_tm1"] = np.stack([moving(w) for w in tm])
    a["w_out1"] = np.stack([weight_units(w, 2) for w in i["w_out"]])
    a["w_ff1"] = np.stack([weight_units(w, 2) for w in i["w_ff1"]])
    a["w_ff2"] = np.stack([weight_units(w, 1) for w in i["w_ff2"]])
    vec = np.zeros((DEPTH, P, VEC1.size), np.float32)
    lam = np.zeros((DEPTH, 4 * DIFF_DIM + 2), np.float32)
    for l in range(DEPTH):
        def put(name, value):
            VEC1(vec[l], name)[...] = value
        put("pre_mix", columns(i["pre_mix_w"][l]))
        put("post_mix", columns(i["post_mix_w"][l]))
        put("pre_mlp", columns(i["pre_mlp_w"][l]))
        put("post_mlp", columns(i["post_mlp_w"][l]))
        put("conv_w", i["conv_dw_w"][l].reshape(CONV_WIDTH, CONV_T, P).transpose(2, 1, 0).reshape(P, -1))
        put("conv_b", columns(i["conv_dw_b"][l]))
        put("ln_w", columns(i["conv_ln_w"][l]))
        put("ln_b", columns(i["conv_ln_b"][l]))
        put("subln", np.tile(i["diff_subln_w"][l], 2)[:, None])
        put("delta_conv", i["delta_conv_w"][l].reshape(SHORT_CONV, 3 * PAIRS1, P).transpose(2, 1, 0).reshape(P, -1))
        put("delta_norm", np.tile(i["delta_norm_w"][l], 2)[:, None])
        init = 0.8 - 0.6 * math.exp(-0.3 * l)
        lam[l] = np.concatenate([i["diff_lambda_q1"][l], i["diff_lambda_k1"][l], i["diff_lambda_q2"][l],
                                 i["diff_lambda_k2"][l], np.array([init, 1.0 - init], np.float32)])
    a["vec1"], a["lam"] = vec, lam
    a["gates"] = np.stack([i["delta_A_log"].reshape(DEPTH, -1), i["delta_dt_bias"].reshape(DEPTH, -1)], axis=1)
    lay_out_second(i, a)
    return {n: np.ascontiguousarray(v, dtype=np.float32) for n, v in a.items()}


def kernel(**inputs):
    import concourse.bacc as bacc
    from concourse.bass_utils import run_bass_kernel_spmd

    arrays = lay_out({n: np.asarray(v) for n, v in inputs.items()})
    nc = bacc.Bacc("TRN2", target_bir_lowering=False, num_devices=1)
    handles = {n: nc.dram_tensor(f"in_{n}", v.shape, F32, kind="ExternalInput").ap() for n, v in arrays.items()}
    out = nc.dram_tensor("out", (P, KD, SEQ), F32, kind="ExternalOutput").ap()
    build(nc, handles, out)
    result = run_bass_kernel_spmd(nc, [{f"in_{n}": v for n, v in arrays.items()}], core_ids=[0])
    y = result.results[0]["out"]
    return np.ascontiguousarray(y.transpose(2, 1, 0).reshape(1, SEQ, D_MODEL))
```
